# Optimizing a Trainium2 kernel written in Bass

```python
import math
import jax
import jax.numpy as jnp
from jax import lax
import numpy as np
import jax, jax.numpy as jnp

D_MODEL = 1024
BATCH = 1
SEQ = 2048
DEPTH = 1

CTX_LEN = 256
GRID_W = 64

A_HEADS = 4
A_DK = 128
A_DV = 128
A_CHUNK = 64
CONV_K = 5
B_HEADS = 4
B_DK = 128
B_DV = 128
B_CHUNK = 16
N_BRANCH = 2

A_QK = A_HEADS * A_DK
A_V = A_HEADS * A_DV
B_QK = B_HEADS * B_DK
B_V = B_HEADS * B_DV
CONV_DIM = 2 * A_QK + A_V
IN_SPLITS = (A_QK, A_QK, A_V, 2 * A_HEADS, 2 * A_HEADS, A_V,
             B_QK, B_QK, B_QK, B_V, B_V, N_BRANCH * D_MODEL)
D_IN = 2 * A_QK + 2 * A_V + 4 * A_HEADS + 3 * B_QK + 2 * B_V + N_BRANCH * D_MODEL

DEEPNORM_ALPHA = (2 * DEPTH) ** 0.25
DEEPNORM_BETA = (8 * DEPTH) ** -0.25
LN_EPS = 1e-6
RMS_EPS = 1e-6
L2_EPS = 1e-6


def layer_norm(t):
    t = t.astype(jnp.float32)
    mu = jnp.mean(t, axis=-1, keepdims=True)
    var = jnp.mean(jnp.square(t - mu), axis=-1, keepdims=True)
    return (t - mu) * lax.rsqrt(var + LN_EPS)

def l2norm(t):
    return t * lax.rsqrt(jnp.sum(t * t, axis=-1, keepdims=True) + L2_EPS)

def rms_norm_gated(o, gain, gate):
    o = o * lax.rsqrt(jnp.mean(o * o, axis=-1, keepdims=True) + RMS_EPS) * gain
    return o.reshape(*o.shape[:-2], -1) * jax.nn.silu(gate)

def split_cols(z):
    out, start = [], 0
    for n in IN_SPLITS:
        out.append(z[..., start:start + n])
        start += n
    return out

def centred_dwconv(u, w):
    u = u.astype(jnp.float32)
    return lax.conv_general_dilated(
        u, w.astype(jnp.float32)[:, None, :], window_strides=(1,),
        padding=((CONV_K // 2, CONV_K // 2),),
        dimension_numbers=('NWC', 'WIO', 'NWC'), feature_group_count=u.shape[-1])

def to_colmajor(t, rows):
    bsz, rest = t.shape[0], t.shape[2:]
    return t.reshape(bsz, rows, GRID_W, *rest).swapaxes(1, 2).reshape(bsz, rows * GRID_W, *rest)

def from_colmajor(t, rows):
    bsz, rest = t.shape[0], t.shape[2:]
    return t.reshape(bsz, GRID_W, rows, *rest).swapaxes(1, 2).reshape(bsz, rows * GRID_W, *rest)

def _to_chunks(t, chunk):
    bsz, length, heads = t.shape[:3]
    t = t.reshape(bsz, length // chunk, chunk, heads, *t.shape[3:])
    return jnp.moveaxis(t, 3, 1)

def _from_chunks(o):
    n, bsz, heads, chunk, dv = o.shape
    return o.transpose(1, 0, 3, 2, 4).reshape(bsz, n * chunk, heads, dv)

def gdn_chunk_scan(q, k, v, g, beta, s0):
    dk = q.shape[-1]
    q, k, v = (_to_chunks(t, A_CHUNK) for t in (q, k, v))
    g, beta = _to_chunks(g, A_CHUNK), _to_chunks(beta, A_CHUNK)
    G = jnp.cumsum(g, axis=-1)
    idx = jnp.arange(A_CHUNK)
    incl = idx[:, None] >= idx[None, :]
    strict = idx[:, None] > idx[None, :]
    diff = G[..., :, None] - G[..., None, :]
    decay = jnp.where(incl, jnp.exp(jnp.where(incl, diff, 0.0)), 0.0)
    kb = k * beta[..., None]
    a_mat = jnp.where(strict, jnp.einsum('bhncd,bhnsd->bhncs', kb, k) * decay, 0.0)
    eye = jnp.eye(A_CHUNK, dtype=a_mat.dtype)
    rhs = jnp.concatenate([kb * jnp.exp(G)[..., None], v * beta[..., None]], axis=-1)
    sol = lax.linalg.triangular_solve(a_mat + eye, rhs, left_side=True, lower=True,
                                      unit_diagonal=True)
    w, u = sol[..., :dk], sol[..., dk:]
    attn = jnp.einsum('bhncd,bhnsd->bhncs', q, k) * decay
    qg = q * jnp.exp(G)[..., None]
    g_last = G[..., -1:]
    kd = k * jnp.exp(g_last - G)[..., None]
    xs = tuple(jnp.moveaxis(t, 2, 0) for t in (w, u, qg, attn, kd, jnp.exp(g_last[..., 0])))

    def step(S, inp):
        w_c, u_c, qg_c, attn_c, kd_c, gl_c = inp
        v_new = u_c - jnp.einsum('bhcd,bhdv->bhcv', w_c, S)
        o_c = jnp.einsum('bhcd,bhdv->bhcv', qg_c, S) + jnp.einsum('bhcs,bhsv->bhcv', attn_c, v_new)
        S = S * gl_c[..., None, None] + jnp.einsum('bhcd,bhcv->bhdv', kd_c, v_new)
        return S, o_c

    s_final, o = lax.scan(step, s0, xs)
    return _from_chunks(o), s_final

def gla_chunk_scan(q, k, v, g, s0):
    q, k, v, g = (_to_chunks(t, B_CHUNK) for t in (q, k, v, g))
    G = jnp.cumsum(g, axis=-2)
    idx = jnp.arange(B_CHUNK)
    incl = idx[:, None] >= idx[None, :]
    qg = q * jnp.exp(G)
    kg = k * jnp.exp(-G)
    attn = jnp.where(incl, jnp.einsum('bhncd,bhnsd->bhncs', qg, kg), 0.0)
    g_last = G[..., -1:, :]
    kd = k * jnp.exp(g_last - G)
    xs = tuple(jnp.moveaxis(t, 2, 0) for t in (qg, attn, v, kd, jnp.exp(g_last[..., 0, :])))

    def step(S, inp):
        qg_c, attn_c, v_c, kd_c, gl_c = inp
        o_c = jnp.einsum('bhcd,bhdv->bhcv', qg_c, S) + jnp.einsum('bhcs,bhsv->bhcv', attn_c, v_c)
        S = S * gl_c[..., :, None] + jnp.einsum('bhcd,bhcv->bhdv', kd_c, v_c)
        return S, o_c

    s_final, o = lax.scan(step, s0, xs)
    return _from_chunks(o), s_final

def prefix_scan(scan_fn, ctx_args, lat_args, s0, reverse):
    flip = (lambda t: jnp.flip(t, axis=1)) if reverse else (lambda t: t)
    o_ctx, s_ctx = scan_fn(*[flip(t) for t in ctx_args], s0)
    o_lat, _ = scan_fn(*[flip(t) for t in lat_args], s_ctx)
    return flip(o_ctx), flip(o_lat)

def project_stream(u, w_in_l, conv_w_l, a_log_l, dt_bias_l, lb_l):
    bsz, length, _ = u.shape
    (a_q, a_k, a_v, a_alpha, a_beta, a_gate,
     b_q, b_f_fwd, b_f_bwd, b_i, b_gate, merge) = split_cols(u @ w_in_l)
    qkv = jax.nn.silu(centred_dwconv(jnp.concatenate([a_q, a_k, a_v], axis=-1), conv_w_l))
    a_q = l2norm(qkv[..., :A_QK].reshape(bsz, length, A_HEADS, A_DK)) * A_DK ** -0.5
    a_k = l2norm(qkv[..., A_QK:2 * A_QK].reshape(bsz, length, A_HEADS, A_DK))
    a_v = qkv[..., 2 * A_QK:].reshape(bsz, length, A_HEADS, A_DV)
    a_g = -jnp.exp(a_log_l) * jax.nn.softplus(a_alpha.reshape(bsz, length, 2, A_HEADS) + dt_bias_l)
    a_b = jax.nn.sigmoid(a_beta.reshape(bsz, length, 2, A_HEADS))
    f_logit = jnp.stack([b_f_fwd, b_f_bwd], axis=2)
    f = lb_l + (1.0 - lb_l) * jax.nn.sigmoid(f_logit)
    b_g = jnp.log(f).reshape(bsz, length, 2, B_HEADS, B_DK)
    b_k = ((1.0 - lb_l) * jax.nn.sigmoid(-f_logit)).reshape(bsz, length, 2, B_HEADS, B_DK)
    b_q = jax.nn.silu(b_q).reshape(bsz, length, B_HEADS, B_DK) * B_DK ** -0.5
    b_i = b_i.reshape(bsz, length, B_HEADS, B_DV)
    return {'a_q': a_q, 'a_k': a_k, 'a_v': a_v, 'a_g': a_g, 'a_b': a_b, 'a_gate': a_gate,
            'b_q': b_q, 'b_k': b_k, 'b_g': b_g, 'b_i': b_i, 'b_gate': b_gate, 'merge': merge}

def merge_branches(o_a, o_b, p, a_norm_l, b_norm_l, w_a_out_l, w_b_out_l, w_out_l):
    y_a = rms_norm_gated(o_a, a_norm_l, p['a_gate']) @ w_a_out_l
    y_b = rms_norm_gated(o_b, b_norm_l, p['b_gate']) @ w_b_out_l
    gates = jax.nn.sigmoid(p['merge'].reshape(*p['merge'].shape[:-1], N_BRANCH, D_MODEL))
    return (gates[..., 0, :] * y_a + gates[..., 1, :] * y_b) @ w_out_l

def first_inputs(seed: int = 0) -> dict:
    key = jax.random.key(seed)
    ks = jax.random.split(key, 20)
    f32 = jnp.float32

    def nrm(k, shape, scale):
        return jax.random.normal(k, shape, f32) * scale

    x = nrm(ks[0], (BATCH, SEQ, D_MODEL), 1.0)
    c = nrm(ks[1], (BATCH, D_MODEL), 1.0)
    ctx = nrm(ks[2], (BATCH, CTX_LEN, D_MODEL), 1.0)
    c_ctx = nrm(ks[3], (D_MODEL,), 1.0)
    w_mod = nrm(ks[4], (DEPTH, D_MODEL, 3 * D_MODEL), D_MODEL ** -0.5)
    b_mod = nrm(ks[5], (DEPTH, 3 * D_MODEL), 0.02)
    w_in = nrm(ks[6], (DEPTH, D_MODEL, D_IN), D_MODEL ** -0.5)
    conv_w = nrm(ks[7], (DEPTH, CONV_K, CONV_DIM), CONV_K ** -0.5)
    a_log = jnp.log(jax.random.uniform(ks[8], (DEPTH, 2, A_HEADS), f32, 1.0, 16.0))
    dt = jnp.exp(jax.random.uniform(ks[9], (DEPTH, 2, A_HEADS), f32, math.log(1e-3), math.log(1e-1)))
    dt_bias = dt + jnp.log(-jnp.expm1(-dt))
    lb_param = nrm(ks[10], (DEPTH + 1, 2, B_QK), 0.1)
    a_norm_g = 1.0 + nrm(ks[11], (DEPTH, A_DV), 0.02)
    b_norm_g = 1.0 + nrm(ks[12], (DEPTH, B_DV), 0.02)
    w_a_out = nrm(ks[13], (DEPTH, A_V, D_MODEL), DEEPNORM_BETA * A_V ** -0.5)
    w_b_out = nrm(ks[14], (DEPTH, B_V, D_MODEL), DEEPNORM_BETA * B_V ** -0.5)
    w_out = nrm(ks[15], (DEPTH, D_MODEL, D_MODEL), DEEPNORM_BETA * D_MODEL ** -0.5)
    ln_g = 1.0 + nrm(ks[16], (DEPTH, D_MODEL), 0.02)
    ln_b = nrm(ks[17], (DEPTH, D_MODEL), 0.02)
    return {'x': x, 'c': c, 'ctx': ctx, 'c_ctx': c_ctx, 'w_mod': w_mod, 'b_mod': b_mod,
            'w_in': w_in, 'conv_w': conv_w, 'a_log': a_log, 'dt_bias': dt_bias,
            'lb_param': lb_param, 'a_norm_g': a_norm_g, 'b_norm_g': b_norm_g,
            'w_a_out': w_a_out, 'w_b_out': w_b_out, 'w_out': w_out, 'ln_g': ln_g, 'ln_b': ln_b}

def first_block(x, c, ctx, c_ctx, w_mod, b_mod, w_in, conv_w, a_log, dt_bias, lb_param,
              a_norm_g, b_norm_g, w_a_out, w_b_out, w_out, ln_g, ln_b):
    f32 = jnp.float32
    bsz = x.shape[0]
    rows = x.shape[1] // GRID_W
    lb_all = jnp.cumsum(jax.nn.softmax(lb_param.astype(f32), axis=0), axis=0)
    h_lat = x.astype(f32)
    h_ctx = ctx.astype(f32)
    s0_a = jnp.zeros((bsz, A_HEADS, A_DK, A_DV), f32)
    s0_b = jnp.zeros((bsz, B_HEADS, B_DK, B_DV), f32)
    cm = lambda t: to_colmajor(t, rows)
    for l in range(DEPTH):
        shift_l, scale_l, gate_l = jnp.split((jax.nn.silu(c) @ w_mod[l] + b_mod[l])[:, None, :], 3, axis=-1)
        shift_c, scale_c, gate_c = jnp.split(jax.nn.silu(c_ctx) @ w_mod[l] + b_mod[l], 3, axis=-1)
        u_lat = layer_norm(h_lat) * (1.0 + scale_l) + shift_l
        u_ctx = layer_norm(h_ctx) * (1.0 + scale_c) + shift_c
        pl = project_stream(u_lat, w_in[l], conv_w[l], a_log[l], dt_bias[l], lb_all[l])
        pc = project_stream(u_ctx, w_in[l], conv_w[l], a_log[l], dt_bias[l], lb_all[l])

        oa_ctx, oa_lat = 0.0, 0.0
        for d in range(2):
            o_c, o_l = prefix_scan(
                gdn_chunk_scan,
                (pc['a_q'], pc['a_k'], pc['a_v'], pc['a_g'][:, :, d], pc['a_b'][:, :, d]),
                (pl['a_q'], pl['a_k'], pl['a_v'], pl['a_g'][:, :, d], pl['a_b'][:, :, d]),
                s0_a, reverse=(d == 1))
            oa_ctx = oa_ctx + o_c
            oa_lat = oa_lat + o_l

        ob_ctx, ob_lat_cm = 0.0, 0.0
        for d in range(2):
            o_c, o_l = prefix_scan(
                gla_chunk_scan,
                (pc['b_q'], pc['b_k'][:, :, d], pc['b_i'], pc['b_g'][:, :, d]),
                (cm(pl['b_q']), cm(pl['b_k'][:, :, d]), cm(pl['b_i']), cm(pl['b_g'][:, :, d])),
                s0_b, reverse=(d == 1))
            ob_ctx = ob_ctx + o_c
            ob_lat_cm = ob_lat_cm + o_l
        ob_lat = from_colmajor(ob_lat_cm, rows)

        sub_lat = merge_branches(oa_lat, ob_lat, pl, a_norm_g[l], b_norm_g[l],
                                 w_a_out[l], w_b_out[l], w_out[l])
        if l < DEPTH - 1:
            sub_ctx = merge_branches(oa_ctx, ob_ctx, pc, a_norm_g[l], b_norm_g[l],
                                     w_a_out[l], w_b_out[l], w_out[l])
            h_ctx = layer_norm(DEEPNORM_ALPHA * h_ctx + gate_c * sub_ctx) * ln_g[l] + ln_b[l]
        h_lat = layer_norm(DEEPNORM_ALPHA * h_lat + gate_l * sub_lat) * ln_g[l] + ln_b[l]
    return h_lat.astype(x.dtype)


_first_inputs = first_inputs


def first_inputs(seed=0):
    import zlib

    import numpy as np

    out = dict(_first_inputs(seed))
    spreads = {}
    factors = {'ctx': 8.0,
     'c_ctx': 8.0,
     'b_mod': 8.0,
     'a_log': 3.944,
     'lb_param': 8.0,
     'a_norm_g': 8.0,
     'b_norm_g': 8.0,
     'ln_g': 2.861,
     'ln_b': 2.874}
    for name, (base, spread) in spreads.items():
        noise = np.random.default_rng([zlib.crc32(name.encode()), seed]).standard_normal(out[name].shape)
        drawn = base * np.exp(spread * noise) if base else spread * noise
        out[name] = jnp.asarray(drawn.astype(out[name].dtype))
    for name, factor in factors.items():
        out[name] = (out[name] * factor).astype(out[name].dtype)
    return out


_narrow_inputs = first_inputs


def first_inputs(seed=0):
    out = dict(_narrow_inputs(seed))
    wider = {'a_norm_g': 6.23, 'b_norm_g': 7.15, 'ln_g': 3.16, 'ln_b': 3.22}
    for name, times in wider.items():
        mean = out[name].mean()
        out[name] = (mean + times * (out[name] - mean)).astype(out[name].dtype)
    return out


D_MIX = D_MODEL
MLA_HEADS = 8
MLA_NOPE = 64
MLA_ROPE = 32
MLA_V = 64
MLA_WIDTH = MLA_HEADS * MLA_V
Q_LORA = 256
KV_LORA = 128
ROPE_THETA = 10000.0
Q_BLOCK = 128
CHUNK = 128
G_HEADS = 8
G_WIDTH = D_MIX - MLA_WIDTH
G_HEAD_DIM = G_WIDTH // G_HEADS
D_IN_2 = Q_LORA + KV_LORA + MLA_ROPE + MLA_WIDTH + 3 * G_WIDTH
DN_ALPHA = (2.0 * DEPTH) ** 0.25
DN_BETA = (8.0 * DEPTH) ** -0.25
EPS = 1e-5


def _rmsnorm(x, g):
    xf = x.astype(jnp.float32)
    y = xf * lax.rsqrt(jnp.mean(xf * xf, axis=-1, keepdims=True) + EPS)
    return (y * g.astype(jnp.float32)).astype(x.dtype)

def _layernorm(x, g, b):
    xf = x.astype(jnp.float32)
    mu = jnp.mean(xf, axis=-1, keepdims=True)
    var = jnp.mean(jnp.square(xf - mu), axis=-1, keepdims=True)
    y = (xf - mu) * lax.rsqrt(var + EPS)
    return (y * g.astype(jnp.float32) + b.astype(jnp.float32)).astype(x.dtype)

def _rope(t, positions):
    half = MLA_ROPE // 2
    inv_freq = 1.0 / (ROPE_THETA ** (jnp.arange(half, dtype=jnp.float32) / half))
    ang = positions.astype(jnp.float32)[..., None] * inv_freq
    cos = jnp.cos(ang)[:, :, None, :].astype(t.dtype)
    sin = jnp.sin(ang)[:, :, None, :].astype(t.dtype)
    t1, t2 = t[..., :half], t[..., half:]
    return jnp.concatenate([t1 * cos - t2 * sin, t1 * sin + t2 * cos], axis=-1)

def _causal_attention(q, k, v):
    b, s, h, dqk = q.shape
    dv = v.shape[-1]
    nb = s // Q_BLOCK
    scale = 1.0 / math.sqrt(dqk)
    qb = q.reshape(b, nb, Q_BLOCK, h, dqk).transpose(1, 0, 2, 3, 4)
    kpos = jnp.arange(s)

    def one_block(args):
        qi, i = args
        sc = jnp.einsum('bqhd,bkhd->bhqk', qi, k).astype(jnp.float32) * scale
        qpos = i * Q_BLOCK + jnp.arange(Q_BLOCK)
        mask = kpos[None, :] <= qpos[:, None]
        sc = jnp.where(mask[None, None], sc, -jnp.inf)
        p = jax.nn.softmax(sc, axis=-1).astype(v.dtype)
        return jnp.einsum('bhqk,bkhd->bqhd', p, v)

    o = lax.map(one_block, (qb, jnp.arange(nb)))
    return o.transpose(1, 0, 2, 3, 4).reshape(b, s, h, dv)

def second_inputs(seed: int = 0) -> dict:
    key = jax.random.key(seed)
    ks = jax.random.split(key, 16)
    f32 = jnp.float32
    x = jax.random.normal(ks[0], (BATCH, SEQ, D_MODEL), f32)
    positions = jnp.broadcast_to(jnp.arange(SEQ, dtype=jnp.int32)[None, :], (BATCH, SEQ))
    w_in = jax.random.normal(ks[1], (D_MODEL, D_IN_2), f32) * D_MODEL ** -0.5
    q_norm_g = 1.0 + 0.02 * jax.random.normal(ks[2], (Q_LORA,), f32)
    w_uq = jax.random.normal(ks[3], (Q_LORA, MLA_HEADS * (MLA_NOPE + MLA_ROPE)), f32) * Q_LORA ** -0.5
    kv_norm_g = 1.0 + 0.02 * jax.random.normal(ks[4], (KV_LORA,), f32)
    w_ukv = jax.random.normal(ks[5], (KV_LORA, MLA_HEADS * (MLA_NOPE + MLA_V)), f32) * KV_LORA ** -0.5
    sgu_norm_g = 1.0 + 0.02 * jax.random.normal(ks[6], (G_WIDTH,), f32)
    sgu_norm_b = 0.02 * jax.random.normal(ks[7], (G_WIDTH,), f32)
    w_spatial = jax.random.normal(ks[8], (G_HEADS, CHUNK, CHUNK), f32) * CHUNK ** -0.5
    b_spatial = 1.0 + 0.02 * jax.random.normal(ks[9], (G_HEADS, CHUNK), f32)
    w_out = jax.random.normal(ks[10], (D_MIX, D_MODEL), f32) * (D_MIX ** -0.5) * DN_BETA
    ln_g = 1.0 + 0.02 * jax.random.normal(ks[11], (D_MODEL,), f32)
    ln_b = 0.02 * jax.random.normal(ks[12], (D_MODEL,), f32)
    return {"x": x, "positions": positions, "w_in": w_in, "q_norm_g": q_norm_g,
            "w_uq": w_uq, "kv_norm_g": kv_norm_g, "w_ukv": w_ukv,
            "sgu_norm_g": sgu_norm_g, "sgu_norm_b": sgu_norm_b,
            "w_spatial": w_spatial, "b_spatial": b_spatial, "w_out": w_out,
            "ln_g": ln_g, "ln_b": ln_b}

def _hybrid_mixer(h, positions, w_in, q_norm_g, w_uq, kv_norm_g, w_ukv,
                  sgu_norm_g, sgu_norm_b, w_spatial, b_spatial, w_out):
    b, s, _ = h.shape
    proj = jnp.einsum('bsd,de->bse', h, w_in)
    splits = np.cumsum([Q_LORA, KV_LORA, MLA_ROPE, MLA_WIDTH, G_WIDTH, G_WIDTH]).tolist()
    c_q, c_kv, k_rope, z_a, u, v = jnp.split(proj, splits, axis=-1)[:6]
    z_b = proj[..., splits[-1]:]

    q = jnp.einsum('bsr,re->bse', _rmsnorm(c_q, q_norm_g), w_uq)
    q = q.reshape(b, s, MLA_HEADS, MLA_NOPE + MLA_ROPE)
    q_nope, q_rope = q[..., :MLA_NOPE], _rope(q[..., MLA_NOPE:], positions)
    kv = jnp.einsum('bsr,re->bse', _rmsnorm(c_kv, kv_norm_g), w_ukv)
    kv = kv.reshape(b, s, MLA_HEADS, MLA_NOPE + MLA_V)
    k_nope, val = kv[..., :MLA_NOPE], kv[..., MLA_NOPE:]
    k_r = jnp.broadcast_to(_rope(k_rope[:, :, None, :], positions), (b, s, MLA_HEADS, MLA_ROPE))
    qf = jnp.concatenate([q_nope, q_rope], axis=-1)
    kf = jnp.concatenate([k_nope, k_r], axis=-1)
    attn = _causal_attention(qf, kf, val).reshape(b, s, MLA_WIDTH)
    out_a = attn * jax.nn.silu(z_a)

    u = jax.nn.gelu(u, approximate=False)
    v = _layernorm(jax.nn.gelu(v, approximate=False), sgu_norm_g, sgu_norm_b)
    nc = s // CHUNK
    vc = v.reshape(b, nc, CHUNK, G_HEADS, G_HEAD_DIM)
    causal = jnp.tril(jnp.ones((CHUNK, CHUNK), dtype=bool))
    w_s = jnp.where(causal[None], w_spatial, 0.0).astype(v.dtype)
    sv = jnp.einsum('hts,bcshd->bcthd', w_s, vc) + b_spatial.T[None, None, :, :, None]
    sgu = u * sv.reshape(b, s, G_WIDTH)
    out_b = sgu * jax.nn.silu(z_b)

    merged = jnp.concatenate([out_a, out_b], axis=-1)
    return jnp.einsum('bse,ed->bsd', merged, w_out)

def second_block(x, positions, w_in, q_norm_g, w_uq, kv_norm_g, w_ukv,
              sgu_norm_g, sgu_norm_b, w_spatial, b_spatial, w_out, ln_g, ln_b):
    h = x
    for _ in range(DEPTH):
        y = _hybrid_mixer(h, positions, w_in, q_norm_g, w_uq, kv_norm_g, w_ukv,
                          sgu_norm_g, sgu_norm_b, w_spatial, b_spatial, w_out)
        h = _layernorm(DN_ALPHA * h + y, ln_g, ln_b)
    return h


_first_inputs_2 = second_inputs


def second_inputs(seed=0):
    import zlib

    import numpy as np

    out = dict(_first_inputs_2(seed))
    spreads = {}
    factors = {'q_norm_g': 8.0,
     'w_uq': 2.752,
     'kv_norm_g': 8.0,
     'sgu_norm_g': 8.0,
     'sgu_norm_b': 8.0,
     'b_spatial': 8.0,
     'ln_g': 2.828,
     'ln_b': 2.887}
    for name, (base, spread) in spreads.items():
        noise = np.random.default_rng([zlib.crc32(name.encode()), seed]).standard_normal(out[name].shape)
        drawn = base * np.exp(spread * noise) if base else spread * noise
        out[name] = __import__('jax').numpy.asarray(drawn.astype(out[name].dtype))
    for name, factor in factors.items():
        out[name] = (out[name] * factor).astype(out[name].dtype)
    return out


_narrow_inputs_2 = second_inputs


def second_inputs(seed=0):

    out = dict(_narrow_inputs_2(seed))
    wider = {'sgu_norm_g': 9.92, 'sgu_norm_b': 9.84, 'b_spatial': 7.05, 'ln_g': 3.18, 'ln_b': 3.18}
    for name, times in wider.items():
        mean = out[name].mean()
        out[name] = (mean + times * (out[name] - mean)).astype(out[name].dtype)
    return out


def setup_inputs(seed=0):
    out = dict(first_inputs(seed))
    for name, value in second_inputs(seed + 1).items():
        if name != "x":
            out[name + "_2"] = value
    return out


def reference(
    x, c, ctx, c_ctx, w_mod, b_mod, w_in, conv_w, a_log, dt_bias, lb_param, a_norm_g, b_norm_g,
    w_a_out, w_b_out, w_out, ln_g, ln_b, positions_2, w_in_2, q_norm_g_2, w_uq_2, kv_norm_g_2,
    w_ukv_2, sgu_norm_g_2, sgu_norm_b_2, w_spatial_2, b_spatial_2, w_out_2, ln_g_2, ln_b_2,
):
    x = first_block(
        x, c, ctx, c_ctx, w_mod, b_mod, w_in, conv_w, a_log, dt_bias, lb_param, a_norm_g,
        b_norm_g, w_a_out, w_b_out, w_out, ln_g, ln_b,
    )
    return second_block(
        x, positions_2, w_in_2, q_norm_g_2, w_uq_2, kv_norm_g_2, w_ukv_2, sgu_norm_g_2,
        sgu_norm_b_2, w_spatial_2, b_spatial_2, w_out_2, ln_g_2, ln_b_2,
    )


_drawn_inputs = setup_inputs


def setup_inputs(seed=0):
    import zlib

    import numpy as np

    out = dict(_drawn_inputs(seed))
    spreads = {}
    factors = {}
    for name, (base, spread) in spreads.items():
        noise = np.random.default_rng([zlib.crc32(name.encode()), seed]).standard_normal(out[name].shape)
        drawn = base * np.exp(spread * noise) if base else spread * noise
        out[name] = jnp.asarray(drawn.astype(out[name].dtype))
    for name, factor in factors.items():
        out[name] = (out[name] * factor).astype(out[name].dtype)
    return out
```

```python
from contextlib import ExitStack

import concourse.bass as bass
from concourse import mybir

F32 = mybir.dt.float32
U32 = mybir.dt.uint32
I32 = mybir.dt.int32
ALU = mybir.AluOpType
ACT = mybir.ActivationFunctionType
AX = mybir.AxisListType

P = 128
BANK = 512
DM = 1024
KT = DM // P
SEQ = 2048
CTX = 256
TOK = CTX + SEQ
NT = TOK // P
GRID_W = 64
ROWS = SEQ // GRID_W
HEADS = 4
NDIR = 2
HD = HEADS * P
C_AQ, C_AV, C_AB = 0, 2 * HD, 3 * HD
C_AGATE = C_AB + 4 * HEADS
C_BQ = C_AGATE + HD
C_BF = C_BQ + HD
C_BI = C_BF + 2 * HD
C_BGATE = C_BI + HD
C_MERGE = C_BGATE + HD
CONV_K = 5
PAD = CONV_K // 2
RAW = TOK + 4 * PAD
EPS1 = 1e-6
LATENT_BLOCKS = SEQ // BANK
BLOCKS = [(0, CTX)] + [(CTX + BANK * n, BANK) for n in range(LATENT_BLOCKS)]
ALPHA = 2.0 ** 0.25


class Stages:

    def __init__(self, sem, names):
        self.sem, self.names, self.turn = sem, names.split(), 0

    def __call__(self, name):
        want = self.names[self.turn % len(self.names)]
        assert name == want, (name, want)
        self.turn += 1
        return self.sem

    def at(self, i, name):
        return i * len(self.names) + self.names.index(name) + 1


class Chip:

    def __init__(self, nc, stack):
        self.nc = nc
        self.bank = stack.enter_context(nc.psum_tensor("bank", [P, 8, BANK], F32))

        def sb(name, shape, dt=F32):
            return stack.enter_context(nc.sbuf_tensor(name, shape, dt))

        self.sb = sb
        self.ident = sb("ident", [P, P])
        self.ones = sb("ones", [P, P])
        self.low = sb("low", [P, P])
        self.up = sb("up", [P, P])
        self.off = sb("off", [P, NDIR, 7, P])
        self.diag16 = sb("diag16", [P, NDIR, P])
        self.modT = sb("modT", [P, 2 * KT, 2])
        self.gate_rows = sb("gate_rows", [P, DM])
        self.lbT = sb("lbT", [P, 2, 2 * HEADS])
        self.decay_tok = sb("decay_tok", [P, NT, 2 * HEADS])
        self.beta_tok = sb("beta_tok", [P, NT, 2 * HEADS])


def bcast(ap, axis, count):
    v = ap.unsqueeze(axis)
    shape = list(v.shape)
    shape[axis] = count
    return v.broadcast_to(shape)


def phase_constants(chip, c, c_ctx, w_mod, b_mod, lb_param):
    nc, bank = chip.nc, chip.bank
    NW = 4
    MODW = 3 * DM
    with ExitStack() as st:
        sb = lambda n, s: st.enter_context(nc.sbuf_tensor("constants_" + n, s, F32))
        sem = lambda n: st.enter_context(nc.semaphore("constants_" + n))
        cond = sb("cond", [2 * KT, P])
        scond = sb("scond", [2 * KT, P])
        condT = sb("condT", [P, 2 * KT])
        wm = sb("wm", [P, NW, MODW])
        bm = sb("bm", [2, MODW])
        mod = sb("mod", [2, MODW])
        lb = sb("lb", [2 * HEADS, 8, P])
        c_loaded, b_loaded, lb_loaded = sem("c_loaded"), sem("b_loaded"), sem("lb_loaded")
        w_loaded = [sem(f"wm_loaded{s}") for s in range(NW)]
        w_used = sem("wm_used")
        pool_step, act_done = sem("pool_step"), sem("act_done")
        masks_ready = sem("masks_ready")
        pe_done, dve_done = sem("pe_done"), sem("dve_done")
        block = st.enter_context(nc.Block())

        @block.sync
        def _(sp):
            sp.dma_start(cond[0:KT, :], c.rearrange("b (k p) -> (b k) p", p=P)).then_inc(c_loaded, 16)
            sp.dma_start(cond[KT:2 * KT, :], c_ctx.rearrange("(k p) -> k p", p=P)).then_inc(c_loaded, 16)
            for r in range(2):
                sp.dma_start(bm[r:r + 1, :], b_mod).then_inc(b_loaded, 16)
            for r in range(2):
                sp.dma_start(lb[:, r, :], lb_param[r].rearrange("d (h p) -> (d h) p", p=P)).then_inc(lb_loaded, 16)
            for k in range(KT):
                if k >= NW:
                    sp.wait_ge(w_used, k - NW + 1)
                sp.dma_start(wm[:, k % NW, :], w_mod[0, k * P:(k + 1) * P, :]).then_inc(w_loaded[k % NW], 16)

        @block.gpsimd
        def _(pool):
            count = [0]

            def step(ins):
                count[0] += 1
                ins.then_inc(pool_step, 1)
                pool.wait_ge(pool_step, count[0])

            def keep(view, pattern, base, mul):
                step(nc.gpsimd.affine_select(out=view, in_=view, compare_op=ALU.is_ge, fill=0.0, base=base,
                                             pattern=pattern, channel_multiplier=mul))

            nc.gpsimd.memset(chip.ones[:], 1.0)
            nc.gpsimd.memset(chip.low[:], 1.0)
            nc.gpsimd.memset(chip.up[:], 1.0)
            nc.gpsimd.memset(chip.off[:], 0.0)
            nc.gpsimd.memset(chip.diag16[:], 1.0)
            step(nc.gpsimd.memset(chip.ident[:], 0.0))
            step(nc.gpsimd.affine_select(out=chip.ident[:], in_=chip.ident[:], compare_op=ALU.not_equal, fill=1.0,
                                         base=0, pattern=[[-1, P]], channel_multiplier=1))
            keep(chip.low[:], [[-1, P]], 0, 1)
            keep(chip.up[:], [[1, P]], 0, -1)
            for n in range(7):
                b = 1 << n
                nb = P // (2 * b)
                for d in range(NDIR):
                    v = chip.off[:, d, n, :].rearrange("p (c j) -> p c j", j=2 * b)[:, :, d * b:(d + 1) * b]
                    lo = b if d == 0 else 0
                    step(nc.gpsimd.memset(v, 1.0))
                    keep(v, [[-2 * b, nb], [0, b]], -lo, 1)
                    keep(v, [[2 * b, nb], [0, b]], lo + b - 1, -1)
            for d in range(NDIR):
                v = chip.diag16[:, d, :].rearrange("p (c j) -> p c j", j=16)
                if d == 0:
                    keep(v, [[16, 8], [1, 16]], 0, -1)
                    keep(v, [[-16, 8], [0, 16]], 0, 1)
                else:
                    keep(v, [[-16, 8], [-1, 16]], 0, 1)
                    keep(v, [[16, 8], [0, 16]], 15, -1)
            nc.gpsimd.memset(chip.decay_tok[:, 0, 0:1], 0.0).then_inc(masks_ready, 1)

        @block.scalar
        def _(act):
            act.wait_ge(c_loaded, 32)
            act.activation(scond[:], cond[:], ACT.Silu).then_inc(act_done, 1)
            for r in range(2):
                act.wait_ge(dve_done, 3 + r)
                act.activation(lb[:, 5 + r, :], lb[:, 3 + r, :], ACT.Exp).then_inc(act_done, 1)

        @block.vector
        def _(dve):
            dve.wait_ge(lb_loaded, 32)
            dve.tensor_tensor(lb[:, 2, :], lb[:, 0, :], lb[:, 1, :], ALU.max).then_inc(dve_done, 1)
            dve.wait_ge(masks_ready, 1)
            dve.wait_ge(pe_done, 1)
            dve.tensor_copy(condT[:], bank[:, 6, 0:2 * KT]).then_inc(dve_done, 1)
            dve.wait_ge(dve_done, 1)
            for r in range(2):
                dve.tensor_tensor(lb[:, 3 + r, :], lb[:, r, :], lb[:, 2, :], ALU.subtract).then_inc(dve_done, 1)
            dve.wait_ge(act_done, 3)
            dve.tensor_tensor(lb[:, 7, :], lb[:, 5, :], lb[:, 6, :], ALU.add).then_inc(dve_done, 1)
            dve.wait_ge(dve_done, 5)
            dve.reciprocal(lb[:, 2, :], lb[:, 7, :]).then_inc(dve_done, 1)
            dve.wait_ge(dve_done, 6)
            dve.tensor_tensor(lb[:, 3, :], lb[:, 5, :], lb[:, 2, :], ALU.mult).then_inc(dve_done, 1)
            dve.wait_ge(dve_done, 7)
            dve.tensor_scalar(lb[:, 4, :], lb[:, 3, :], -1.0, 1.0, ALU.mult, ALU.add).then_inc(dve_done, 1)
            dve.wait_ge(b_loaded, 32)
            dve.wait_ge(pe_done, 3)
            for n in range(6):
                dve.tensor_tensor(mod[:, n * BANK:(n + 1) * BANK], bank[0:2, n, :], bm[:, n * BANK:(n + 1) * BANK],
                                  ALU.add).then_inc(dve_done, 1)
            dve.wait_ge(pe_done, 4)
            mT = bank[:, 7, 0:4 * KT].rearrange("p (k s) -> p k s", s=2)
            dve.tensor_copy(chip.modT[:, 0:KT, :], mT[:, 0:KT, :])
            dve.tensor_scalar(chip.modT[:, KT:2 * KT, :], mT[:, KT:2 * KT, :], 1.0, None, ALU.add)
            for r in range(2):
                dve.tensor_copy(chip.lbT[:, r, :], bank[:, 6, 64 + 8 * r:72 + 8 * r])
            dve.wait_ge(pe_done, 5)
            for n in range(2):
                dve.tensor_copy(chip.gate_rows[:, n * BANK:(n + 1) * BANK], bank[:, n, :])

        @block.tensor
        def _(pe):
            pe.wait_ge(masks_ready, 1)
            pe.wait_ge(act_done, 1)
            pe.transpose(bank[:, 6, 0:2 * KT], scond[:], chip.ident[0:2 * KT, 0:2 * KT]).then_inc(pe_done, 1)
            pe.wait_ge(dve_done, 8)
            for r in range(2):
                t = pe.transpose(bank[:, 6, 64 + 8 * r:72 + 8 * r], lb[:, 3 + r, :], chip.ident[0:8, 0:8])
            t.then_inc(pe_done, 1)
            cT = condT[:].rearrange("p (s k) -> p k s", k=KT)
            for k in range(KT):
                pe.wait_ge(w_loaded[k % NW], 16 * (k // NW + 1))
                for n in range(6):
                    mm = pe.matmul(bank[0:2, n, :], cT[:, k, :], wm[:, k % NW, n * BANK:(n + 1) * BANK],
                                   start=(k == 0), stop=(k == KT - 1))
                mm.then_inc(w_used, 1)
            pe.wait_ge(w_used, KT)
            pe.nop().then_inc(pe_done, 1)
            pe.wait_ge(dve_done, 14)
            for j in range(2 * KT):
                t = pe.transpose(bank[:, 7, 2 * j:2 * j + 2], mod[:, j * P:(j + 1) * P], chip.ident[0:2, 0:2])
            t.then_inc(pe_done, 1)
            for n in range(2):
                mm = pe.matmul(bank[:, n, :], chip.ones[0:1, :], mod[0:1, 2 * DM + n * BANK:2 * DM + (n + 1) * BANK],
                               start=True, stop=True)
            mm.then_inc(pe_done, 1)


def phase_modulated_norm(chip, uT, x, ctx_in):
    nc, bank = chip.nc, chip.bank
    with ExitStack() as st:
        sb = lambda n, s: st.enter_context(nc.sbuf_tensor("modulated_norm_" + n, s, F32))
        sem = lambda n: st.enter_context(nc.semaphore("modulated_norm_" + n))
        xin = sb("xin", [P, 2, DM])
        xh = sb("xh", [P, 2, DM])
        stats = sb("stats", [P, 2, 12])
        mv = sb("mv", [P, 2, 2])
        inv = sb("inv", [P, 2, 1])
        rstd = sb("rstd", [P, 2, 1])
        x_loaded = [sem(f"x_loaded{s}") for s in range(2)]
        D = Stages(sem("dve_stage"), "stats0 mv0 var0 inv0 xh0 uT0 stats1 mv1 var1 inv1 xh1 uT1")
        A = Stages(sem("act_stage"), "rstd0 uT0 rstd1 uT1")
        T = Stages(sem("pe_stage"), "turned0 turned1")
        block = st.enter_context(nc.Block())
        pairs = SEQ // (2 * P)

        def turns(eng, body):
            body(0, True)
            with eng.Fori(1, pairs + 1) as i:
                body(i, False)

        @block.sync
        def _(sp):
            def body(i, first):
                for s in range(2):
                    if not first:
                        sp.wait_ge(D.sem, D.at(i - 1, f"xh{s}"))
                    src = ctx_in[s * P:(s + 1) * P, :] if first else x[bass.ds((i - 1) * 2 * P + s * P, P), :]
                    sp.dma_start(xin[:, s, :], src).then_inc(x_loaded[s], 16)
            turns(sp, body)

        @block.vector
        def _(dve):
            def body(i, first):
                stream = 1 if first else 0
                for s in range(2):
                    dve.wait_ge(x_loaded[s], i * 16 + 16)
                    dve.bn_stats(stats[:, s, 0:6], xin[:, s, 0:BANK])
                    dve.bn_stats(stats[:, s, 6:12], xin[:, s, BANK:DM]).then_inc(D(f"stats{s}"), 1)
                    dve.wait_ge(D.sem, D.at(i, f"stats{s}"))
                    dve.nop(nofuse=True)
                    dve.bn_aggr(mv[:, s, :], stats[:, s, :]).then_inc(D(f"mv{s}"), 1)
                    dve.wait_ge(D.sem, D.at(i, f"mv{s}"))
                    dve.tensor_scalar(mv[:, s, 1:2], mv[:, s, 1:2], EPS1, None, ALU.add).then_inc(D(f"var{s}"), 1)
                    dve.wait_ge(D.sem, D.at(i, f"var{s}"))
                    dve.reciprocal(inv[:, s, :], mv[:, s, 1:2]).then_inc(D(f"inv{s}"), 1)
                    dve.wait_ge(A.sem, A.at(i, f"rstd{s}"))
                    if not first:
                        dve.wait_ge(T.sem, T.at(i - 1, f"turned{s}"))
                    dve.tensor_scalar(xh[:, s, :], xin[:, s, :], mv[:, s, 0:1], rstd[:, s, :], ALU.subtract,
                                      ALU.mult).then_inc(D(f"xh{s}"), 1)
                    dve.wait_ge(T.sem, T.at(i, f"turned{s}"))
                    for k in range(KT // 2):
                        ev = dve.tensor_scalar(uT[:, k, bass.ds(i * 2 * P + s * P, P)], bank[:, 2 * s, k * P:(k + 1) * P],
                                               chip.modT[:, KT + k, stream:stream + 1],
                                               chip.modT[:, k, stream:stream + 1], ALU.mult, ALU.add)
                    ev.then_inc(D(f"uT{s}"), 1)
            turns(dve, body)

        @block.scalar
        def _(act):
            def body(i, first):
                stream = 1 if first else 0
                for s in range(2):
                    act.wait_ge(D.sem, D.at(i, f"inv{s}"))
                    act.activation(rstd[:, s, :], inv[:, s, :], ACT.Sqrt).then_inc(A(f"rstd{s}"), 1)
                    act.wait_ge(T.sem, T.at(i, f"turned{s}"))
                    for k in range(KT // 2, KT):
                        ev = act.activation(uT[:, k, bass.ds(i * 2 * P + s * P, P)],
                                            bank[:, 2 * s + 1, (k - KT // 2) * P:(k - KT // 2 + 1) * P], ACT.Identity,
                                            bias=chip.modT[:, k, stream:stream + 1],
                                            scale=chip.modT[:, KT + k, stream:stream + 1])
                    ev.then_inc(A(f"uT{s}"), 1)
            turns(act, body)

        @block.tensor
        def _(pe):
            def body(i, first):
                for s in range(2):
                    pe.wait_ge(D.sem, D.at(i, f"xh{s}"))
                    if not first:
                        pe.wait_ge(D.sem, D.at(i - 1, f"uT{s}"))
                        pe.wait_ge(A.sem, A.at(i - 1, f"uT{s}"))
                    for k in range(KT):
                        t = pe.transpose(bank[:, 2 * s + k // 4, (k % 4) * P:(k % 4 + 1) * P],
                                         xh[:, s, k * P:(k + 1) * P], chip.ident[:])
                    t.then_inc(T(f"turned{s}"), 1)
            turns(pe, body)


def phase_conv(chip, uT, w_in, conv_w, sa):
    nc, bank = chip.nc, chip.bank
    NF = 3 * HEADS
    with ExitStack() as st:
        sb = lambda n, s: st.enter_context(nc.sbuf_tensor("conv_" + n, s, F32))
        sem = lambda n: st.enter_context(nc.semaphore("conv_" + n))
        W = sb("W", [P, 2, KT, P])
        taps = sb("taps", [P, NF, CONV_K])
        tap_rows = sb("tap_rows", [NF * CONV_K, P])
        raw = sb("raw", [P, 2, RAW])
        acc = sb("acc", [P, RAW])
        y = sb("y", [P, 2, TOK])
        sq = sb("sq", [P, TOK])
        inv = sb("inv", [P, TOK])
        w_loaded = [sem(f"w_loaded{s}") for s in range(2)]
        y_stored = [sem(f"y_stored{s}") for s in range(2)]
        taps_loaded, taps_ready, taps_turned = sem("taps_loaded"), sem("taps_ready"), sem("taps_turned")
        T = Stages(sem("pe_stage"), " ".join([f"proj{b}" for b in range(5)] + [f"sum{b}" for b in range(5)]))
        D = Stages(sem("dve_stage"), "t0 t1 t2 t3 conv " + " ".join(f"ss{b}" for b in range(5)) + " inv y")
        A = Stages(sem("act_stage"), " ".join(f"raw{b}" for b in range(5)) + " silu sq rinv")
        block = st.enter_context(nc.Block())
        rcol = [PAD + t0 + (2 * PAD if t0 else 0) for t0, _ in BLOCKS]
        WIDE = RAW - 2 * PAD

        @block.sync
        def _(sp):
            sp.dma_start(tap_rows[:], conv_w[0].rearrange("t (f p) -> (t f) p", p=P)).then_inc(taps_loaded, 16)

            def body(i, s, first):
                f = 2 * i + s
                if not first:
                    sp.wait_ge(T.sem, T.at(f - 2, "proj4"))
                sp.dma_start(W[:, s], w_in[:, bass.ds(f * P, P)].rearrange("(k p) n -> p k n", p=P)
                             ).then_inc(w_loaded[s], 16)

            def store(i, s):
                f = 2 * i + s
                sp.wait_ge(D.sem, D.at(f, "y"))
                sp.dma_start(sa[bass.ds(f, 1)].rearrange("a p t -> (a p) t"), y[:, s, :]).then_inc(y_stored[s], 16)
            body(0, 0, True)
            body(0, 1, True)
            with sp.Fori(0, NF // 2 - 1) as i:
                for s in range(2):
                    body(i + 1, s, False)
                    store(i, s)
            for s in range(2):
                store(NF // 2 - 1, s)
                sp.wait_ge(y_stored[s], 16 * (NF // 2))

        @block.tensor
        def _(pe):
            pe.wait_ge(taps_loaded, 16)
            pe.transpose(bank[:, 7, 0:NF * CONV_K], tap_rows[:], chip.ident[0:NF * CONV_K, 0:NF * CONV_K]
                         ).then_inc(taps_turned, 1)

            def body(i, s, first):
                f = 2 * i + s
                pe.wait_ge(w_loaded[s], i * 16 + 16)
                for b, (t0, n) in enumerate(BLOCKS):
                    if not first:
                        pe.wait_ge(A.sem, A.at(f - 1, f"raw{b}"))
                    for k in range(KT):
                        mm = pe.matmul(bank[:, b, 0:n], W[:, s, k, :], uT[:, k, t0:t0 + n], start=(k == 0),
                                       stop=(k == KT - 1))
                    mm.then_inc(T(f"proj{b}"), 1)
                pe.wait_ge(A.sem, A.at(f, "sq"))
                if first:
                    pe.wait_ge(taps_ready, 1)
                for b, (t0, n) in enumerate(BLOCKS):
                    if b >= 3:
                        pe.wait_ge(D.sem, D.at(f, f"ss{b - 3}"))
                    elif not first:
                        pe.wait_ge(D.sem, D.at(f - 1, f"ss{min(b + 3, 4)}"))
                    pe.matmul(bank[:, 5 + b % 3, 0:n], chip.ones[:], sq[:, t0:t0 + n], start=True, stop=True
                              ).then_inc(T(f"sum{b}"), 1)
            body(0, 0, True)
            body(0, 1, False)
            with pe.Fori(1, NF // 2) as i:
                body(i, 0, False)
                body(i, 1, False)

        @block.scalar
        def _(act):
            def body(i, s, first):
                f = 2 * i + s
                for b, (t0, n) in enumerate(BLOCKS):
                    act.wait_ge(T.sem, T.at(f, f"proj{b}"))
                    if not first:
                        act.wait_ge(D.sem, D.at(f - 2, "conv"))
                    act.activation(raw[:, s, rcol[b]:rcol[b] + n], bank[:, b, 0:n], ACT.Copy).then_inc(A(f"raw{b}"), 1)
                act.wait_ge(D.sem, D.at(f, "conv"))
                if not first:
                    act.wait_ge(y_stored[s], i * 16)
                act.activation(y[:, s, 0:CTX], acc[:, 0:CTX], ACT.Silu)
                act.activation(y[:, s, CTX:TOK], acc[:, CTX + 2 * PAD:WIDE], ACT.Silu).then_inc(A("silu"), 1)
                act.wait_ge(A.sem, A.at(f, "silu"))
                if not (first and s == 0):
                    act.wait_ge(T.sem, T.at(f - 1, "sum4"))
                act.activation(sq[:], y[:, s, :], ACT.Square).then_inc(A("sq"), 1)
                act.wait_ge(D.sem, D.at(f, "inv"))
                act.activation(inv[:], inv[:], ACT.Sqrt, scale=scale_of[0]).then_inc(A("rinv"), 1)
            scale_of = [1.0 / P]
            for s in range(2):
                body(0, s, True)
            with act.Fori(1, HEADS // 2) as i:
                for s in range(2):
                    body(i, s, False)
            scale_of[0] = 1.0
            with act.Fori(HEADS // 2, NF // 2) as i:
                for s in range(2):
                    body(i, s, False)

        @block.vector
        def _(dve):
            for s in range(2):
                dve.memset(raw[:, s, 0:PAD], 0.0)
                dve.memset(raw[:, s, PAD + CTX:3 * PAD + CTX], 0.0)
                dve.memset(raw[:, s, RAW - PAD:RAW], 0.0)
            dve.wait_ge(taps_turned, 1)
            dve.tensor_copy(taps[:].rearrange("p f t -> p t f"),
                            bank[:, 7, 0:NF * CONV_K].rearrange("p (t f) -> p t f", f=NF)).then_inc(taps_ready, 1)
            dve.wait_ge(taps_ready, 1)

            def body(i, s, first, norm):
                f = 2 * i + s
                tap = taps[:, bass.ds(f, 1), :].rearrange("p a t -> p (a t)")
                dve.wait_ge(A.sem, A.at(f, "raw4"))
                if not (first and s == 0):
                    dve.wait_ge(A.sem, A.at(f - 1, "silu"))
                dve.tensor_scalar(acc[:, 0:WIDE], raw[:, s, 0:WIDE], tap[:, 0:1], None, ALU.mult
                                  ).then_inc(D("t0"), 1)
                for t in range(1, CONV_K):
                    dve.wait_ge(D.sem, D.at(f, f"t{t - 1}"))
                    dve.scalar_tensor_tensor(out=acc[:, 0:WIDE], in0=raw[:, s, t:t + WIDE], scalar=tap[:, t:t + 1],
                                             in1=acc[:, 0:WIDE], op0=ALU.mult, op1=ALU.add
                                             ).then_inc(D(f"t{t}" if t < CONV_K - 1 else "conv"), 1)
                for b, (t0, n) in enumerate(BLOCKS):
                    dve.wait_ge(T.sem, T.at(f, f"sum{b}"))
                    if norm:
                        dve.tensor_scalar(inv[:, t0:t0 + n], bank[:, 5 + b % 3, 0:n], EPS1, None, ALU.add
                                          ).then_inc(D(f"ss{b}"), 1)
                    else:
                        dve.tensor_scalar(inv[:, t0:t0 + n], bank[:, 5 + b % 3, 0:n], 0.0, 1.0, ALU.mult, ALU.add
                                          ).then_inc(D(f"ss{b}"), 1)
                dve.wait_ge(D.sem, D.at(f, "ss4"))
                dve.reciprocal(inv[:], inv[:]).then_inc(D("inv"), 1)
                dve.wait_ge(A.sem, A.at(f, "rinv"))
                if norm:
                    dve.tensor_tensor(y[:, s, :], y[:, s, :], inv[:], ALU.mult).then_inc(D("y"), 1)
                else:
                    dve.memset(inv[:, 0:1], 1.0).then_inc(D("y"), 1)
            body(0, 0, True, True)
            body(0, 1, True, True)
            with dve.Fori(1, HEADS) as i:
                body(i, 0, False, True)
                body(i, 1, False, True)
            with dve.Fori(HEADS, NF // 2) as i:
                body(i, 0, False, False)
                body(i, 1, False, False)


def phase_decay_beta(chip, uT, w_in, a_log, dt_bias):
    nc, bank = chip.nc, chip.bank
    NH2 = 2 * HEADS
    with ExitStack() as st:
        sb = lambda n, s: st.enter_context(nc.sbuf_tensor("decay_beta_" + n, s, F32))
        sem = lambda n: st.enter_context(nc.semaphore("decay_beta_" + n))
        W = sb("Wab", [P, KT, 2 * NH2])
        z16 = sb("z16", [2 * NH2, TOK])
        z = sb("z", [P, NT, 2 * NH2])
        par = sb("par", [P, 2, NH2])
        w = [sb(f"w{n}", [P, NT, NH2]) for n in range(6)]
        loaded, act_done, pe_done, dve_done = sem("loaded"), sem("act_done"), sem("pe_done"), sem("dve_done")
        block = st.enter_context(nc.Block())

        @block.sync
        def _(sp):
            sp.dma_start(W[:], w_in[:, C_AB:C_AB + 2 * NH2].rearrange("(k p) n -> p k n", p=P)).then_inc(loaded, 16)
            for n, src in enumerate((dt_bias, a_log)):
                sp.dma_start(par[:, n, :], src.rearrange("l d h -> l (d h)").broadcast_to([P, NH2])
                             ).then_inc(loaded, 16)

        @block.tensor
        def _(pe):
            pe.wait_ge(loaded, 48)
            for b, (t0, n) in enumerate(BLOCKS):
                for k in range(KT):
                    mm = pe.matmul(bank[0:2 * NH2, b, 0:n], W[:, k, :], uT[:, k, t0:t0 + n], start=(k == 0),
                                   stop=(k == KT - 1))
                mm.then_inc(pe_done, 1)
            pe.wait_ge(act_done, 5)
            for t in range(NT):
                tr = pe.transpose(bank[:, 7, t * 2 * NH2:(t + 1) * 2 * NH2], z16[:, t * P:(t + 1) * P],
                                  chip.ident[0:2 * NH2, 0:2 * NH2])
            tr.then_inc(pe_done, 1)

        @block.scalar
        def _(act):
            for b, (t0, n) in enumerate(BLOCKS):
                act.wait_ge(pe_done, b + 1)
                act.activation(z16[:, t0:t0 + n], bank[0:2 * NH2, b, 0:n], ACT.Copy).then_inc(act_done, 1)
            act.wait_ge(dve_done, 1)
            act.activation(chip.beta_tok[:], z[:, :, NH2:], ACT.Sigmoid)
            act.wait_ge(dve_done, 2)
            act.activation(w[0][:], z[:, :, 0:NH2], ACT.Abs).then_inc(act_done, 1)
            act.wait_ge(act_done, 6)
            act.activation(w[1][:], w[0][:], ACT.Exp, scale=-1.0).then_inc(act_done, 1)
            act.activation(par[:, 1, :], par[:, 1, :], ACT.Exp).then_inc(act_done, 1)
            act.wait_ge(dve_done, 3)
            act.activation(w[0][:], w[2][:], ACT.Ln).then_inc(act_done, 1)

        @block.vector
        def _(dve):
            n = [0]

            def link(ins):
                n[0] += 1
                ins.then_inc(dve_done, 1)
                dve.wait_ge(dve_done, n[0])
            dve.wait_ge(pe_done, 6)
            link(dve.tensor_copy(z[:], bank[:, 7, 0:NT * 2 * NH2].rearrange("p (t c) -> p t c", t=NT)))
            link(dve.tensor_tensor(z[:, :, 0:NH2], z[:, :, 0:NH2], bcast(par[:, 0, :], 1, NT), ALU.add))
            dve.wait_ge(act_done, 8)
            link(dve.tensor_scalar(w[2][:], w[1][:], 1.0, None, ALU.add))
            link(dve.tensor_scalar(w[3][:], w[2][:], 1.0, None, ALU.subtract))
            link(dve.tensor_scalar(w[4][:], w[3][:], 0.0, None, ALU.is_equal))
            link(dve.tensor_tensor(w[3][:], w[3][:], w[4][:], ALU.add))
            link(dve.reciprocal(w[5][:], w[3][:]))
            dve.wait_ge(act_done, 9)
            link(dve.tensor_tensor(w[0][:], w[0][:], w[4][:], ALU.add))
            link(dve.tensor_tensor(w[0][:], w[0][:], w[5][:], ALU.mult))
            link(dve.tensor_tensor(w[0][:], w[0][:], w[1][:], ALU.mult))
            link(dve.tensor_scalar(w[1][:], z[:, :, 0:NH2], 0.0, None, ALU.max))
            link(dve.tensor_tensor(w[0][:], w[0][:], w[1][:], ALU.add))
            link(dve.tensor_scalar(w[0][:], w[0][:], -1.0, None, ALU.mult))
            link(dve.tensor_tensor(chip.decay_tok[:], w[0][:], bcast(par[:, 1, :], 1, NT), ALU.mult))


def phase_gla_inputs(chip, uT, w_in, sq_, sv, sk, sg):
    nc, bank = chip.nc, chip.bank
    NF = 4 * HEADS
    with ExitStack() as st:
        sb = lambda n, s: st.enter_context(nc.sbuf_tensor("gla_inputs_" + n, s, F32))
        sem = lambda n: st.enter_context(nc.semaphore("gla_inputs_" + n))
        W = sb("W", [P, 2, KT, P])
        reset = sb("reset", [P, NDIR, TOK])
        a = sb("a", [P, 2, TOK])
        b_ = sb("b_", [P, 2, TOK])
        lf = sb("lf", [P, TOK])
        w_loaded = [sem(f"w_loaded{s}") for s in range(2)]
        stored = [sem(f"stored{s}") for s in range(2)]
        reset_ready = sem("reset_ready")
        T = Stages(sem("pe_stage"), " ".join(f"proj{b}" for b in range(5)))
        D = Stages(sem("dve_stage"), "f k g")
        A = Stages(sem("act_stage"), " ".join(f"out{b}" for b in range(5)) + " ln")
        block = st.enter_context(nc.Block())
        groups = [(0, C_BQ), (HEADS // 2, C_BI), (HEADS, C_BF)]

        def to(dst, b):
            t0, n = BLOCKS[b]
            if b == 0:
                return dst[:, 0:CTX]
            r = GRID_W // 8 * 0 + (n // GRID_W)
            return dst[:, CTX:TOK].rearrange("p (w r) -> p r w", r=ROWS)[:, (b - 1) * r:b * r, :]

        def frm(b):
            n = BLOCKS[b][1]
            v = bank[:, b, 0:n]
            return v if b == 0 else v.rearrange("p (r w) -> p r w", w=GRID_W)

        @block.sync
        def _(sp):
            def body(i, s, col, first):
                f = 2 * i + s
                if not first:
                    sp.wait_ge(T.sem, T.at(f - 2, "proj4"))
                sp.dma_start(W[:, s], w_in[:, bass.ds(col + s * P, P)].rearrange("(k p) n -> p k n", p=P)
                             ).then_inc(w_loaded[s], 16)
            for n, (i0, col) in enumerate(groups):
                i1 = groups[n + 1][0] if n < 2 else NF // 2
                start = i0
                if n == 0:
                    for s in range(2):
                        body(0, s, col, True)
                    start = 1
                with sp.Fori(start, i1) as i:
                    for s in range(2):
                        body(i, s, col + (i - i0) * 2 * P, False)

        @block.gpsimd
        def _(sp):
            def row(dram, r):
                return dram[bass.ds(r, 1)].rearrange("a p t -> (a p) t")

            for dram, i0 in ((sq_, 0), (sv, HEADS // 2)):
                with sp.Fori(i0, i0 + HEADS // 2) as i:
                    for s in range(2):
                        sp.wait_ge(A.sem, A.at(2 * i + s, "ln"))
                        sp.dma_start(row(dram, 2 * (i - i0) + s), a[:, s, :]).then_inc(stored[s], 16)
            with sp.Fori(HEADS, NF // 2) as i:
                for s in range(2):
                    sp.wait_ge(D.sem, D.at(2 * (i - HEADS) + s, "g"))
                    sp.dma_start(row(sk, 2 * (i - HEADS) + s), b_[:, s, :]).then_inc(stored[s], 16)
                    sp.dma_start(row(sg, 2 * (i - HEADS) + s), a[:, s, :]).then_inc(stored[s], 16)
            for s in range(2):
                sp.wait_ge(stored[s], 16 * HEADS + 32 * HEADS)

        @block.tensor
        def _(pe):
            def body(i, s, first):
                f = 2 * i + s
                pe.wait_ge(w_loaded[s], i * 16 + 16)
                for b, (t0, n) in enumerate(BLOCKS):
                    if not first:
                        pe.wait_ge(A.sem, A.at(f - 1, f"out{b}"))
                    for k in range(KT):
                        mm = pe.matmul(bank[:, b, 0:n], W[:, s, k, :], uT[:, k, t0:t0 + n], start=(k == 0),
                                       stop=(k == KT - 1))
                    mm.then_inc(T(f"proj{b}"), 1)
            body(0, 0, True)
            body(0, 1, False)
            with pe.Fori(1, NF // 2) as i:
                body(i, 0, False)
                body(i, 1, False)

        @block.scalar
        def _(act):
            def plain(i, s, first, func):
                f = 2 * i + s
                if not first:
                    act.wait_ge(stored[s], i * 16)
                for b in range(5):
                    act.wait_ge(T.sem, T.at(f, f"proj{b}"))
                    act.activation(to(a[:, s, :], b), frm(b), func).then_inc(A(f"out{b}"), 1)
                act.wait_ge(A.sem, A.at(f, "out4"))
                act.activation(a[:, s, :], a[:, s, :], ACT.Copy, scale=P ** -0.5 if func == ACT.Silu else 1.0
                               ).then_inc(A("ln"), 1)

            def forget(i, s):
                f = 2 * i + s
                act.wait_ge(stored[s], (i - HEADS) * 32 + 16 * HEADS)
                for b in range(5):
                    act.wait_ge(T.sem, T.at(f, f"proj{b}"))
                    act.activation(to(a[:, s, :], b), frm(b), ACT.Sigmoid)
                    act.activation(to(b_[:, s, :], b), frm(b), ACT.Sigmoid, scale=-1.0).then_inc(A(f"out{b}"), 1)
                act.wait_ge(D.sem, D.at(2 * (i - HEADS) + s, "f"))
                act.activation(lf[:], a[:, s, :], ACT.Ln).then_inc(A("ln"), 1)
            for s in range(2):
                plain(0, s, True, ACT.Silu)
            with act.Fori(1, HEADS // 2) as i:
                for s in range(2):
                    plain(i, s, False, ACT.Silu)
            with act.Fori(HEADS // 2, HEADS) as i:
                for s in range(2):
                    plain(i, s, False, ACT.Copy)
            with act.Fori(HEADS, NF // 2) as i:
                for s in range(2):
                    forget(i, s)

        @block.vector
        def _(dve):
            dve.memset(reset[:], 1.0).then_inc(reset_ready, 1)
            dve.wait_ge(reset_ready, 1)
            for d in range(NDIR):
                v = reset[:, d, :].rearrange("p (t c) -> p t c", c=P)
                dve.memset(v[:, :, d * (P - 1):d * (P - 1) + 1], 0.0).then_inc(reset_ready, 1)
            dve.wait_ge(reset_ready, 3)

            def body(i, s, d):
                g = 2 * i + s
                dve.wait_ge(A.sem, A.at(g + 2 * HEADS, "out4"))
                one_less = chip.lbT[:, 1, bass.ds(g, 1)]
                dve.tensor_scalar(a[:, s, :], a[:, s, :], one_less, chip.lbT[:, 0, bass.ds(g, 1)], ALU.mult,
                                  ALU.add).then_inc(D("f"), 1)
                dve.tensor_scalar(b_[:, s, :], b_[:, s, :], one_less, None, ALU.mult).then_inc(D("k"), 1)
                dve.wait_ge(A.sem, A.at(g + 2 * HEADS, "ln"))
                step = 1 if d == 0 else -1
                dve.tensor_tensor_scan(a[:, s, ::step], reset[:, d, ::step], lf[:, ::step], 0.0, ALU.mult,
                                       ALU.add).then_inc(D("g"), 1)
            for d in range(NDIR):
                with dve.Fori(d * HEADS // 2, (d + 1) * HEADS // 2) as i:
                    for s in range(2):
                        body(i, s, d)


def phase_delta_rule(chip, sa, so_a):
    nc, bank = chip.nc, chip.bank
    LEVELS = range(1, 7)
    with ExitStack() as st:
        sb = lambda n, s: st.enter_context(nc.sbuf_tensor("delta_" + n, s, F32))
        sem = lambda n: st.enter_context(nc.semaphore("delta_" + n))
        mat = lambda n: [sb(f"{n}{d}", [P, HEADS, P]) for d in range(NDIR)]
        qkv = [[sb(f"qkv{d}{s}", [P, 3 * HEADS, P]) for s in range(2)] for d in range(NDIR)]
        kd, kbe, vb, Dm, A_, AT, T_, TT = (mat(n) for n in ("kd", "kbe", "vb", "Dm", "A", "AT", "T", "TT"))
        attnT, qg, vnew, S = (mat(n) for n in ("attnT", "qg", "vnew", "S"))
        M1, WT = A_, T_
        small = sb("small", [P, NDIR, 8, HEADS])
        g_, beta, Gc, gd, eGc, egd, beg, eGl = ([small[:, d, n, :] for d in range(NDIR)] for n in range(8))
        o = sb("o", [P, HEADS, SEQ])
        none = sb("none", [P, NDIR])
        loaded = [sem(f"loaded{s}") for s in range(2)]
        zeroed, o_stored = sem("zeroed"), sem("o_stored")
        both = lambda names: " ".join(f"{x}{d}" for x in names.split() for d in range(NDIR))
        D = Stages(sem("dve_stage"), both("gb Gc gd E0_ E kd kbe vb eGl qg Dm A attn Ti T0_ TTi TT0_ "
                                          + " ".join(f"M{n}_ T{n}_ TT{n}_" for n in LEVELS) + " S o"))
        A = Stages(sem("act_stage"), both("eGc egd E eGr AT attnT WT vnew"))
        T = Stages(sem("pe_stage"), both("tok sum gram flip " + " ".join(f"a{n}_ b{n}_" for n in LEVELS) + " w v os"))
        block = st.enter_context(nc.Block())
        last = (P - 1, 0)
        cum = (chip.up, chip.low)
        seen = (chip.low, chip.up)
        B = [[bank[:, 4 * d + n, :] for n in range(4)] for d in range(NDIR)]
        B3 = [[b.rearrange("p (h c) -> p h c", h=HEADS) for b in bs] for bs in B]

        def turns(eng, body):
            for n in range(2):
                body(n, n, n)
            with eng.Fori(1, NT // 2) as i:
                for s in range(2):
                    body(2 * i + s, s, None)

        def tile(n, ctx, d):
            if d == 0:
                return n
            return 1 - n if ctx is not None else NT + 1 - n

        @block.sync
        def _(sp):
            def body(n, s, ctx):
                if ctx is None:
                    sp.wait_ge(D.sem, D.at(n - 2, "attn1"))
                for d in range(NDIR):
                    sp.dma_start(qkv[d][s][:], sa[:, :, bass.ds(tile(n, ctx, d) * P, P)].rearrange("a p t -> p a t")
                                 ).then_inc(loaded[s], 16)
            turns(sp, body)
            sp.wait_ge(D.sem, D.at(NT - 1, "o1"))
            sp.dma_start(so_a.rearrange("h p t -> p h t"), o[:]).then_inc(o_stored, 16)
            sp.wait_ge(o_stored, 16)

        @block.gpsimd
        def _(pool):
            nc.gpsimd.memset(o[:], 0.0)
            for d in range(NDIR):
                z = nc.gpsimd.memset(S[d][:], 0.0)
            z.then_inc(zeroed, 1)

        @block.tensor
        def _(pe):
            pe.wait_ge(zeroed, 1)

            def heads(fn):
                for h in range(HEADS):
                    m = fn(h)
                return m

            def body(n, s, ctx):
                pe.wait_ge(loaded[s], (n // 2 if ctx is not None else (n - s) // 2) * 32 + 32)
                for d in range(NDIR):
                    x = qkv[d][s]
                    if ctx != 0:
                        pe.wait_ge(A.sem, A.at(n - 1, f"vnew{d}"))
                    heads(lambda h: pe.transpose(B3[d][0][:, h, :], x[:, HEADS + h, :], chip.ident[:]))
                    heads(lambda h: pe.transpose(B3[d][1][:, h, :], x[:, 2 * HEADS + h, :], chip.ident[:])
                          ).then_inc(T(f"tok{d}"), 1)
                for d in range(NDIR):
                    pe.wait_ge(D.sem, D.at(n, f"gb{d}"))
                    pe.matmul(B[d][2][:, 0:HEADS], cum[d][:], g_[d], start=True, stop=True)
                    heads(lambda h: pe.matmul(B3[d][3][:, h, :], g_[d][:, h:h + 1].broadcast_to([P, P]), cum[d][:],
                                              start=True, stop=True)).then_inc(T(f"sum{d}"), 1)
                for d in range(NDIR):
                    x = qkv[d][s]
                    pe.wait_ge(D.sem, D.at(n, f"Gc{d}"))
                    heads(lambda h: pe.matmul(B3[d][2][:, h, :], x[:, HEADS + h, :], x[:, HEADS + h, :], start=True,
                                              stop=True))
                    pe.wait_ge(D.sem, D.at(n, f"kbe{d}"))
                    heads(lambda h: pe.matmul(B3[d][0][:, h, :], x[:, h, :], x[:, HEADS + h, :], start=True,
                                              stop=True)).then_inc(T(f"gram{d}"), 1)
                for d in range(NDIR):
                    pe.wait_ge(D.sem, D.at(n, f"A{d}"))
                    heads(lambda h: pe.transpose(B3[d][1][:, h, :], A_[d][:, h, :], chip.ident[:]))
                    pe.wait_ge(A.sem, A.at(n, f"eGr{d}"))
                    pe.wait_ge(D.sem, D.at(n, f"attn{d}"))
                    heads(lambda h: pe.transpose(B3[d][3][:, h, :], Dm[d][:, h, :], chip.ident[:])
                          ).then_inc(T(f"flip{d}"), 1)
                for lv in LEVELS:
                    for d in range(NDIR):
                        if lv == 1:
                            pe.wait_ge(A.sem, A.at(n, f"AT{d}"))
                        pe.wait_ge(D.sem, D.at(n, f"TT{lv - 1}_{d}"))
                        heads(lambda h: pe.matmul(B3[d][0][:, h, :], AT[d][:, h, :], T_[d][:, h, :], start=True,
                                                  stop=True)).then_inc(T(f"a{lv}_{d}"), 1)
                    for d in range(NDIR):
                        pe.wait_ge(D.sem, D.at(n, f"M{lv}_{d}"))
                        if lv < 6:
                            heads(lambda h: pe.matmul(B3[d][1][:, h, :], TT[d][:, h, :], M1[d][:, h, :], start=True,
                                                      stop=True))
                        heads(lambda h: pe.matmul(B3[d][2][:, h, :], M1[d][:, h, :], TT[d][:, h, :], start=True,
                                                  stop=True)).then_inc(T(f"b{lv}_{d}"), 1)
                for d in range(NDIR):
                    pe.wait_ge(D.sem, D.at(n, f"TT6_{d}"))
                    heads(lambda h: pe.matmul(B3[d][1][:, h, :], kbe[d][:, h, :], TT[d][:, h, :], start=True,
                                              stop=True)).then_inc(T(f"w{d}"), 1)
                for d in range(NDIR):
                    pe.wait_ge(A.sem, A.at(n, f"WT{d}"))
                    if ctx != 0:
                        pe.wait_ge(D.sem, D.at(n - 1, f"S{d}"))
                    for h in range(HEADS):
                        pe.matmul(B3[d][0][:, h, :], TT[d][:, h, :], vb[d][:, h, :], start=True, stop=False)
                        m = pe.matmul(B3[d][0][:, h, :], WT[d][:, h, :], S[d][:, h, :], start=False, stop=True)
                    m.then_inc(T(f"v{d}"), 1)
                for d in range(NDIR):
                    pe.wait_ge(A.sem, A.at(n, f"attnT{d}"))
                    pe.wait_ge(A.sem, A.at(n, f"vnew{d}"))
                    for h in range(HEADS):
                        pe.matmul(B3[d][2][:, h, :], S[d][:, h, :], qg[d][:, h, :], start=True, stop=False)
                        pe.matmul(B3[d][2][:, h, :], vnew[d][:, h, :], attnT[d][:, h, :], start=False, stop=True)
                    heads(lambda h: pe.matmul(B3[d][3][:, h, :], kd[d][:, h, :], vnew[d][:, h, :], start=True,
                                              stop=True)).then_inc(T(f"os{d}"), 1)
            turns(pe, body)

        @block.scalar
        def _(act):
            def body(n, s, ctx):
                for d in range(NDIR):
                    act.wait_ge(D.sem, D.at(n, f"Gc{d}"))
                    act.activation(eGc[d], Gc[d], ACT.Exp).then_inc(A(f"eGc{d}"), 1)
                for d in range(NDIR):
                    act.wait_ge(D.sem, D.at(n, f"gd{d}"))
                    act.activation(egd[d], gd[d], ACT.Exp).then_inc(A(f"egd{d}"), 1)
                for d in range(NDIR):
                    act.wait_ge(D.sem, D.at(n, f"E{d}"))
                    act.activation(Dm[d][:], Dm[d][:], ACT.Exp).then_inc(A(f"E{d}"), 1)
                for d in range(NDIR):
                    act.activation(qg[d][:], B3[d][3][:], ACT.Exp).then_inc(A(f"eGr{d}"), 1)
                for d in range(NDIR):
                    act.wait_ge(T.sem, T.at(n, f"flip{d}"))
                    act.activation(AT[d][:], B3[d][1][:], ACT.Copy).then_inc(A(f"AT{d}"), 1)
                for d in range(NDIR):
                    act.activation(attnT[d][:], B3[d][3][:], ACT.Copy).then_inc(A(f"attnT{d}"), 1)
                for d in range(NDIR):
                    act.wait_ge(T.sem, T.at(n, f"w{d}"))
                    act.activation(WT[d][:], B3[d][1][:], ACT.Copy, scale=-1.0).then_inc(A(f"WT{d}"), 1)
                for d in range(NDIR):
                    act.wait_ge(T.sem, T.at(n, f"v{d}"))
                    act.activation(vnew[d][:], B3[d][0][:], ACT.Copy).then_inc(A(f"vnew{d}"), 1)
            turns(act, body)

        @block.vector
        def _(dve):
            dve.wait_ge(zeroed, 1)
            per_token = lambda col: bcast(col, 2, P)
            per_pair = lambda m: bcast(m, 1, HEADS)

            def body(n, s, ctx):
                for d in range(NDIR):
                    t = tile(n, ctx, d)
                    row = lambda src: src[:, bass.ds(t, 1), d * HEADS:(d + 1) * HEADS].rearrange("p a h -> p (a h)")
                    dve.tensor_copy(beta[d], row(chip.beta_tok))
                    dve.tensor_copy(g_[d], row(chip.decay_tok)).then_inc(D(f"gb{d}"), 1)
                for d in range(NDIR):
                    dve.wait_ge(T.sem, T.at(n, f"sum{d}"))
                    dve.tensor_copy(Gc[d], B[d][2][:, 0:HEADS]).then_inc(D(f"Gc{d}"), 1)
                for d in range(NDIR):
                    dve.wait_ge(D.sem, D.at(n, f"Gc{d}"))
                    dve.tensor_tensor(gd[d], B3[d][3][:, :, last[d]], Gc[d], ALU.subtract).then_inc(D(f"gd{d}"), 1)
                for d in range(NDIR):
                    dve.scalar_tensor_tensor(out=Dm[d][:], in0=B3[d][3][:], scalar=-1.0, in1=per_token(Gc[d]),
                                             op0=ALU.mult, op1=ALU.add).then_inc(D(f"E0_{d}"), 1)
                for d in range(NDIR):
                    dve.wait_ge(D.sem, D.at(n, f"E0_{d}"))
                    dve.tensor_scalar(Dm[d][:], Dm[d][:], 0.0, None, ALU.min).then_inc(D(f"E{d}"), 1)
                for d in range(NDIR):
                    dve.wait_ge(A.sem, A.at(n, f"egd{d}"))
                    dve.tensor_tensor(beg[d], eGc[d], beta[d], ALU.mult)
                    dve.tensor_tensor(kd[d][:], B3[d][0][:], per_token(egd[d]), ALU.mult).then_inc(D(f"kd{d}"), 1)
                for d in range(NDIR):
                    dve.wait_ge(D.sem, D.at(n, f"kd{d}"))
                    dve.tensor_tensor(kbe[d][:], B3[d][0][:], per_token(beg[d]), ALU.mult).then_inc(D(f"kbe{d}"), 1)
                for d in range(NDIR):
                    dve.tensor_tensor(vb[d][:], B3[d][1][:], per_token(beta[d]), ALU.mult).then_inc(D(f"vb{d}"), 1)
                for d in range(NDIR):
                    dve.wait_ge(A.sem, A.at(n, f"eGr{d}"))
                    dve.tensor_copy(eGl[d], qg[d][:, :, last[d]]).then_inc(D(f"eGl{d}"), 1)
                for d in range(NDIR):
                    dve.wait_ge(D.sem, D.at(n, f"eGl{d}"))
                    dve.tensor_tensor(qg[d][:], qg[d][:], qkv[d][s][:, 0:HEADS, :], ALU.mult).then_inc(D(f"qg{d}"), 1)
                for d in range(NDIR):
                    dve.tensor_tensor(Dm[d][:], Dm[d][:], per_pair(seen[d][:]), ALU.mult).then_inc(D(f"Dm{d}"), 1)
                for d in range(NDIR):
                    dve.wait_ge(T.sem, T.at(n, f"gram{d}"))
                    dve.wait_ge(D.sem, D.at(n, f"Dm{d}"))
                    for h in range(HEADS):
                        m = dve.scalar_tensor_tensor(out=A_[d][:, h, :], in0=B3[d][2][:, h, :],
                                                     scalar=beta[d][:, h:h + 1], in1=Dm[d][:, h, :], op0=ALU.mult,
                                                     op1=ALU.mult)
                    m.then_inc(D(f"A{d}"), 1)
                for d in range(NDIR):
                    dve.wait_ge(D.sem, D.at(n, f"A{d}"))
                    dve.tensor_tensor(Dm[d][:], B3[d][0][:], Dm[d][:], ALU.mult).then_inc(D(f"attn{d}"), 1)
                for d in range(NDIR):
                    dve.scalar_tensor_tensor(out=T_[d][:], in0=A_[d][:], scalar=-1.0,
                                             in1=per_pair(chip.off[:, d, 0, :]), op0=ALU.mult, op1=ALU.mult
                                             ).then_inc(D(f"Ti{d}"), 1)
                for d in range(NDIR):
                    dve.wait_ge(D.sem, D.at(n, f"Ti{d}"))
                    dve.tensor_tensor(T_[d][:], T_[d][:], per_pair(chip.ident[:]), ALU.add).then_inc(D(f"T0_{d}"), 1)
                for d in range(NDIR):
                    dve.wait_ge(A.sem, A.at(n, f"AT{d}"))
                    dve.scalar_tensor_tensor(out=TT[d][:], in0=AT[d][:], scalar=-1.0,
                                             in1=per_pair(chip.off[:, 1 - d, 0, :]), op0=ALU.mult, op1=ALU.mult
                                             ).then_inc(D(f"TTi{d}"), 1)
                for d in range(NDIR):
                    dve.wait_ge(D.sem, D.at(n, f"TTi{d}"))
                    dve.tensor_tensor(TT[d][:], TT[d][:], per_pair(chip.ident[:]), ALU.add).then_inc(D(f"TT0_{d}"), 1)
                for lv in LEVELS:
                    for d in range(NDIR):
                        dve.wait_ge(T.sem, T.at(n, f"a{lv}_{d}"))
                        dve.tensor_tensor(M1[d][:], B3[d][0][:], per_pair(chip.off[:, d, lv, :]), ALU.mult
                                          ).then_inc(D(f"M{lv}_{d}"), 1)
                    for d in range(NDIR):
                        dve.wait_ge(T.sem, T.at(n, f"b{lv}_{d}"))
                        if lv < 6:
                            dve.tensor_tensor(T_[d][:], T_[d][:], B3[d][1][:], ALU.subtract
                                              ).then_inc(D(f"T{lv}_{d}"), 1)
                        else:
                            dve.memset(none[:, d:d + 1], 0.0).then_inc(D(f"T{lv}_{d}"), 1)
                    for d in range(NDIR):
                        dve.tensor_tensor(TT[d][:], TT[d][:], B3[d][2][:], ALU.subtract
                                          ).then_inc(D(f"TT{lv}_{d}"), 1)
                for d in range(NDIR):
                    dve.wait_ge(T.sem, T.at(n, f"os{d}"))
                    for h in range(HEADS):
                        m = dve.scalar_tensor_tensor(out=S[d][:, h, :], in0=S[d][:, h, :], scalar=eGl[d][:, h:h + 1],
                                                     in1=B3[d][3][:, h, :], op0=ALU.mult, op1=ALU.add)
                    m.then_inc(D(f"S{d}"), 1)
                for d in range(NDIR):
                    if ctx is not None:
                        dve.memset(none[:, d:d + 1], 0.0).then_inc(D(f"o{d}"), 1)
                        continue
                    t = o[:, :, bass.ds((tile(n, ctx, d) - CTX // P) * P, P)]
                    dve.tensor_tensor(t, t, B3[d][2][:], ALU.add).then_inc(D(f"o{d}"), 1)
            turns(dve, body)


def phase_gla(chip, sq_, sv, sk, sg, so_b):
    nc, bank = chip.nc, chip.bank
    HALF = (64, 32, 16)
    with ExitStack() as st:
        sb = lambda n, s: st.enter_context(nc.sbuf_tensor("gla_" + n, s, F32))
        sem = lambda n: st.enter_context(nc.semaphore("gla_" + n))
        mat = lambda n: [sb(f"{n}{d}", [P, HEADS, P]) for d in range(NDIR)]
        qvkg = [[sb(f"qvkg{d}{s}", [P, 4, HEADS, P]) for s in range(2)] for d in range(NDIR)]
        qg, kdT, dq, dk, v, kd, attnT, S = (mat(n) for n in ("qg", "kdT", "dq", "dk", "v", "kd", "attnT", "S"))
        X = [mat(f"X{L}_") for L in HALF]
        eGl = [sb(f"eGl{d}", [P, HEADS]) for d in range(NDIR)]
        o = sb("o", [P, HEADS, SEQ])
        none = sb("none", [P, NDIR])
        loaded = [sem(f"loaded{s}") for s in range(2)]
        zeroed, o_stored = sem("zeroed"), sem("o_stored")
        both = lambda names: " ".join(f"{x}{d}" for x in names.split() for d in range(NDIR))
        D = Stages(sem("dve_stage"), both("ekd ex0_ ex1_ ex2_ edq") + " "
                   + both("qg kd x0_ x1_ x2_ dq dk diag lv0_ lv1_ lv2_ S o"))
        A = Stages(sem("act_stage"), both("qg kd x0_ x1_ x2_ dk dq v kdtok"))
        T = Stages(sem("pe_stage"), both("v kd lv diag os"))
        block = st.enter_context(nc.Block())
        last = (P - 1, 0)
        B = [[bank[:, 4 * d + n, :] for n in range(4)] for d in range(NDIR)]
        B3 = [[b.rearrange("p (h c) -> p h c", h=HEADS) for b in bs] for bs in B]

        def turns(eng, body):
            for n in range(2):
                body(n, n, n)
            with eng.Fori(1, NT // 2) as i:
                for s in range(2):
                    body(2 * i + s, s, None)

        def tile(n, ctx, d):
            if d == 0:
                return n
            return 1 - n if ctx is not None else NT + 1 - n

        def halves(m, L):
            return m.rearrange("p h c -> p (h c)").rearrange("p (b e l) -> p b e l", e=2, l=L)

        def where(d, n):
            L = HALF[n]
            b = B[d][3][:, 256 * n:256 * n + 256] if n < 2 else B[d][0][:, 0:256]
            return b.rearrange("p (h b l) -> p h b l", h=HEADS, l=L)

        @block.sync
        def _(sp):
            def body(n, s, ctx):
                if ctx is None:
                    sp.wait_ge(D.sem, D.at(n - 2, "dk1"))
                    sp.wait_ge(T.sem, T.at(n - 2, "v1"))
                for d in range(NDIR):
                    hs = slice(d * HEADS, (d + 1) * HEADS)
                    for m, src in enumerate((sq_, sv, sk[hs], sg[hs])):
                        sp.dma_start(qvkg[d][s][:, m], src[:, :, bass.ds(tile(n, ctx, d) * P, P)].rearrange(
                            "h p t -> p h t")).then_inc(loaded[s], 16)
            turns(sp, body)
            sp.wait_ge(D.sem, D.at(NT - 1, "o1"))
            sp.dma_start(so_b.rearrange("h p t -> p h t"), o[:]).then_inc(o_stored, 16)
            sp.wait_ge(o_stored, 16)

        @block.gpsimd
        def _(pool):
            nc.gpsimd.memset(o[:], 0.0)
            for d in range(NDIR):
                z = nc.gpsimd.memset(S[d][:], 0.0)
            z.then_inc(zeroed, 1)

        def land(eng, n, s, ctx):
            eng.wait_ge(loaded[s], (n // 2 if ctx is not None else (n - s) // 2) * 128 + 128)

        @block.tensor
        def _(pe):
            pe.wait_ge(zeroed, 1)

            def body(n, s, ctx):
                land(pe, n, s, ctx)
                for d in range(NDIR):
                    if ctx != 0:
                        pe.wait_ge(D.sem, D.at(n - 1, f"o{d}"))
                    for h in range(HEADS):
                        m = pe.transpose(B3[d][0][:, h, :], qvkg[d][s][:, 1, h, :], chip.ident[:])
                    m.then_inc(T(f"v{d}"), 1)
                for d in range(NDIR):
                    pe.wait_ge(D.sem, D.at(n, f"kd{d}"))
                    for h in range(HEADS):
                        m = pe.transpose(B3[d][1][:, h, :], kdT[d][:, h, :], chip.ident[:])
                    m.then_inc(T(f"kd{d}"), 1)
                for d in range(NDIR):
                    pe.wait_ge(A.sem, A.at(n, f"v{d}"))
                    for lv, L in enumerate(HALF):
                        pe.wait_ge(D.sem, D.at(n, f"x{lv}_{d}"))
                        xs = X[lv][d][:].rearrange("p h (b e l) -> p h b e l", e=2, l=L)
                        for h in range(HEADS):
                            m = pe.matmul(where(d, lv)[:, h], X[lv][d][:, h, :], xs[:, h, :, 1 - d, :], start=True,
                                          stop=True)
                    m.then_inc(T(f"lv{d}"), 1)
                for d in range(NDIR):
                    pe.wait_ge(D.sem, D.at(n, f"dk{d}"))
                    for h in range(HEADS):
                        m = pe.matmul(B3[d][2][:, h, :], dk[d][:, h, :], dq[d][:, h, :], start=True, stop=True)
                    m.then_inc(T(f"diag{d}"), 1)
                for d in range(NDIR):
                    pe.wait_ge(A.sem, A.at(n, f"kdtok{d}"))
                    pe.wait_ge(D.sem, D.at(n, f"lv2_{d}"))
                    for h in range(HEADS):
                        pe.matmul(B3[d][1][:, h, :], S[d][:, h, :], qg[d][:, h, :], start=True, stop=False)
                        pe.matmul(B3[d][1][:, h, :], v[d][:, h, :], attnT[d][:, h, :], start=False, stop=True)
                    for h in range(HEADS):
                        m = pe.matmul(B3[d][2][:, h, :], kd[d][:, h, :], v[d][:, h, :], start=True, stop=True)
                    m.then_inc(T(f"os{d}"), 1)
            turns(pe, body)

        @block.scalar
        def _(act):
            def body(n, s, ctx):
                land(act, n, s, ctx)
                for d in range(NDIR):
                    if ctx != 0:
                        act.wait_ge(T.sem, T.at(n - 1, f"os{d}"))
                    act.activation(qg[d][:], qvkg[d][s][:, 3], ACT.Exp).then_inc(A(f"qg{d}"), 1)
                for d in range(NDIR):
                    act.wait_ge(D.sem, D.at(n, f"ekd{d}"))
                    act.activation(kdT[d][:], kdT[d][:], ACT.Exp).then_inc(A(f"kd{d}"), 1)
                for lv in range(3):
                    for d in range(NDIR):
                        act.wait_ge(D.sem, D.at(n, f"ex{lv}_{d}"))
                        act.activation(X[lv][d][:], X[lv][d][:], ACT.Exp).then_inc(A(f"x{lv}_{d}"), 1)
                for d in range(NDIR):
                    act.wait_ge(D.sem, D.at(n, f"edq{d}"))
                    act.activation(dk[d][:], dq[d][:], ACT.Exp, scale=-1.0).then_inc(A(f"dk{d}"), 1)
                for d in range(NDIR):
                    act.wait_ge(A.sem, A.at(n, f"dk{d}"))
                    act.activation(dq[d][:], dq[d][:], ACT.Exp).then_inc(A(f"dq{d}"), 1)
                for d in range(NDIR):
                    act.wait_ge(T.sem, T.at(n, f"v{d}"))
                    act.activation(v[d][:], B3[d][0][:], ACT.Copy).then_inc(A(f"v{d}"), 1)
                for d in range(NDIR):
                    act.wait_ge(T.sem, T.at(n, f"kd{d}"))
                    act.activation(kd[d][:], B3[d][1][:], ACT.Copy).then_inc(A(f"kdtok{d}"), 1)
            turns(act, body)

        @block.vector
        def _(dve):
            dve.wait_ge(zeroed, 1)

            def body(n, s, ctx):
                land(dve, n, s, ctx)
                for d in range(NDIR):
                    G = qvkg[d][s][:, 3]
                    dve.tensor_tensor(kdT[d][:], G[:, :, last[d]:last[d] + 1].broadcast_to([P, HEADS, P]), G,
                                      ALU.subtract).then_inc(D(f"ekd{d}"), 1)
                for lv, L in enumerate(HALF):
                    for d in range(NDIR):
                        g, x = halves(qvkg[d][s][:, 3], L), halves(X[lv][d][:], L)
                        nb = HEADS * P // (2 * L)
                        ref = (g[:, :, 0, L - 1:L] if d == 0 else g[:, :, 1, 0:1]).broadcast_to([P, nb, L])
                        ask, key = 1 - d, d
                        dve.tensor_tensor(x[:, :, ask, :], g[:, :, ask, :], ref, ALU.subtract)
                        dve.tensor_tensor(x[:, :, key, :], ref, g[:, :, key, :], ALU.subtract
                                          ).then_inc(D(f"ex{lv}_{d}"), 1)
                for d in range(NDIR):
                    g = qvkg[d][s][:, 3].rearrange("p h c -> p (h c)").rearrange("p (b l) -> p b l", l=16)
                    x = dq[d][:].rearrange("p h c -> p (h c)").rearrange("p (b l) -> p b l", l=16)
                    e = 15 * d
                    dve.tensor_tensor(x, g, g[:, :, e:e + 1].broadcast_to([P, HEADS * 8, 16]), ALU.subtract
                                      ).then_inc(D(f"edq{d}"), 1)
                for d in range(NDIR):
                    dve.wait_ge(A.sem, A.at(n, f"qg{d}"))
                    if ctx != 0:
                        dve.wait_ge(D.sem, D.at(n - 1, f"S{d}"))
                    dve.tensor_copy(eGl[d][:], qg[d][:, :, last[d]]).then_inc(D(f"qg{d}"), 1)
                for d in range(NDIR):
                    dve.wait_ge(A.sem, A.at(n, f"kd{d}"))
                    dve.wait_ge(D.sem, D.at(n, f"qg{d}"))
                    dve.tensor_tensor(qg[d][:], qg[d][:], qvkg[d][s][:, 0], ALU.mult)
                    dve.tensor_tensor(kdT[d][:], kdT[d][:], qvkg[d][s][:, 2], ALU.mult).then_inc(D(f"kd{d}"), 1)
                for lv, L in enumerate(HALF):
                    for d in range(NDIR):
                        dve.wait_ge(A.sem, A.at(n, f"x{lv}_{d}"))
                        x = halves(X[lv][d][:], L)
                        dve.tensor_tensor(x[:, :, 1 - d, :], x[:, :, 1 - d, :],
                                          halves(qvkg[d][s][:, 0], L)[:, :, 1 - d, :], ALU.mult)
                        dve.tensor_tensor(x[:, :, d, :], x[:, :, d, :], halves(qvkg[d][s][:, 2], L)[:, :, d, :],
                                          ALU.mult).then_inc(D(f"x{lv}_{d}"), 1)
                for d in range(NDIR):
                    dve.wait_ge(A.sem, A.at(n, f"dq{d}"))
                    dve.tensor_tensor(dq[d][:], dq[d][:], qvkg[d][s][:, 0], ALU.mult).then_inc(D(f"dq{d}"), 1)
                for d in range(NDIR):
                    dve.tensor_tensor(dk[d][:], dk[d][:], qvkg[d][s][:, 2], ALU.mult).then_inc(D(f"dk{d}"), 1)
                for d in range(NDIR):
                    dve.wait_ge(T.sem, T.at(n, f"diag{d}"))
                    dve.tensor_tensor(attnT[d][:], B3[d][2][:], bcast(chip.diag16[:, d, :], 1, HEADS), ALU.mult
                                      ).then_inc(D(f"diag{d}"), 1)
                for lv, L in enumerate(HALF):
                    for d in range(NDIR):
                        ask = 1 - d
                        dve.wait_ge(D.sem, D.at(n, f"lv{lv - 1}_{d}" if lv else f"diag{d}"))
                        dve.nop(nofuse=True)
                        mask = chip.off[:, 1 - d, 6 - lv, :].bitcast(U32).rearrange("p (b e l) -> p b e l", e=2, l=L)
                        out = attnT[d][:].rearrange("p h (b e l) -> p h b e l", e=2, l=L)[:, :, :, ask, :]
                        dve.copy_predicated(out, bcast(mask[:, :, ask, :], 1, HEADS), where(d, lv)
                                            ).then_inc(D(f"lv{lv}_{d}"), 1)
                for d in range(NDIR):
                    dve.wait_ge(T.sem, T.at(n, f"os{d}"))
                    for h in range(HEADS):
                        m = dve.scalar_tensor_tensor(out=S[d][:, h, :], in0=S[d][:, h, :], scalar=eGl[d][:, h:h + 1],
                                                     in1=B3[d][2][:, h, :], op0=ALU.mult, op1=ALU.add)
                    m.then_inc(D(f"S{d}"), 1)
                for d in range(NDIR):
                    if ctx is not None:
                        dve.memset(none[:, d:d + 1], 0.0).then_inc(D(f"o{d}"), 1)
                        continue
                    t = o[:, :, bass.ds((tile(n, ctx, d) - CTX // P) * P, P)]
                    dve.tensor_tensor(t, t, B3[d][1][:], ALU.add).then_inc(D(f"o{d}"), 1)
            turns(dve, body)


def phase_branch_gates(chip, uT, w_in, so_a, so_b, a_norm_g, b_norm_g, yT):
    nc, bank = chip.nc, chip.bank
    NF = 2 * HEADS
    NB = LATENT_BLOCKS
    with ExitStack() as st:
        sb = lambda n, s: st.enter_context(nc.sbuf_tensor("gates_" + n, s, F32))
        sem = lambda n: st.enter_context(nc.semaphore("gates_" + n))
        W = sb("W", [P, 2, KT, P])
        o = sb("o", [P, 2, SEQ])
        sq = sb("sq", [P, SEQ])
        inv = sb("inv", [P, SEQ])
        silu = sb("silu", [P, SEQ])
        gain = sb("gain", [P, 2])
        w_loaded = [sem(f"w_loaded{s}") for s in range(2)]
        o_loaded = [sem(f"o_loaded{s}") for s in range(2)]
        gain_loaded = sem("gain_loaded")
        T = Stages(sem("pe_stage"), " ".join([f"proj{b}" for b in range(NB)] + [f"sum{b}" for b in range(NB)]))
        A = Stages(sem("act_stage"), "sq " + " ".join(f"silu{b}" for b in range(NB)) + " rinv")
        D = Stages(sem("dve_stage"), " ".join(f"ss{b}" for b in range(NB)) + " inv o y")
        block = st.enter_context(nc.Block())

        def turns(eng, body):
            body(0, 0, 0)
            body(0, 1, 0)
            for br in range(2):
                with eng.Fori(max(1, br * HEADS // 2), (br + 1) * HEADS // 2) as i:
                    for s in range(2):
                        body(i, s, br)

        def first(i):
            return isinstance(i, int) and i == 0

        @block.sync
        def _(sp):
            for br, g in enumerate((a_norm_g, b_norm_g)):
                sp.dma_start(gain[:, br:br + 1], g[0].rearrange("(p a) -> p a", a=1)).then_inc(gain_loaded, 16)

            def body(i, s, br):
                f = 2 * i + s
                if not first(i):
                    sp.wait_ge(T.sem, T.at(f - 2, f"proj{NB - 1}"))
                base = (C_AGATE, C_BGATE - HD)[br]
                sp.dma_start(W[:, s], w_in[:, bass.ds(f * P + base, P)].rearrange("(k p) n -> p k n", p=P)
                             ).then_inc(w_loaded[s], 16)
                if not first(i):
                    sp.wait_ge(D.sem, D.at(f - 2, "y"))
                sp.dma_start(o[:, s, :], (so_a, so_b)[br][bass.ds(f - br * HEADS, 1)].rearrange("a p t -> (a p) t")
                             ).then_inc(o_loaded[s], 16)
            turns(sp, body)

        @block.tensor
        def _(pe):
            def body(i, s, br):
                f = 2 * i + s
                pe.wait_ge(w_loaded[s], i * 16 + 16)
                for b in range(NB):
                    if not (first(i) and s == 0):
                        pe.wait_ge(A.sem, A.at(f - 1, f"silu{b}"))
                    for k in range(KT):
                        mm = pe.matmul(bank[:, b, :], W[:, s, k, :], uT[:, k, CTX + b * BANK:CTX + (b + 1) * BANK],
                                       start=(k == 0), stop=(k == KT - 1))
                    mm.then_inc(T(f"proj{b}"), 1)
                pe.wait_ge(A.sem, A.at(f, "sq"))
                for b in range(NB):
                    if not (first(i) and s == 0):
                        pe.wait_ge(D.sem, D.at(f - 1, f"ss{b}"))
                    pe.matmul(bank[:, 4 + b, :], chip.ones[:], sq[:, b * BANK:(b + 1) * BANK], start=True, stop=True
                              ).then_inc(T(f"sum{b}"), 1)
            turns(pe, body)

        @block.scalar
        def _(act):
            def body(i, s, br):
                f = 2 * i + s
                act.wait_ge(o_loaded[s], i * 16 + 16)
                if not (first(i) and s == 0):
                    act.wait_ge(T.sem, T.at(f - 1, f"sum{NB - 1}"))
                act.activation(sq[:], o[:, s, :], ACT.Square).then_inc(A("sq"), 1)
                for b in range(NB):
                    act.wait_ge(T.sem, T.at(f, f"proj{b}"))
                    if not (first(i) and s == 0):
                        act.wait_ge(D.sem, D.at(f - 1, "y"))
                    act.activation(silu[:, b * BANK:(b + 1) * BANK], bank[:, b, :], ACT.Silu).then_inc(A(f"silu{b}"), 1)
                act.wait_ge(D.sem, D.at(f, "inv"))
                act.activation(inv[:], inv[:], ACT.Sqrt).then_inc(A("rinv"), 1)
            turns(act, body)

        @block.vector
        def _(dve):
            dve.wait_ge(gain_loaded, 32)

            def body(i, s, br):
                f = 2 * i + s
                if not (first(i) and s == 0):
                    dve.wait_ge(D.sem, D.at(f - 1, "o"))
                for b in range(NB):
                    dve.wait_ge(T.sem, T.at(f, f"sum{b}"))
                    dve.tensor_scalar(inv[:, b * BANK:(b + 1) * BANK], bank[:, 4 + b, :], 1.0 / P, EPS1, ALU.mult,
                                      ALU.add).then_inc(D(f"ss{b}"), 1)
                dve.wait_ge(D.sem, D.at(f, f"ss{NB - 1}"))
                dve.reciprocal(inv[:], inv[:]).then_inc(D("inv"), 1)
                dve.wait_ge(A.sem, A.at(f, "rinv"))
                dve.scalar_tensor_tensor(out=o[:, s, :], in0=o[:, s, :], scalar=gain[:, br:br + 1], in1=inv[:],
                                         op0=ALU.mult, op1=ALU.mult).then_inc(D("o"), 1)
                dve.wait_ge(D.sem, D.at(f, "o"))
                grid = lambda v: v.rearrange("p (r w) -> p r w", w=GRID_W)
                by_row = grid(o[:, s, :]) if br == 0 else o[:, s, :].rearrange("p (w r) -> p r w", r=ROWS)
                dve.tensor_tensor(grid(yT[:, bass.ds(f, 1), :].rearrange("p a t -> p (a t)")), by_row, grid(silu[:]),
                                  ALU.mult).then_inc(D("y"), 1)
            turns(dve, body)


def phase_merge(chip, uT, w_in, yT, w_a_out, w_b_out, smT):
    nc, bank = chip.nc, chip.bank
    NB = LATENT_BLOCKS
    with ExitStack() as st:
        sb = lambda n, s: st.enter_context(nc.sbuf_tensor("merge_" + n, s, F32))
        sem = lambda n: st.enter_context(nc.semaphore("merge_" + n))
        WG = sb("WG", [P, 2, 2, KT, P])
        WY = sb("WY", [P, 2, 2, HEADS, P])
        sig = sb("sig", [P, 2, 2, BANK])
        row = sb("row", [P, 2, SEQ])
        loaded = [sem(f"loaded{s}") for s in range(2)]
        stored = [sem(f"stored{s}") for s in range(2)]
        T = Stages(sem("pe_stage"), " ".join(f"gate{b} y{b}" for b in range(NB)))
        A = Stages(sem("act_stage"), " ".join(f"sig{b}" for b in range(NB)))
        D = Stages(sem("dve_stage"), " ".join(f"a{b} b{b} sum{b}" for b in range(NB)))
        block = st.enter_context(nc.Block())

        def turns(eng, body):
            body(0, 0)
            body(0, 1)
            with eng.Fori(1, KT // 2) as i:
                for s in range(2):
                    body(i, s)

        first = lambda i: isinstance(i, int) and i == 0

        @block.sync
        def _(sp):
            def body(i, s):
                j = 2 * i + s
                if not first(i):
                    sp.wait_ge(T.sem, T.at(j - 2, f"y{NB - 1}"))
                for br in range(2):
                    sp.dma_start(WG[:, s, br], w_in[:, bass.ds(j * P + C_MERGE + br * DM, P)].rearrange(
                        "(k p) n -> p k n", p=P)).then_inc(loaded[s], 16)
                    sp.dma_start(WY[:, s, br], (w_a_out, w_b_out)[br][:, bass.ds(j * P, P)].rearrange(
                        "(k p) n -> p k n", p=P)).then_inc(loaded[s], 16)
            turns(sp, body)

        @block.gpsimd
        def _(pool):
            def body(i, s):
                j = 2 * i + s
                pool.wait_ge(D.sem, D.at(j, f"sum{NB - 1}"))
                pool.dma_start(smT[bass.ds(j, 1)].rearrange("a p t -> (a p) t"), row[:, s, :]).then_inc(stored[s], 16)
            turns(pool, body)
            for s in range(2):
                pool.wait_ge(stored[s], 16 * KT // 2)

        @block.tensor
        def _(pe):
            def body(i, s):
                j = 2 * i + s
                pe.wait_ge(loaded[s], i * 64 + 64)
                for b in range(NB):
                    q = 4 * (b % 2)
                    if b >= 2:
                        pe.wait_ge(D.sem, D.at(j, f"sum{b - 2}"))
                    elif not (first(i) and s == 0):
                        pe.wait_ge(D.sem, D.at(j - 1, f"sum{b + 2}"))
                    t = slice(CTX + b * BANK, CTX + (b + 1) * BANK)
                    for br in range(2):
                        for k in range(KT):
                            mm = pe.matmul(bank[:, q + br, :], WG[:, s, br, k, :], uT[:, k, t], start=(k == 0),
                                           stop=(k == KT - 1))
                    mm.then_inc(T(f"gate{b}"), 1)
                    for br in range(2):
                        for k in range(HEADS):
                            mm = pe.matmul(bank[:, q + 2 + br, :], WY[:, s, br, k, :],
                                           yT[:, br * HEADS + k, b * BANK:(b + 1) * BANK], start=(k == 0),
                                           stop=(k == HEADS - 1))
                    mm.then_inc(T(f"y{b}"), 1)
            turns(pe, body)

        @block.scalar
        def _(act):
            def body(i, s):
                j = 2 * i + s
                for b in range(NB):
                    act.wait_ge(T.sem, T.at(j, f"gate{b}"))
                    for br in range(2):
                        m = act.activation(sig[:, b % 2, br, :], bank[:, 4 * (b % 2) + br, :], ACT.Sigmoid)
                    m.then_inc(A(f"sig{b}"), 1)
            turns(act, body)

        @block.vector
        def _(dve):
            def body(i, s):
                j = 2 * i + s
                if not first(i):
                    dve.wait_ge(stored[s], i * 16)
                for b in range(NB):
                    q, t = b % 2, slice(b * BANK, (b + 1) * BANK)
                    dve.wait_ge(A.sem, A.at(j, f"sig{b}"))
                    dve.wait_ge(T.sem, T.at(j, f"y{b}"))
                    dve.tensor_tensor(row[:, s, t], bank[:, 4 * q + 2, :], sig[:, q, 0, :], ALU.mult
                                      ).then_inc(D(f"a{b}"), 1)
                    dve.tensor_tensor(sig[:, q, 1, :], bank[:, 4 * q + 3, :], sig[:, q, 1, :], ALU.mult
                                      ).then_inc(D(f"b{b}"), 1)
                    dve.wait_ge(D.sem, D.at(j, f"b{b}"))
                    dve.tensor_tensor(row[:, s, t], row[:, s, t], sig[:, q, 1, :], ALU.add).then_inc(D(f"sum{b}"), 1)
            turns(dve, body)


def layer_norm_steps(dve, D, A, t, x, stats, mv, inv, rstd, eps, g_row):
    width = x.shape[-1]
    for n in range(width // BANK):
        m = dve.bn_stats(stats[:, 6 * n:6 * n + 6], x[:, n * BANK:(n + 1) * BANK])
    m.then_inc(D("stats"), 1)
    dve.wait_ge(D.sem, D.at(t, "stats"))
    dve.nop(nofuse=True)
    dve.bn_aggr(mv, stats[:, 0:6 * (width // BANK)]).then_inc(D("mv"), 1)
    dve.wait_ge(D.sem, D.at(t, "mv"))
    dve.tensor_scalar(mv[:, 1:2], mv[:, 1:2], eps, None, ALU.add).then_inc(D("var"), 1)
    dve.wait_ge(D.sem, D.at(t, "var"))
    dve.reciprocal(inv, mv[:, 1:2]).then_inc(D("inv"), 1)
    dve.wait_ge(A.sem, A.at(t, "rstd"))
    dve.tensor_scalar(x, x, mv[:, 0:1], rstd, ALU.subtract, ALU.mult).then_inc(D("n"), 1)
    dve.wait_ge(D.sem, D.at(t, "n"))
    dve.tensor_tensor(x, x, g_row, ALU.mult).then_inc(D("scaled"), 1)
    dve.wait_ge(D.sem, D.at(t, "scaled"))


def phase_residual(chip, x, smT, w_out, ln_g, ln_b, sh, hT):
    nc, bank = chip.nc, chip.bank
    NTL = SEQ // P
    with ExitStack() as st:
        sb = lambda n, s: st.enter_context(nc.sbuf_tensor("residual_" + n, s, F32))
        sem = lambda n: st.enter_context(nc.semaphore("residual_" + n))
        W = sb("W", [P, KT, DM])
        mT = sb("mT", [P, 2, KT, P])
        xs = sb("xs", [P, 2, DM])
        r = sb("r", [P, 2, DM])
        h = sb("h", [P, 2, DM])
        rows = sb("rows", [P, 2, DM])
        stats, mv, inv, rstd = (sb(n, [P, w]) for n, w in (("stats", 12), ("mv", 2), ("inv", 1), ("rstd", 1)))
        once = sem("once")
        loaded = [sem(f"loaded{s}") for s in range(2)]
        stored = [sem(f"stored{s}") for s in range(2)]
        T = Stages(sem("pe_stage"), "mm turned")
        A = Stages(sem("act_stage"), "rstd hT")
        D = Stages(sem("dve_stage"), "gated sum stats mv var inv n scaled h")
        block = st.enter_context(nc.Block())

        def turns(eng, body):
            body(0, 0)
            body(0, 1)
            with eng.Fori(1, NTL // 2) as i:
                for s in range(2):
                    body(i, s)

        first = lambda i: isinstance(i, int) and i == 0

        @block.sync
        def _(sp):
            sp.dma_start(W[:], w_out.rearrange("(k p) n -> p k n", p=P)).then_inc(once, 16)
            for n, src in enumerate((ln_g, ln_b)):
                sp.dma_start(rows[:, n, :], src.broadcast_to([P, DM])).then_inc(once, 16)

            def body(i, s):
                t = 2 * i + s
                if not first(i):
                    sp.wait_ge(T.sem, T.at(t - 2, "mm"))
                    sp.wait_ge(D.sem, D.at(t - 2, "sum"))
                sp.dma_start(mT[:, s], smT[:, :, bass.ds(t * P, P)].rearrange("k p t -> p k t")).then_inc(loaded[s], 16)
                sp.dma_start(xs[:, s], x[bass.ds(t * P, P), :]).then_inc(loaded[s], 16)
            turns(sp, body)

        @block.gpsimd
        def _(pool):
            def body(i, s):
                t = 2 * i + s
                pool.wait_ge(D.sem, D.at(t, "h"))
                pool.dma_start(sh[bass.ds(t * P, P), :], h[:, s, :]).then_inc(stored[s], 16)
            turns(pool, body)
            for s in range(2):
                pool.wait_ge(stored[s], 16 * NTL // 2)

        @block.tensor
        def _(pe):
            pe.wait_ge(once, 48)

            def mm(i, s):
                t = 2 * i + s
                pe.wait_ge(loaded[s], i * 32 + 32)
                if not first(i):
                    pe.wait_ge(D.sem, D.at(t - 2, "gated"))
                for n in range(2):
                    for k in range(KT):
                        m = pe.matmul(bank[:, 2 * s + n, :], mT[:, s, k, :], W[:, k, n * BANK:(n + 1) * BANK],
                                      start=(k == 0), stop=(k == KT - 1))
                m.then_inc(T("mm"), 1)

            def turn(i, s):
                t = 2 * i + s
                pe.wait_ge(D.sem, D.at(t, "h"))
                if not first(i):
                    pe.wait_ge(A.sem, A.at(t - 2, "hT"))
                for k in range(KT):
                    m = pe.transpose(bank[:, 4 + 2 * s + k // 4, (k % 4) * P:(k % 4 + 1) * P],
                                     h[:, s, k * P:(k + 1) * P], chip.ident[:])
                m.then_inc(T("turned"), 1)

            def body(i, s):
                mm(i, s)
                turn(i, s)
            turns(pe, body)

        @block.scalar
        def _(act):
            def body(i, s):
                t = 2 * i + s
                act.wait_ge(D.sem, D.at(t, "inv"))
                act.activation(rstd[:], inv[:], ACT.Sqrt).then_inc(A("rstd"), 1)
                act.wait_ge(T.sem, T.at(t, "turned"))
                for n in range(2):
                    m = act.activation(hT[:, 4 * n:4 * n + 4, bass.ds(t * P, P)],
                                       bank[:, 4 + 2 * s + n, :].rearrange("p (k t) -> p k t", k=4), ACT.Copy)
                m.then_inc(A("hT"), 1)
            turns(act, body)

        @block.vector
        def _(dve):
            dve.wait_ge(once, 48)

            def body(i, s):
                t = 2 * i + s
                dve.wait_ge(T.sem, T.at(t, "mm"))
                for n in range(2):
                    c = slice(n * BANK, (n + 1) * BANK)
                    m = dve.tensor_tensor(r[:, s, c], bank[:, 2 * s + n, :], chip.gate_rows[:, c], ALU.mult)
                m.then_inc(D("gated"), 1)
                dve.wait_ge(D.sem, D.at(t, "gated"))
                dve.scalar_tensor_tensor(out=r[:, s, :], in0=xs[:, s, :], scalar=ALPHA, in1=r[:, s, :], op0=ALU.mult,
                                         op1=ALU.add).then_inc(D("sum"), 1)
                dve.wait_ge(D.sem, D.at(t, "sum"))
                layer_norm_steps(dve, D, A, t, r[:, s, :], stats[:], mv[:], inv[:], rstd[:], EPS1, rows[:, 0, :])
                if not first(i):
                    dve.wait_ge(stored[s], i * 16)
                    dve.wait_ge(T.sem, T.at(t - 2, "turned"))
                dve.tensor_tensor(h[:, s, :], r[:, s, :], rows[:, 1, :], ALU.add).then_inc(D("h"), 1)
            turns(dve, body)


EPS2 = 1e-5
Q_LORA, KV_LORA, ROPE, NOPE = 256, 128, 32, 64
QK = NOPE + ROPE
AH = 8
DV = 64
WIDTH = AH * DV
C_KV, C_KR, C_ZA = Q_LORA, Q_LORA + KV_LORA, Q_LORA + KV_LORA + ROPE
C_U, C_V, C_ZB = C_ZA + WIDTH, C_ZA + 2 * WIDTH, C_ZA + 3 * WIDTH
QT = SEQ // P
NEG = -1e30
TWO_PI = 6.283185307179586


def phase_rotation(chip, positions, inv_freq, rot):
    nc, bank = chip.nc, chip.bank
    R = slice(NOPE, QK)
    HALF = ROPE // 2
    with ExitStack() as st:
        sb = lambda n, s, dt=F32: st.enter_context(nc.sbuf_tensor("rotation_" + n, s, dt))
        sem = lambda n: st.enter_context(nc.semaphore("rotation_" + n))
        consts = sb("consts", [1, 2, QK])
        cols = sb("cols", [QK, 2])
        pos = sb("pos", [QK, SEQ], I32)
        ang, turns_, tmp = (sb(n, [QK, SEQ]) for n in ("ang", "turns", "tmp"))
        pos_loaded, consts_ready, cols_turned = sem("pos_loaded"), sem("consts_ready"), sem("cols_turned")
        table, table_act = sem("table"), sem("table_act")
        block = st.enter_context(nc.Block())

        @block.sync
        def _(sp):
            sp.dma_start(pos[R, :], positions.broadcast_to([ROPE, SEQ])).then_inc(pos_loaded, 16)
            sp.dma_start(consts[:, 0, NOPE:NOPE + HALF], inv_freq).then_inc(pos_loaded, 16)
            sp.dma_start(consts[:, 0, NOPE + HALF:QK], inv_freq).then_inc(pos_loaded, 16)

        @block.gpsimd
        def _(pool):
            nc.gpsimd.memset(consts[:, 1, NOPE:NOPE + HALF], -1.0)
            nc.gpsimd.memset(consts[:, 1, NOPE + HALF:QK], 1.0)
            nc.gpsimd.memset(consts[:, :, 0:NOPE], 0.0).then_inc(consts_ready, 1)

        @block.tensor
        def _(pe):
            pe.wait_ge(consts_ready, 1)
            pe.wait_ge(pos_loaded, 48)
            for n in range(2):
                m = pe.transpose(bank[0:QK, 7, n:n + 1], consts[:, n, :], chip.ident[0:1, 0:1])
            m.then_inc(cols_turned, 1)

        @block.scalar
        def _(act):
            for n in range(2):
                act.wait_ge(table, (9, 13)[n])
                act.activation((tmp, ang)[n][R, :], (tmp, ang)[n][R, :], ACT.Sin).then_inc(table_act, 1)

        @block.vector
        def _(dve):
            count = [0]

            def link(ins):
                count[0] += 1
                ins.then_inc(table, 1)
                dve.wait_ge(table, count[0])
            dve.wait_ge(cols_turned, 1)
            dve.wait_ge(pos_loaded, 48)
            link(dve.tensor_copy(cols[:], bank[0:QK, 7, 0:2]))
            link(dve.tensor_copy(ang[R, :], pos[R, :]))
            link(dve.tensor_scalar(ang[R, :], ang[R, :], cols[R, 0:1], None, ALU.mult))
            link(dve.tensor_scalar(turns_[R, :], ang[R, :], 1.0 / TWO_PI, 12582912.0, ALU.mult, ALU.add))
            link(dve.tensor_scalar(turns_[R, :], turns_[R, :], 12582912.0, None, ALU.subtract))
            parts = (6.28125, 1.9340515136718750e-3, TWO_PI - 6.28125 - 1.9340515136718750e-3)
            for part in parts:
                link(dve.scalar_tensor_tensor(out=ang[R, :], in0=turns_[R, :], scalar=-part, in1=ang[R, :],
                                              op0=ALU.mult, op1=ALU.add))
            PI = 3.1415925
            link(dve.tensor_scalar(tmp[R, :], ang[R, :], PI, -PI, ALU.min, ALU.max))
            link(dve.tensor_scalar(ang[R, :], ang[R, :], TWO_PI / 4, None, ALU.add))
            link(dve.tensor_scalar(turns_[R, :], ang[R, :], PI, -TWO_PI, ALU.is_gt, ALU.mult))
            link(dve.tensor_tensor(ang[R, :], ang[R, :], turns_[R, :], ALU.add))
            link(dve.tensor_scalar(ang[R, :], ang[R, :], PI, -PI, ALU.min, ALU.max))
            dve.wait_ge(table_act, 1)
            link(dve.tensor_scalar(rot[R, 1, :], tmp[R, :], cols[R, 1:2], None, ALU.mult))
            dve.wait_ge(table_act, 2)
            link(dve.tensor_copy(rot[R, 0, :], ang[R, :]))


def phase_latents(chip, hT, w_in, q_norm_g, kv_norm_g, cqT, ckvT, kT, rot, shT):
    nc, bank = chip.nc, chip.bank
    NB = LATENT_BLOCKS
    R = slice(NOPE, QK)
    HALF = ROPE // 2
    with ExitStack() as st:
        sb = lambda n, s, dt=F32: st.enter_context(nc.sbuf_tensor("latents_" + n, s, dt))
        sem = lambda n: st.enter_context(nc.semaphore("latents_" + n))
        W = sb("W", [P, KT, 3 * P])
        WR = sb("WR", [P, KT, 2, QK])
        gains = sb("gains", [P, 3])
        sq = sb("sq", [P, 3, BANK])
        v = sb("v", [P, 2, BANK])
        kr = sb("kr", [QK, 2, BANK])
        once, shT_stored = sem("once"), sem("shT_stored")
        T = Stages(sem("pe_stage"), "proj0 proj1 proj2 kr krs sumq sumkv")
        A = Stages(sem("act_stage"), "raw0 raw1 raw2 sq0 sq1 sq2 rinv")
        D = Stages(sem("dve_stage"), "vq vkv inv q0 q1 kv krc krs kr")
        block = st.enter_context(nc.Block())

        @block.sync
        def _(sp):
            v_ = lambda ap: ap.rearrange("(k p) n -> p k n", p=P)
            sp.dma_start(W[:], v_(w_in[:, 0:3 * P])).then_inc(once, 16)
            sp.dma_start(WR[:, :, 0, :], v_(w_in[:, C_KR - NOPE:C_KR + ROPE])).then_inc(once, 16)
            sp.dma_start(WR[:, :, 1, 0:NOPE], v_(w_in[:, C_KR - NOPE:C_KR])).then_inc(once, 16)
            for half in range(2):
                sp.dma_start(WR[:, :, 1, NOPE + half * HALF:NOPE + (half + 1) * HALF],
                             v_(w_in[:, C_KR + (1 - half) * HALF:C_KR + (2 - half) * HALF])).then_inc(once, 16)
            for f in range(2):
                sp.dma_start(gains[:, f:f + 1], q_norm_g[f * P:(f + 1) * P].rearrange("(p a) -> p a", a=1)
                             ).then_inc(once, 16)
            sp.dma_start(gains[:, 2:3], kv_norm_g.rearrange("(p a) -> p a", a=1)).then_inc(once, 16)
            with sp.Fori(0, QT) as t:
                sp.dma_start(shT[bass.ds(t, 1)].rearrange("a p (k c) -> (a p) k c", k=KT),
                             hT[:, :, bass.ds(t * P, P)]).then_inc(shT_stored, 16)
            sp.wait_ge(shT_stored, 16 * QT)

        @block.tensor
        def _(pe):
            pe.wait_ge(once, 16 * 8)

            def body(b, first):
                rhs = lambda k: hT[:, k, bass.ds(b * BANK, BANK)]
                for f in range(3):
                    if not first:
                        pe.wait_ge(A.sem, A.at(b - 1, f"raw{f}"))
                        pe.wait_ge(A.sem, A.at(b - 1, f"sq{f}"))
                    for k in range(KT):
                        m = pe.matmul(bank[:, f, :], W[:, k, f * P:(f + 1) * P], rhs(k), start=(k == 0),
                                      stop=(k == KT - 1))
                    m.then_inc(T(f"proj{f}"), 1)
                for n, name in enumerate(("kr", "krs")):
                    if not first:
                        pe.wait_ge(D.sem, D.at(b - 1, name if n else "krc"))
                    for k in range(KT):
                        m = pe.matmul(bank[0:QK, 3 + n, :], WR[:, k, n, :], rhs(k), start=(k == 0),
                                      stop=(k == KT - 1))
                    m.then_inc(T(name), 1)
                pe.wait_ge(A.sem, A.at(b, "sq1"))
                if not first:
                    pe.wait_ge(D.sem, D.at(b - 1, "vkv"))
                for f in range(2):
                    m = pe.matmul(bank[:, 5, :], chip.ones[:], sq[:, f, :], start=(f == 0), stop=(f == 1))
                m.then_inc(T("sumq"), 1)
                pe.wait_ge(A.sem, A.at(b, "sq2"))
                pe.matmul(bank[:, 6, :], chip.ones[:], sq[:, 2, :], start=True, stop=True).then_inc(T("sumkv"), 1)
            body(0, True)
            with pe.Fori(1, NB) as b:
                body(b, False)

        @block.scalar
        def _(act):
            def body(b, first):
                for f in range(3):
                    act.wait_ge(T.sem, T.at(b, f"proj{f}"))
                    out = cqT[:, f, bass.ds(b * BANK, BANK)] if f < 2 else ckvT[:, bass.ds(b * BANK, BANK)]
                    act.activation(out, bank[:, f, :], ACT.Copy).then_inc(A(f"raw{f}"), 1)
                for f in range(3):
                    if not first and f == 0:
                        act.wait_ge(T.sem, T.at(b - 1, "sumkv"))
                    act.activation(sq[:, f, :], bank[:, f, :], ACT.Square).then_inc(A(f"sq{f}"), 1)
                act.wait_ge(D.sem, D.at(b, "inv"))
                act.activation(v[:], v[:], ACT.Sqrt).then_inc(A("rinv"), 1)
            body(0, True)
            with act.Fori(1, NB) as b:
                body(b, False)

        @block.vector
        def _(dve):
            dve.wait_ge(once, 16 * 8)

            def body(b, first):
                t = bass.ds(b * BANK, BANK)
                dve.wait_ge(T.sem, T.at(b, "sumq"))
                if not first:
                    dve.wait_ge(D.sem, D.at(b - 1, "kv"))
                dve.tensor_scalar(v[:, 0, :], bank[:, 5, :], 1.0 / Q_LORA, EPS2, ALU.mult, ALU.add
                                  ).then_inc(D("vq"), 1)
                dve.wait_ge(T.sem, T.at(b, "sumkv"))
                dve.tensor_scalar(v[:, 1, :], bank[:, 6, :], 1.0 / KV_LORA, EPS2, ALU.mult, ALU.add
                                  ).then_inc(D("vkv"), 1)
                dve.wait_ge(D.sem, D.at(b, "vkv"))
                dve.reciprocal(v[:], v[:]).then_inc(D("inv"), 1)
                dve.wait_ge(A.sem, A.at(b, "rinv"))
                for f in range(3):
                    c = cqT[:, f, t] if f < 2 else ckvT[:, t]
                    dve.scalar_tensor_tensor(out=c, in0=c, scalar=gains[:, f:f + 1], in1=v[:, f // 2, :],
                                             op0=ALU.mult, op1=ALU.mult).then_inc(D(("q0", "q1", "kv")[f]), 1)
                dve.tensor_tensor(kr[R, 0, :], bank[R, 3, :], rot[R, 0, t], ALU.mult).then_inc(D("krc"), 1)
                dve.tensor_tensor(kr[R, 1, :], bank[R, 4, :], rot[R, 1, t], ALU.mult).then_inc(D("krs"), 1)
                dve.wait_ge(D.sem, D.at(b, "krs"))
                dve.tensor_tensor(kT[R, t], kr[R, 0, :], kr[R, 1, :], ALU.add).then_inc(D("kr"), 1)
            body(0, True)
            with dve.Fori(1, NB) as b:
                body(b, False)


def phase_attention(chip, cqT, ckvT, kT, rot, w_uq, w_ukv, oall):
    nc, bank = chip.nc, chip.bank
    NB = LATENT_BLOCKS
    R = slice(NOPE, QK)
    HALF = ROPE // 2
    SCALE = QK ** -0.5
    NS, NTB = 3, 3
    SC0, TB0, OB0 = 0, 3, 6
    chunks = {i: (i + 4) // 4 for i in range(QT)}
    with ExitStack() as st:
        sb = lambda n, s: st.enter_context(nc.sbuf_tensor("attn_" + n, s, F32))
        sem = lambda n: st.enter_context(nc.semaphore("attn_" + n))
        WQ = sb("WQ", [P, 2, 2, QK])
        WKV = sb("WKV", [P, NOPE + DV])
        qT = sb("qT", [QK, SEQ])
        v = sb("v", [P, QT, DV])
        ahead = sb("ahead", [P, P])
        sc = sb("sc", [P, 2, SEQ])
        pT = sb("pT", [P, NTB, BANK])
        tmp = sb("tmp", [QK, 2, 2, BANK])
        mx = sb("mx", [P, 2, 4])
        top = sb("top", [P, 2])
        total = sb("total", [P, 2])
        share = sb("share", [P, 2])
        w_loaded, mask_ready = sem("w_loaded"), sem("mask_ready")
        tiles = range(QT)
        groups = [(i, g) for i in tiles for g in range(chunks[i])]
        gi = {ig: n for n, ig in enumerate(groups)}
        T = Stages(sem("pe_stage"), " ".join([f"q{b} k{b}" for b in range(NB)] + ["v0 v1"])
                   + " " + " ".join(x for i in range(QT + 1) for x in (
                       [f"s{i}_{g}" for g in range(chunks.get(i, 0))]
                       + ([y for g in range(chunks[i - 1] + 1) for y in (
                           ([f"t{i - 1}_{g}"] if g < chunks[i - 1] else []) + ([f"o{i - 1}_{g - 1}"] if g else []))]
                          if i else []))))
        D = Stages(sem("dve_stage"), " ".join(f"qc{b} qs{b} q{b}" for b in range(NB)) + " v0 v1 " + " ".join(
            x for i in range(QT + 1) for x in (
                ([f"m{i}_{g}" for g in range(chunks[i])] + [f"top{i}"] if i < QT else [])
                + ([f"t{i - 1}_{g}" for g in range(chunks[i - 1])] + [f"share{i - 1}", f"o{i - 1}"] if i else []))))
        A = Stages(sem("act_stage"), " ".join(f"q{b} k{b}" for b in range(NB)) + " " + " ".join(
            f"e{i}" for i in tiles))
        block = st.enter_context(nc.Block())

        def turns(eng, body):
            body(0, True)
            with eng.Fori(1, AH) as h:
                body(h, False)

        @block.sync
        def _(sp):
            def body(h, first):
                if not first:
                    sp.wait_ge(T.sem, T.at(h - 1, "v1"))
                q = w_uq.rearrange("(k p) n -> p k n", p=P)
                sp.dma_start(WQ[:, :, 0, :], q[:, :, bass.ds(h * QK, QK)]).then_inc(w_loaded, 16)
                sp.dma_start(WQ[:, :, 1, 0:NOPE], q[:, :, bass.ds(h * QK, NOPE)]).then_inc(w_loaded, 16)
                for half in range(2):
                    sp.dma_start(WQ[:, :, 1, NOPE + half * HALF:NOPE + (half + 1) * HALF],
                                 q[:, :, bass.ds(h * QK + NOPE + (1 - half) * HALF, HALF)]).then_inc(w_loaded, 16)
                sp.dma_start(WKV[:], w_ukv[:, bass.ds(h * (NOPE + DV), NOPE + DV)]).then_inc(w_loaded, 16)
            turns(sp, body)

        @block.gpsimd
        def _(pool):
            nc.gpsimd.memset(ahead[:], 0.0).then_inc(mask_ready, 1)
            pool.wait_ge(mask_ready, 1)
            nc.gpsimd.affine_select(out=ahead[:], in_=ahead[:], compare_op=ALU.is_ge, fill=NEG, base=0,
                                    pattern=[[-1, P]], channel_multiplier=1).then_inc(mask_ready, 1)

        @block.tensor
        def _(pe):
            pe.wait_ge(mask_ready, 2)

            def body(h, first):
                pe.wait_ge(w_loaded, h * 80 + 80)
                for b in range(NB):
                    t = slice(b * BANK, (b + 1) * BANK)
                    if not first and b == 0:
                        pe.wait_ge(D.sem, D.at(h - 1, f"o{QT - 1}"))
                    if b > 0:
                        pe.wait_ge(A.sem, A.at(h, f"q{b - 1}"))
                        pe.wait_ge(D.sem, D.at(h, f"qs{b - 1}"))
                    for n in range(2):
                        for k in range(2):
                            m = pe.matmul(bank[0:QK, n, :], WQ[:, k, n, :], cqT[:, k, t], start=(k == 0), stop=(k == 1))
                    m.then_inc(T(f"q{b}"), 1)
                    if b > 0:
                        pe.wait_ge(A.sem, A.at(h, f"k{b - 1}"))
                    pe.matmul(bank[0:NOPE, 2, :], WKV[:, 0:NOPE], ckvT[:, t], start=True, stop=True
                              ).then_inc(T(f"k{b}"), 1)
                for n in range(2):
                    for t in range(8 * n, 8 * n + 8):
                        m = pe.matmul(bank[:, 3 + n, (t % 8) * DV:(t % 8 + 1) * DV], ckvT[:, t * P:(t + 1) * P],
                                      WKV[:, NOPE:NOPE + DV], start=True, stop=True)
                    m.then_inc(T(f"v{n}"), 1)

                def scores(i):
                    q = qT[:, i * P:(i + 1) * P]
                    for g in range(chunks[i]):
                        n = gi[i, g]
                        if n >= NS:
                            pe.wait_ge(D.sem, D.at(h, "m%d_%d" % groups[n - NS]))
                        else:
                            pe.wait_ge(A.sem, A.at(h, f"k{NB - 1}"))
                            pe.wait_ge(D.sem, D.at(h, f"q{NB - 1}"))
                        lo, hi = g * BANK, min((g + 1) * BANK, i * P)
                        bk = bank[:, SC0 + n % NS, :]
                        if hi > lo:
                            m = pe.matmul(bk[:, 0:hi - lo], q, kT[:, lo:hi], start=True, stop=True)
                        if (i + 1) * P <= (g + 1) * BANK:
                            d = slice(i * P - lo, (i + 1) * P - lo)
                            pe.matmul(bk[:, d], q, kT[:, i * P:(i + 1) * P], start=True, stop=False)
                            m = pe.matmul(bk[:, d], chip.ident[:], ahead[:], start=False, stop=True)
                        m.then_inc(T(f"s{i}_{g}"), 1)

                def rest(i):
                    for g in range(chunks[i] + 1):
                        if g < chunks[i]:
                            n = gi[i, g]
                            if g == 0:
                                pe.wait_ge(A.sem, A.at(h, f"e{i}"))
                            if n >= NTB:
                                pe.wait_ge(D.sem, D.at(h, "t%d_%d" % groups[n - NTB]))
                            else:
                                pe.wait_ge(D.sem, D.at(h, "v1"))
                            for c in range(4 * g, min(4 * g + 4, i + 1)):
                                m = pe.transpose(bank[:, TB0 + n % NTB, (c % 4) * P:(c % 4 + 1) * P],
                                                 sc[:, i % 2, c * P:(c + 1) * P], chip.ident[:])
                            m.then_inc(T(f"t{i}_{g}"), 1)
                        if g > 0:
                            n = gi[i, g - 1]
                            pe.wait_ge(D.sem, D.at(h, f"t{i}_{g - 1}"))
                            if g == 1 and i >= 2:
                                pe.wait_ge(D.sem, D.at(h, f"o{i - 2}"))
                            for c in range(4 * (g - 1), min(4 * g, i + 1)):
                                m = pe.matmul(bank[:, OB0 + i % 2, 0:DV], pT[:, n % NTB, (c % 4) * P:(c % 4 + 1) * P],
                                              v[:, c, :], start=(c == 0), stop=(c == i))
                            m.then_inc(T(f"o{i}_{g - 1}"), 1)
                for i in range(QT + 1):
                    if i < QT:
                        scores(i)
                    if i:
                        rest(i - 1)
            turns(pe, body)

        @block.scalar
        def _(act):
            def body(h, first):
                for b in range(NB):
                    t = slice(b * BANK, (b + 1) * BANK)
                    act.wait_ge(T.sem, T.at(h, f"q{b}"))
                    act.activation(qT[0:NOPE, t], bank[0:NOPE, 0, :], ACT.Copy).then_inc(A(f"q{b}"), 1)
                    act.wait_ge(T.sem, T.at(h, f"k{b}"))
                    act.activation(kT[0:NOPE, t], bank[0:NOPE, 2, :], ACT.Copy).then_inc(A(f"k{b}"), 1)
                for i in tiles:
                    act.wait_ge(D.sem, D.at(h, f"top{i}"))
                    n = (i + 1) * P
                    act.activation(sc[:, i % 2, 0:n], sc[:, i % 2, 0:n], ACT.Exp, bias=top[:, i % 2:i % 2 + 1],
                                   accum_out=total[:, i % 2:i % 2 + 1]).then_inc(A(f"e{i}"), 1)
            turns(act, body)

        @block.vector
        def _(dve):
            def body(h, first):
                for b in range(NB):
                    t = slice(b * BANK, (b + 1) * BANK)
                    dve.wait_ge(T.sem, T.at(h, f"q{b}"))
                    dve.wait_ge(A.sem, A.at(h, f"q{b}"))
                    if b or not first:
                        prev = D.at(h, f"q{b - 1}") if b else D.at(h - 1, f"q{NB - 1}")
                        dve.wait_ge(D.sem, prev)
                    dve.tensor_tensor(tmp[R, b % 2, 0, :], bank[R, 0, :], rot[R, 0, t], ALU.mult
                                      ).then_inc(D(f"qc{b}"), 1)
                    dve.tensor_tensor(tmp[R, b % 2, 1, :], bank[R, 1, :], rot[R, 1, t], ALU.mult
                                      ).then_inc(D(f"qs{b}"), 1)
                    dve.wait_ge(D.sem, D.at(h, f"qs{b}"))
                    dve.tensor_tensor(qT[R, t], tmp[R, b % 2, 0, :], tmp[R, b % 2, 1, :], ALU.add
                                      ).then_inc(D(f"q{b}"), 1)
                for n in range(2):
                    dve.wait_ge(T.sem, T.at(h, f"v{n}"))
                    dve.tensor_copy(v[:, 8 * n:8 * n + 8, :], bank[:, 3 + n, :].rearrange("p (t c) -> p t c", c=DV)
                                    ).then_inc(D(f"v{n}"), 1)
                for i in range(QT + 1):
                    if i < QT:
                        for g in range(chunks[i]):
                            n = gi[i, g]
                            w = min(BANK, (i + 1) * P - g * BANK)
                            dve.wait_ge(T.sem, T.at(h, f"s{i}_{g}"))
                            dve.tensor_scalar(sc[:, i % 2, g * BANK:g * BANK + w], bank[:, SC0 + n % NS, 0:w], SCALE,
                                              None, ALU.mult, ALU.max, accum_out=mx[:, i % 2, g:g + 1]
                                              ).then_inc(D(f"m{i}_{g}"), 1)
                        dve.wait_ge(D.sem, D.at(h, f"m{i}_{chunks[i] - 1}"))
                        dve.tensor_reduce(top[:, i % 2:i % 2 + 1], mx[:, i % 2, 0:chunks[i]], AX.X, ALU.max,
                                          negate=True).then_inc(D(f"top{i}"), 1)
                    if i:
                        j = i - 1
                        for g in range(chunks[j]):
                            n = gi[j, g]
                            w = min(BANK, (j + 1) * P - g * BANK)
                            dve.wait_ge(T.sem, T.at(h, f"t{j}_{g}"))
                            if n >= NTB:
                                dve.wait_ge(T.sem, T.at(h, "o%d_%d" % groups[n - NTB]))
                            dve.tensor_copy(pT[:, n % NTB, 0:w], bank[:, TB0 + n % NTB, 0:w]).then_inc(D(f"t{j}_{g}"), 1)
                        dve.wait_ge(T.sem, T.at(h, f"o{j}_{chunks[j] - 1}"))
                        dve.reciprocal(share[:, j % 2:j % 2 + 1], total[:, j % 2:j % 2 + 1]).then_inc(D(f"share{j}"), 1)
                        dve.wait_ge(D.sem, D.at(h, f"share{j}"))
                        dve.tensor_scalar(oall[:, j, bass.ds(h * DV, DV)], bank[:, OB0 + j % 2, 0:DV],
                                          share[:, j % 2:j % 2 + 1], None, ALU.mult).then_inc(D(f"o{j}"), 1)
            turns(dve, body)


def phase_output(chip, oall, shT, sh, w_in, sgu_g, sgu_b, w_spatial, b_spatial, w_out, ln_g, ln_b, out):
    nc, bank = chip.nc, chip.bank
    COLS = (C_V, C_U, C_ZB, C_ZA)
    with ExitStack() as st:
        sb = lambda n, s: st.enter_context(nc.sbuf_tensor("out_" + n, s, F32))
        sem = lambda n: st.enter_context(nc.semaphore("out_" + n))
        W = sb("W", [P, KT, 4, WIDTH])
        WO = sb("WO", [P, KT, DM])
        wsT = sb("wsT", [P, AH, P])
        bs = sb("bs", [AH, P])
        bsT = sb("bsT", [P, AH])
        srows = sb("srows", [P, 2, WIDTH])
        rows = sb("rows", [P, 2, DM])
        xT = sb("xT", [P, 2, KT, P])
        hs = sb("hs", [P, DM])
        v, u, zb, za = (sb(n, [P, 2, WIDTH]) for n in ("v", "u", "zb", "za"))
        m_ = sb("m", [P, 2 * WIDTH])
        ws = m_[:].rearrange("p (h s) -> p h s", h=AH)
        mT = sb("mT", [P, KT, P])
        r = sb("r", [P, DM])
        stats, mv, inv, rstd = (sb(n, [P, 2, w]) for n, w in (("stats", 12), ("mv", 2), ("inv", 1), ("rstd", 1)))
        once, w_loaded, prep, prep_pe = sem("once"), sem("w_loaded"), sem("prep"), sem("prep_pe")
        x_loaded = [sem(f"x_loaded{s}") for s in range(2)]
        h_loaded, stored = sem("h_loaded"), sem("stored")
        TH_ = Stages(sem("pe_head"), "proj0 proj1 proj2 proj3")
        TT_ = Stages(sem("pe_tail"), "spatial turned mm")
        AH_ = Stages(sem("act_head"), "v u zb za rstd")
        AT_ = Stages(sem("act_tail"), "mT rstd")
        DH_ = Stages(sem("dve_head"), "stats mv var inv n scaled vn")
        DT_ = Stages(sem("dve_tail"), "sv su b a sum stats mv var inv n scaled y")
        block = st.enter_context(nc.Block())

        def turns(eng, head, tail):
            head(0, 0, True)
            head(1, 1, False)
            tail(0, 0, True)
            with eng.Fori(1, QT // 2) as i:
                head(2 * i, 0, False)
                tail(2 * i - 1, 1, False)
                head(2 * i + 1, 1, False)
                tail(2 * i, 0, False)
            tail(QT - 1, 1, False)

        @block.sync
        def _(sp):
            sp.dma_start(ws, w_spatial.rearrange("h t s -> t h s")).then_inc(once, 16)
            sp.dma_start(bs[:], b_spatial).then_inc(once, 16)
            for n, c in enumerate(COLS):
                sp.dma_start(W[:, :, n, :], w_in[:, c:c + WIDTH].rearrange("(k p) n -> p k n", p=P)
                             ).then_inc(w_loaded, 16)
            for n, src in enumerate((sgu_g, sgu_b)):
                sp.dma_start(srows[:, n, :], src.broadcast_to([P, WIDTH])).then_inc(w_loaded, 16)
            for n, src in enumerate((ln_g, ln_b)):
                sp.dma_start(rows[:, n, :], src.broadcast_to([P, DM])).then_inc(w_loaded, 16)
            sp.dma_start(WO[:], w_out.rearrange("(k p) n -> p k n", p=P)).then_inc(w_loaded, 16)

            def head(t, s, first):
                if not isinstance(t, int):
                    sp.wait_ge(TH_.sem, TH_.at(t - 2, "proj3"))
                sp.dma_start(xT[:, s], shT[bass.ds(t, 1)].rearrange("a p (k c) -> (a p) k c", k=KT)
                             ).then_inc(x_loaded[s], 16)

            def tail(t, s, first):
                if not first:
                    sp.wait_ge(DT_.sem, DT_.at(t - 1, "sum"))
                sp.dma_start(hs[:], sh[bass.ds(t * P, P), :]).then_inc(h_loaded, 16)
                sp.wait_ge(DT_.sem, DT_.at(t, "y"))
                sp.dma_start(out[bass.ds(t * P, P), :], r[:]).then_inc(stored, 16)
            turns(sp, head, tail)
            sp.wait_ge(stored, 16 * QT)

        @block.tensor
        def _(pe):
            pe.wait_ge(once, 32)
            pe.transpose(bank[:, 7, 0:AH], bs[:], chip.ident[0:AH, 0:AH]).then_inc(prep_pe, 1)
            pe.wait_ge(prep, 1)
            for h in range(AH):
                m = pe.transpose(bank[:, 5 + h // 4, (h % 4) * P:(h % 4 + 1) * P], ws[:, h, :], chip.ident[:])
            m.then_inc(prep_pe, 1)
            pe.wait_ge(w_loaded, 16 * 9)

            def head(t, s, first):
                pe.wait_ge(x_loaded[s], (t - s) // 2 * 16 + 16)
                for n in range(4):
                    if not first:
                        pe.wait_ge(AH_.sem, AH_.at(t - 1, ("v", "u", "zb", "za")[n]))
                    for k in range(KT):
                        m = pe.matmul(bank[:, n, :], xT[:, s, k, :], W[:, k, n, :], start=(k == 0), stop=(k == KT - 1))
                    m.then_inc(TH_(f"proj{n}"), 1)

            def tail(t, s, first):
                pe.wait_ge(DH_.sem, DH_.at(t, "vn"))
                if first:
                    pe.wait_ge(prep, 3)
                else:
                    pe.wait_ge(DT_.sem, DT_.at(t - 1, "sum"))
                for h in range(AH):
                    m = pe.matmul(bank[:, 4, h * DV:(h + 1) * DV], wsT[:, h, :], v[:, s, h * DV:(h + 1) * DV], start=True,
                                  stop=True)
                m.then_inc(TT_("spatial"), 1)
                pe.wait_ge(DT_.sem, DT_.at(t, "a"))
                for k in range(KT):
                    m = pe.transpose(bank[:, 5 + k // 4, (k % 4) * P:(k % 4 + 1) * P], m_[:, k * P:(k + 1) * P],
                                     chip.ident[:])
                m.then_inc(TT_("turned"), 1)
                pe.wait_ge(AT_.sem, AT_.at(t, "mT"))
                for n in range(2):
                    for k in range(KT):
                        m = pe.matmul(bank[:, (7, 4)[n], :], mT[:, k, :], WO[:, k, n * BANK:(n + 1) * BANK],
                                      start=(k == 0), stop=(k == KT - 1))
                m.then_inc(TT_("mm"), 1)
            turns(pe, head, tail)

        @block.scalar
        def _(act):
            def head(t, s, first):
                if not isinstance(t, int):
                    act.wait_ge(TT_.sem, TT_.at(t - 2, "spatial"))
                act.wait_ge(TH_.sem, TH_.at(t, "proj0"))
                act.activation(v[:, s], bank[:, 0, :], ACT.Gelu).then_inc(AH_("v"), 1)
                if not isinstance(t, int):
                    act.wait_ge(DT_.sem, DT_.at(t - 2, "a"))
                act.wait_ge(TH_.sem, TH_.at(t, "proj1"))
                act.activation(u[:, s], bank[:, 1, :], ACT.Gelu).then_inc(AH_("u"), 1)
                act.wait_ge(TH_.sem, TH_.at(t, "proj2"))
                act.activation(zb[:, s], bank[:, 2, :], ACT.Silu).then_inc(AH_("zb"), 1)
                act.wait_ge(TH_.sem, TH_.at(t, "proj3"))
                act.activation(za[:, s], bank[:, 3, :], ACT.Silu).then_inc(AH_("za"), 1)
                act.wait_ge(DH_.sem, DH_.at(t, "inv"))
                act.activation(rstd[:, 0, :], inv[:, 0, :], ACT.Sqrt).then_inc(AH_("rstd"), 1)

            def tail(t, s, first):
                act.wait_ge(TT_.sem, TT_.at(t, "turned"))
                for n in range(2):
                    m = act.activation(mT[:, 4 * n:4 * n + 4, :], bank[:, 5 + n, :].rearrange("p (k c) -> p k c", k=4),
                                       ACT.Copy)
                m.then_inc(AT_("mT"), 1)
                act.wait_ge(DT_.sem, DT_.at(t, "inv"))
                act.activation(rstd[:, 1, :], inv[:, 1, :], ACT.Sqrt).then_inc(AT_("rstd"), 1)
            turns(act, head, tail)

        @block.vector
        def _(dve):
            dve.wait_ge(once, 32)
            dve.tensor_tensor(ws, ws, bcast(chip.low[:], 1, AH), ALU.mult).then_inc(prep, 1)
            dve.wait_ge(prep_pe, 1)
            dve.tensor_copy(bsT[:], bank[:, 7, 0:AH]).then_inc(prep, 1)
            dve.wait_ge(prep_pe, 2)
            for n in range(2):
                m = dve.tensor_copy(wsT[:, 4 * n:4 * n + 4, :], bank[:, 5 + n, :].rearrange("p (h c) -> p h c", h=4))
            m.then_inc(prep, 1)
            dve.wait_ge(w_loaded, 16 * 9)
            dve.wait_ge(prep, 3)

            def head(t, s, first):
                dve.wait_ge(AH_.sem, AH_.at(t, "v"))
                layer_norm_steps(dve, DH_, AH_, t, v[:, s], stats[:, 0], mv[:, 0], inv[:, 0], rstd[:, 0], EPS2,
                                 srows[:, 0, :])
                dve.tensor_tensor(v[:, s], v[:, s], srows[:, 1, :], ALU.add).then_inc(DH_("vn"), 1)

            def tail(t, s, first):
                by_head = lambda ap: ap.rearrange("p (h d) -> p h d", h=AH)
                a, b = m_[:, 0:WIDTH], m_[:, WIDTH:2 * WIDTH]
                dve.wait_ge(TT_.sem, TT_.at(t, "spatial"))
                if not first:
                    dve.wait_ge(TT_.sem, TT_.at(t - 1, "turned"))
                dve.tensor_tensor(by_head(b), by_head(bank[:, 4, :]), bcast(bsT[:], 2, DV), ALU.add
                                  ).then_inc(DT_("sv"), 1)
                dve.wait_ge(AH_.sem, AH_.at(t, "za"))
                dve.wait_ge(DT_.sem, DT_.at(t, "sv"))
                dve.tensor_tensor(b, b, u[:, s], ALU.mult).then_inc(DT_("su"), 1)
                dve.wait_ge(DT_.sem, DT_.at(t, "su"))
                dve.tensor_tensor(b, b, zb[:, s], ALU.mult).then_inc(DT_("b"), 1)
                dve.tensor_tensor(a, oall[:, bass.ds(t, 1), :].rearrange("p a n -> p (a n)"), za[:, s], ALU.mult
                                  ).then_inc(DT_("a"), 1)
                dve.wait_ge(TT_.sem, TT_.at(t, "mm"))
                dve.wait_ge(h_loaded, t * 16 + 16)
                if not first:
                    dve.wait_ge(stored, t * 16)
                for n in range(2):
                    c = slice(n * BANK, (n + 1) * BANK)
                    m = dve.scalar_tensor_tensor(out=r[:, c], in0=hs[:, c], scalar=ALPHA, in1=bank[:, (7, 4)[n], :],
                                                 op0=ALU.mult, op1=ALU.add)
                m.then_inc(DT_("sum"), 1)
                dve.wait_ge(DT_.sem, DT_.at(t, "sum"))
                layer_norm_steps(dve, DT_, AT_, t, r[:], stats[:, 1], mv[:, 1], inv[:, 1], rstd[:, 1], EPS2,
                                 rows[:, 0, :])
                dve.tensor_tensor(r[:], r[:], rows[:, 1, :], ALU.add).then_inc(DT_("y"), 1)
            turns(dve, head, tail)


def build(nc, a, out):
    def scratch(name, shape):
        return nc.dram_tensor(name, shape, F32, kind="Internal").ap()

    sa = scratch("delta_qkv", [3 * HEADS, P, TOK])
    sq_, sv = scratch("gla_queries", [HEADS, P, TOK]), scratch("gla_values", [HEADS, P, TOK])
    sk, sg = scratch("gla_keys", [2 * HEADS, P, TOK]), scratch("gla_decays", [2 * HEADS, P, TOK])
    so_a, so_b = scratch("delta_outputs", [HEADS, P, SEQ]), scratch("gla_outputs", [HEADS, P, SEQ])
    smT = scratch("merged", [KT, P, SEQ])
    sh = scratch("hidden", [SEQ, DM])
    shT = scratch("hidden_turned", [QT, P, DM])
    with ExitStack() as stack:
        chip = Chip(nc, stack)
        w_in = a["w_in"][0]
        with ExitStack() as st:
            uT = st.enter_context(nc.sbuf_tensor("uT", [P, KT, TOK], F32))
            phase_constants(chip, a["c"], a["c_ctx"], a["w_mod"], a["b_mod"], a["lb_param"])
            phase_modulated_norm(chip, uT, a["x"][0], a["ctx"][0])
            phase_conv(chip, uT, w_in, a["conv_w"], sa)
            phase_decay_beta(chip, uT, w_in, a["a_log"], a["dt_bias"])
            phase_gla_inputs(chip, uT, w_in, sq_, sv, sk, sg)
            phase_delta_rule(chip, sa, so_a)
            phase_gla(chip, sq_, sv, sk, sg, so_b)
            yT = st.enter_context(nc.sbuf_tensor("yT", [P, 2 * HEADS, SEQ], F32))
            phase_branch_gates(chip, uT, w_in, so_a, so_b, a["a_norm_g"], a["b_norm_g"], yT)
            phase_merge(chip, uT, w_in, yT, a["w_a_out"][0], a["w_b_out"][0], smT)
        oall = stack.enter_context(nc.sbuf_tensor("oall", [P, QT, WIDTH], F32))
        with ExitStack() as st:
            sb = lambda n, s: st.enter_context(nc.sbuf_tensor(n, s, F32))
            hT = sb("hT", [P, KT, SEQ])
            phase_residual(chip, a["x"][0], smT, a["w_out"][0], a["ln_g"], a["ln_b"], sh, hT)
            cqT, ckvT = sb("cqT", [P, 2, SEQ]), sb("ckvT", [P, SEQ])
            kT, rot = sb("kT", [QK, SEQ]), sb("rot", [QK, 2, SEQ])
            phase_rotation(chip, a["positions_2"], a["inv_freq"], rot)
            phase_latents(chip, hT, a["w_in_2"], a["q_norm_g_2"], a["kv_norm_g_2"], cqT, ckvT, kT, rot, shT)
            phase_attention(chip, cqT, ckvT, kT, rot, a["w_uq_2"], a["w_ukv_2"], oall)
        row = lambda n: a[n].rearrange("(a n) -> a n", a=1)
        phase_output(chip, oall, shT, sh, a["w_in_2"], row("sgu_norm_g_2"), row("sgu_norm_b_2"), a["w_spatial_2"],
                     a["b_spatial_2"], a["w_out_2"], row("ln_g_2"), row("ln_b_2"), out[0])


INPUTS = ["x", "c", "ctx", "c_ctx", "w_mod", "b_mod", "w_in", "conv_w", "a_log", "dt_bias", "lb_param", "a_norm_g",
          "b_norm_g", "w_a_out", "w_b_out", "w_out", "ln_g", "ln_b", "positions_2", "w_in_2", "q_norm_g_2", "w_uq_2",
          "kv_norm_g_2", "w_ukv_2", "sgu_norm_g_2", "sgu_norm_b_2", "w_spatial_2", "b_spatial_2", "w_out_2", "ln_g_2",
          "ln_b_2"]


def kernel(**inputs):
    import numpy as np
    import concourse.bacc as bacc
    from concourse.bass_utils import run_bass_kernel_spmd

    arrays = {name: np.ascontiguousarray(inputs[name]) for name in INPUTS}
    half = ROPE // 2
    arrays["inv_freq"] = (np.float32(1.0) / np.float32(10000.0) ** (np.arange(half, dtype=np.float32)
                                                                   / np.float32(half))).reshape(1, half)
    nc = bacc.Bacc("TRN2", target_bir_lowering=False, num_devices=1)
    aps = {name: nc.dram_tensor(f"in_{name}", v.shape, mybir.dt.from_np(v.dtype), kind="ExternalInput").ap()
           for name, v in arrays.items()}
    out = nc.dram_tensor("out", (1, SEQ, DM), F32, kind="ExternalOutput").ap()
    build(nc, aps, out)
    result = run_bass_kernel_spmd(nc, [{f"in_{name}": v for name, v in arrays.items()}], core_ids=[0])
    return result.results[0]["out"]
```

```python
from contextlib import ExitStack

import concourse.bass as bass
from concourse import mybir

F32 = mybir.dt.float32
U32 = mybir.dt.uint32
I32 = mybir.dt.int32
ALU = mybir.AluOpType
ACT = mybir.ActivationFunctionType
AX = mybir.AxisListType

P = 128
BANK = 512
DM = 1024
KT = DM // P
SEQ = 2048
CTX = 256
TOK = CTX + SEQ
NT = TOK // P
GRID_W = 64
ROWS = SEQ // GRID_W
HEADS = 4
NDIR = 2
HD = HEADS * P
C_AQ, C_AV, C_AB = 0, 2 * HD, 3 * HD
C_AGATE = C_AB + 4 * HEADS
C_BQ = C_AGATE + HD
C_BF = C_BQ + HD
C_BI = C_BF + 2 * HD
C_BGATE = C_BI + HD
C_MERGE = C_BGATE + HD
CONV_K = 5
PAD = CONV_K // 2
RAW = TOK + 4 * PAD
EPS1 = 1e-6
LATENT_BLOCKS = SEQ // BANK
BLOCKS = [(0, CTX)] + [(CTX + BANK * n, BANK) for n in range(LATENT_BLOCKS)]
ALPHA = 2.0 ** 0.25


class Stages:

    def __init__(self, sem, names):
        self.sem, self.names, self.turn = sem, names.split(), 0

    def __call__(self, name):
        want = self.names[self.turn % len(self.names)]
        assert name == want, (name, want)
        self.turn += 1
        return self.sem

    def at(self, i, name):
        return i * len(self.names) + self.names.index(name) + 1


class Chip:

    def __init__(self, nc, stack):
        self.nc = nc
        self.bank = stack.enter_context(nc.psum_tensor("bank", [P, 8, BANK], F32))

        def sb(name, shape, dt=F32):
            return stack.enter_context(nc.sbuf_tensor(name, shape, dt))

        self.sb = sb
        self.ident = sb("ident", [P, P])
        self.ones = sb("ones", [P, P])
        self.low = sb("low", [P, P])
        self.up = sb("up", [P, P])
        self.off = sb("off", [P, NDIR, 7, P])
        self.diag16 = sb("diag16", [P, NDIR, P])
        self.modT = sb("modT", [P, 2 * KT, 2])
        self.gate_rows = sb("gate_rows", [P, DM])
        self.lbT = sb("lbT", [P, 2, 2 * HEADS])
        self.decay_tok = sb("decay_tok", [P, NT, 2 * HEADS])
        self.beta_tok = sb("beta_tok", [P, NT, 2 * HEADS])


def bcast(ap, axis, count):
    v = ap.unsqueeze(axis)
    shape = list(v.shape)
    shape[axis] = count
    return v.broadcast_to(shape)


def phase_constants(chip, c, c_ctx, w_mod, b_mod, lb_param):
    nc, bank = chip.nc, chip.bank
    NW = 4
    MODW = 3 * DM
    with ExitStack() as st:
        sb = lambda n, s: st.enter_context(nc.sbuf_tensor("constants_" + n, s, F32))
        sem = lambda n: st.enter_context(nc.semaphore("constants_" + n))
        cond = sb("cond", [2 * KT, P])
        scond = sb("scond", [2 * KT, P])
        condT = sb("condT", [P, 2 * KT])
        wm = sb("wm", [P, NW, MODW])
        bm = sb("bm", [2, MODW])
        mod = sb("mod", [2, MODW])
        lb = sb("lb", [2 * HEADS, 8, P])
        c_loaded, b_loaded, lb_loaded = sem("c_loaded"), sem("b_loaded"), sem("lb_loaded")
        w_loaded = [sem(f"wm_loaded{s}") for s in range(NW)]
        w_used = sem("wm_used")
        pool_step, act_done = sem("pool_step"), sem("act_done")
        masks_ready = sem("masks_ready")
        pe_done, dve_done = sem("pe_done"), sem("dve_done")
        block = st.enter_context(nc.Block())

        @block.sync
        def _(sp):
            sp.dma_start(cond[0:KT, :], c.rearrange("b (k p) -> (b k) p", p=P)).then_inc(c_loaded, 16)
            sp.dma_start(cond[KT:2 * KT, :], c_ctx.rearrange("(k p) -> k p", p=P)).then_inc(c_loaded, 16)
            for r in range(2):
                sp.dma_start(bm[r:r + 1, :], b_mod).then_inc(b_loaded, 16)
            for r in range(2):
                sp.dma_start(lb[:, r, :], lb_param[r].rearrange("d (h p) -> (d h) p", p=P)).then_inc(lb_loaded, 16)
            for k in range(KT):
                if k >= NW:
                    sp.wait_ge(w_used, k - NW + 1)
                sp.dma_start(wm[:, k % NW, :], w_mod[0, k * P:(k + 1) * P, :]).then_inc(w_loaded[k % NW], 16)

        @block.gpsimd
        def _(pool):
            count = [0]

            def step(ins):
                count[0] += 1
                ins.then_inc(pool_step, 1)
                pool.wait_ge(pool_step, count[0])

            def keep(view, pattern, base, mul):
                step(nc.gpsimd.affine_select(out=view, in_=view, compare_op=ALU.is_ge, fill=0.0, base=base,
                                             pattern=pattern, channel_multiplier=mul))

            nc.gpsimd.memset(chip.ones[:], 1.0)
            nc.gpsimd.memset(chip.low[:], 1.0)
            nc.gpsimd.memset(chip.up[:], 1.0)
            nc.gpsimd.memset(chip.off[:], 0.0)
            nc.gpsimd.memset(chip.diag16[:], 1.0)
            step(nc.gpsimd.memset(chip.ident[:], 0.0))
            step(nc.gpsimd.affine_select(out=chip.ident[:], in_=chip.ident[:], compare_op=ALU.not_equal, fill=1.0,
                                         base=0, pattern=[[-1, P]], channel_multiplier=1))
            keep(chip.low[:], [[-1, P]], 0, 1)
            keep(chip.up[:], [[1, P]], 0, -1)
            for n in range(7):
                b = 1 << n
                nb = P // (2 * b)
                for d in range(NDIR):
                    v = chip.off[:, d, n, :].rearrange("p (c j) -> p c j", j=2 * b)[:, :, d * b:(d + 1) * b]
                    lo = b if d == 0 else 0
                    step(nc.gpsimd.memset(v, 1.0))
                    keep(v, [[-2 * b, nb], [0, b]], -lo, 1)
                    keep(v, [[2 * b, nb], [0, b]], lo + b - 1, -1)
            for d in range(NDIR):
                v = chip.diag16[:, d, :].rearrange("p (c j) -> p c j", j=16)
                if d == 0:
                    keep(v, [[16, 8], [1, 16]], 0, -1)
                    keep(v, [[-16, 8], [0, 16]], 0, 1)
                else:
                    keep(v, [[-16, 8], [-1, 16]], 0, 1)
                    keep(v, [[16, 8], [0, 16]], 15, -1)
            nc.gpsimd.memset(chip.decay_tok[:, 0, 0:1], 0.0).then_inc(masks_ready, 1)

        @block.scalar
        def _(act):
            act.wait_ge(c_loaded, 32)
            act.activation(scond[:], cond[:], ACT.Silu).then_inc(act_done, 1)
            for r in range(2):
                act.wait_ge(dve_done, 3 + r)
                act.activation(lb[:, 5 + r, :], lb[:, 3 + r, :], ACT.Exp).then_inc(act_done, 1)

        @block.vector
        def _(dve):
            dve.wait_ge(lb_loaded, 32)
            dve.tensor_tensor(lb[:, 2, :], lb[:, 0, :], lb[:, 1, :], ALU.max).then_inc(dve_done, 1)
            dve.wait_ge(masks_ready, 1)
            dve.wait_ge(pe_done, 1)
            dve.tensor_copy(condT[:], bank[:, 6, 0:2 * KT]).then_inc(dve_done, 1)
            dve.wait_ge(dve_done, 1)
            for r in range(2):
                dve.tensor_tensor(lb[:, 3 + r, :], lb[:, r, :], lb[:, 2, :], ALU.subtract).then_inc(dve_done, 1)
            dve.wait_ge(act_done, 3)
            dve.tensor_tensor(lb[:, 7, :], lb[:, 5, :], lb[:, 6, :], ALU.add).then_inc(dve_done, 1)
            dve.wait_ge(dve_done, 5)
            dve.reciprocal(lb[:, 2, :], lb[:, 7, :]).then_inc(dve_done, 1)
            dve.wait_ge(dve_done, 6)
            dve.tensor_tensor(lb[:, 3, :], lb[:, 5, :], lb[:, 2, :], ALU.mult).then_inc(dve_done, 1)
            dve.wait_ge(dve_done, 7)
            dve.tensor_scalar(lb[:, 4, :], lb[:, 3, :], -1.0, 1.0, ALU.mult, ALU.add).then_inc(dve_done, 1)
            dve.wait_ge(b_loaded, 32)
            dve.wait_ge(pe_done, 3)
            for n in range(6):
                dve.tensor_tensor(mod[:, n * BANK:(n + 1) * BANK], bank[0:2, n, :], bm[:, n * BANK:(n + 1) * BANK],
                                  ALU.add).then_inc(dve_done, 1)
            dve.wait_ge(pe_done, 4)
            mT = bank[:, 7, 0:4 * KT].rearrange("p (k s) -> p k s", s=2)
            dve.tensor_copy(chip.modT[:, 0:KT, :], mT[:, 0:KT, :])
            dve.tensor_scalar(chip.modT[:, KT:2 * KT, :], mT[:, KT:2 * KT, :], 1.0, None, ALU.add)
            for r in range(2):
                dve.tensor_copy(chip.lbT[:, r, :], bank[:, 6, 64 + 8 * r:72 + 8 * r])
            dve.wait_ge(pe_done, 5)
            for n in range(2):
                dve.tensor_copy(chip.gate_rows[:, n * BANK:(n + 1) * BANK], bank[:, n, :])

        @block.tensor
        def _(pe):
            pe.wait_ge(masks_ready, 1)
            pe.wait_ge(act_done, 1)
            pe.transpose(bank[:, 6, 0:2 * KT], scond[:], chip.ident[0:2 * KT, 0:2 * KT]).then_inc(pe_done, 1)
            pe.wait_ge(dve_done, 8)
            for r in range(2):
                t = pe.transpose(bank[:, 6, 64 + 8 * r:72 + 8 * r], lb[:, 3 + r, :], chip.ident[0:8, 0:8])
            t.then_inc(pe_done, 1)
            cT = condT[:].rearrange("p (s k) -> p k s", k=KT)
            for k in range(KT):
                pe.wait_ge(w_loaded[k % NW], 16 * (k // NW + 1))
                for n in range(6):
                    mm = pe.matmul(bank[0:2, n, :], cT[:, k, :], wm[:, k % NW, n * BANK:(n + 1) * BANK],
                                   start=(k == 0), stop=(k == KT - 1))
                mm.then_inc(w_used, 1)
            pe.wait_ge(w_used, KT)
            pe.nop().then_inc(pe_done, 1)
            pe.wait_ge(dve_done, 14)
            for j in range(2 * KT):
                t = pe.transpose(bank[:, 7, 2 * j:2 * j + 2], mod[:, j * P:(j + 1) * P], chip.ident[0:2, 0:2])
            t.then_inc(pe_done, 1)
            for n in range(2):
                mm = pe.matmul(bank[:, n, :], chip.ones[0:1, :], mod[0:1, 2 * DM + n * BANK:2 * DM + (n + 1) * BANK],
                               start=True, stop=True)
            mm.then_inc(pe_done, 1)


def phase_modulated_norm(chip, uT, x, ctx_in):
    nc, bank = chip.nc, chip.bank
    with ExitStack() as st:
        sb = lambda n, s: st.enter_context(nc.sbuf_tensor("modulated_norm_" + n, s, F32))
        sem = lambda n: st.enter_context(nc.semaphore("modulated_norm_" + n))
        xin = sb("xin", [P, 2, DM])
        xh = sb("xh", [P, 2, DM])
        stats = sb("stats", [P, 2, 12])
        mv = sb("mv", [P, 2, 2])
        inv = sb("inv", [P, 2, 1])
        rstd = sb("rstd", [P, 2, 1])
        x_loaded = [sem(f"x_loaded{s}") for s in range(2)]
        D = Stages(sem("dve_stage"), "stats0 mv0 var0 inv0 xh0 uT0 stats1 mv1 var1 inv1 xh1 uT1")
        A = Stages(sem("act_stage"), "rstd0 uT0 rstd1 uT1")
        T = Stages(sem("pe_stage"), "turned0 turned1")
        block = st.enter_context(nc.Block())
        pairs = SEQ // (2 * P)

        def turns(eng, body):
            body(0, True)
            with eng.Fori(1, pairs + 1) as i:
                body(i, False)

        @block.sync
        def _(sp):
            def body(i, first):
                for s in range(2):
                    if not first:
                        sp.wait_ge(D.sem, D.at(i - 1, f"xh{s}"))
                    src = ctx_in[s * P:(s + 1) * P, :] if first else x[bass.ds((i - 1) * 2 * P + s * P, P), :]
                    sp.dma_start(xin[:, s, :], src).then_inc(x_loaded[s], 16)
            turns(sp, body)

        @block.vector
        def _(dve):
            def body(i, first):
                stream = 1 if first else 0
                for s in range(2):
                    dve.wait_ge(x_loaded[s], i * 16 + 16)
                    dve.bn_stats(stats[:, s, 0:6], xin[:, s, 0:BANK])
                    dve.bn_stats(stats[:, s, 6:12], xin[:, s, BANK:DM]).then_inc(D(f"stats{s}"), 1)
                    dve.wait_ge(D.sem, D.at(i, f"stats{s}"))
                    dve.nop(nofuse=True)
                    dve.bn_aggr(mv[:, s, :], stats[:, s, :]).then_inc(D(f"mv{s}"), 1)
                    dve.wait_ge(D.sem, D.at(i, f"mv{s}"))
                    dve.tensor_scalar(mv[:, s, 1:2], mv[:, s, 1:2], EPS1, None, ALU.add).then_inc(D(f"var{s}"), 1)
                    dve.wait_ge(D.sem, D.at(i, f"var{s}"))
                    dve.reciprocal(inv[:, s, :], mv[:, s, 1:2]).then_inc(D(f"inv{s}"), 1)
                    dve.wait_ge(A.sem, A.at(i, f"rstd{s}"))
                    if not first:
                        dve.wait_ge(T.sem, T.at(i - 1, f"turned{s}"))
                    dve.tensor_scalar(xh[:, s, :], xin[:, s, :], mv[:, s, 0:1], rstd[:, s, :], ALU.subtract,
                                      ALU.mult).then_inc(D(f"xh{s}"), 1)
                    dve.wait_ge(T.sem, T.at(i, f"turned{s}"))
                    for k in range(KT // 2):
                        ev = dve.tensor_scalar(uT[:, k, bass.ds(i * 2 * P + s * P, P)], bank[:, 2 * s, k * P:(k + 1) * P],
                                               chip.modT[:, KT + k, stream:stream + 1],
                                               chip.modT[:, k, stream:stream + 1], ALU.mult, ALU.add)
                    ev.then_inc(D(f"uT{s}"), 1)
            turns(dve, body)

        @block.scalar
        def _(act):
            def body(i, first):
                stream = 1 if first else 0
                for s in range(2):
                    act.wait_ge(D.sem, D.at(i, f"inv{s}"))
                    act.activation(rstd[:, s, :], inv[:, s, :], ACT.Sqrt).then_inc(A(f"rstd{s}"), 1)
                    act.wait_ge(T.sem, T.at(i, f"turned{s}"))
                    for k in range(KT // 2, KT):
                        ev = act.activation(uT[:, k, bass.ds(i * 2 * P + s * P, P)],
                                            bank[:, 2 * s + 1, (k - KT // 2) * P:(k - KT // 2 + 1) * P], ACT.Identity,
                                            bias=chip.modT[:, k, stream:stream + 1],
                                            scale=chip.modT[:, KT + k, stream:stream + 1])
                    ev.then_inc(A(f"uT{s}"), 1)
            turns(act, body)

        @block.tensor
        def _(pe):
            def body(i, first):
                for s in range(2):
                    pe.wait_ge(D.sem, D.at(i, f"xh{s}"))
                    if not first:
                        pe.wait_ge(D.sem, D.at(i - 1, f"uT{s}"))
                        pe.wait_ge(A.sem, A.at(i - 1, f"uT{s}"))
                    for k in range(KT):
                        t = pe.transpose(bank[:, 2 * s + k // 4, (k % 4) * P:(k % 4 + 1) * P],
                                         xh[:, s, k * P:(k + 1) * P], chip.ident[:])
                    t.then_inc(T(f"turned{s}"), 1)
            turns(pe, body)


def phase_conv(chip, uT, w_in, conv_w, sa):
    nc, bank = chip.nc, chip.bank
    NF = 3 * HEADS
    with ExitStack() as st:
        sb = lambda n, s: st.enter_context(nc.sbuf_tensor("conv_" + n, s, F32))
        sem = lambda n: st.enter_context(nc.semaphore("conv_" + n))
        W = sb("W", [P, 2, KT, P])
        taps = sb("taps", [P, NF, CONV_K])
        tap_rows = sb("tap_rows", [NF * CONV_K, P])
        raw = sb("raw", [P, 2, RAW])
        acc = sb("acc", [P, RAW])
        y = sb("y", [P, 2, TOK])
        sq = sb("sq", [P, TOK])
        inv = sb("inv", [P, TOK])
        w_loaded = [sem(f"w_loaded{s}") for s in range(2)]
        y_stored = [sem(f"y_stored{s}") for s in range(2)]
        taps_loaded, taps_ready, taps_turned = sem("taps_loaded"), sem("taps_ready"), sem("taps_turned")
        T, TS = Stages(sem("pe_proj"), " ".join(f"proj{b}" for b in range(5))), Stages(
            sem("pe_sums"), " ".join(f"sum{b}" for b in range(5)))
        D = Stages(sem("dve_conv"), " ".join(f"t{t}" for t in range(CONV_K - 1)) + " conv")
        DS, DY = Stages(sem("dve_sums"), " ".join(f"ss{b}" for b in range(5))), Stages(sem("dve_scale"), "inv y")
        A, AS = Stages(sem("act_raw"), " ".join(f"raw{b}" for b in range(5))), Stages(sem("act_silu"), "silu")
        AQ, AR = Stages(sem("act_square"), "sq"), Stages(sem("act_root"), "rinv")
        block = st.enter_context(nc.Block())
        def steps(eng, step):
            for f in range(2):
                step(f, f)
            with eng.Fori(1, HEADS // 2 + 1) as i:
                for s in range(2):
                    step(2 * i + s, s)
            for f in range(HEADS + 2, NF + 2):
                step(f, f % 2)
        num = lambda f: isinstance(f, int)
        exists = lambda f: not num(f) or 0 <= f < NF
        normed = lambda f: not num(f) or f < 2 * HEADS
        rcol = [PAD + t0 + (2 * PAD if t0 else 0) for t0, _ in BLOCKS]
        WIDE = RAW - 2 * PAD

        @block.sync
        def _(sp):
            sp.dma_start(tap_rows[:], conv_w[0].rearrange("t (f p) -> (t f) p", p=P)).then_inc(taps_loaded, 16)

            def step(f, s):
                g = f + 1
                if not num(f) or (f > 0 and exists(g)):
                    sp.wait_ge(T.sem, T.at(g - 2, "proj4"))
                if exists(g):
                    sp.dma_start(W[:, 1 - s], w_in[:, bass.ds(g * P, P)].rearrange("(k p) n -> p k n", p=P)
                                 ).then_inc(w_loaded[1 - s], 16)
                g = f - 2
                if exists(g):
                    if normed(g):
                        sp.wait_ge(DY.sem, DY.at(g, "y"))
                    else:
                        sp.wait_ge(AS.sem, AS.at(g, "silu"))
                    sp.dma_start(sa[bass.ds(g, 1)].rearrange("a p t -> (a p) t"), y[:, s, :]).then_inc(y_stored[s], 16)
            sp.dma_start(W[:, 0], w_in[:, 0:P].rearrange("(k p) n -> p k n", p=P)).then_inc(w_loaded[0], 16)
            steps(sp, step)
            for s in range(2):
                sp.wait_ge(y_stored[s], 16 * (NF // 2))

        @block.tensor
        def _(pe):
            pe.wait_ge(taps_loaded, 16)
            pe.transpose(bank[:, 7, 0:NF * CONV_K], tap_rows[:], chip.ident[0:NF * CONV_K, 0:NF * CONV_K]
                         ).then_inc(taps_turned, 1)

            def step(f, s):
                def project(blocks):
                    for b in blocks:
                        t0, n = BLOCKS[b]
                        if not (num(f) and f == 0):
                            pe.wait_ge(A.sem, A.at(f - 1, f"raw{b}"))
                        for k in range(KT):
                            mm = pe.matmul(bank[:, b, 0:n], W[:, s, k, :], uT[:, k, t0:t0 + n], start=(k == 0),
                                           stop=(k == KT - 1))
                        mm.then_inc(T(f"proj{b}"), 1)

                def sums(blocks):
                    g = f - 1
                    for b in blocks:
                        t0, n = BLOCKS[b]
                        if b == 0:
                            pe.wait_ge(AQ.sem, AQ.at(g, "sq"))
                        if b >= 3:
                            pe.wait_ge(DS.sem, DS.at(g, f"ss{b - 3}"))
                        elif not (num(g) and g == 0):
                            pe.wait_ge(DS.sem, DS.at(g - 1, f"ss{min(b + 3, 4)}"))
                        elif b == 2:
                            pe.wait_ge(taps_ready, 1)
                        pe.matmul(bank[:, 5 + b % 3, 0:n], chip.ones[:], sq[:, t0:t0 + n], start=True, stop=True
                                  ).then_inc(TS(f"sum{b}"), 1)

                if exists(f):
                    pe.wait_ge(w_loaded[s], (f - s) // 2 * 16 + 16)
                    project(range(4))
                if exists(f - 1) and normed(f - 1):
                    sums(range(3))
                if exists(f):
                    project((4,))
                if exists(f - 1) and normed(f - 1):
                    sums((3, 4))
            steps(pe, step)

        @block.scalar
        def _(act):
            def step(f, s):
                def copy(b):
                    if exists(f):
                        t0, n = BLOCKS[b]
                        act.wait_ge(T.sem, T.at(f, f"proj{b}"))
                        if b == 0 and not (num(f) and f < 2):
                            act.wait_ge(D.sem, D.at(f - 2, "conv"))
                        act.activation(raw[:, s, rcol[b]:rcol[b] + n], bank[:, b, 0:n], ACT.Copy
                                       ).then_inc(A(f"raw{b}"), 1)

                copy(0)
                copy(1)
                g, u = f - 1, 1 - s
                if exists(g):
                    act.wait_ge(D.sem, D.at(g, "conv"))
                    if not (num(g) and g < 2):
                        act.wait_ge(y_stored[u], (g - u) // 2 * 16)
                    act.activation(y[:, u, 0:CTX], acc[:, 0:CTX], ACT.Silu)
                    act.activation(y[:, u, CTX:TOK], acc[:, CTX + 2 * PAD:WIDE], ACT.Silu).then_inc(AS("silu"), 1)
                    if normed(g):
                        act.wait_ge(AS.sem, AS.at(g, "silu"))
                        if not (num(g) and g == 0):
                            act.wait_ge(TS.sem, TS.at(g - 1, "sum4"))
                        act.activation(sq[:], y[:, u, :], ACT.Square).then_inc(AQ("sq"), 1)
                copy(2)
                g = f - 2
                if exists(g) and normed(g):
                    act.wait_ge(DY.sem, DY.at(g, "inv"))
                    act.activation(inv[:], inv[:], ACT.Sqrt, scale=1.0 / P if not num(g) or g < HEADS else 1.0
                                   ).then_inc(AR("rinv"), 1)
                copy(3)
                copy(4)
            steps(act, step)

        @block.vector
        def _(dve):
            for s in range(2):
                dve.memset(raw[:, s, 0:PAD], 0.0)
                dve.memset(raw[:, s, PAD + CTX:3 * PAD + CTX], 0.0)
                dve.memset(raw[:, s, RAW - PAD:RAW], 0.0)
            dve.wait_ge(taps_turned, 1)
            dve.tensor_copy(taps[:].rearrange("p f t -> p t f"),
                            bank[:, 7, 0:NF * CONV_K].rearrange("p (t f) -> p t f", f=NF)).then_inc(taps_ready, 1)
            dve.wait_ge(taps_ready, 1)

            def step(f, s):
                g, u = f - 1, 1 - s
                if exists(g):
                    tap = taps[:, bass.ds(g, 1), :].rearrange("p a t -> p (a t)")
                    dve.wait_ge(A.sem, A.at(g, "raw4"))
                    if not (num(g) and g == 0):
                        dve.wait_ge(AS.sem, AS.at(g - 1, "silu"))
                    dve.tensor_scalar(acc[:, 0:WIDE], raw[:, u, 0:WIDE], tap[:, 0:1], None, ALU.mult
                                      ).then_inc(D("t0"), 1)
                    for t in range(1, CONV_K):
                        dve.wait_ge(D.sem, D.at(g, f"t{t - 1}"))
                        dve.scalar_tensor_tensor(out=acc[:, 0:WIDE], in0=raw[:, u, t:t + WIDE], scalar=tap[:, t:t + 1],
                                                 in1=acc[:, 0:WIDE], op0=ALU.mult, op1=ALU.add
                                                 ).then_inc(D(f"t{t}" if t < CONV_K - 1 else "conv"), 1)
                g = f - 2
                if exists(g) and normed(g):
                    dve.wait_ge(DS.sem, DS.at(g, "ss4"))
                    dve.reciprocal(inv[:], inv[:]).then_inc(DY("inv"), 1)
                    dve.wait_ge(AR.sem, AR.at(g, "rinv"))
                    dve.tensor_tensor(y[:, s, :], y[:, s, :], inv[:], ALU.mult).then_inc(DY("y"), 1)
                g = f - 1
                if exists(g) and normed(g):
                    if exists(f - 2):
                        dve.wait_ge(DY.sem, DY.at(f - 2, "y"))
                    for b, (t0, n) in enumerate(BLOCKS):
                        dve.wait_ge(TS.sem, TS.at(g, f"sum{b}"))
                        dve.tensor_scalar(inv[:, t0:t0 + n], bank[:, 5 + b % 3, 0:n], EPS1, None, ALU.add
                                          ).then_inc(DS(f"ss{b}"), 1)
            steps(dve, step)


def phase_decay_beta(chip, uT, w_in, a_log, dt_bias):
    nc, bank = chip.nc, chip.bank
    NH2 = 2 * HEADS
    with ExitStack() as st:
        sb = lambda n, s: st.enter_context(nc.sbuf_tensor("decay_beta_" + n, s, F32))
        sem = lambda n: st.enter_context(nc.semaphore("decay_beta_" + n))
        W = sb("Wab", [P, KT, 2 * NH2])
        z16 = sb("z16", [2 * NH2, TOK])
        z = sb("z", [P, NT, 2 * NH2])
        par = sb("par", [P, 2, NH2])
        w = [sb(f"w{n}", [P, NT, NH2]) for n in range(6)]
        loaded, act_done, pe_done, dve_done = sem("loaded"), sem("act_done"), sem("pe_done"), sem("dve_done")
        block = st.enter_context(nc.Block())

        @block.sync
        def _(sp):
            sp.dma_start(W[:], w_in[:, C_AB:C_AB + 2 * NH2].rearrange("(k p) n -> p k n", p=P)).then_inc(loaded, 16)
            for n, src in enumerate((dt_bias, a_log)):
                sp.dma_start(par[:, n, :], src.rearrange("l d h -> l (d h)").broadcast_to([P, NH2])
                             ).then_inc(loaded, 16)

        @block.tensor
        def _(pe):
            pe.wait_ge(loaded, 48)
            for b, (t0, n) in enumerate(BLOCKS):
                for k in range(KT):
                    mm = pe.matmul(bank[0:2 * NH2, b, 0:n], W[:, k, :], uT[:, k, t0:t0 + n], start=(k == 0),
                                   stop=(k == KT - 1))
                mm.then_inc(pe_done, 1)
            pe.wait_ge(act_done, 5)
            for t in range(NT):
                tr = pe.transpose(bank[:, 7, t * 2 * NH2:(t + 1) * 2 * NH2], z16[:, t * P:(t + 1) * P],
                                  chip.ident[0:2 * NH2, 0:2 * NH2])
            tr.then_inc(pe_done, 1)

        @block.scalar
        def _(act):
            for b, (t0, n) in enumerate(BLOCKS):
                act.wait_ge(pe_done, b + 1)
                act.activation(z16[:, t0:t0 + n], bank[0:2 * NH2, b, 0:n], ACT.Copy).then_inc(act_done, 1)
            act.wait_ge(dve_done, 1)
            act.activation(chip.beta_tok[:], z[:, :, NH2:], ACT.Sigmoid)
            act.wait_ge(dve_done, 2)
            act.activation(w[0][:], z[:, :, 0:NH2], ACT.Abs).then_inc(act_done, 1)
            act.wait_ge(act_done, 6)
            act.activation(w[1][:], w[0][:], ACT.Exp, scale=-1.0).then_inc(act_done, 1)
            act.activation(par[:, 1, :], par[:, 1, :], ACT.Exp).then_inc(act_done, 1)
            act.wait_ge(dve_done, 3)
            act.activation(w[0][:], w[2][:], ACT.Ln).then_inc(act_done, 1)

        @block.vector
        def _(dve):
            n = [0]

            def link(ins):
                n[0] += 1
                ins.then_inc(dve_done, 1)
                dve.wait_ge(dve_done, n[0])
            dve.wait_ge(pe_done, 6)
            link(dve.tensor_copy(z[:], bank[:, 7, 0:NT * 2 * NH2].rearrange("p (t c) -> p t c", t=NT)))
            link(dve.tensor_tensor(z[:, :, 0:NH2], z[:, :, 0:NH2], bcast(par[:, 0, :], 1, NT), ALU.add))
            dve.wait_ge(act_done, 8)
            link(dve.tensor_scalar(w[2][:], w[1][:], 1.0, None, ALU.add))
            link(dve.tensor_scalar(w[3][:], w[2][:], 1.0, None, ALU.subtract))
            link(dve.tensor_scalar(w[4][:], w[3][:], 0.0, None, ALU.is_equal))
            link(dve.tensor_tensor(w[3][:], w[3][:], w[4][:], ALU.add))
            link(dve.reciprocal(w[5][:], w[3][:]))
            dve.wait_ge(act_done, 9)
            link(dve.tensor_tensor(w[0][:], w[0][:], w[4][:], ALU.add))
            link(dve.tensor_tensor(w[0][:], w[0][:], w[5][:], ALU.mult))
            link(dve.tensor_tensor(w[0][:], w[0][:], w[1][:], ALU.mult))
            link(dve.tensor_scalar(w[1][:], z[:, :, 0:NH2], 0.0, None, ALU.max))
            link(dve.tensor_tensor(w[0][:], w[0][:], w[1][:], ALU.add))
            link(dve.tensor_scalar(w[0][:], w[0][:], -1.0, None, ALU.mult))
            link(dve.tensor_tensor(chip.decay_tok[:], w[0][:], bcast(par[:, 1, :], 1, NT), ALU.mult))


def phase_gla_inputs(chip, uT, w_in, sq_, sv, sk, sg):
    nc, bank = chip.nc, chip.bank
    NF = 4 * HEADS
    with ExitStack() as st:
        sb = lambda n, s: st.enter_context(nc.sbuf_tensor("gla_inputs_" + n, s, F32))
        sem = lambda n: st.enter_context(nc.semaphore("gla_inputs_" + n))
        W = sb("W", [P, 2, KT, P])
        reset = sb("reset", [P, NDIR, TOK])
        a = sb("a", [P, 2, TOK])
        b_ = sb("b_", [P, 2, TOK])
        lf = sb("lf", [P, TOK])
        w_loaded = [sem(f"w_loaded{s}") for s in range(2)]
        stored = [sem(f"stored{s}") for s in range(2)]
        reset_ready = sem("reset_ready")
        T = Stages(sem("pe_stage"), " ".join(f"proj{b}" for b in range(5)))
        D = Stages(sem("dve_stage"), "f k g")
        A = Stages(sem("act_stage"), " ".join(f"out{b}" for b in range(5)) + " ln")
        block = st.enter_context(nc.Block())
        groups = [(0, C_BQ), (HEADS // 2, C_BI), (HEADS, C_BF)]

        def to(dst, b):
            t0, n = BLOCKS[b]
            if b == 0:
                return dst[:, 0:CTX]
            r = GRID_W // 8 * 0 + (n // GRID_W)
            return dst[:, CTX:TOK].rearrange("p (w r) -> p r w", r=ROWS)[:, (b - 1) * r:b * r, :]

        def frm(b):
            n = BLOCKS[b][1]
            v = bank[:, b, 0:n]
            return v if b == 0 else v.rearrange("p (r w) -> p r w", w=GRID_W)

        @block.sync
        def _(sp):
            def body(i, s, col, first):
                f = 2 * i + s
                if not first:
                    sp.wait_ge(T.sem, T.at(f - 2, "proj4"))
                sp.dma_start(W[:, s], w_in[:, bass.ds(col + s * P, P)].rearrange("(k p) n -> p k n", p=P)
                             ).then_inc(w_loaded[s], 16)
            for n, (i0, col) in enumerate(groups):
                i1 = groups[n + 1][0] if n < 2 else NF // 2
                start = i0
                if n == 0:
                    for s in range(2):
                        body(0, s, col, True)
                    start = 1
                with sp.Fori(start, i1) as i:
                    for s in range(2):
                        body(i, s, col + (i - i0) * 2 * P, False)

        @block.gpsimd
        def _(sp):
            def row(dram, r):
                return dram[bass.ds(r, 1)].rearrange("a p t -> (a p) t")

            for dram, i0 in ((sq_, 0), (sv, HEADS // 2)):
                with sp.Fori(i0, i0 + HEADS // 2) as i:
                    for s in range(2):
                        sp.wait_ge(A.sem, A.at(2 * i + s, "ln"))
                        sp.dma_start(row(dram, 2 * (i - i0) + s), a[:, s, :]).then_inc(stored[s], 16)
            with sp.Fori(HEADS, NF // 2) as i:
                for s in range(2):
                    sp.wait_ge(D.sem, D.at(2 * (i - HEADS) + s, "g"))
                    sp.dma_start(row(sk, 2 * (i - HEADS) + s), b_[:, s, :]).then_inc(stored[s], 16)
                    sp.dma_start(row(sg, 2 * (i - HEADS) + s), a[:, s, :]).then_inc(stored[s], 16)
            for s in range(2):
                sp.wait_ge(stored[s], 16 * HEADS + 32 * HEADS)

        @block.tensor
        def _(pe):
            def body(i, s, first):
                f = 2 * i + s
                pe.wait_ge(w_loaded[s], i * 16 + 16)
                for b, (t0, n) in enumerate(BLOCKS):
                    if not first:
                        pe.wait_ge(A.sem, A.at(f - 1, f"out{b}"))
                    for k in range(KT):
                        mm = pe.matmul(bank[:, b, 0:n], W[:, s, k, :], uT[:, k, t0:t0 + n], start=(k == 0),
                                       stop=(k == KT - 1))
                    mm.then_inc(T(f"proj{b}"), 1)
            body(0, 0, True)
            body(0, 1, False)
            with pe.Fori(1, NF // 2) as i:
                body(i, 0, False)
                body(i, 1, False)

        @block.scalar
        def _(act):
            def plain(i, s, first, func):
                f = 2 * i + s
                if not first:
                    act.wait_ge(stored[s], i * 16)
                for b in range(5):
                    act.wait_ge(T.sem, T.at(f, f"proj{b}"))
                    act.activation(to(a[:, s, :], b), frm(b), func).then_inc(A(f"out{b}"), 1)
                act.wait_ge(A.sem, A.at(f, "out4"))
                act.activation(a[:, s, :], a[:, s, :], ACT.Copy, scale=P ** -0.5 if func == ACT.Silu else 1.0
                               ).then_inc(A("ln"), 1)

            def forget(i, s):
                f = 2 * i + s
                act.wait_ge(stored[s], (i - HEADS) * 32 + 16 * HEADS)
                for b in range(5):
                    act.wait_ge(T.sem, T.at(f, f"proj{b}"))
                    act.activation(to(a[:, s, :], b), frm(b), ACT.Sigmoid)
                    act.activation(to(b_[:, s, :], b), frm(b), ACT.Sigmoid, scale=-1.0).then_inc(A(f"out{b}"), 1)
                act.wait_ge(D.sem, D.at(2 * (i - HEADS) + s, "f"))
                act.activation(lf[:], a[:, s, :], ACT.Ln).then_inc(A("ln"), 1)
            for s in range(2):
                plain(0, s, True, ACT.Silu)
            with act.Fori(1, HEADS // 2) as i:
                for s in range(2):
                    plain(i, s, False, ACT.Silu)
            with act.Fori(HEADS // 2, HEADS) as i:
                for s in range(2):
                    plain(i, s, False, ACT.Copy)
            with act.Fori(HEADS, NF // 2) as i:
                for s in range(2):
                    forget(i, s)

        @block.vector
        def _(dve):
            dve.memset(reset[:], 1.0).then_inc(reset_ready, 1)
            dve.wait_ge(reset_ready, 1)
            for d in range(NDIR):
                v = reset[:, d, :].rearrange("p (t c) -> p t c", c=P)
                dve.memset(v[:, :, d * (P - 1):d * (P - 1) + 1], 0.0).then_inc(reset_ready, 1)
            dve.wait_ge(reset_ready, 3)

            def body(i, s, d):
                g = 2 * i + s
                dve.wait_ge(A.sem, A.at(g + 2 * HEADS, "out4"))
                one_less = chip.lbT[:, 1, bass.ds(g, 1)]
                dve.tensor_scalar(a[:, s, :], a[:, s, :], one_less, chip.lbT[:, 0, bass.ds(g, 1)], ALU.mult,
                                  ALU.add).then_inc(D("f"), 1)
                dve.tensor_scalar(b_[:, s, :], b_[:, s, :], one_less, None, ALU.mult).then_inc(D("k"), 1)
                dve.wait_ge(A.sem, A.at(g + 2 * HEADS, "ln"))
                step = 1 if d == 0 else -1
                dve.tensor_tensor_scan(a[:, s, ::step], reset[:, d, ::step], lf[:, ::step], 0.0, ALU.mult,
                                       ALU.add).then_inc(D("g"), 1)
            for d in range(NDIR):
                with dve.Fori(d * HEADS // 2, (d + 1) * HEADS // 2) as i:
                    for s in range(2):
                        body(i, s, d)


def phase_delta_rule(chip, sa, so_a):
    nc, bank = chip.nc, chip.bank
    LEVELS = range(1, 7)
    with ExitStack() as st:
        sb = lambda n, s: st.enter_context(nc.sbuf_tensor("delta_" + n, s, F32))
        sem = lambda n: st.enter_context(nc.semaphore("delta_" + n))
        mat = lambda n: [sb(f"{n}{d}", [P, HEADS, P]) for d in range(NDIR)]
        qkv = [[sb(f"qkv{d}{s}", [P, 3 * HEADS, P]) for s in range(2)] for d in range(NDIR)]
        kd, kbe, vb, Dm, A_, AT, T_, TT = (mat(n) for n in ("kd", "kbe", "vb", "Dm", "A", "AT", "T", "TT"))
        attnT, qg, vnew, S = (mat(n) for n in ("attnT", "qg", "vnew", "S"))
        WT = T_
        OWN = LEVELS[:4]
        M1 = [[sb(f"M1_{d}{lv}", [P, HEADS, P]) for lv in OWN] + [A_[d]] * (len(LEVELS) - len(OWN))
              for d in range(NDIR)]
        small = sb("small", [P, NDIR, 8, HEADS])
        g_, beta, Gc, gd, eGc, egd, beg, eGl = ([small[:, d, n, :] for d in range(NDIR)] for n in range(8))
        o = sb("o", [P, HEADS, SEQ])
        none = sb("none", [P, NDIR])
        loaded = [sem(f"loaded{s}") for s in range(2)]
        zeroed, o_stored = sem("zeroed"), sem("o_stored")
        both = lambda names: " ".join(f"{x}{d}" for x in names.split() for d in range(NDIR))
        D = Stages(sem("dve_stage"), both("gb Gc gd E0_ E kd kbe vb eGl qg Dm A attn Ti T0_ TTi TT0_ "
                                          + " ".join(f"M{n}_ T{n}_ TT{n}_" for n in LEVELS) + " S o"))
        A = Stages(sem("act_stage"), both("eGc egd E eGr AT attnT WT vnew"))
        T = Stages(sem("pe_stage"), both("tok sum gram flip " + " ".join(f"a{n}_ b{n}_" for n in LEVELS) + " w v os"))
        block = st.enter_context(nc.Block())
        last = (P - 1, 0)
        cum = (chip.up, chip.low)
        seen = (chip.low, chip.up)
        B = [[bank[:, 4 * d + n, :] for n in range(4)] for d in range(NDIR)]
        B3 = [[b.rearrange("p (h c) -> p h c", h=HEADS) for b in bs] for bs in B]

        def half(x, lv, side):
            return x.rearrange("p h (g two b) -> p h g two b", two=2, b=2 ** lv)[:, :, :, side, :]

        def turns(eng, body):
            for n in range(2):
                body(n, n, n)
            with eng.Fori(1, NT // 2) as i:
                for s in range(2):
                    body(2 * i + s, s, None)

        def tile(n, ctx, d):
            if d == 0:
                return n
            return 1 - n if ctx is not None else NT + 1 - n

        @block.sync
        def _(sp):
            def body(n, s, ctx):
                if ctx is None:
                    sp.wait_ge(D.sem, D.at(n - 2, "attn1"))
                for d in range(NDIR):
                    sp.dma_start(qkv[d][s][:], sa[:, :, bass.ds(tile(n, ctx, d) * P, P)].rearrange("a p t -> p a t")
                                 ).then_inc(loaded[s], 16)
            turns(sp, body)
            sp.wait_ge(D.sem, D.at(NT - 1, "o1"))
            sp.dma_start(so_a.rearrange("h p t -> p h t"), o[:]).then_inc(o_stored, 16)
            sp.wait_ge(o_stored, 16)

        @block.gpsimd
        def _(pool):
            nc.gpsimd.memset(o[:], 0.0)
            for d in range(NDIR):
                for m in [S[d]] + M1[d][:len(OWN)]:
                    z = nc.gpsimd.memset(m[:], 0.0)
            z.then_inc(zeroed, 1)

        @block.tensor
        def _(pe):
            pe.wait_ge(zeroed, 1)

            def heads(fn):
                for h in range(HEADS):
                    m = fn(h)
                return m

            def body(n, s, ctx):
                pe.wait_ge(loaded[s], (n // 2 if ctx is not None else (n - s) // 2) * 32 + 32)
                for d in range(NDIR):
                    x = qkv[d][s]
                    if ctx != 0:
                        pe.wait_ge(A.sem, A.at(n - 1, f"vnew{d}"))
                    heads(lambda h: pe.transpose(B3[d][0][:, h, :], x[:, HEADS + h, :], chip.ident[:]))
                    heads(lambda h: pe.transpose(B3[d][1][:, h, :], x[:, 2 * HEADS + h, :], chip.ident[:])
                          ).then_inc(T(f"tok{d}"), 1)
                for d in range(NDIR):
                    pe.wait_ge(D.sem, D.at(n, f"gb{d}"))
                    pe.matmul(B[d][2][:, 0:HEADS], cum[d][:], g_[d], start=True, stop=True)
                    heads(lambda h: pe.matmul(B3[d][3][:, h, :], g_[d][:, h:h + 1].broadcast_to([P, P]), cum[d][:],
                                              start=True, stop=True)).then_inc(T(f"sum{d}"), 1)
                for d in range(NDIR):
                    x = qkv[d][s]
                    pe.wait_ge(D.sem, D.at(n, f"Gc{d}"))
                    heads(lambda h: pe.matmul(B3[d][2][:, h, :], x[:, HEADS + h, :], x[:, HEADS + h, :], start=True,
                                              stop=True))
                    pe.wait_ge(D.sem, D.at(n, f"kbe{d}"))
                    heads(lambda h: pe.matmul(B3[d][0][:, h, :], x[:, h, :], x[:, HEADS + h, :], start=True,
                                              stop=True)).then_inc(T(f"gram{d}"), 1)
                for d in range(NDIR):
                    pe.wait_ge(D.sem, D.at(n, f"A{d}"))
                    heads(lambda h: pe.transpose(B3[d][1][:, h, :], A_[d][:, h, :], chip.ident[:]))
                    pe.wait_ge(A.sem, A.at(n, f"eGr{d}"))
                    pe.wait_ge(D.sem, D.at(n, f"attn{d}"))
                    heads(lambda h: pe.transpose(B3[d][3][:, h, :], Dm[d][:, h, :], chip.ident[:])
                          ).then_inc(T(f"flip{d}"), 1)
                for lv in LEVELS:
                    for d in range(NDIR):
                        if lv == 1:
                            pe.wait_ge(A.sem, A.at(n, f"AT{d}"))
                        pe.wait_ge(D.sem, D.at(n, f"TT{lv - 1}_{d}"))
                        heads(lambda h: pe.matmul(B3[d][0][:, h, :], AT[d][:, h, :], T_[d][:, h, :], start=True,
                                                  stop=True)).then_inc(T(f"a{lv}_{d}"), 1)
                    for d in range(NDIR):
                        m1 = M1[d][lv - 1]
                        pe.wait_ge(D.sem, D.at(n, f"M{lv}_{d}"))
                        if lv < 6:
                            heads(lambda h: pe.matmul(B3[d][1][:, h, :], TT[d][:, h, :], m1[:, h, :], start=True,
                                                      stop=True))
                        heads(lambda h: pe.matmul(B3[d][2][:, h, :], m1[:, h, :], TT[d][:, h, :], start=True,
                                                  stop=True)).then_inc(T(f"b{lv}_{d}"), 1)
                for d in range(NDIR):
                    pe.wait_ge(D.sem, D.at(n, f"TT6_{d}"))
                    heads(lambda h: pe.matmul(B3[d][1][:, h, :], kbe[d][:, h, :], TT[d][:, h, :], start=True,
                                              stop=True)).then_inc(T(f"w{d}"), 1)
                for d in range(NDIR):
                    pe.wait_ge(A.sem, A.at(n, f"WT{d}"))
                    if ctx != 0:
                        pe.wait_ge(D.sem, D.at(n - 1, f"S{d}"))
                    for h in range(HEADS):
                        pe.matmul(B3[d][0][:, h, :], TT[d][:, h, :], vb[d][:, h, :], start=True, stop=False)
                        m = pe.matmul(B3[d][0][:, h, :], WT[d][:, h, :], S[d][:, h, :], start=False, stop=True)
                    m.then_inc(T(f"v{d}"), 1)
                for d in range(NDIR):
                    pe.wait_ge(A.sem, A.at(n, f"attnT{d}"))
                    pe.wait_ge(A.sem, A.at(n, f"vnew{d}"))
                    for h in range(HEADS):
                        pe.matmul(B3[d][2][:, h, :], S[d][:, h, :], qg[d][:, h, :], start=True, stop=False)
                        pe.matmul(B3[d][2][:, h, :], vnew[d][:, h, :], attnT[d][:, h, :], start=False, stop=True)
                    heads(lambda h: pe.matmul(B3[d][3][:, h, :], kd[d][:, h, :], vnew[d][:, h, :], start=True,
                                              stop=True)).then_inc(T(f"os{d}"), 1)
            turns(pe, body)

        @block.scalar
        def _(act):
            def body(n, s, ctx):
                for d in range(NDIR):
                    act.wait_ge(D.sem, D.at(n, f"Gc{d}"))
                    act.activation(eGc[d], Gc[d], ACT.Exp).then_inc(A(f"eGc{d}"), 1)
                for d in range(NDIR):
                    act.wait_ge(D.sem, D.at(n, f"gd{d}"))
                    act.activation(egd[d], gd[d], ACT.Exp).then_inc(A(f"egd{d}"), 1)
                for d in range(NDIR):
                    act.wait_ge(D.sem, D.at(n, f"E{d}"))
                    act.activation(Dm[d][:], Dm[d][:], ACT.Exp).then_inc(A(f"E{d}"), 1)
                for d in range(NDIR):
                    act.activation(qg[d][:], B3[d][3][:], ACT.Exp).then_inc(A(f"eGr{d}"), 1)
                for d in range(NDIR):
                    act.wait_ge(T.sem, T.at(n, f"flip{d}"))
                    act.activation(AT[d][:], B3[d][1][:], ACT.Copy).then_inc(A(f"AT{d}"), 1)
                for d in range(NDIR):
                    act.activation(attnT[d][:], B3[d][3][:], ACT.Copy).then_inc(A(f"attnT{d}"), 1)
                for d in range(NDIR):
                    act.wait_ge(T.sem, T.at(n, f"w{d}"))
                    act.activation(WT[d][:], B3[d][1][:], ACT.Copy, scale=-1.0).then_inc(A(f"WT{d}"), 1)
                for d in range(NDIR):
                    act.wait_ge(T.sem, T.at(n, f"v{d}"))
                    act.activation(vnew[d][:], B3[d][0][:], ACT.Copy).then_inc(A(f"vnew{d}"), 1)
            turns(act, body)

        @block.vector
        def _(dve):
            dve.wait_ge(zeroed, 1)
            per_token = lambda col: bcast(col, 2, P)
            per_pair = lambda m: bcast(m, 1, HEADS)

            def body(n, s, ctx):
                for d in range(NDIR):
                    t = tile(n, ctx, d)
                    row = lambda src: src[:, bass.ds(t, 1), d * HEADS:(d + 1) * HEADS].rearrange("p a h -> p (a h)")
                    dve.tensor_copy(beta[d], row(chip.beta_tok))
                    dve.tensor_copy(g_[d], row(chip.decay_tok)).then_inc(D(f"gb{d}"), 1)
                for d in range(NDIR):
                    dve.wait_ge(T.sem, T.at(n, f"sum{d}"))
                    dve.tensor_copy(Gc[d], B[d][2][:, 0:HEADS]).then_inc(D(f"Gc{d}"), 1)
                for d in range(NDIR):
                    dve.wait_ge(D.sem, D.at(n, f"Gc{d}"))
                    dve.tensor_tensor(gd[d], B3[d][3][:, :, last[d]], Gc[d], ALU.subtract).then_inc(D(f"gd{d}"), 1)
                for d in range(NDIR):
                    dve.scalar_tensor_tensor(out=Dm[d][:], in0=B3[d][3][:], scalar=-1.0, in1=per_token(Gc[d]),
                                             op0=ALU.mult, op1=ALU.add).then_inc(D(f"E0_{d}"), 1)
                for d in range(NDIR):
                    dve.wait_ge(D.sem, D.at(n, f"E0_{d}"))
                    dve.tensor_scalar(Dm[d][:], Dm[d][:], 0.0, None, ALU.min).then_inc(D(f"E{d}"), 1)
                for d in range(NDIR):
                    dve.wait_ge(A.sem, A.at(n, f"egd{d}"))
                    dve.tensor_tensor(beg[d], eGc[d], beta[d], ALU.mult)
                    dve.tensor_tensor(kd[d][:], B3[d][0][:], per_token(egd[d]), ALU.mult).then_inc(D(f"kd{d}"), 1)
                for d in range(NDIR):
                    dve.wait_ge(D.sem, D.at(n, f"kd{d}"))
                    dve.tensor_tensor(kbe[d][:], B3[d][0][:], per_token(beg[d]), ALU.mult).then_inc(D(f"kbe{d}"), 1)
                for d in range(NDIR):
                    dve.tensor_tensor(vb[d][:], B3[d][1][:], per_token(beta[d]), ALU.mult).then_inc(D(f"vb{d}"), 1)
                for d in range(NDIR):
                    dve.wait_ge(A.sem, A.at(n, f"eGr{d}"))
                    dve.tensor_copy(eGl[d], qg[d][:, :, last[d]]).then_inc(D(f"eGl{d}"), 1)
                for d in range(NDIR):
                    dve.wait_ge(D.sem, D.at(n, f"eGl{d}"))
                    dve.tensor_tensor(qg[d][:], qg[d][:], qkv[d][s][:, 0:HEADS, :], ALU.mult).then_inc(D(f"qg{d}"), 1)
                for d in range(NDIR):
                    dve.tensor_tensor(Dm[d][:], Dm[d][:], per_pair(seen[d][:]), ALU.mult).then_inc(D(f"Dm{d}"), 1)
                for d in range(NDIR):
                    dve.wait_ge(T.sem, T.at(n, f"gram{d}"))
                    dve.wait_ge(D.sem, D.at(n, f"Dm{d}"))
                    for h in range(HEADS):
                        m = dve.scalar_tensor_tensor(out=A_[d][:, h, :], in0=B3[d][2][:, h, :],
                                                     scalar=beta[d][:, h:h + 1], in1=Dm[d][:, h, :], op0=ALU.mult,
                                                     op1=ALU.mult)
                    m.then_inc(D(f"A{d}"), 1)
                for d in range(NDIR):
                    dve.wait_ge(D.sem, D.at(n, f"A{d}"))
                    dve.tensor_tensor(Dm[d][:], B3[d][0][:], Dm[d][:], ALU.mult).then_inc(D(f"attn{d}"), 1)
                for d in range(NDIR):
                    dve.scalar_tensor_tensor(out=T_[d][:], in0=A_[d][:], scalar=-1.0,
                                             in1=per_pair(chip.off[:, d, 0, :]), op0=ALU.mult, op1=ALU.mult
                                             ).then_inc(D(f"Ti{d}"), 1)
                for d in range(NDIR):
                    dve.wait_ge(D.sem, D.at(n, f"Ti{d}"))
                    dve.tensor_tensor(T_[d][:], T_[d][:], per_pair(chip.ident[:]), ALU.add).then_inc(D(f"T0_{d}"), 1)
                for d in range(NDIR):
                    dve.wait_ge(A.sem, A.at(n, f"AT{d}"))
                    dve.scalar_tensor_tensor(out=TT[d][:], in0=AT[d][:], scalar=-1.0,
                                             in1=per_pair(chip.off[:, 1 - d, 0, :]), op0=ALU.mult, op1=ALU.mult
                                             ).then_inc(D(f"TTi{d}"), 1)
                for d in range(NDIR):
                    dve.wait_ge(D.sem, D.at(n, f"TTi{d}"))
                    dve.tensor_tensor(TT[d][:], TT[d][:], per_pair(chip.ident[:]), ALU.add).then_inc(D(f"TT0_{d}"), 1)
                for lv in LEVELS:
                    for d in range(NDIR):
                        dve.wait_ge(T.sem, T.at(n, f"a{lv}_{d}"))
                        if lv in OWN:
                            off = half(chip.off[:, d, lv:lv + 1, :], lv, d)
                            off = off.broadcast_to([P, HEADS, *off.shape[2:]])
                            dve.tensor_tensor(half(M1[d][lv - 1], lv, d), half(B3[d][0], lv, d), off, ALU.mult
                                              ).then_inc(D(f"M{lv}_{d}"), 1)
                        else:
                            dve.tensor_tensor(M1[d][lv - 1][:], B3[d][0][:], per_pair(chip.off[:, d, lv, :]), ALU.mult
                                              ).then_inc(D(f"M{lv}_{d}"), 1)
                    for d in range(NDIR):
                        dve.wait_ge(T.sem, T.at(n, f"b{lv}_{d}"))
                        if lv < 6:
                            t = half(T_[d], lv, d)
                            dve.tensor_tensor(t, t, half(B3[d][1], lv, d), ALU.subtract
                                              ).then_inc(D(f"T{lv}_{d}"), 1)
                        else:
                            dve.memset(none[:, d:d + 1], 0.0).then_inc(D(f"T{lv}_{d}"), 1)
                    for d in range(NDIR):
                        t = half(TT[d], lv, 1 - d)
                        dve.tensor_tensor(t, t, half(B3[d][2], lv, 1 - d), ALU.subtract
                                          ).then_inc(D(f"TT{lv}_{d}"), 1)
                for d in range(NDIR):
                    dve.wait_ge(T.sem, T.at(n, f"os{d}"))
                    for h in range(HEADS):
                        m = dve.scalar_tensor_tensor(out=S[d][:, h, :], in0=S[d][:, h, :], scalar=eGl[d][:, h:h + 1],
                                                     in1=B3[d][3][:, h, :], op0=ALU.mult, op1=ALU.add)
                    m.then_inc(D(f"S{d}"), 1)
                for d in range(NDIR):
                    if ctx is not None:
                        dve.memset(none[:, d:d + 1], 0.0).then_inc(D(f"o{d}"), 1)
                        continue
                    t = o[:, :, bass.ds((tile(n, ctx, d) - CTX // P) * P, P)]
                    dve.tensor_tensor(t, t, B3[d][2][:], ALU.add).then_inc(D(f"o{d}"), 1)
            turns(dve, body)


def phase_gla(chip, sq_, sv, sk, sg, so_b):
    nc, bank = chip.nc, chip.bank
    HALF = (64, 32, 16)
    with ExitStack() as st:
        sb = lambda n, s: st.enter_context(nc.sbuf_tensor("gla_" + n, s, F32))
        sem = lambda n: st.enter_context(nc.semaphore("gla_" + n))
        mat = lambda n: [sb(f"{n}{d}", [P, HEADS, P]) for d in range(NDIR)]
        qvkg = [[sb(f"qvkg{d}{s}", [P, 4, HEADS, P]) for s in range(2)] for d in range(NDIR)]
        qg, kdT, dq, dk, v, kd, attnT, S = (mat(n) for n in ("qg", "kdT", "dq", "dk", "v", "kd", "attnT", "S"))
        X = [mat(f"X{L}_") for L in HALF]
        eGl = [sb(f"eGl{d}", [P, HEADS]) for d in range(NDIR)]
        o = sb("o", [P, HEADS, SEQ])
        none = sb("none", [P, NDIR])
        loaded = [sem(f"loaded{s}") for s in range(2)]
        zeroed, o_stored = sem("zeroed"), sem("o_stored")
        both = lambda names: " ".join(f"{x}{d}" for x in names.split() for d in range(NDIR))
        D = Stages(sem("dve_stage"), both("ekd ex0_ ex1_ ex2_ edq") + " "
                   + both("qg kd x0_ x1_ x2_ dq dk diag lv0_ lv1_ lv2_ S o"))
        A = Stages(sem("act_stage"), both("qg kd x0_ x1_ x2_ dk dq v kdtok"))
        T = Stages(sem("pe_stage"), both("v kd lv diag os"))
        block = st.enter_context(nc.Block())
        last = (P - 1, 0)
        B = [[bank[:, 4 * d + n, :] for n in range(4)] for d in range(NDIR)]
        B3 = [[b.rearrange("p (h c) -> p h c", h=HEADS) for b in bs] for bs in B]

        def turns(eng, body):
            for n in range(2):
                body(n, n, n)
            with eng.Fori(1, NT // 2) as i:
                for s in range(2):
                    body(2 * i + s, s, None)

        def tile(n, ctx, d):
            if d == 0:
                return n
            return 1 - n if ctx is not None else NT + 1 - n

        def halves(m, L):
            return m.rearrange("p h c -> p (h c)").rearrange("p (b e l) -> p b e l", e=2, l=L)

        def where(d, n):
            L = HALF[n]
            b = B[d][3][:, 256 * n:256 * n + 256] if n < 2 else B[d][0][:, 0:256]
            return b.rearrange("p (h b l) -> p h b l", h=HEADS, l=L)

        @block.sync
        def _(sp):
            def body(n, s, ctx):
                if ctx is None:
                    sp.wait_ge(D.sem, D.at(n - 2, "dk1"))
                    sp.wait_ge(T.sem, T.at(n - 2, "v1"))
                for d in range(NDIR):
                    hs = slice(d * HEADS, (d + 1) * HEADS)
                    for m, src in enumerate((sq_, sv, sk[hs], sg[hs])):
                        sp.dma_start(qvkg[d][s][:, m], src[:, :, bass.ds(tile(n, ctx, d) * P, P)].rearrange(
                            "h p t -> p h t")).then_inc(loaded[s], 16)
            turns(sp, body)
            sp.wait_ge(D.sem, D.at(NT - 1, "o1"))
            sp.dma_start(so_b.rearrange("h p t -> p h t"), o[:]).then_inc(o_stored, 16)
            sp.wait_ge(o_stored, 16)

        @block.gpsimd
        def _(pool):
            nc.gpsimd.memset(o[:], 0.0)
            for d in range(NDIR):
                z = nc.gpsimd.memset(S[d][:], 0.0)
            z.then_inc(zeroed, 1)

        def land(eng, n, s, ctx):
            eng.wait_ge(loaded[s], (n // 2 if ctx is not None else (n - s) // 2) * 128 + 128)

        @block.tensor
        def _(pe):
            pe.wait_ge(zeroed, 1)

            def body(n, s, ctx):
                land(pe, n, s, ctx)
                for d in range(NDIR):
                    if ctx != 0:
                        pe.wait_ge(D.sem, D.at(n - 1, f"o{d}"))
                    for h in range(HEADS):
                        m = pe.transpose(B3[d][0][:, h, :], qvkg[d][s][:, 1, h, :], chip.ident[:])
                    m.then_inc(T(f"v{d}"), 1)
                for d in range(NDIR):
                    pe.wait_ge(D.sem, D.at(n, f"kd{d}"))
                    for h in range(HEADS):
                        m = pe.transpose(B3[d][1][:, h, :], kdT[d][:, h, :], chip.ident[:])
                    m.then_inc(T(f"kd{d}"), 1)
                for d in range(NDIR):
                    pe.wait_ge(A.sem, A.at(n, f"v{d}"))
                    for lv, L in enumerate(HALF):
                        pe.wait_ge(D.sem, D.at(n, f"x{lv}_{d}"))
                        xs = X[lv][d][:].rearrange("p h (b e l) -> p h b e l", e=2, l=L)
                        for h in range(HEADS):
                            m = pe.matmul(where(d, lv)[:, h], X[lv][d][:, h, :], xs[:, h, :, 1 - d, :], start=True,
                                          stop=True)
                    m.then_inc(T(f"lv{d}"), 1)
                for d in range(NDIR):
                    pe.wait_ge(D.sem, D.at(n, f"dk{d}"))
                    for h in range(HEADS):
                        m = pe.matmul(B3[d][2][:, h, :], dk[d][:, h, :], dq[d][:, h, :], start=True, stop=True)
                    m.then_inc(T(f"diag{d}"), 1)
                for d in range(NDIR):
                    pe.wait_ge(A.sem, A.at(n, f"kdtok{d}"))
                    pe.wait_ge(D.sem, D.at(n, f"lv2_{d}"))
                    for h in range(HEADS):
                        pe.matmul(B3[d][1][:, h, :], S[d][:, h, :], qg[d][:, h, :], start=True, stop=False)
                        pe.matmul(B3[d][1][:, h, :], v[d][:, h, :], attnT[d][:, h, :], start=False, stop=True)
                    for h in range(HEADS):
                        m = pe.matmul(B3[d][2][:, h, :], kd[d][:, h, :], v[d][:, h, :], start=True, stop=True)
                    m.then_inc(T(f"os{d}"), 1)
            turns(pe, body)

        @block.scalar
        def _(act):
            def body(n, s, ctx):
                land(act, n, s, ctx)
                for d in range(NDIR):
                    if ctx != 0:
                        act.wait_ge(T.sem, T.at(n - 1, f"os{d}"))
                    act.activation(qg[d][:], qvkg[d][s][:, 3], ACT.Exp).then_inc(A(f"qg{d}"), 1)
                for d in range(NDIR):
                    act.wait_ge(D.sem, D.at(n, f"ekd{d}"))
                    act.activation(kdT[d][:], kdT[d][:], ACT.Exp).then_inc(A(f"kd{d}"), 1)
                for lv in range(3):
                    for d in range(NDIR):
                        act.wait_ge(D.sem, D.at(n, f"ex{lv}_{d}"))
                        act.activation(X[lv][d][:], X[lv][d][:], ACT.Exp).then_inc(A(f"x{lv}_{d}"), 1)
                for d in range(NDIR):
                    act.wait_ge(D.sem, D.at(n, f"edq{d}"))
                    act.activation(dk[d][:], dq[d][:], ACT.Exp, scale=-1.0).then_inc(A(f"dk{d}"), 1)
                for d in range(NDIR):
                    act.wait_ge(A.sem, A.at(n, f"dk{d}"))
                    act.activation(dq[d][:], dq[d][:], ACT.Exp).then_inc(A(f"dq{d}"), 1)
                for d in range(NDIR):
                    act.wait_ge(T.sem, T.at(n, f"v{d}"))
                    act.activation(v[d][:], B3[d][0][:], ACT.Copy).then_inc(A(f"v{d}"), 1)
                for d in range(NDIR):
                    act.wait_ge(T.sem, T.at(n, f"kd{d}"))
                    act.activation(kd[d][:], B3[d][1][:], ACT.Copy).then_inc(A(f"kdtok{d}"), 1)
            turns(act, body)

        @block.vector
        def _(dve):
            dve.wait_ge(zeroed, 1)

            def body(n, s, ctx):
                land(dve, n, s, ctx)
                for d in range(NDIR):
                    G = qvkg[d][s][:, 3]
                    dve.tensor_tensor(kdT[d][:], G[:, :, last[d]:last[d] + 1].broadcast_to([P, HEADS, P]), G,
                                      ALU.subtract).then_inc(D(f"ekd{d}"), 1)
                for lv, L in enumerate(HALF):
                    for d in range(NDIR):
                        g, x = halves(qvkg[d][s][:, 3], L), halves(X[lv][d][:], L)
                        nb = HEADS * P // (2 * L)
                        ref = (g[:, :, 0, L - 1:L] if d == 0 else g[:, :, 1, 0:1]).broadcast_to([P, nb, L])
                        ask, key = 1 - d, d
                        dve.tensor_tensor(x[:, :, ask, :], g[:, :, ask, :], ref, ALU.subtract)
                        dve.tensor_tensor(x[:, :, key, :], ref, g[:, :, key, :], ALU.subtract
                                          ).then_inc(D(f"ex{lv}_{d}"), 1)
                for d in range(NDIR):
                    g = qvkg[d][s][:, 3].rearrange("p h c -> p (h c)").rearrange("p (b l) -> p b l", l=16)
                    x = dq[d][:].rearrange("p h c -> p (h c)").rearrange("p (b l) -> p b l", l=16)
                    e = 15 * d
                    dve.tensor_tensor(x, g, g[:, :, e:e + 1].broadcast_to([P, HEADS * 8, 16]), ALU.subtract
                                      ).then_inc(D(f"edq{d}"), 1)
                for d in range(NDIR):
                    dve.wait_ge(A.sem, A.at(n, f"qg{d}"))
                    if ctx != 0:
                        dve.wait_ge(D.sem, D.at(n - 1, f"S{d}"))
                    dve.tensor_copy(eGl[d][:], qg[d][:, :, last[d]]).then_inc(D(f"qg{d}"), 1)
                for d in range(NDIR):
                    dve.wait_ge(A.sem, A.at(n, f"kd{d}"))
                    dve.wait_ge(D.sem, D.at(n, f"qg{d}"))
                    dve.tensor_tensor(qg[d][:], qg[d][:], qvkg[d][s][:, 0], ALU.mult)
                    dve.tensor_tensor(kdT[d][:], kdT[d][:], qvkg[d][s][:, 2], ALU.mult).then_inc(D(f"kd{d}"), 1)
                for lv, L in enumerate(HALF):
                    for d in range(NDIR):
                        dve.wait_ge(A.sem, A.at(n, f"x{lv}_{d}"))
                        x = halves(X[lv][d][:], L)
                        dve.tensor_tensor(x[:, :, 1 - d, :], x[:, :, 1 - d, :],
                                          halves(qvkg[d][s][:, 0], L)[:, :, 1 - d, :], ALU.mult)
                        dve.tensor_tensor(x[:, :, d, :], x[:, :, d, :], halves(qvkg[d][s][:, 2], L)[:, :, d, :],
                                          ALU.mult).then_inc(D(f"x{lv}_{d}"), 1)
                for d in range(NDIR):
                    dve.wait_ge(A.sem, A.at(n, f"dq{d}"))
                    dve.tensor_tensor(dq[d][:], dq[d][:], qvkg[d][s][:, 0], ALU.mult).then_inc(D(f"dq{d}"), 1)
                for d in range(NDIR):
                    dve.tensor_tensor(dk[d][:], dk[d][:], qvkg[d][s][:, 2], ALU.mult).then_inc(D(f"dk{d}"), 1)
                for d in range(NDIR):
                    dve.wait_ge(T.sem, T.at(n, f"diag{d}"))
                    dve.tensor_tensor(attnT[d][:], B3[d][2][:], bcast(chip.diag16[:, d, :], 1, HEADS), ALU.mult
                                      ).then_inc(D(f"diag{d}"), 1)
                for lv, L in enumerate(HALF):
                    for d in range(NDIR):
                        ask = 1 - d
                        dve.wait_ge(D.sem, D.at(n, f"lv{lv - 1}_{d}" if lv else f"diag{d}"))
                        dve.nop(nofuse=True)
                        mask = chip.off[:, 1 - d, 6 - lv, :].bitcast(U32).rearrange("p (b e l) -> p b e l", e=2, l=L)
                        out = attnT[d][:].rearrange("p h (b e l) -> p h b e l", e=2, l=L)[:, :, :, ask, :]
                        dve.copy_predicated(out, bcast(mask[:, :, ask, :], 1, HEADS), where(d, lv)
                                            ).then_inc(D(f"lv{lv}_{d}"), 1)
                for d in range(NDIR):
                    dve.wait_ge(T.sem, T.at(n, f"os{d}"))
                    for h in range(HEADS):
                        m = dve.scalar_tensor_tensor(out=S[d][:, h, :], in0=S[d][:, h, :], scalar=eGl[d][:, h:h + 1],
                                                     in1=B3[d][2][:, h, :], op0=ALU.mult, op1=ALU.add)
                    m.then_inc(D(f"S{d}"), 1)
                for d in range(NDIR):
                    if ctx is not None:
                        dve.memset(none[:, d:d + 1], 0.0).then_inc(D(f"o{d}"), 1)
                        continue
                    t = o[:, :, bass.ds((tile(n, ctx, d) - CTX // P) * P, P)]
                    dve.tensor_tensor(t, t, B3[d][1][:], ALU.add).then_inc(D(f"o{d}"), 1)
            turns(dve, body)


def phase_branch_gates(chip, uT, w_in, so_a, so_b, a_norm_g, b_norm_g, yT):
    nc, bank = chip.nc, chip.bank
    NF = 2 * HEADS
    NB = LATENT_BLOCKS
    with ExitStack() as st:
        sb = lambda n, s: st.enter_context(nc.sbuf_tensor("gates_" + n, s, F32))
        sem = lambda n: st.enter_context(nc.semaphore("gates_" + n))
        W = sb("W", [P, 2, KT, P])
        o = sb("o", [P, 2, SEQ])
        sq = sb("sq", [P, SEQ])
        inv = sb("inv", [P, SEQ])
        silu = sb("silu", [P, SEQ])
        gain = sb("gain", [P, 2])
        w_loaded = [sem(f"w_loaded{s}") for s in range(2)]
        o_loaded = [sem(f"o_loaded{s}") for s in range(2)]
        gain_loaded = sem("gain_loaded")
        T = Stages(sem("pe_stage"), " ".join([f"proj{b}" for b in range(NB)] + [f"sum{b}" for b in range(NB)]))
        A = Stages(sem("act_stage"), "sq " + " ".join(f"silu{b}" for b in range(NB)) + " rinv")
        D = Stages(sem("dve_stage"), " ".join(f"ss{b}" for b in range(NB)) + " inv o y")
        block = st.enter_context(nc.Block())

        def turns(eng, body):
            body(0, 0, 0)
            body(0, 1, 0)
            for br in range(2):
                with eng.Fori(max(1, br * HEADS // 2), (br + 1) * HEADS // 2) as i:
                    for s in range(2):
                        body(i, s, br)

        def first(i):
            return isinstance(i, int) and i == 0

        @block.sync
        def _(sp):
            for br, g in enumerate((a_norm_g, b_norm_g)):
                sp.dma_start(gain[:, br:br + 1], g[0].rearrange("(p a) -> p a", a=1)).then_inc(gain_loaded, 16)

            def body(i, s, br):
                f = 2 * i + s
                if not first(i):
                    sp.wait_ge(T.sem, T.at(f - 2, f"proj{NB - 1}"))
                base = (C_AGATE, C_BGATE - HD)[br]
                sp.dma_start(W[:, s], w_in[:, bass.ds(f * P + base, P)].rearrange("(k p) n -> p k n", p=P)
                             ).then_inc(w_loaded[s], 16)
                if not first(i):
                    sp.wait_ge(D.sem, D.at(f - 2, "y"))
                sp.dma_start(o[:, s, :], (so_a, so_b)[br][bass.ds(f - br * HEADS, 1)].rearrange("a p t -> (a p) t")
                             ).then_inc(o_loaded[s], 16)
            turns(sp, body)

        @block.tensor
        def _(pe):
            def body(i, s, br):
                f = 2 * i + s
                pe.wait_ge(w_loaded[s], i * 16 + 16)
                for b in range(NB):
                    if not (first(i) and s == 0):
                        pe.wait_ge(A.sem, A.at(f - 1, f"silu{b}"))
                    for k in range(KT):
                        mm = pe.matmul(bank[:, b, :], W[:, s, k, :], uT[:, k, CTX + b * BANK:CTX + (b + 1) * BANK],
                                       start=(k == 0), stop=(k == KT - 1))
                    mm.then_inc(T(f"proj{b}"), 1)
                pe.wait_ge(A.sem, A.at(f, "sq"))
                for b in range(NB):
                    if not (first(i) and s == 0):
                        pe.wait_ge(D.sem, D.at(f - 1, f"ss{b}"))
                    pe.matmul(bank[:, 4 + b, :], chip.ones[:], sq[:, b * BANK:(b + 1) * BANK], start=True, stop=True
                              ).then_inc(T(f"sum{b}"), 1)
            turns(pe, body)

        @block.scalar
        def _(act):
            def body(i, s, br):
                f = 2 * i + s
                act.wait_ge(o_loaded[s], i * 16 + 16)
                if not (first(i) and s == 0):
                    act.wait_ge(T.sem, T.at(f - 1, f"sum{NB - 1}"))
                act.activation(sq[:], o[:, s, :], ACT.Square).then_inc(A("sq"), 1)
                for b in range(NB):
                    act.wait_ge(T.sem, T.at(f, f"proj{b}"))
                    if not (first(i) and s == 0):
                        act.wait_ge(D.sem, D.at(f - 1, "y"))
                    act.activation(silu[:, b * BANK:(b + 1) * BANK], bank[:, b, :], ACT.Silu).then_inc(A(f"silu{b}"), 1)
                act.wait_ge(D.sem, D.at(f, "inv"))
                act.activation(inv[:], inv[:], ACT.Sqrt).then_inc(A("rinv"), 1)
            turns(act, body)

        @block.vector
        def _(dve):
            dve.wait_ge(gain_loaded, 32)

            def body(i, s, br):
                f = 2 * i + s
                if not (first(i) and s == 0):
                    dve.wait_ge(D.sem, D.at(f - 1, "o"))
                for b in range(NB):
                    dve.wait_ge(T.sem, T.at(f, f"sum{b}"))
                    dve.tensor_scalar(inv[:, b * BANK:(b + 1) * BANK], bank[:, 4 + b, :], 1.0 / P, EPS1, ALU.mult,
                                      ALU.add).then_inc(D(f"ss{b}"), 1)
                dve.wait_ge(D.sem, D.at(f, f"ss{NB - 1}"))
                dve.reciprocal(inv[:], inv[:]).then_inc(D("inv"), 1)
                dve.wait_ge(A.sem, A.at(f, "rinv"))
                dve.scalar_tensor_tensor(out=o[:, s, :], in0=o[:, s, :], scalar=gain[:, br:br + 1], in1=inv[:],
                                         op0=ALU.mult, op1=ALU.mult).then_inc(D("o"), 1)
                dve.wait_ge(D.sem, D.at(f, "o"))
                grid = lambda v: v.rearrange("p (r w) -> p r w", w=GRID_W)
                by_row = grid(o[:, s, :]) if br == 0 else o[:, s, :].rearrange("p (w r) -> p r w", r=ROWS)
                dve.tensor_tensor(grid(yT[:, bass.ds(f, 1), :].rearrange("p a t -> p (a t)")), by_row, grid(silu[:]),
                                  ALU.mult).then_inc(D("y"), 1)
            turns(dve, body)


def phase_merge(chip, uT, w_in, yT, w_a_out, w_b_out, smT):
    nc, bank = chip.nc, chip.bank
    NB = LATENT_BLOCKS
    with ExitStack() as st:
        sb = lambda n, s: st.enter_context(nc.sbuf_tensor("merge_" + n, s, F32))
        sem = lambda n: st.enter_context(nc.semaphore("merge_" + n))
        WG = sb("WG", [P, 2, 2, KT, P])
        WY = sb("WY", [P, 2, 2, HEADS, P])
        sig = sb("sig", [P, 2, 2, BANK])
        row = sb("row", [P, 2, SEQ])
        loaded = [sem(f"loaded{s}") for s in range(2)]
        stored = [sem(f"stored{s}") for s in range(2)]
        T = Stages(sem("pe_stage"), " ".join(f"gate{b} y{b}" for b in range(NB)))
        A = Stages(sem("act_stage"), " ".join(f"sig{b}" for b in range(NB)))
        D = Stages(sem("dve_stage"), " ".join(f"a{b} b{b} sum{b}" for b in range(NB)))
        block = st.enter_context(nc.Block())

        def turns(eng, body):
            body(0, 0)
            body(0, 1)
            with eng.Fori(1, KT // 2) as i:
                for s in range(2):
                    body(i, s)

        first = lambda i: isinstance(i, int) and i == 0

        @block.sync
        def _(sp):
            def body(i, s):
                j = 2 * i + s
                if not first(i):
                    sp.wait_ge(T.sem, T.at(j - 2, f"y{NB - 1}"))
                for br in range(2):
                    sp.dma_start(WG[:, s, br], w_in[:, bass.ds(j * P + C_MERGE + br * DM, P)].rearrange(
                        "(k p) n -> p k n", p=P)).then_inc(loaded[s], 16)
                    sp.dma_start(WY[:, s, br], (w_a_out, w_b_out)[br][:, bass.ds(j * P, P)].rearrange(
                        "(k p) n -> p k n", p=P)).then_inc(loaded[s], 16)
            turns(sp, body)

        @block.gpsimd
        def _(pool):
            def body(i, s):
                j = 2 * i + s
                pool.wait_ge(D.sem, D.at(j, f"sum{NB - 1}"))
                pool.dma_start(smT[bass.ds(j, 1)].rearrange("a p t -> (a p) t"), row[:, s, :]).then_inc(stored[s], 16)
            turns(pool, body)
            for s in range(2):
                pool.wait_ge(stored[s], 16 * KT // 2)

        @block.tensor
        def _(pe):
            def body(i, s):
                j = 2 * i + s
                pe.wait_ge(loaded[s], i * 64 + 64)
                for b in range(NB):
                    q = 4 * (b % 2)
                    if b >= 2:
                        pe.wait_ge(D.sem, D.at(j, f"sum{b - 2}"))
                    elif not (first(i) and s == 0):
                        pe.wait_ge(D.sem, D.at(j - 1, f"sum{b + 2}"))
                    t = slice(CTX + b * BANK, CTX + (b + 1) * BANK)
                    for br in range(2):
                        for k in range(KT):
                            mm = pe.matmul(bank[:, q + br, :], WG[:, s, br, k, :], uT[:, k, t], start=(k == 0),
                                           stop=(k == KT - 1))
                    mm.then_inc(T(f"gate{b}"), 1)
                    for br in range(2):
                        for k in range(HEADS):
                            mm = pe.matmul(bank[:, q + 2 + br, :], WY[:, s, br, k, :],
                                           yT[:, br * HEADS + k, b * BANK:(b + 1) * BANK], start=(k == 0),
                                           stop=(k == HEADS - 1))
                    mm.then_inc(T(f"y{b}"), 1)
            turns(pe, body)

        @block.scalar
        def _(act):
            def body(i, s):
                j = 2 * i + s
                for b in range(NB):
                    act.wait_ge(T.sem, T.at(j, f"gate{b}"))
                    for br in range(2):
                        m = act.activation(sig[:, b % 2, br, :], bank[:, 4 * (b % 2) + br, :], ACT.Sigmoid)
                    m.then_inc(A(f"sig{b}"), 1)
            turns(act, body)

        @block.vector
        def _(dve):
            def body(i, s):
                j = 2 * i + s
                if not first(i):
                    dve.wait_ge(stored[s], i * 16)
                for b in range(NB):
                    q, t = b % 2, slice(b * BANK, (b + 1) * BANK)
                    dve.wait_ge(A.sem, A.at(j, f"sig{b}"))
                    dve.wait_ge(T.sem, T.at(j, f"y{b}"))
                    dve.tensor_tensor(row[:, s, t], bank[:, 4 * q + 2, :], sig[:, q, 0, :], ALU.mult
                                      ).then_inc(D(f"a{b}"), 1)
                    dve.tensor_tensor(sig[:, q, 1, :], bank[:, 4 * q + 3, :], sig[:, q, 1, :], ALU.mult
                                      ).then_inc(D(f"b{b}"), 1)
                    dve.wait_ge(D.sem, D.at(j, f"b{b}"))
                    dve.tensor_tensor(row[:, s, t], row[:, s, t], sig[:, q, 1, :], ALU.add).then_inc(D(f"sum{b}"), 1)
            turns(dve, body)


def layer_norm_steps(dve, D, A, t, x, stats, mv, inv, rstd, eps, g_row):
    width = x.shape[-1]
    for n in range(width // BANK):
        m = dve.bn_stats(stats[:, 6 * n:6 * n + 6], x[:, n * BANK:(n + 1) * BANK])
    m.then_inc(D("stats"), 1)
    dve.wait_ge(D.sem, D.at(t, "stats"))
    dve.nop(nofuse=True)
    dve.bn_aggr(mv, stats[:, 0:6 * (width // BANK)]).then_inc(D("mv"), 1)
    dve.wait_ge(D.sem, D.at(t, "mv"))
    dve.tensor_scalar(mv[:, 1:2], mv[:, 1:2], eps, None, ALU.add).then_inc(D("var"), 1)
    dve.wait_ge(D.sem, D.at(t, "var"))
    dve.reciprocal(inv, mv[:, 1:2]).then_inc(D("inv"), 1)
    dve.wait_ge(A.sem, A.at(t, "rstd"))
    dve.tensor_scalar(x, x, mv[:, 0:1], rstd, ALU.subtract, ALU.mult).then_inc(D("n"), 1)
    dve.wait_ge(D.sem, D.at(t, "n"))
    dve.tensor_tensor(x, x, g_row, ALU.mult).then_inc(D("scaled"), 1)
    dve.wait_ge(D.sem, D.at(t, "scaled"))


def phase_residual(chip, x, smT, w_out, ln_g, ln_b, sh, hT):
    nc, bank = chip.nc, chip.bank
    NTL = SEQ // P
    with ExitStack() as st:
        sb = lambda n, s: st.enter_context(nc.sbuf_tensor("residual_" + n, s, F32))
        sem = lambda n: st.enter_context(nc.semaphore("residual_" + n))
        W = sb("W", [P, KT, DM])
        mT = sb("mT", [P, 2, KT, P])
        xs = sb("xs", [P, 2, DM])
        r = sb("r", [P, 2, DM])
        h = sb("h", [P, 2, DM])
        rows = sb("rows", [P, 2, DM])
        stats, mv, inv, rstd = (sb(n, [P, w]) for n, w in (("stats", 12), ("mv", 2), ("inv", 1), ("rstd", 1)))
        once = sem("once")
        loaded = [sem(f"loaded{s}") for s in range(2)]
        stored = [sem(f"stored{s}") for s in range(2)]
        T, TU = Stages(sem("pe_mm"), "mm"), Stages(sem("pe_turned"), "turned")
        A = Stages(sem("act_stage"), "rstd hT")
        D = Stages(sem("dve_stage"), "gated sum stats mv var inv n scaled h")
        block = st.enter_context(nc.Block())

        def turns(eng, body):
            body(0, 0)
            body(0, 1)
            with eng.Fori(1, NTL // 2) as i:
                for s in range(2):
                    body(i, s)

        first = lambda i: isinstance(i, int) and i == 0

        @block.sync
        def _(sp):
            sp.dma_start(W[:], w_out.rearrange("(k p) n -> p k n", p=P)).then_inc(once, 16)
            for n, src in enumerate((ln_g, ln_b)):
                sp.dma_start(rows[:, n, :], src.broadcast_to([P, DM])).then_inc(once, 16)

            def body(i, s):
                t = 2 * i + s
                if not first(i):
                    sp.wait_ge(T.sem, T.at(t - 2, "mm"))
                    sp.wait_ge(D.sem, D.at(t - 2, "sum"))
                sp.dma_start(mT[:, s], smT[:, :, bass.ds(t * P, P)].rearrange("k p t -> p k t")).then_inc(loaded[s], 16)
                sp.dma_start(xs[:, s], x[bass.ds(t * P, P), :]).then_inc(loaded[s], 16)
            turns(sp, body)

        @block.gpsimd
        def _(pool):
            def body(i, s):
                t = 2 * i + s
                pool.wait_ge(D.sem, D.at(t, "h"))
                pool.dma_start(sh[bass.ds(t * P, P), :], h[:, s, :]).then_inc(stored[s], 16)
            turns(pool, body)
            for s in range(2):
                pool.wait_ge(stored[s], 16 * NTL // 2)

        @block.tensor
        def _(pe):
            pe.wait_ge(once, 48)

            def mm(i, s):
                t = 2 * i + s
                pe.wait_ge(loaded[s], i * 32 + 32)
                if not first(i):
                    pe.wait_ge(D.sem, D.at(t - 2, "gated"))
                for n in range(2):
                    for k in range(KT):
                        m = pe.matmul(bank[:, 2 * s + n, :], mT[:, s, k, :], W[:, k, n * BANK:(n + 1) * BANK],
                                      start=(k == 0), stop=(k == KT - 1))
                m.then_inc(T("mm"), 1)

            def turn(i, s):
                t = 2 * i + s
                pe.wait_ge(D.sem, D.at(t, "h"))
                if not first(i):
                    pe.wait_ge(A.sem, A.at(t - 2, "hT"))
                for k in range(KT):
                    m = pe.transpose(bank[:, 4 + 2 * s + k // 4, (k % 4) * P:(k % 4 + 1) * P],
                                     h[:, s, k * P:(k + 1) * P], chip.ident[:])
                m.then_inc(TU("turned"), 1)

            mm(0, 0)
            mm(0, 1)
            turn(0, 0)
            with pe.Fori(1, NTL // 2) as i:
                mm(i, 0)
                turn(i - 1, 1)
                mm(i, 1)
                turn(i, 0)
            turn(NTL // 2 - 1, 1)

        @block.scalar
        def _(act):
            def body(i, s):
                t = 2 * i + s
                act.wait_ge(D.sem, D.at(t, "inv"))
                act.activation(rstd[:], inv[:], ACT.Sqrt).then_inc(A("rstd"), 1)
                act.wait_ge(TU.sem, TU.at(t, "turned"))
                for n in range(2):
                    m = act.activation(hT[:, 4 * n:4 * n + 4, bass.ds(t * P, P)],
                                       bank[:, 4 + 2 * s + n, :].rearrange("p (k t) -> p k t", k=4), ACT.Copy)
                m.then_inc(A("hT"), 1)
            turns(act, body)

        @block.vector
        def _(dve):
            dve.wait_ge(once, 48)

            def body(i, s):
                t = 2 * i + s
                dve.wait_ge(T.sem, T.at(t, "mm"))
                for n in range(2):
                    c = slice(n * BANK, (n + 1) * BANK)
                    m = dve.tensor_tensor(r[:, s, c], bank[:, 2 * s + n, :], chip.gate_rows[:, c], ALU.mult)
                m.then_inc(D("gated"), 1)
                dve.wait_ge(D.sem, D.at(t, "gated"))
                dve.scalar_tensor_tensor(out=r[:, s, :], in0=xs[:, s, :], scalar=ALPHA, in1=r[:, s, :], op0=ALU.mult,
                                         op1=ALU.add).then_inc(D("sum"), 1)
                dve.wait_ge(D.sem, D.at(t, "sum"))
                layer_norm_steps(dve, D, A, t, r[:, s, :], stats[:], mv[:], inv[:], rstd[:], EPS1, rows[:, 0, :])
                if not first(i):
                    dve.wait_ge(stored[s], i * 16)
                    dve.wait_ge(TU.sem, TU.at(t - 2, "turned"))
                dve.tensor_tensor(h[:, s, :], r[:, s, :], rows[:, 1, :], ALU.add).then_inc(D("h"), 1)
            turns(dve, body)


EPS2 = 1e-5
Q_LORA, KV_LORA, ROPE, NOPE = 256, 128, 32, 64
QK = NOPE + ROPE
AH = 8
DV = 64
WIDTH = AH * DV
C_KV, C_KR, C_ZA = Q_LORA, Q_LORA + KV_LORA, Q_LORA + KV_LORA + ROPE
C_U, C_V, C_ZB = C_ZA + WIDTH, C_ZA + 2 * WIDTH, C_ZA + 3 * WIDTH
QT = SEQ // P
NEG = -1e30
TWO_PI = 6.283185307179586


def phase_rotation(chip, positions, inv_freq, rot):
    nc, bank = chip.nc, chip.bank
    R = slice(NOPE, QK)
    HALF = ROPE // 2
    with ExitStack() as st:
        sb = lambda n, s, dt=F32: st.enter_context(nc.sbuf_tensor("rotation_" + n, s, dt))
        sem = lambda n: st.enter_context(nc.semaphore("rotation_" + n))
        consts = sb("consts", [1, 2, QK])
        cols = sb("cols", [QK, 2])
        pos = sb("pos", [QK, SEQ], I32)
        ang, turns_, tmp = (sb(n, [QK, SEQ]) for n in ("ang", "turns", "tmp"))
        pos_loaded, consts_ready, cols_turned = sem("pos_loaded"), sem("consts_ready"), sem("cols_turned")
        table, table_act = sem("table"), sem("table_act")
        block = st.enter_context(nc.Block())

        @block.sync
        def _(sp):
            sp.dma_start(pos[R, :], positions.broadcast_to([ROPE, SEQ])).then_inc(pos_loaded, 16)
            sp.dma_start(consts[:, 0, NOPE:NOPE + HALF], inv_freq).then_inc(pos_loaded, 16)
            sp.dma_start(consts[:, 0, NOPE + HALF:QK], inv_freq).then_inc(pos_loaded, 16)

        @block.gpsimd
        def _(pool):
            nc.gpsimd.memset(consts[:, 1, NOPE:NOPE + HALF], -1.0)
            nc.gpsimd.memset(consts[:, 1, NOPE + HALF:QK], 1.0)
            nc.gpsimd.memset(consts[:, :, 0:NOPE], 0.0).then_inc(consts_ready, 1)

        @block.tensor
        def _(pe):
            pe.wait_ge(consts_ready, 1)
            pe.wait_ge(pos_loaded, 48)
            for n in range(2):
                m = pe.transpose(bank[0:QK, 7, n:n + 1], consts[:, n, :], chip.ident[0:1, 0:1])
            m.then_inc(cols_turned, 1)

        @block.scalar
        def _(act):
            for n in range(2):
                act.wait_ge(table, (9, 13)[n])
                act.activation((tmp, ang)[n][R, :], (tmp, ang)[n][R, :], ACT.Sin).then_inc(table_act, 1)

        @block.vector
        def _(dve):
            count = [0]

            def link(ins):
                count[0] += 1
                ins.then_inc(table, 1)
                dve.wait_ge(table, count[0])
            dve.wait_ge(cols_turned, 1)
            dve.wait_ge(pos_loaded, 48)
            link(dve.tensor_copy(cols[:], bank[0:QK, 7, 0:2]))
            link(dve.tensor_copy(ang[R, :], pos[R, :]))
            link(dve.tensor_scalar(ang[R, :], ang[R, :], cols[R, 0:1], None, ALU.mult))
            link(dve.tensor_scalar(turns_[R, :], ang[R, :], 1.0 / TWO_PI, 12582912.0, ALU.mult, ALU.add))
            link(dve.tensor_scalar(turns_[R, :], turns_[R, :], 12582912.0, None, ALU.subtract))
            parts = (6.28125, 1.9340515136718750e-3, TWO_PI - 6.28125 - 1.9340515136718750e-3)
            for part in parts:
                link(dve.scalar_tensor_tensor(out=ang[R, :], in0=turns_[R, :], scalar=-part, in1=ang[R, :],
                                              op0=ALU.mult, op1=ALU.add))
            PI = 3.1415925
            link(dve.tensor_scalar(tmp[R, :], ang[R, :], PI, -PI, ALU.min, ALU.max))
            link(dve.tensor_scalar(ang[R, :], ang[R, :], TWO_PI / 4, None, ALU.add))
            link(dve.tensor_scalar(turns_[R, :], ang[R, :], PI, -TWO_PI, ALU.is_gt, ALU.mult))
            link(dve.tensor_tensor(ang[R, :], ang[R, :], turns_[R, :], ALU.add))
            link(dve.tensor_scalar(ang[R, :], ang[R, :], PI, -PI, ALU.min, ALU.max))
            dve.wait_ge(table_act, 1)
            link(dve.tensor_scalar(rot[R, 1, :], tmp[R, :], cols[R, 1:2], None, ALU.mult))
            dve.wait_ge(table_act, 2)
            link(dve.tensor_copy(rot[R, 0, :], ang[R, :]))


def phase_latents(chip, hT, w_in, q_norm_g, kv_norm_g, cqT, ckvT, kT, rot, shT):
    nc, bank = chip.nc, chip.bank
    NB = LATENT_BLOCKS
    R = slice(NOPE, QK)
    HALF = ROPE // 2
    with ExitStack() as st:
        sb = lambda n, s, dt=F32: st.enter_context(nc.sbuf_tensor("latents_" + n, s, dt))
        sem = lambda n: st.enter_context(nc.semaphore("latents_" + n))
        W = sb("W", [P, KT, 3 * P])
        WR = sb("WR", [P, KT, 2, QK])
        gains = sb("gains", [P, 3])
        sq = sb("sq", [P, 3, BANK])
        v = sb("v", [P, 2, BANK])
        kr = sb("kr", [QK, 2, BANK])
        once, shT_stored = sem("once"), sem("shT_stored")
        T = Stages(sem("pe_stage"), "proj0 proj1 proj2 kr krs sumq sumkv")
        A = Stages(sem("act_stage"), "raw0 raw1 raw2 sq0 sq1 sq2 rinv")
        D = Stages(sem("dve_stage"), "vq vkv inv q0 q1 kv krc krs kr")
        block = st.enter_context(nc.Block())

        @block.sync
        def _(sp):
            v_ = lambda ap: ap.rearrange("(k p) n -> p k n", p=P)
            sp.dma_start(W[:], v_(w_in[:, 0:3 * P])).then_inc(once, 16)
            sp.dma_start(WR[:, :, 0, :], v_(w_in[:, C_KR - NOPE:C_KR + ROPE])).then_inc(once, 16)
            sp.dma_start(WR[:, :, 1, 0:NOPE], v_(w_in[:, C_KR - NOPE:C_KR])).then_inc(once, 16)
            for half in range(2):
                sp.dma_start(WR[:, :, 1, NOPE + half * HALF:NOPE + (half + 1) * HALF],
                             v_(w_in[:, C_KR + (1 - half) * HALF:C_KR + (2 - half) * HALF])).then_inc(once, 16)
            for f in range(2):
                sp.dma_start(gains[:, f:f + 1], q_norm_g[f * P:(f + 1) * P].rearrange("(p a) -> p a", a=1)
                             ).then_inc(once, 16)
            sp.dma_start(gains[:, 2:3], kv_norm_g.rearrange("(p a) -> p a", a=1)).then_inc(once, 16)
            with sp.Fori(0, QT) as t:
                sp.dma_start(shT[bass.ds(t, 1)].rearrange("a p (k c) -> (a p) k c", k=KT),
                             hT[:, :, bass.ds(t * P, P)]).then_inc(shT_stored, 16)
            sp.wait_ge(shT_stored, 16 * QT)

        @block.tensor
        def _(pe):
            pe.wait_ge(once, 16 * 8)

            def body(b, first):
                rhs = lambda k: hT[:, k, bass.ds(b * BANK, BANK)]
                for f in range(3):
                    if not first:
                        pe.wait_ge(A.sem, A.at(b - 1, f"raw{f}"))
                        pe.wait_ge(A.sem, A.at(b - 1, f"sq{f}"))
                    for k in range(KT):
                        m = pe.matmul(bank[:, f, :], W[:, k, f * P:(f + 1) * P], rhs(k), start=(k == 0),
                                      stop=(k == KT - 1))
                    m.then_inc(T(f"proj{f}"), 1)
                for n, name in enumerate(("kr", "krs")):
                    if not first:
                        pe.wait_ge(D.sem, D.at(b - 1, name if n else "krc"))
                    for k in range(KT):
                        m = pe.matmul(bank[0:QK, 3 + n, :], WR[:, k, n, :], rhs(k), start=(k == 0),
                                      stop=(k == KT - 1))
                    m.then_inc(T(name), 1)
                pe.wait_ge(A.sem, A.at(b, "sq1"))
                if not first:
                    pe.wait_ge(D.sem, D.at(b - 1, "vkv"))
                for f in range(2):
                    m = pe.matmul(bank[:, 5, :], chip.ones[:], sq[:, f, :], start=(f == 0), stop=(f == 1))
                m.then_inc(T("sumq"), 1)
                pe.wait_ge(A.sem, A.at(b, "sq2"))
                pe.matmul(bank[:, 6, :], chip.ones[:], sq[:, 2, :], start=True, stop=True).then_inc(T("sumkv"), 1)
            body(0, True)
            with pe.Fori(1, NB) as b:
                body(b, False)

        @block.scalar
        def _(act):
            def body(b, first):
                for f in range(3):
                    act.wait_ge(T.sem, T.at(b, f"proj{f}"))
                    out = cqT[:, f, bass.ds(b * BANK, BANK)] if f < 2 else ckvT[:, bass.ds(b * BANK, BANK)]
                    act.activation(out, bank[:, f, :], ACT.Copy).then_inc(A(f"raw{f}"), 1)
                for f in range(3):
                    if not first and f == 0:
                        act.wait_ge(T.sem, T.at(b - 1, "sumkv"))
                    act.activation(sq[:, f, :], bank[:, f, :], ACT.Square).then_inc(A(f"sq{f}"), 1)
                act.wait_ge(D.sem, D.at(b, "inv"))
                act.activation(v[:], v[:], ACT.Sqrt).then_inc(A("rinv"), 1)
            body(0, True)
            with act.Fori(1, NB) as b:
                body(b, False)

        @block.vector
        def _(dve):
            dve.wait_ge(once, 16 * 8)

            def body(b, first):
                t = bass.ds(b * BANK, BANK)
                dve.wait_ge(T.sem, T.at(b, "sumq"))
                if not first:
                    dve.wait_ge(D.sem, D.at(b - 1, "kv"))
                dve.tensor_scalar(v[:, 0, :], bank[:, 5, :], 1.0 / Q_LORA, EPS2, ALU.mult, ALU.add
                                  ).then_inc(D("vq"), 1)
                dve.wait_ge(T.sem, T.at(b, "sumkv"))
                dve.tensor_scalar(v[:, 1, :], bank[:, 6, :], 1.0 / KV_LORA, EPS2, ALU.mult, ALU.add
                                  ).then_inc(D("vkv"), 1)
                dve.wait_ge(D.sem, D.at(b, "vkv"))
                dve.reciprocal(v[:], v[:]).then_inc(D("inv"), 1)
                dve.wait_ge(A.sem, A.at(b, "rinv"))
                for f in range(3):
                    c = cqT[:, f, t] if f < 2 else ckvT[:, t]
                    dve.scalar_tensor_tensor(out=c, in0=c, scalar=gains[:, f:f + 1], in1=v[:, f // 2, :],
                                             op0=ALU.mult, op1=ALU.mult).then_inc(D(("q0", "q1", "kv")[f]), 1)
                dve.tensor_tensor(kr[R, 0, :], bank[R, 3, :], rot[R, 0, t], ALU.mult).then_inc(D("krc"), 1)
                dve.tensor_tensor(kr[R, 1, :], bank[R, 4, :], rot[R, 1, t], ALU.mult).then_inc(D("krs"), 1)
                dve.wait_ge(D.sem, D.at(b, "krs"))
                dve.tensor_tensor(kT[R, t], kr[R, 0, :], kr[R, 1, :], ALU.add).then_inc(D("kr"), 1)
            body(0, True)
            with dve.Fori(1, NB) as b:
                body(b, False)


def phase_attention(chip, cqT, ckvT, kT, rot, w_uq, w_ukv, vall, oall):
    nc, bank = chip.nc, chip.bank
    NB = LATENT_BLOCKS
    R = slice(NOPE, QK)
    HALF = ROPE // 2
    SCALE = QK ** -0.5
    AHEAD, NSC = 2, 3
    NS, NTB = 3, 3
    SC0, TB0, OB0 = 0, 3, 6
    chunks = {i: (i + 4) // 4 for i in range(QT)}
    with ExitStack() as st:
        sb = lambda n, s: st.enter_context(nc.sbuf_tensor("attn_" + n, s, F32))
        sem = lambda n: st.enter_context(nc.semaphore("attn_" + n))
        WQ = sb("WQ", [P, 2, 2, QK])
        WK = sb("WK", [P, NOPE])
        WV = sb("WV", [P, AH, DV])
        qT = sb("qT", [QK, SEQ])
        v = sb("v", [P, QT, DV])
        ahead = sb("ahead", [P, P])
        sc = sb("sc", [P, NSC, SEQ])
        pT = sb("pT", [P, NTB, BANK])
        tmp = sb("tmp", [QK, 2, 2, BANK])
        mx = sb("mx", [P, NSC, 4])
        top = sb("top", [P, NSC])
        total = sb("total", [P, NSC])
        share = sb("share", [P, NSC])
        w_loaded, mask_ready = sem("w_loaded"), sem("mask_ready")
        wv_loaded, vall_ready, vall_copied = sem("wv_loaded"), sem("vall_ready"), sem("vall_copied")
        order = [i for n in range(QT // 2) for i in (QT - 1 - n, n)]
        at = {i: n for n, i in enumerate(order)}
        slot = {i: n % NSC for i, n in at.items()}
        steps = [(order[n] if n < QT else None, order[n - AHEAD] if n >= AHEAD else None) for n in range(QT + AHEAD)]
        groups = [(i, g) for i in order for g in range(chunks[i])]
        gi = {ig: n for n, ig in enumerate(groups)}
        T = Stages(sem("pe_stage"), " ".join([f"q{b} k{b}" for b in range(NB)])
                   + " " + " ".join(x for i, j in steps for x in (
                       [f"s{i}_{g}" for g in range(chunks.get(i, 0))]
                       + ([y for g in range(chunks[j] + 1) for y in (
                           ([f"t{j}_{g}"] if g < chunks[j] else []) + ([f"o{j}_{g - 1}"] if g else []))]
                          if j is not None else []))))
        D = Stages(sem("dve_stage"), " ".join(f"qc{b} qs{b} q{b}" for b in range(NB)) + " " + " ".join(
            x for i, j in steps for x in (
                ([f"m{i}_{g}" for g in range(chunks[i])] + [f"top{i}"] if i is not None else [])
                + ([f"share{j}", f"o{j}"] if j is not None else []))))
        A = Stages(sem("act_stage"), "v " + " ".join(f"q{b} k{b}" for b in range(NB)) + " " + " ".join(
            x for i, j in steps for x in (([f"t{j}_{g}" for g in range(chunks[j])] if j is not None else [])
                                          + ([f"e{i}"] if i is not None else []))))
        ended = lambda f: f"o{f}_{chunks[f] - 1}"
        block = st.enter_context(nc.Block())

        def turns(eng, body):
            body(0, True)
            with eng.Fori(1, AH) as h:
                body(h, False)

        @block.sync
        def _(sp):
            sp.dma_start(WV[:], w_ukv.rearrange("k (h n) -> k h n", h=AH)[:, :, NOPE:NOPE + DV]).then_inc(wv_loaded, 16)

            def body(h, first):
                if not first:
                    sp.wait_ge(T.sem, T.at(h - 1, f"k{NB - 1}"))
                q = w_uq.rearrange("(k p) n -> p k n", p=P)
                sp.dma_start(WQ[:, :, 0, :], q[:, :, bass.ds(h * QK, QK)]).then_inc(w_loaded, 16)
                sp.dma_start(WQ[:, :, 1, 0:NOPE], q[:, :, bass.ds(h * QK, NOPE)]).then_inc(w_loaded, 16)
                for half in range(2):
                    sp.dma_start(WQ[:, :, 1, NOPE + half * HALF:NOPE + (half + 1) * HALF],
                                 q[:, :, bass.ds(h * QK + NOPE + (1 - half) * HALF, HALF)]).then_inc(w_loaded, 16)
                sp.dma_start(WK[:], w_ukv[:, bass.ds(h * (NOPE + DV), NOPE)]).then_inc(w_loaded, 16)
            turns(sp, body)

        @block.gpsimd
        def _(pool):
            nc.gpsimd.memset(ahead[:], 0.0).then_inc(mask_ready, 1)
            pool.wait_ge(mask_ready, 1)
            nc.gpsimd.affine_select(out=ahead[:], in_=ahead[:], compare_op=ALU.is_ge, fill=NEG, base=0,
                                    pattern=[[-1, P]], channel_multiplier=1).then_inc(mask_ready, 1)

        @block.tensor
        def _(pe):
            pe.wait_ge(mask_ready, 2)
            pe.wait_ge(wv_loaded, 16)
            for t in range(QT):
                if t >= 4:
                    pe.wait_ge(vall_copied, t - 3)
                pe.matmul(bank[:, 4 + t % 4, :], ckvT[:, t * P:(t + 1) * P], WV[:].rearrange("p h n -> p (h n)"),
                          start=True, stop=True).then_inc(vall_ready, 1)

            def body(h, first):
                pe.wait_ge(w_loaded, h * 80 + 80)
                for b in range(NB):
                    t = slice(b * BANK, (b + 1) * BANK)
                    b0 = 3 * (b % 2)
                    if b >= 2:
                        pe.wait_ge(A.sem, A.at(h, f"k{b - 2}"))
                        pe.wait_ge(D.sem, D.at(h, f"qs{b - 2}"))
                    elif not first:
                        pe.wait_ge(D.sem, D.at(h - 1, ("m%d_%d" % groups[-1], f"o{order[-1]}")[b]))
                    elif b == 1:
                        pe.wait_ge(vall_copied, QT)
                    for n in range(2):
                        for k in range(2):
                            m = pe.matmul(bank[0:QK, b0 + n, :], WQ[:, k, n, :], cqT[:, k, t], start=(k == 0),
                                          stop=(k == 1))
                    m.then_inc(T(f"q{b}"), 1)
                    pe.matmul(bank[0:NOPE, b0 + 2, :], WK[:], ckvT[:, t], start=True, stop=True).then_inc(T(f"k{b}"), 1)

                def scores(i):
                    q = qT[:, i * P:(i + 1) * P]
                    for g in range(chunks[i]):
                        n = gi[i, g]
                        if n >= NS:
                            pe.wait_ge(D.sem, D.at(h, "m%d_%d" % groups[n - NS]))
                        else:
                            pe.wait_ge(A.sem, A.at(h, f"k{NB - 1}"))
                            pe.wait_ge(D.sem, D.at(h, f"q{NB - 1}"))
                        lo, hi = g * BANK, min((g + 1) * BANK, i * P)
                        bk = bank[:, SC0 + n % NS, :]
                        if hi > lo:
                            m = pe.matmul(bk[:, 0:hi - lo], q, kT[:, lo:hi], start=True, stop=True)
                        if (i + 1) * P <= (g + 1) * BANK:
                            d = slice(i * P - lo, (i + 1) * P - lo)
                            pe.matmul(bk[:, d], q, kT[:, i * P:(i + 1) * P], start=True, stop=False)
                            m = pe.matmul(bk[:, d], chip.ident[:], ahead[:], start=False, stop=True)
                        m.then_inc(T(f"s{i}_{g}"), 1)

                def rest(i):
                    for g in range(chunks[i] + 1):
                        if g < chunks[i]:
                            n = gi[i, g]
                            if g == 0:
                                pe.wait_ge(A.sem, A.at(h, f"e{i}"))
                            if n >= NTB:
                                pe.wait_ge(A.sem, A.at(h, "t%d_%d" % groups[n - NTB]))
                            for c in range(4 * g, min(4 * g + 4, i + 1)):
                                m = pe.transpose(bank[:, TB0 + n % NTB, (c % 4) * P:(c % 4 + 1) * P],
                                                 sc[:, slot[i], c * P:(c + 1) * P], chip.ident[:])
                            m.then_inc(T(f"t{i}_{g}"), 1)
                        if g > 0:
                            n = gi[i, g - 1]
                            pe.wait_ge(A.sem, A.at(h, f"t{i}_{g - 1}"))
                            if g == 1 and at[i] >= 2:
                                pe.wait_ge(D.sem, D.at(h, f"o{order[at[i] - 2]}"))
                            if g == 1 and at[i] == 0:
                                pe.wait_ge(A.sem, A.at(h, "v"))
                            for c in range(4 * (g - 1), min(4 * g, i + 1)):
                                m = pe.matmul(bank[:, OB0 + at[i] % 2, 0:DV], pT[:, n % NTB, (c % 4) * P:(c % 4 + 1) * P],
                                              v[:, c, :], start=(c == 0), stop=(c == i))
                            m.then_inc(T(f"o{i}_{g - 1}"), 1)
                for i, j in steps:
                    if i is not None:
                        scores(i)
                    if j is not None:
                        rest(j)
            turns(pe, body)

        @block.scalar
        def _(act):
            for t in range(QT):
                act.wait_ge(vall_ready, t + 1)
                act.activation(vall[:, t, :], bank[:, 4 + t % 4, :], ACT.Copy).then_inc(vall_copied, 1)

            def body(h, first):
                if first:
                    act.wait_ge(vall_copied, QT)
                else:
                    act.wait_ge(T.sem, T.at(h - 1, ended(order[-1])))
                act.activation(v[:], vall[:, :, bass.ds(h * DV, DV)], ACT.Copy).then_inc(A("v"), 1)
                for b in range(NB):
                    t = slice(b * BANK, (b + 1) * BANK)
                    act.wait_ge(T.sem, T.at(h, f"q{b}"))
                    act.activation(qT[0:NOPE, t], bank[0:NOPE, 3 * (b % 2), :], ACT.Copy).then_inc(A(f"q{b}"), 1)
                    act.wait_ge(T.sem, T.at(h, f"k{b}"))
                    act.activation(kT[0:NOPE, t], bank[0:NOPE, 3 * (b % 2) + 2, :], ACT.Copy).then_inc(A(f"k{b}"), 1)
                for i, j in steps:
                    for g in range(chunks[j] if j is not None else 0):
                        n = gi[j, g]
                        w = min(BANK, (j + 1) * P - g * BANK)
                        act.wait_ge(T.sem, T.at(h, f"t{j}_{g}"))
                        if n >= NTB:
                            act.wait_ge(T.sem, T.at(h, "o%d_%d" % groups[n - NTB]))
                        act.activation(pT[:, n % NTB, 0:w], bank[:, TB0 + n % NTB, 0:w], ACT.Copy
                                       ).then_inc(A(f"t{j}_{g}"), 1)
                    if i is None:
                        continue
                    act.wait_ge(D.sem, D.at(h, f"top{i}"))
                    n = (i + 1) * P
                    act.activation(sc[:, slot[i], 0:n], sc[:, slot[i], 0:n], ACT.Exp,
                                   bias=top[:, slot[i]:slot[i] + 1], accum_out=total[:, slot[i]:slot[i] + 1]
                                   ).then_inc(A(f"e{i}"), 1)
            turns(act, body)

        @block.vector
        def _(dve):
            def body(h, first):
                for b in range(NB):
                    t = slice(b * BANK, (b + 1) * BANK)
                    dve.wait_ge(T.sem, T.at(h, f"q{b}"))
                    dve.wait_ge(A.sem, A.at(h, f"q{b}"))
                    if b or not first:
                        prev = D.at(h, f"q{b - 1}") if b else D.at(h - 1, f"q{NB - 1}")
                        dve.wait_ge(D.sem, prev)
                    dve.tensor_tensor(tmp[R, b % 2, 0, :], bank[R, 3 * (b % 2), :], rot[R, 0, t], ALU.mult
                                      ).then_inc(D(f"qc{b}"), 1)
                    dve.tensor_tensor(tmp[R, b % 2, 1, :], bank[R, 3 * (b % 2) + 1, :], rot[R, 1, t], ALU.mult
                                      ).then_inc(D(f"qs{b}"), 1)
                    dve.wait_ge(D.sem, D.at(h, f"qs{b}"))
                    dve.tensor_tensor(qT[R, t], tmp[R, b % 2, 0, :], tmp[R, b % 2, 1, :], ALU.add
                                      ).then_inc(D(f"q{b}"), 1)
                for i, j in steps:
                    if i is not None:
                        for g in range(chunks[i]):
                            n = gi[i, g]
                            w = min(BANK, (i + 1) * P - g * BANK)
                            dve.wait_ge(T.sem, T.at(h, f"s{i}_{g}"))
                            dve.tensor_scalar(sc[:, slot[i], g * BANK:g * BANK + w], bank[:, SC0 + n % NS, 0:w], SCALE,
                                              None, ALU.mult, ALU.max, accum_out=mx[:, slot[i], g:g + 1]
                                              ).then_inc(D(f"m{i}_{g}"), 1)
                        dve.wait_ge(D.sem, D.at(h, f"m{i}_{chunks[i] - 1}"))
                        dve.tensor_reduce(top[:, slot[i]:slot[i] + 1], mx[:, slot[i], 0:chunks[i]], AX.X, ALU.max,
                                          negate=True).then_inc(D(f"top{i}"), 1)
                    if j is not None:
                        u = slice(slot[j], slot[j] + 1)
                        dve.wait_ge(T.sem, T.at(h, f"o{j}_{chunks[j] - 1}"))
                        dve.reciprocal(share[:, u], total[:, u]).then_inc(D(f"share{j}"), 1)
                        dve.wait_ge(D.sem, D.at(h, f"share{j}"))
                        dve.tensor_scalar(oall[:, j, bass.ds(h * DV, DV)], bank[:, OB0 + at[j] % 2, 0:DV],
                                          share[:, u], None, ALU.mult).then_inc(D(f"o{j}"), 1)
            turns(dve, body)


def phase_output(chip, oall, WO, shT, sh, w_in, sgu_g, sgu_b, w_spatial, b_spatial, w_out, ln_g, ln_b, out):
    nc, bank = chip.nc, chip.bank
    COLS = (C_V, C_U, C_ZB, C_ZA)
    with ExitStack() as st:
        sb = lambda n, s: st.enter_context(nc.sbuf_tensor("out_" + n, s, F32))
        sem = lambda n: st.enter_context(nc.semaphore("out_" + n))
        W = sb("W", [P, KT, 4, WIDTH])
        wsT = sb("wsT", [P, AH, P])
        bs = sb("bs", [AH, P])
        bsT = sb("bsT", [P, AH])
        srows = sb("srows", [P, 2, WIDTH])
        rows = sb("rows", [P, 2, DM])
        xT = sb("xT", [P, 2, KT, P])
        hs = sb("hs", [P, DM])
        v, u, zb, za = (sb(n, [P, 2, WIDTH]) for n in ("v", "u", "zb", "za"))
        m_ = sb("m", [P, 2 * WIDTH])
        ws = m_[:].rearrange("p (h s) -> p h s", h=AH)
        mT = sb("mT", [P, KT, P])
        r = sb("r", [P, DM])
        stats, mv, inv, rstd = (sb(n, [P, 2, w]) for n, w in (("stats", 12), ("mv", 2), ("inv", 1), ("rstd", 1)))
        once, rows_loaded, wo_loaded, prep, prep_pe = (sem(n) for n in ("once", "rows_loaded", "wo_loaded", "prep",
                                                                        "prep_pe"))
        w_loaded = [sem(f"w_loaded{n}") for n in range(4)]
        x_loaded = [sem(f"x_loaded{s}") for s in range(2)]
        h_loaded, stored = sem("h_loaded"), sem("stored")
        TH_ = Stages(sem("pe_head"), "proj0 proj1 proj2 proj3")
        TT_ = Stages(sem("pe_tail"), "spatial turned mm")
        AH_ = Stages(sem("act_head"), "v u zb rstd za")
        AT_ = Stages(sem("act_tail"), "mT rstd")
        DH_ = Stages(sem("dve_head"), "stats mv var inv n scaled vn")
        DT_ = Stages(sem("dve_tail"), "sv su b a sum stats mv var inv n scaled y")
        block = st.enter_context(nc.Block())

        def steps(eng, step):
            step(0, 0, True, False)
            step(1, 1, True, True)
            with eng.Fori(1, QT // 2) as i:
                step(2 * i, 0, True, True)
                step(2 * i + 1, 1, True, True)
            step(QT, 0, False, True)
        early = lambda t: isinstance(t, int) and t < 2

        @block.sync
        def _(sp):
            sp.dma_start(ws, w_spatial.rearrange("h t s -> t h s")).then_inc(once, 16)
            sp.dma_start(bs[:], b_spatial).then_inc(once, 16)
            for s in range(2):
                sp.dma_start(xT[:, s], shT[s:s + 1].rearrange("a p (k c) -> (a p) k c", k=KT)).then_inc(x_loaded[s], 16)
            for n, c in enumerate(COLS):
                sp.dma_start(W[:, :, n, :], w_in[:, c:c + WIDTH].rearrange("(k p) n -> p k n", p=P)
                             ).then_inc(w_loaded[n], 16)
            for n, src in enumerate((sgu_g, sgu_b)):
                sp.dma_start(srows[:, n, :], src.broadcast_to([P, WIDTH])).then_inc(rows_loaded, 16)
            for n, src in enumerate((ln_g, ln_b)):
                sp.dma_start(rows[:, n, :], src.broadcast_to([P, DM])).then_inc(rows_loaded, 16)
            sp.dma_start(WO, w_out.rearrange("(k p) n -> p k n", p=P)).then_inc(wo_loaded, 16)

            def step(t, s, new, old):
                if new and not early(t):
                    sp.wait_ge(TH_.sem, TH_.at(t - 2, "proj3"))
                    sp.dma_start(xT[:, s], shT[bass.ds(t, 1)].rearrange("a p (k c) -> (a p) k c", k=KT)
                                 ).then_inc(x_loaded[s], 16)
                if old:
                    if not early(t):
                        sp.wait_ge(DT_.sem, DT_.at(t - 2, "sum"))
                    sp.dma_start(hs[:], sh[bass.ds((t - 1) * P, P), :]).then_inc(h_loaded, 16)
            steps(sp, step)

        @block.gpsimd
        def _(pool):
            def step(t, s, new, old):
                if old:
                    pool.wait_ge(DT_.sem, DT_.at(t - 1, "y"))
                    pool.dma_start(out[bass.ds((t - 1) * P, P), :], r[:]).then_inc(stored, 16)
            steps(pool, step)
            pool.wait_ge(stored, 16 * QT)

        @block.tensor
        def _(pe):
            pe.wait_ge(once, 32)
            pe.transpose(bank[:, 7, 0:AH], bs[:], chip.ident[0:AH, 0:AH]).then_inc(prep_pe, 1)
            pe.wait_ge(prep, 1)
            for h in range(AH):
                m = pe.transpose(bank[:, 5 + h // 4, (h % 4) * P:(h % 4 + 1) * P], ws[:, h, :], chip.ident[:])
            m.then_inc(prep_pe, 1)

            def step(t, s, new, old):
                def project(n):
                    if not new:
                        return
                    if isinstance(t, int) and t == 0:
                        pe.wait_ge(w_loaded[n], 16)
                    else:
                        pe.wait_ge(AH_.sem, AH_.at(t - 1, ("v", "u", "zb", "za")[n]))
                    for k in range(KT):
                        m = pe.matmul(bank[:, n, :], xT[:, s, k, :], W[:, k, n, :], start=(k == 0), stop=(k == KT - 1))
                    m.then_inc(TH_(f"proj{n}"), 1)

                if new:
                    pe.wait_ge(x_loaded[s], (t - s) // 2 * 16 + 16)
                project(0)
                if old:
                    pe.wait_ge(DH_.sem, DH_.at(t - 1, "vn"))
                    if early(t):
                        pe.wait_ge(prep, 3)
                    else:
                        pe.wait_ge(DT_.sem, DT_.at(t - 2, "sum"))
                    for h in range(AH):
                        m = pe.matmul(bank[:, 4, h * DV:(h + 1) * DV], wsT[:, h, :], v[:, 1 - s, h * DV:(h + 1) * DV],
                                      start=True, stop=True)
                    m.then_inc(TT_("spatial"), 1)
                project(1)
                project(2)
                if old:
                    pe.wait_ge(DT_.sem, DT_.at(t - 1, "a"))
                    for k in range(KT):
                        m = pe.transpose(bank[:, 5 + k // 4, (k % 4) * P:(k % 4 + 1) * P], m_[:, k * P:(k + 1) * P],
                                         chip.ident[:])
                    m.then_inc(TT_("turned"), 1)
                project(3)
                if old:
                    if early(t):
                        pe.wait_ge(wo_loaded, 16)
                    pe.wait_ge(AT_.sem, AT_.at(t - 1, "mT"))
                    for n in range(2):
                        for k in range(KT):
                            m = pe.matmul(bank[:, (7, 4)[n], :], mT[:, k, :], WO[:, k, n * BANK:(n + 1) * BANK],
                                          start=(k == 0), stop=(k == KT - 1))
                    m.then_inc(TT_("mm"), 1)
            steps(pe, step)

        @block.scalar
        def _(act):
            def step(t, s, new, old):
                if new:
                    if not early(t):
                        act.wait_ge(TT_.sem, TT_.at(t - 2, "spatial"))
                    act.wait_ge(TH_.sem, TH_.at(t, "proj0"))
                    act.activation(v[:, s], bank[:, 0, :], ACT.Gelu).then_inc(AH_("v"), 1)
                    if not early(t):
                        act.wait_ge(DT_.sem, DT_.at(t - 2, "a"))
                    act.wait_ge(TH_.sem, TH_.at(t, "proj1"))
                    act.activation(u[:, s], bank[:, 1, :], ACT.Gelu).then_inc(AH_("u"), 1)
                    act.wait_ge(TH_.sem, TH_.at(t, "proj2"))
                    act.activation(zb[:, s], bank[:, 2, :], ACT.Silu).then_inc(AH_("zb"), 1)
                    act.wait_ge(DH_.sem, DH_.at(t, "inv"))
                    act.activation(rstd[:, 0, :], inv[:, 0, :], ACT.Sqrt).then_inc(AH_("rstd"), 1)
                if old:
                    act.wait_ge(TT_.sem, TT_.at(t - 1, "turned"))
                    for n in range(2):
                        m = act.activation(mT[:, 4 * n:4 * n + 4, :],
                                           bank[:, 5 + n, :].rearrange("p (k c) -> p k c", k=4), ACT.Copy)
                    m.then_inc(AT_("mT"), 1)
                if new:
                    act.wait_ge(TH_.sem, TH_.at(t, "proj3"))
                    act.activation(za[:, s], bank[:, 3, :], ACT.Silu).then_inc(AH_("za"), 1)
                if old:
                    act.wait_ge(DT_.sem, DT_.at(t - 1, "inv"))
                    act.activation(rstd[:, 1, :], inv[:, 1, :], ACT.Sqrt).then_inc(AT_("rstd"), 1)
            steps(act, step)

        @block.vector
        def _(dve):
            dve.wait_ge(once, 32)
            dve.tensor_tensor(ws, ws, bcast(chip.low[:], 1, AH), ALU.mult).then_inc(prep, 1)
            dve.wait_ge(prep_pe, 1)
            dve.tensor_copy(bsT[:], bank[:, 7, 0:AH]).then_inc(prep, 1)
            dve.wait_ge(prep_pe, 2)
            for n in range(2):
                m = dve.tensor_copy(wsT[:, 4 * n:4 * n + 4, :], bank[:, 5 + n, :].rearrange("p (h c) -> p h c", h=4))
            m.then_inc(prep, 1)
            dve.wait_ge(rows_loaded, 64)
            dve.wait_ge(prep, 3)

            def step(t, s, new, old):
                by_head = lambda ap: ap.rearrange("p (h d) -> p h d", h=AH)
                a, b = m_[:, 0:WIDTH], m_[:, WIDTH:2 * WIDTH]
                if old:
                    dve.wait_ge(TT_.sem, TT_.at(t - 1, "spatial"))
                    if not early(t):
                        dve.wait_ge(TT_.sem, TT_.at(t - 2, "turned"))
                    dve.tensor_tensor(by_head(b), by_head(bank[:, 4, :]), bcast(bsT[:], 2, DV), ALU.add
                                      ).then_inc(DT_("sv"), 1)
                    dve.wait_ge(AH_.sem, AH_.at(t - 1, "za"))
                    dve.wait_ge(DT_.sem, DT_.at(t - 1, "sv"))
                    dve.tensor_tensor(b, b, u[:, 1 - s], ALU.mult).then_inc(DT_("su"), 1)
                    dve.wait_ge(DT_.sem, DT_.at(t - 1, "su"))
                    dve.tensor_tensor(b, b, zb[:, 1 - s], ALU.mult).then_inc(DT_("b"), 1)
                    dve.tensor_tensor(a, oall[:, bass.ds(t - 1, 1), :].rearrange("p a n -> p (a n)"), za[:, 1 - s],
                                      ALU.mult).then_inc(DT_("a"), 1)
                if new:
                    dve.wait_ge(AH_.sem, AH_.at(t, "v"))
                    layer_norm_steps(dve, DH_, AH_, t, v[:, s], stats[:, 0], mv[:, 0], inv[:, 0], rstd[:, 0], EPS2,
                                     srows[:, 0, :])
                    dve.tensor_tensor(v[:, s], v[:, s], srows[:, 1, :], ALU.add).then_inc(DH_("vn"), 1)
                if old:
                    dve.wait_ge(TT_.sem, TT_.at(t - 1, "mm"))
                    dve.wait_ge(h_loaded, t * 16)
                    if not early(t):
                        dve.wait_ge(stored, (t - 1) * 16)
                    for n in range(2):
                        c = slice(n * BANK, (n + 1) * BANK)
                        m = dve.scalar_tensor_tensor(out=r[:, c], in0=hs[:, c], scalar=ALPHA,
                                                     in1=bank[:, (7, 4)[n], :], op0=ALU.mult, op1=ALU.add)
                    m.then_inc(DT_("sum"), 1)
                    dve.wait_ge(DT_.sem, DT_.at(t - 1, "sum"))
                    layer_norm_steps(dve, DT_, AT_, t - 1, r[:], stats[:, 1], mv[:, 1], inv[:, 1], rstd[:, 1], EPS2,
                                     rows[:, 0, :])
                    dve.tensor_tensor(r[:], r[:], rows[:, 1, :], ALU.add).then_inc(DT_("y"), 1)
            steps(dve, step)


def build(nc, a, out):
    def scratch(name, shape):
        return nc.dram_tensor(name, shape, F32, kind="Internal").ap()

    sa = scratch("delta_qkv", [3 * HEADS, P, TOK])
    sq_, sv = scratch("gla_queries", [HEADS, P, TOK]), scratch("gla_values", [HEADS, P, TOK])
    sk, sg = scratch("gla_keys", [2 * HEADS, P, TOK]), scratch("gla_decays", [2 * HEADS, P, TOK])
    so_a, so_b = scratch("delta_outputs", [HEADS, P, SEQ]), scratch("gla_outputs", [HEADS, P, SEQ])
    smT = scratch("merged", [KT, P, SEQ])
    sh = scratch("hidden", [SEQ, DM])
    shT = scratch("hidden_turned", [QT, P, DM])
    with ExitStack() as stack:
        chip = Chip(nc, stack)
        w_in = a["w_in"][0]
        with ExitStack() as st:
            uT = st.enter_context(nc.sbuf_tensor("uT", [P, KT, TOK], F32))
            phase_constants(chip, a["c"], a["c_ctx"], a["w_mod"], a["b_mod"], a["lb_param"])
            phase_modulated_norm(chip, uT, a["x"][0], a["ctx"][0])
            phase_conv(chip, uT, w_in, a["conv_w"], sa)
            phase_decay_beta(chip, uT, w_in, a["a_log"], a["dt_bias"])
            phase_gla_inputs(chip, uT, w_in, sq_, sv, sk, sg)
            phase_delta_rule(chip, sa, so_a)
            phase_gla(chip, sq_, sv, sk, sg, so_b)
            yT = st.enter_context(nc.sbuf_tensor("yT", [P, 2 * HEADS, SEQ], F32))
            phase_branch_gates(chip, uT, w_in, so_a, so_b, a["a_norm_g"], a["b_norm_g"], yT)
            phase_merge(chip, uT, w_in, yT, a["w_a_out"][0], a["w_b_out"][0], smT)
        hT = stack.enter_context(nc.sbuf_tensor("hT", [P, KT, SEQ], F32))
        oall = hT[:, 0:KT // 2, :].rearrange("p k t -> p (k t)").rearrange("p (a n) -> p a n", n=WIDTH)
        vall = hT[:, KT // 2:KT, :].rearrange("p k t -> p (k t)").rearrange("p (a n) -> p a n", n=WIDTH)
        WO = hT[:, KT // 2:KT, :].rearrange("p k t -> p (k t)").rearrange("p (a n) -> p a n", n=DM)
        phase_residual(chip, a["x"][0], smT, a["w_out"][0], a["ln_g"], a["ln_b"], sh, hT)
        with ExitStack() as st:
            sb = lambda n, s: st.enter_context(nc.sbuf_tensor(n, s, F32))
            cqT, ckvT = sb("cqT", [P, 2, SEQ]), sb("ckvT", [P, SEQ])
            kT, rot = sb("kT", [QK, SEQ]), sb("rot", [QK, 2, SEQ])
            phase_rotation(chip, a["positions_2"], a["inv_freq"], rot)
            phase_latents(chip, hT, a["w_in_2"], a["q_norm_g_2"], a["kv_norm_g_2"], cqT, ckvT, kT, rot, shT)
            phase_attention(chip, cqT, ckvT, kT, rot, a["w_uq_2"], a["w_ukv_2"], vall, oall)
        row = lambda n: a[n].rearrange("(a n) -> a n", a=1)
        phase_output(chip, oall, WO, shT, sh, a["w_in_2"], row("sgu_norm_g_2"), row("sgu_norm_b_2"), a["w_spatial_2"],
                     a["b_spatial_2"], a["w_out_2"], row("ln_g_2"), row("ln_b_2"), out[0])


INPUTS = ["x", "c", "ctx", "c_ctx", "w_mod", "b_mod", "w_in", "conv_w", "a_log", "dt_bias", "lb_param", "a_norm_g",
          "b_norm_g", "w_a_out", "w_b_out", "w_out", "ln_g", "ln_b", "positions_2", "w_in_2", "q_norm_g_2", "w_uq_2",
          "kv_norm_g_2", "w_ukv_2", "sgu_norm_g_2", "sgu_norm_b_2", "w_spatial_2", "b_spatial_2", "w_out_2", "ln_g_2",
          "ln_b_2"]


def kernel(**inputs):
    import numpy as np
    import concourse.bacc as bacc
    from concourse.bass_utils import run_bass_kernel_spmd

    arrays = {name: np.ascontiguousarray(inputs[name]) for name in INPUTS}
    half = ROPE // 2
    arrays["inv_freq"] = (np.float32(1.0) / np.float32(10000.0) ** (np.arange(half, dtype=np.float32)
                                                                   / np.float32(half))).reshape(1, half)
    nc = bacc.Bacc("TRN2", target_bir_lowering=False, num_devices=1)
    aps = {name: nc.dram_tensor(f"in_{name}", v.shape, mybir.dt.from_np(v.dtype), kind="ExternalInput").ap()
           for name, v in arrays.items()}
    out = nc.dram_tensor("out", (1, SEQ, DM), F32, kind="ExternalOutput").ap()
    build(nc, aps, out)
    result = run_bass_kernel_spmd(nc, [{f"in_{name}": v for name, v in arrays.items()}], core_ids=[0])
    return result.results[0]["out"]
```

```python
from contextlib import ExitStack

import concourse.bass as bass
from concourse import mybir

F32 = mybir.dt.float32
U32 = mybir.dt.uint32
I32 = mybir.dt.int32
ALU = mybir.AluOpType
ACT = mybir.ActivationFunctionType
AX = mybir.AxisListType

P = 128
BANK = 512
DM = 1024
KT = DM // P
SEQ = 2048
CTX = 256
TOK = CTX + SEQ
NT = TOK // P
GRID_W = 64
ROWS = SEQ // GRID_W
HEADS = 4
NDIR = 2
HD = HEADS * P
C_AQ, C_AV, C_AB = 0, 2 * HD, 3 * HD
C_AGATE = C_AB + 4 * HEADS
C_BQ = C_AGATE + HD
C_BF = C_BQ + HD
C_BI = C_BF + 2 * HD
C_BGATE = C_BI + HD
C_MERGE = C_BGATE + HD
CONV_K = 5
PAD = CONV_K // 2
RAW = TOK + 4 * PAD
EPS1 = 1e-6
LATENT_BLOCKS = SEQ // BANK
BLOCKS = [(0, CTX)] + [(CTX + BANK * n, BANK) for n in range(LATENT_BLOCKS)]
ALPHA = 2.0 ** 0.25


class Stages:

    def __init__(self, sem, names):
        self.sem, self.names, self.turn = sem, names.split(), 0

    def __call__(self, name):
        want = self.names[self.turn % len(self.names)]
        assert name == want, (name, want)
        self.turn += 1
        return self.sem

    def at(self, i, name):
        return i * len(self.names) + self.names.index(name) + 1


class Chip:

    def __init__(self, nc, stack):
        self.nc = nc
        self.bank = stack.enter_context(nc.psum_tensor("bank", [P, 8, BANK], F32))

        def sb(name, shape, dt=F32):
            return stack.enter_context(nc.sbuf_tensor(name, shape, dt))

        self.sb = sb
        self.ident = sb("ident", [P, P])
        self.ones = sb("ones", [P, P])
        self.low = sb("low", [P, P])
        self.up = sb("up", [P, P])
        self.off = sb("off", [P, NDIR, 7, P])
        self.diag16 = sb("diag16", [P, NDIR, P])
        self.modT = sb("modT", [P, 2 * KT, 2])
        self.gate_rows = sb("gate_rows", [P, DM])
        self.lbT = sb("lbT", [P, 2, 2 * HEADS])
        self.decay_tok = sb("decay_tok", [P, NT, 2 * HEADS])
        self.beta_tok = sb("beta_tok", [P, NT, 2 * HEADS])


def bcast(ap, axis, count):
    v = ap.unsqueeze(axis)
    shape = list(v.shape)
    shape[axis] = count
    return v.broadcast_to(shape)


def phase_constants(chip, c, c_ctx, w_mod, b_mod, lb_param):
    nc, bank = chip.nc, chip.bank
    NW = 4
    MODW = 3 * DM
    with ExitStack() as st:
        sb = lambda n, s: st.enter_context(nc.sbuf_tensor("constants_" + n, s, F32))
        sem = lambda n: st.enter_context(nc.semaphore("constants_" + n))
        cond = sb("cond", [2 * KT, P])
        scond = sb("scond", [2 * KT, P])
        condT = sb("condT", [P, 2 * KT])
        wm = sb("wm", [P, NW, MODW])
        bm = sb("bm", [2, MODW])
        mod = sb("mod", [2, MODW])
        lb = sb("lb", [2 * HEADS, 8, P])
        c_loaded, b_loaded, lb_loaded = sem("c_loaded"), sem("b_loaded"), sem("lb_loaded")
        w_loaded = [sem(f"wm_loaded{s}") for s in range(NW)]
        w_used = sem("wm_used")
        pool_step, act_done = sem("pool_step"), sem("act_done")
        masks_ready = sem("masks_ready")
        pe_done, dve_done = sem("pe_done"), sem("dve_done")
        block = st.enter_context(nc.Block())

        @block.sync
        def _(sp):
            sp.dma_start(cond[0:KT, :], c.rearrange("b (k p) -> (b k) p", p=P)).then_inc(c_loaded, 16)
            sp.dma_start(cond[KT:2 * KT, :], c_ctx.rearrange("(k p) -> k p", p=P)).then_inc(c_loaded, 16)
            for r in range(2):
                sp.dma_start(bm[r:r + 1, :], b_mod).then_inc(b_loaded, 16)
            for r in range(2):
                sp.dma_start(lb[:, r, :], lb_param[r].rearrange("d (h p) -> (d h) p", p=P)).then_inc(lb_loaded, 16)
            for k in range(KT):
                if k >= NW:
                    sp.wait_ge(w_used, k - NW + 1)
                sp.dma_start(wm[:, k % NW, :], w_mod[0, k * P:(k + 1) * P, :]).then_inc(w_loaded[k % NW], 16)

        @block.gpsimd
        def _(pool):
            count = [0]

            def step(ins):
                count[0] += 1
                ins.then_inc(pool_step, 1)
                pool.wait_ge(pool_step, count[0])

            def keep(view, pattern, base, mul):
                step(nc.gpsimd.affine_select(out=view, in_=view, compare_op=ALU.is_ge, fill=0.0, base=base,
                                             pattern=pattern, channel_multiplier=mul))

            nc.gpsimd.memset(chip.ones[:], 1.0)
            nc.gpsimd.memset(chip.low[:], 1.0)
            nc.gpsimd.memset(chip.up[:], 1.0)
            nc.gpsimd.memset(chip.off[:], 0.0)
            nc.gpsimd.memset(chip.diag16[:], 1.0)
            step(nc.gpsimd.memset(chip.ident[:], 0.0))
            step(nc.gpsimd.affine_select(out=chip.ident[:], in_=chip.ident[:], compare_op=ALU.not_equal, fill=1.0,
                                         base=0, pattern=[[-1, P]], channel_multiplier=1))
            keep(chip.low[:], [[-1, P]], 0, 1)
            keep(chip.up[:], [[1, P]], 0, -1)
            for n in range(7):
                b = 1 << n
                nb = P // (2 * b)
                for d in range(NDIR):
                    v = chip.off[:, d, n, :].rearrange("p (c j) -> p c j", j=2 * b)[:, :, d * b:(d + 1) * b]
                    lo = b if d == 0 else 0
                    step(nc.gpsimd.memset(v, 1.0))
                    keep(v, [[-2 * b, nb], [0, b]], -lo, 1)
                    keep(v, [[2 * b, nb], [0, b]], lo + b - 1, -1)
            for d in range(NDIR):
                v = chip.diag16[:, d, :].rearrange("p (c j) -> p c j", j=16)
                if d == 0:
                    keep(v, [[16, 8], [1, 16]], 0, -1)
                    keep(v, [[-16, 8], [0, 16]], 0, 1)
                else:
                    keep(v, [[-16, 8], [-1, 16]], 0, 1)
                    keep(v, [[16, 8], [0, 16]], 15, -1)
            nc.gpsimd.memset(chip.decay_tok[:, 0, 0:1], 0.0).then_inc(masks_ready, 1)

        @block.scalar
        def _(act):
            act.wait_ge(c_loaded, 32)
            act.activation(scond[:], cond[:], ACT.Silu).then_inc(act_done, 1)
            for r in range(2):
                act.wait_ge(dve_done, 3 + r)
                act.activation(lb[:, 5 + r, :], lb[:, 3 + r, :], ACT.Exp).then_inc(act_done, 1)

        @block.vector
        def _(dve):
            dve.wait_ge(lb_loaded, 32)
            dve.tensor_tensor(lb[:, 2, :], lb[:, 0, :], lb[:, 1, :], ALU.max).then_inc(dve_done, 1)
            dve.wait_ge(masks_ready, 1)
            dve.wait_ge(pe_done, 1)
            dve.tensor_copy(condT[:], bank[:, 6, 0:2 * KT]).then_inc(dve_done, 1)
            dve.wait_ge(dve_done, 1)
            for r in range(2):
                dve.tensor_tensor(lb[:, 3 + r, :], lb[:, r, :], lb[:, 2, :], ALU.subtract).then_inc(dve_done, 1)
            dve.wait_ge(act_done, 3)
            dve.tensor_tensor(lb[:, 7, :], lb[:, 5, :], lb[:, 6, :], ALU.add).then_inc(dve_done, 1)
            dve.wait_ge(dve_done, 5)
            dve.reciprocal(lb[:, 2, :], lb[:, 7, :]).then_inc(dve_done, 1)
            dve.wait_ge(dve_done, 6)
            dve.tensor_tensor(lb[:, 3, :], lb[:, 5, :], lb[:, 2, :], ALU.mult).then_inc(dve_done, 1)
            dve.wait_ge(dve_done, 7)
            dve.tensor_scalar(lb[:, 4, :], lb[:, 3, :], -1.0, 1.0, ALU.mult, ALU.add).then_inc(dve_done, 1)
            dve.wait_ge(b_loaded, 32)
            dve.wait_ge(pe_done, 3)
            for n in range(6):
                dve.tensor_tensor(mod[:, n * BANK:(n + 1) * BANK], bank[0:2, n, :], bm[:, n * BANK:(n + 1) * BANK],
                                  ALU.add).then_inc(dve_done, 1)
            dve.wait_ge(pe_done, 4)
            mT = bank[:, 7, 0:4 * KT].rearrange("p (k s) -> p k s", s=2)
            dve.tensor_copy(chip.modT[:, 0:KT, :], mT[:, 0:KT, :])
            dve.tensor_scalar(chip.modT[:, KT:2 * KT, :], mT[:, KT:2 * KT, :], 1.0, None, ALU.add)
            for r in range(2):
                dve.tensor_copy(chip.lbT[:, r, :], bank[:, 6, 64 + 8 * r:72 + 8 * r])
            dve.wait_ge(pe_done, 5)
            for n in range(2):
                dve.tensor_copy(chip.gate_rows[:, n * BANK:(n + 1) * BANK], bank[:, n, :])

        @block.tensor
        def _(pe):
            pe.wait_ge(masks_ready, 1)
            pe.wait_ge(act_done, 1)
            pe.transpose(bank[:, 6, 0:2 * KT], scond[:], chip.ident[0:2 * KT, 0:2 * KT]).then_inc(pe_done, 1)
            pe.wait_ge(dve_done, 8)
            for r in range(2):
                t = pe.transpose(bank[:, 6, 64 + 8 * r:72 + 8 * r], lb[:, 3 + r, :], chip.ident[0:8, 0:8])
            t.then_inc(pe_done, 1)
            cT = condT[:].rearrange("p (s k) -> p k s", k=KT)
            for k in range(KT):
                pe.wait_ge(w_loaded[k % NW], 16 * (k // NW + 1))
                for n in range(6):
                    mm = pe.matmul(bank[0:2, n, :], cT[:, k, :], wm[:, k % NW, n * BANK:(n + 1) * BANK],
                                   start=(k == 0), stop=(k == KT - 1))
                mm.then_inc(w_used, 1)
            pe.wait_ge(w_used, KT)
            pe.nop().then_inc(pe_done, 1)
            pe.wait_ge(dve_done, 14)
            for j in range(2 * KT):
                t = pe.transpose(bank[:, 7, 2 * j:2 * j + 2], mod[:, j * P:(j + 1) * P], chip.ident[0:2, 0:2])
            t.then_inc(pe_done, 1)
            for n in range(2):
                mm = pe.matmul(bank[:, n, :], chip.ones[0:1, :], mod[0:1, 2 * DM + n * BANK:2 * DM + (n + 1) * BANK],
                               start=True, stop=True)
            mm.then_inc(pe_done, 1)


def phase_modulated_norm(chip, uT, x, ctx_in):
    nc, bank = chip.nc, chip.bank
    with ExitStack() as st:
        sb = lambda n, s: st.enter_context(nc.sbuf_tensor("modulated_norm_" + n, s, F32))
        sem = lambda n: st.enter_context(nc.semaphore("modulated_norm_" + n))
        xin = sb("xin", [P, 2, DM])
        xh = sb("xh", [P, 2, DM])
        stats = sb("stats", [P, 2, 12])
        mv = sb("mv", [P, 2, 2])
        inv = sb("inv", [P, 2, 1])
        rstd = sb("rstd", [P, 2, 1])
        x_loaded = [sem(f"x_loaded{s}") for s in range(2)]
        D, DU = Stages(sem("dve_norm"), "stats mv var inv xh"), Stages(sem("dve_out"), "uT")
        A, AU = Stages(sem("act_norm"), "rstd"), Stages(sem("act_out"), "uT")
        T = Stages(sem("pe_stage"), "turned")
        block = st.enter_context(nc.Block())
        num = lambda t: isinstance(t, int)
        in_context = lambda t: num(t) and t < CTX // P

        def turns(eng, body):
            for t in range(3):
                body(t, t % 2)
            with eng.Fori(0, (NT - 4) // 2) as i:
                body(2 * i + 3, 1)
                body(2 * i + 4, 0)
            body(NT - 1, 1)

        @block.sync
        def _(sp):
            def body(t, s):
                if not (num(t) and t < 2):
                    sp.wait_ge(D.sem, D.at(t - 2, "xh"))
                src = ctx_in[t * P:(t + 1) * P, :] if in_context(t) else x[bass.ds((t - CTX // P) * P, P), :]
                sp.dma_start(xin[:, s, :], src).then_inc(x_loaded[s], 16)
            turns(sp, body)

        @block.vector
        def _(dve):
            def copy_out(t, s):
                stream = 1 if in_context(t) else 0
                dve.wait_ge(T.sem, T.at(t, "turned"))
                for k in range(KT // 2):
                    ev = dve.tensor_scalar(uT[:, k, bass.ds(t * P, P)], bank[:, 2 * s, k * P:(k + 1) * P],
                                           chip.modT[:, KT + k, stream:stream + 1],
                                           chip.modT[:, k, stream:stream + 1], ALU.mult, ALU.add)
                ev.then_inc(DU("uT"), 1)

            def body(t, s):
                dve.wait_ge(x_loaded[s], (t - s) // 2 * 16 + 16)
                dve.bn_stats(stats[:, s, 0:6], xin[:, s, 0:BANK])
                dve.bn_stats(stats[:, s, 6:12], xin[:, s, BANK:DM]).then_inc(D("stats"), 1)
                dve.wait_ge(D.sem, D.at(t, "stats"))
                dve.nop(nofuse=True)
                dve.bn_aggr(mv[:, s, :], stats[:, s, :]).then_inc(D("mv"), 1)
                dve.wait_ge(D.sem, D.at(t, "mv"))
                dve.tensor_scalar(mv[:, s, 1:2], mv[:, s, 1:2], EPS1, None, ALU.add).then_inc(D("var"), 1)
                dve.wait_ge(D.sem, D.at(t, "var"))
                dve.reciprocal(inv[:, s, :], mv[:, s, 1:2]).then_inc(D("inv"), 1)
                dve.wait_ge(A.sem, A.at(t, "rstd"))
                if not (num(t) and t < 2):
                    dve.wait_ge(T.sem, T.at(t - 2, "turned"))
                dve.tensor_scalar(xh[:, s, :], xin[:, s, :], mv[:, s, 0:1], rstd[:, s, :], ALU.subtract,
                                  ALU.mult).then_inc(D("xh"), 1)
                if not (num(t) and t == 0):
                    copy_out(t - 1, 1 - s)
            turns(dve, body)
            copy_out(NT - 1, 1)

        @block.scalar
        def _(act):
            def copy_out(t, s):
                stream = 1 if in_context(t) else 0
                act.wait_ge(T.sem, T.at(t, "turned"))
                for k in range(KT // 2, KT):
                    ev = act.activation(uT[:, k, bass.ds(t * P, P)],
                                        bank[:, 2 * s + 1, (k - KT // 2) * P:(k - KT // 2 + 1) * P], ACT.Identity,
                                        bias=chip.modT[:, k, stream:stream + 1],
                                        scale=chip.modT[:, KT + k, stream:stream + 1])
                ev.then_inc(AU("uT"), 1)

            def body(t, s):
                act.wait_ge(D.sem, D.at(t, "inv"))
                act.activation(rstd[:, s, :], inv[:, s, :], ACT.Sqrt).then_inc(A("rstd"), 1)
                if not (num(t) and t == 0):
                    copy_out(t - 1, 1 - s)
            turns(act, body)
            copy_out(NT - 1, 1)

        @block.tensor
        def _(pe):
            def body(t, s):
                pe.wait_ge(D.sem, D.at(t, "xh"))
                if not (num(t) and t < 2):
                    pe.wait_ge(DU.sem, DU.at(t - 2, "uT"))
                    pe.wait_ge(AU.sem, AU.at(t - 2, "uT"))
                for k in range(KT):
                    m = pe.transpose(bank[:, 2 * s + k // 4, (k % 4) * P:(k % 4 + 1) * P],
                                     xh[:, s, k * P:(k + 1) * P], chip.ident[:])
                m.then_inc(T("turned"), 1)
            turns(pe, body)


def phase_conv(chip, uT, w_in, conv_w, sa):
    nc, bank = chip.nc, chip.bank
    NF = 3 * HEADS
    with ExitStack() as st:
        sb = lambda n, s: st.enter_context(nc.sbuf_tensor("conv_" + n, s, F32))
        sem = lambda n: st.enter_context(nc.semaphore("conv_" + n))
        W = sb("W", [P, 2, KT, P])
        taps = sb("taps", [P, NF, CONV_K])
        tap_rows = sb("tap_rows", [NF * CONV_K, P])
        raw = sb("raw", [P, 2, RAW])
        acc = sb("acc", [P, RAW])
        y = sb("y", [P, 2, TOK])
        sq = sb("sq", [P, TOK])
        inv = sb("inv", [P, TOK])
        w_loaded = [sem(f"w_loaded{s}") for s in range(2)]
        y_stored = [sem(f"y_stored{s}") for s in range(2)]
        taps_loaded, taps_ready, taps_turned = sem("taps_loaded"), sem("taps_ready"), sem("taps_turned")
        T, TS = Stages(sem("pe_proj"), " ".join(f"proj{b}" for b in range(5))), Stages(
            sem("pe_sums"), " ".join(f"sum{b}" for b in range(5)))
        D = Stages(sem("dve_conv"), " ".join(f"t{t}" for t in range(CONV_K - 1)) + " conv")
        DS, DY = Stages(sem("dve_sums"), " ".join(f"ss{b}" for b in range(5))), Stages(sem("dve_scale"), "inv y")
        A, AS = Stages(sem("act_raw"), " ".join(f"raw{b}" for b in range(5))), Stages(sem("act_silu"), "silu")
        AQ, AR = Stages(sem("act_square"), "sq"), Stages(sem("act_root"), "rinv")
        block = st.enter_context(nc.Block())
        def steps(eng, step):
            for f in range(2):
                step(f, f)
            with eng.Fori(1, HEADS // 2 + 1) as i:
                for s in range(2):
                    step(2 * i + s, s)
            for f in range(HEADS + 2, NF + 2):
                step(f, f % 2)
        num = lambda f: isinstance(f, int)
        exists = lambda f: not num(f) or 0 <= f < NF
        normed = lambda f: not num(f) or f < 2 * HEADS
        rcol = [PAD + t0 + (2 * PAD if t0 else 0) for t0, _ in BLOCKS]
        WIDE = RAW - 2 * PAD

        @block.sync
        def _(sp):
            sp.dma_start(tap_rows[:], conv_w[0].rearrange("t (f p) -> (t f) p", p=P)).then_inc(taps_loaded, 16)

            def step(f, s):
                g = f + 1
                if not num(f) or (f > 0 and exists(g)):
                    sp.wait_ge(T.sem, T.at(g - 2, "proj4"))
                if exists(g):
                    sp.dma_start(W[:, 1 - s], w_in[:, bass.ds(g * P, P)].rearrange("(k p) n -> p k n", p=P)
                                 ).then_inc(w_loaded[1 - s], 16)
                g = f - 2
                if exists(g):
                    if normed(g):
                        sp.wait_ge(DY.sem, DY.at(g, "y"))
                    else:
                        sp.wait_ge(AS.sem, AS.at(g, "silu"))
                    sp.dma_start(sa[bass.ds(g, 1)].rearrange("a p t -> (a p) t"), y[:, s, :]).then_inc(y_stored[s], 16)
            sp.dma_start(W[:, 0], w_in[:, 0:P].rearrange("(k p) n -> p k n", p=P)).then_inc(w_loaded[0], 16)
            steps(sp, step)
            for s in range(2):
                sp.wait_ge(y_stored[s], 16 * (NF // 2))

        @block.tensor
        def _(pe):
            pe.wait_ge(taps_loaded, 16)
            pe.transpose(bank[:, 7, 0:NF * CONV_K], tap_rows[:], chip.ident[0:NF * CONV_K, 0:NF * CONV_K]
                         ).then_inc(taps_turned, 1)

            def step(f, s):
                def project(blocks):
                    for b in blocks:
                        t0, n = BLOCKS[b]
                        if not (num(f) and f == 0):
                            pe.wait_ge(A.sem, A.at(f - 1, f"raw{b}"))
                        for k in range(KT):
                            mm = pe.matmul(bank[:, b, 0:n], W[:, s, k, :], uT[:, k, t0:t0 + n], start=(k == 0),
                                           stop=(k == KT - 1))
                        mm.then_inc(T(f"proj{b}"), 1)

                def sums(blocks):
                    g = f - 1
                    for b in blocks:
                        t0, n = BLOCKS[b]
                        if b == 0:
                            pe.wait_ge(AQ.sem, AQ.at(g, "sq"))
                        if b >= 3:
                            pe.wait_ge(DS.sem, DS.at(g, f"ss{b - 3}"))
                        elif not (num(g) and g == 0):
                            pe.wait_ge(DS.sem, DS.at(g - 1, f"ss{min(b + 3, 4)}"))
                        elif b == 2:
                            pe.wait_ge(taps_ready, 1)
                        pe.matmul(bank[:, 5 + b % 3, 0:n], chip.ones[:], sq[:, t0:t0 + n], start=True, stop=True
                                  ).then_inc(TS(f"sum{b}"), 1)

                if exists(f):
                    pe.wait_ge(w_loaded[s], (f - s) // 2 * 16 + 16)
                    project(range(4))
                if exists(f - 1) and normed(f - 1):
                    sums(range(3))
                if exists(f):
                    project((4,))
                if exists(f - 1) and normed(f - 1):
                    sums((3, 4))
            steps(pe, step)

        @block.scalar
        def _(act):
            def step(f, s):
                def copy(b):
                    if exists(f):
                        t0, n = BLOCKS[b]
                        act.wait_ge(T.sem, T.at(f, f"proj{b}"))
                        if b == 0 and not (num(f) and f < 2):
                            act.wait_ge(D.sem, D.at(f - 2, "conv"))
                        act.activation(raw[:, s, rcol[b]:rcol[b] + n], bank[:, b, 0:n], ACT.Copy
                                       ).then_inc(A(f"raw{b}"), 1)

                copy(0)
                copy(1)
                g, u = f - 1, 1 - s
                if exists(g):
                    act.wait_ge(D.sem, D.at(g, "conv"))
                    if not (num(g) and g < 2):
                        act.wait_ge(y_stored[u], (g - u) // 2 * 16)
                    act.activation(y[:, u, 0:CTX], acc[:, 0:CTX], ACT.Silu)
                    act.activation(y[:, u, CTX:TOK], acc[:, CTX + 2 * PAD:WIDE], ACT.Silu).then_inc(AS("silu"), 1)
                    if normed(g):
                        act.wait_ge(AS.sem, AS.at(g, "silu"))
                        if not (num(g) and g == 0):
                            act.wait_ge(TS.sem, TS.at(g - 1, "sum4"))
                        act.activation(sq[:], y[:, u, :], ACT.Square).then_inc(AQ("sq"), 1)
                copy(2)
                g = f - 2
                if exists(g) and normed(g):
                    act.wait_ge(DY.sem, DY.at(g, "inv"))
                    act.activation(inv[:], inv[:], ACT.Sqrt, scale=1.0 / P if not num(g) or g < HEADS else 1.0
                                   ).then_inc(AR("rinv"), 1)
                copy(3)
                copy(4)
            steps(act, step)

        @block.vector
        def _(dve):
            for s in range(2):
                dve.memset(raw[:, s, 0:PAD], 0.0)
                dve.memset(raw[:, s, PAD + CTX:3 * PAD + CTX], 0.0)
                dve.memset(raw[:, s, RAW - PAD:RAW], 0.0)
            dve.wait_ge(taps_turned, 1)
            dve.tensor_copy(taps[:].rearrange("p f t -> p t f"),
                            bank[:, 7, 0:NF * CONV_K].rearrange("p (t f) -> p t f", f=NF)).then_inc(taps_ready, 1)
            dve.wait_ge(taps_ready, 1)

            def step(f, s):
                g, u = f - 1, 1 - s
                if exists(g):
                    tap = taps[:, bass.ds(g, 1), :].rearrange("p a t -> p (a t)")
                    dve.wait_ge(A.sem, A.at(g, "raw4"))
                    if not (num(g) and g == 0):
                        dve.wait_ge(AS.sem, AS.at(g - 1, "silu"))
                    dve.tensor_scalar(acc[:, 0:WIDE], raw[:, u, 0:WIDE], tap[:, 0:1], None, ALU.mult
                                      ).then_inc(D("t0"), 1)
                    for t in range(1, CONV_K):
                        dve.wait_ge(D.sem, D.at(g, f"t{t - 1}"))
                        dve.scalar_tensor_tensor(out=acc[:, 0:WIDE], in0=raw[:, u, t:t + WIDE], scalar=tap[:, t:t + 1],
                                                 in1=acc[:, 0:WIDE], op0=ALU.mult, op1=ALU.add
                                                 ).then_inc(D(f"t{t}" if t < CONV_K - 1 else "conv"), 1)
                g = f - 2
                if exists(g) and normed(g):
                    dve.wait_ge(DS.sem, DS.at(g, "ss4"))
                    dve.reciprocal(inv[:], inv[:]).then_inc(DY("inv"), 1)
                    dve.wait_ge(AR.sem, AR.at(g, "rinv"))
                    dve.tensor_tensor(y[:, s, :], y[:, s, :], inv[:], ALU.mult).then_inc(DY("y"), 1)
                g = f - 1
                if exists(g) and normed(g):
                    if exists(f - 2):
                        dve.wait_ge(DY.sem, DY.at(f - 2, "y"))
                    for b, (t0, n) in enumerate(BLOCKS):
                        dve.wait_ge(TS.sem, TS.at(g, f"sum{b}"))
                        dve.tensor_scalar(inv[:, t0:t0 + n], bank[:, 5 + b % 3, 0:n], EPS1, None, ALU.add
                                          ).then_inc(DS(f"ss{b}"), 1)
            steps(dve, step)


def phase_decay_beta(chip, uT, w_in, a_log, dt_bias):
    nc, bank = chip.nc, chip.bank
    NH2 = 2 * HEADS
    with ExitStack() as st:
        sb = lambda n, s: st.enter_context(nc.sbuf_tensor("decay_beta_" + n, s, F32))
        sem = lambda n: st.enter_context(nc.semaphore("decay_beta_" + n))
        W = sb("Wab", [P, KT, 2 * NH2])
        z16 = sb("z16", [2 * NH2, TOK])
        z = sb("z", [P, NT, 2 * NH2])
        par = sb("par", [P, 2, NH2])
        w = [sb(f"w{n}", [P, NT, NH2]) for n in range(6)]
        loaded, act_done, pe_done, dve_done = sem("loaded"), sem("act_done"), sem("pe_done"), sem("dve_done")
        block = st.enter_context(nc.Block())

        @block.sync
        def _(sp):
            sp.dma_start(W[:], w_in[:, C_AB:C_AB + 2 * NH2].rearrange("(k p) n -> p k n", p=P)).then_inc(loaded, 16)
            for n, src in enumerate((dt_bias, a_log)):
                sp.dma_start(par[:, n, :], src.rearrange("l d h -> l (d h)").broadcast_to([P, NH2])
                             ).then_inc(loaded, 16)

        @block.tensor
        def _(pe):
            pe.wait_ge(loaded, 48)
            for b, (t0, n) in enumerate(BLOCKS):
                for k in range(KT):
                    mm = pe.matmul(bank[0:2 * NH2, b, 0:n], W[:, k, :], uT[:, k, t0:t0 + n], start=(k == 0),
                                   stop=(k == KT - 1))
                mm.then_inc(pe_done, 1)
            pe.wait_ge(act_done, 5)
            for t in range(NT):
                tr = pe.transpose(bank[:, 7, t * 2 * NH2:(t + 1) * 2 * NH2], z16[:, t * P:(t + 1) * P],
                                  chip.ident[0:2 * NH2, 0:2 * NH2])
            tr.then_inc(pe_done, 1)

        @block.scalar
        def _(act):
            for b, (t0, n) in enumerate(BLOCKS):
                act.wait_ge(pe_done, b + 1)
                act.activation(z16[:, t0:t0 + n], bank[0:2 * NH2, b, 0:n], ACT.Copy).then_inc(act_done, 1)
            act.wait_ge(dve_done, 1)
            act.activation(chip.beta_tok[:], z[:, :, NH2:], ACT.Sigmoid)
            act.wait_ge(dve_done, 2)
            act.activation(w[0][:], z[:, :, 0:NH2], ACT.Abs).then_inc(act_done, 1)
            act.wait_ge(act_done, 6)
            act.activation(w[1][:], w[0][:], ACT.Exp, scale=-1.0).then_inc(act_done, 1)
            act.activation(par[:, 1, :], par[:, 1, :], ACT.Exp).then_inc(act_done, 1)
            act.wait_ge(dve_done, 3)
            act.activation(w[0][:], w[2][:], ACT.Ln).then_inc(act_done, 1)

        @block.vector
        def _(dve):
            n = [0]

            def link(ins):
                n[0] += 1
                ins.then_inc(dve_done, 1)
                dve.wait_ge(dve_done, n[0])
            dve.wait_ge(pe_done, 6)
            link(dve.tensor_copy(z[:], bank[:, 7, 0:NT * 2 * NH2].rearrange("p (t c) -> p t c", t=NT)))
            link(dve.tensor_tensor(z[:, :, 0:NH2], z[:, :, 0:NH2], bcast(par[:, 0, :], 1, NT), ALU.add))
            dve.wait_ge(act_done, 8)
            link(dve.tensor_scalar(w[2][:], w[1][:], 1.0, None, ALU.add))
            link(dve.tensor_scalar(w[3][:], w[2][:], 1.0, None, ALU.subtract))
            link(dve.tensor_scalar(w[4][:], w[3][:], 0.0, None, ALU.is_equal))
            link(dve.tensor_tensor(w[3][:], w[3][:], w[4][:], ALU.add))
            link(dve.reciprocal(w[5][:], w[3][:]))
            dve.wait_ge(act_done, 9)
            link(dve.tensor_tensor(w[0][:], w[0][:], w[4][:], ALU.add))
            link(dve.tensor_tensor(w[0][:], w[0][:], w[5][:], ALU.mult))
            link(dve.tensor_tensor(w[0][:], w[0][:], w[1][:], ALU.mult))
            link(dve.tensor_scalar(w[1][:], z[:, :, 0:NH2], 0.0, None, ALU.max))
            link(dve.tensor_tensor(w[0][:], w[0][:], w[1][:], ALU.add))
            link(dve.tensor_scalar(w[0][:], w[0][:], -1.0, None, ALU.mult))
            link(dve.tensor_tensor(chip.decay_tok[:], w[0][:], bcast(par[:, 1, :], 1, NT), ALU.mult))


def phase_gla_inputs(chip, uT, w_in, sq_, sv, sk, sg):
    nc, bank = chip.nc, chip.bank
    NF = 4 * HEADS
    with ExitStack() as st:
        sb = lambda n, s: st.enter_context(nc.sbuf_tensor("gla_inputs_" + n, s, F32))
        sem = lambda n: st.enter_context(nc.semaphore("gla_inputs_" + n))
        W = sb("W", [P, 2, KT, P])
        reset = sb("reset", [P, NDIR, TOK])
        a = sb("a", [P, 2, TOK])
        b_ = sb("b_", [P, 2, TOK])
        lf = sb("lf", [P, TOK])
        w_loaded = [sem(f"w_loaded{s}") for s in range(2)]
        stored = [sem(f"stored{s}") for s in range(2)]
        reset_ready = sem("reset_ready")
        T = Stages(sem("pe_stage"), " ".join(f"proj{b}" for b in range(5)))
        D = Stages(sem("dve_stage"), "f k g")
        A = Stages(sem("act_stage"), " ".join(f"out{b}" for b in range(5)) + " ln")
        block = st.enter_context(nc.Block())
        groups = [(0, C_BQ), (HEADS // 2, C_BI), (HEADS, C_BF)]

        def to(dst, b):
            t0, n = BLOCKS[b]
            if b == 0:
                return dst[:, 0:CTX]
            r = GRID_W // 8 * 0 + (n // GRID_W)
            return dst[:, CTX:TOK].rearrange("p (w r) -> p r w", r=ROWS)[:, (b - 1) * r:b * r, :]

        def frm(b):
            n = BLOCKS[b][1]
            v = bank[:, b, 0:n]
            return v if b == 0 else v.rearrange("p (r w) -> p r w", w=GRID_W)

        @block.sync
        def _(sp):
            def body(i, s, col, first):
                f = 2 * i + s
                if not first:
                    sp.wait_ge(T.sem, T.at(f - 2, "proj4"))
                sp.dma_start(W[:, s], w_in[:, bass.ds(col + s * P, P)].rearrange("(k p) n -> p k n", p=P)
                             ).then_inc(w_loaded[s], 16)
            for n, (i0, col) in enumerate(groups):
                i1 = groups[n + 1][0] if n < 2 else NF // 2
                start = i0
                if n == 0:
                    for s in range(2):
                        body(0, s, col, True)
                    start = 1
                with sp.Fori(start, i1) as i:
                    for s in range(2):
                        body(i, s, col + (i - i0) * 2 * P, False)

        @block.gpsimd
        def _(sp):
            def row(dram, r):
                return dram[bass.ds(r, 1)].rearrange("a p t -> (a p) t")

            for dram, i0 in ((sq_, 0), (sv, HEADS // 2)):
                with sp.Fori(i0, i0 + HEADS // 2) as i:
                    for s in range(2):
                        sp.wait_ge(A.sem, A.at(2 * i + s, "ln"))
                        sp.dma_start(row(dram, 2 * (i - i0) + s), a[:, s, :]).then_inc(stored[s], 16)
            with sp.Fori(HEADS, NF // 2) as i:
                for s in range(2):
                    sp.wait_ge(D.sem, D.at(2 * (i - HEADS) + s, "g"))
                    sp.dma_start(row(sk, 2 * (i - HEADS) + s), b_[:, s, :]).then_inc(stored[s], 16)
                    sp.dma_start(row(sg, 2 * (i - HEADS) + s), a[:, s, :]).then_inc(stored[s], 16)
            for s in range(2):
                sp.wait_ge(stored[s], 16 * HEADS + 32 * HEADS)

        @block.tensor
        def _(pe):
            def body(i, s, first):
                f = 2 * i + s
                pe.wait_ge(w_loaded[s], i * 16 + 16)
                for b, (t0, n) in enumerate(BLOCKS):
                    if not first:
                        pe.wait_ge(A.sem, A.at(f - 1, f"out{b}"))
                    for k in range(KT):
                        mm = pe.matmul(bank[:, b, 0:n], W[:, s, k, :], uT[:, k, t0:t0 + n], start=(k == 0),
                                       stop=(k == KT - 1))
                    mm.then_inc(T(f"proj{b}"), 1)
            body(0, 0, True)
            body(0, 1, False)
            with pe.Fori(1, NF // 2) as i:
                body(i, 0, False)
                body(i, 1, False)

        @block.scalar
        def _(act):
            def plain(i, s, first, func):
                f = 2 * i + s
                if not first:
                    act.wait_ge(stored[s], i * 16)
                for b in range(5):
                    act.wait_ge(T.sem, T.at(f, f"proj{b}"))
                    act.activation(to(a[:, s, :], b), frm(b), func).then_inc(A(f"out{b}"), 1)
                act.wait_ge(A.sem, A.at(f, "out4"))
                act.activation(a[:, s, :], a[:, s, :], ACT.Copy, scale=P ** -0.5 if func == ACT.Silu else 1.0
                               ).then_inc(A("ln"), 1)

            def forget(i, s):
                f = 2 * i + s
                act.wait_ge(stored[s], (i - HEADS) * 32 + 16 * HEADS)
                for b in range(5):
                    act.wait_ge(T.sem, T.at(f, f"proj{b}"))
                    act.activation(to(a[:, s, :], b), frm(b), ACT.Sigmoid)
                    act.activation(to(b_[:, s, :], b), frm(b), ACT.Sigmoid, scale=-1.0).then_inc(A(f"out{b}"), 1)
                act.wait_ge(D.sem, D.at(2 * (i - HEADS) + s, "f"))
                act.activation(lf[:], a[:, s, :], ACT.Ln).then_inc(A("ln"), 1)
            for s in range(2):
                plain(0, s, True, ACT.Silu)
            with act.Fori(1, HEADS // 2) as i:
                for s in range(2):
                    plain(i, s, False, ACT.Silu)
            with act.Fori(HEADS // 2, HEADS) as i:
                for s in range(2):
                    plain(i, s, False, ACT.Copy)
            with act.Fori(HEADS, NF // 2) as i:
                for s in range(2):
                    forget(i, s)

        @block.vector
        def _(dve):
            dve.memset(reset[:], 1.0).then_inc(reset_ready, 1)
            dve.wait_ge(reset_ready, 1)
            for d in range(NDIR):
                v = reset[:, d, :].rearrange("p (t c) -> p t c", c=P)
                dve.memset(v[:, :, d * (P - 1):d * (P - 1) + 1], 0.0).then_inc(reset_ready, 1)
            dve.wait_ge(reset_ready, 3)

            def body(i, s, d):
                g = 2 * i + s
                dve.wait_ge(A.sem, A.at(g + 2 * HEADS, "out4"))
                one_less = chip.lbT[:, 1, bass.ds(g, 1)]
                dve.tensor_scalar(a[:, s, :], a[:, s, :], one_less, chip.lbT[:, 0, bass.ds(g, 1)], ALU.mult,
                                  ALU.add).then_inc(D("f"), 1)
                dve.tensor_scalar(b_[:, s, :], b_[:, s, :], one_less, None, ALU.mult).then_inc(D("k"), 1)
                dve.wait_ge(A.sem, A.at(g + 2 * HEADS, "ln"))
                step = 1 if d == 0 else -1
                dve.tensor_tensor_scan(a[:, s, ::step], reset[:, d, ::step], lf[:, ::step], 0.0, ALU.mult,
                                       ALU.add).then_inc(D("g"), 1)
            for d in range(NDIR):
                with dve.Fori(d * HEADS // 2, (d + 1) * HEADS // 2) as i:
                    for s in range(2):
                        body(i, s, d)


def phase_delta_rule(chip, sa, so_a):
    nc, bank = chip.nc, chip.bank
    LEVELS = range(1, 7)
    with ExitStack() as st:
        sb = lambda n, s: st.enter_context(nc.sbuf_tensor("delta_" + n, s, F32))
        sem = lambda n: st.enter_context(nc.semaphore("delta_" + n))
        mat = lambda n: [sb(f"{n}{d}", [P, HEADS, P]) for d in range(NDIR)]
        qkv = [[sb(f"qkv{d}{s}", [P, 3 * HEADS, P]) for s in range(2)] for d in range(NDIR)]
        kd, kbe, vb, Dm, A_, AT, T_, TT = (mat(n) for n in ("kd", "kbe", "vb", "Dm", "A", "AT", "T", "TT"))
        attnT, qg, vnew, S = (mat(n) for n in ("attnT", "qg", "vnew", "S"))
        WT = T_
        OWN = LEVELS[:4]
        M1 = [[sb(f"M1_{d}{lv}", [P, HEADS, P]) for lv in OWN] + [A_[d]] * (len(LEVELS) - len(OWN))
              for d in range(NDIR)]
        small = sb("small", [P, NDIR, 8, HEADS])
        g_, beta, Gc, gd, eGc, egd, beg, eGl = ([small[:, d, n, :] for d in range(NDIR)] for n in range(8))
        o = sb("o", [P, HEADS, SEQ])
        none = sb("none", [P, NDIR])
        loaded = [sem(f"loaded{s}") for s in range(2)]
        zeroed, o_zeroed, o_stored = sem("zeroed"), sem("o_zeroed"), sem("o_stored")
        both = lambda names: " ".join(f"{x}{d}" for x in names.split() for d in range(NDIR))
        D = Stages(sem("dve_stage"), both("Gc gd E0_ E kd kbe vb eGl qg Dm A attn Ti T0_ TTi TT0_") + " " + " ".join(
            f"M{n}_0 M{n}_1 " + " ".join((f"T{n}_{d} " if n < LEVELS[-1] else "") + f"TT{n}_{d}" for d in range(NDIR))
            for n in LEVELS) + " " + both("S o"))
        DG = Stages(sem("dve_gb"), both("gb"))
        A = Stages(sem("act_stage"), both("eGc egd E eGr AT attnT WT vnew"))
        T = Stages(sem("pe_stage"), both("gram flip") + " " + " ".join(
            f"a{n}_0 a{n}_1 " + " ".join((f"t{n}_{d} " if n < LEVELS[-1] else "") + f"b{n}_{d}" for d in range(NDIR))
            for n in LEVELS) + " " + both("w v os"))
        TR, TC, TK = Stages(sem("pe_rows"), both("rows")), Stages(sem("pe_columns"), both("cols")), Stages(
            sem("pe_tokens"), both("tok"))
        block = st.enter_context(nc.Block())
        last = (P - 1, 0)
        cum = (chip.up, chip.low)
        seen = (chip.low, chip.up)
        B = [[bank[:, 4 * d + n, :] for n in range(4)] for d in range(NDIR)]
        B3 = [[b.rearrange("p (h c) -> p h c", h=HEADS) for b in bs] for bs in B]

        def half(x, lv, side):
            return x.rearrange("p h (g two b) -> p h g two b", two=2, b=2 ** lv)[:, :, :, side, :]

        LAST = "last"

        def turns(eng, body):
            for n in range(2):
                body(n, n, n)
            with eng.Fori(1, NT // 2 - 1) as i:
                for s in range(2):
                    body(2 * i + s, s, None)
            body(NT - 2, 0, None)
            body(NT - 1, 1, LAST)

        in_context = lambda ctx: isinstance(ctx, int)

        def tile(n, ctx, d):
            if d == 0:
                return n
            return 1 - n if in_context(ctx) else NT + 1 - n

        @block.sync
        def _(sp):
            def body(n, s, ctx):
                if not in_context(ctx):
                    sp.wait_ge(D.sem, D.at(n - 2, "attn1"))
                for d in range(NDIR):
                    sp.dma_start(qkv[d][s][:], sa[:, :, bass.ds(tile(n, ctx, d) * P, P)].rearrange("a p t -> p a t")
                                 ).then_inc(loaded[s], 16)
            turns(sp, body)
            sp.wait_ge(D.sem, D.at(NT - 1, "o1"))
            sp.dma_start(so_a.rearrange("h p t -> p h t"), o[:]).then_inc(o_stored, 16)
            sp.wait_ge(o_stored, 16)

        @block.gpsimd
        def _(pool):
            for d in range(NDIR):
                for m in [S[d]] + M1[d][:len(OWN)]:
                    z = nc.gpsimd.memset(m[:], 0.0)
            z.then_inc(zeroed, 1)
            nc.gpsimd.memset(o[:], 0.0).then_inc(o_zeroed, 1)

        @block.tensor
        def _(pe):
            pe.wait_ge(zeroed, 1)

            def heads(fn):
                for h in range(HEADS):
                    m = fn(h)
                return m

            def rows(n):
                for d in range(NDIR):
                    pe.wait_ge(DG.sem, DG.at(n, f"gb{d}"))
                    heads(lambda h: pe.matmul(B3[d][1][:, h, :], g_[d][:, h:h + 1].broadcast_to([P, P]), cum[d][:],
                                              start=True, stop=True)).then_inc(TR(f"rows{d}"), 1)

            def body(n, s, ctx):
                pe.wait_ge(loaded[s], (n - s) // 2 * 32 + 32)
                for d in range(NDIR):
                    if ctx != 0:
                        pe.wait_ge(A.sem, A.at(n - 1, f"vnew{d}"))
                    pe.matmul(B[d][0][:, 0:HEADS], cum[d][:], g_[d], start=True, stop=True
                              ).then_inc(TC(f"cols{d}"), 1)
                for d in range(NDIR):
                    x = qkv[d][s]
                    if ctx != 0:
                        pe.wait_ge(D.sem, D.at(n - 1, f"o{d}"))
                    heads(lambda h: pe.transpose(B3[d][2][:, h, :], x[:, HEADS + h, :], chip.ident[:]))
                    heads(lambda h: pe.transpose(B3[d][3][:, h, :], x[:, 2 * HEADS + h, :], chip.ident[:])
                          ).then_inc(TK(f"tok{d}"), 1)
                for d in range(NDIR):
                    x = qkv[d][s]
                    pe.wait_ge(D.sem, D.at(n, f"Gc{d}"))
                    heads(lambda h: pe.matmul(B3[d][0][:, h, :], x[:, HEADS + h, :], x[:, HEADS + h, :], start=True,
                                              stop=True))
                    pe.wait_ge(D.sem, D.at(n, f"E0_{d}"))
                    pe.wait_ge(A.sem, A.at(n, f"eGr{d}"))
                    heads(lambda h: pe.matmul(B3[d][1][:, h, :], x[:, h, :], x[:, HEADS + h, :], start=True,
                                              stop=True)).then_inc(T(f"gram{d}"), 1)
                for d in range(NDIR):
                    pe.wait_ge(D.sem, D.at(n, f"A{d}"))
                    heads(lambda h: pe.transpose(B3[d][0][:, h, :], A_[d][:, h, :], chip.ident[:]))
                    pe.wait_ge(D.sem, D.at(n, f"attn{d}"))
                    heads(lambda h: pe.transpose(B3[d][2][:, h, :], Dm[d][:, h, :], chip.ident[:])
                          ).then_inc(T(f"flip{d}"), 1)
                for lv in LEVELS:
                    for d in range(NDIR):
                        if lv == 1:
                            pe.wait_ge(A.sem, A.at(n, f"AT{d}"))
                        pe.wait_ge(D.sem, D.at(n, f"T{lv - 1}_{d}"))
                        heads(lambda h: pe.matmul(B3[d][0][:, h, :], AT[d][:, h, :], T_[d][:, h, :], start=True,
                                                  stop=True)).then_inc(T(f"a{lv}_{d}"), 1)
                    for d in range(NDIR):
                        m1 = M1[d][lv - 1]
                        if lv == 1:
                            pe.wait_ge(A.sem, A.at(n, f"attnT{d}"))
                        pe.wait_ge(D.sem, D.at(n, f"M{lv}_{d}"))
                        if lv < 6:
                            heads(lambda h: pe.matmul(B3[d][1][:, h, :], TT[d][:, h, :], m1[:, h, :], start=True,
                                                      stop=True)).then_inc(T(f"t{lv}_{d}"), 1)
                        heads(lambda h: pe.matmul(B3[d][2][:, h, :], m1[:, h, :], TT[d][:, h, :], start=True,
                                                  stop=True)).then_inc(T(f"b{lv}_{d}"), 1)
                for d in range(NDIR):
                    pe.wait_ge(D.sem, D.at(n, f"TT6_{d}"))
                    heads(lambda h: pe.matmul(B3[d][1][:, h, :], kbe[d][:, h, :], TT[d][:, h, :], start=True,
                                              stop=True)).then_inc(T(f"w{d}"), 1)
                for d in range(NDIR):
                    pe.wait_ge(A.sem, A.at(n, f"WT{d}"))
                    if ctx != 0:
                        pe.wait_ge(D.sem, D.at(n - 1, f"S{d}"))
                    for h in range(HEADS):
                        pe.matmul(B3[d][0][:, h, :], TT[d][:, h, :], vb[d][:, h, :], start=True, stop=False)
                        m = pe.matmul(B3[d][0][:, h, :], WT[d][:, h, :], S[d][:, h, :], start=False, stop=True)
                    m.then_inc(T(f"v{d}"), 1)
                if ctx is not LAST:
                    rows(n + 1)
                for d in range(NDIR):
                    pe.wait_ge(A.sem, A.at(n, f"vnew{d}"))
                    for h in range(HEADS):
                        pe.matmul(B3[d][2][:, h, :], S[d][:, h, :], qg[d][:, h, :], start=True, stop=False)
                        pe.matmul(B3[d][2][:, h, :], vnew[d][:, h, :], attnT[d][:, h, :], start=False, stop=True)
                    heads(lambda h: pe.matmul(B3[d][3][:, h, :], kd[d][:, h, :], vnew[d][:, h, :], start=True,
                                              stop=True)).then_inc(T(f"os{d}"), 1)
            rows(0)
            turns(pe, body)

        @block.scalar
        def _(act):
            def body(n, s, ctx):
                for d in range(NDIR):
                    act.wait_ge(D.sem, D.at(n, f"Gc{d}"))
                    act.activation(eGc[d], Gc[d], ACT.Exp).then_inc(A(f"eGc{d}"), 1)
                for d in range(NDIR):
                    act.wait_ge(D.sem, D.at(n, f"gd{d}"))
                    act.activation(egd[d], gd[d], ACT.Exp).then_inc(A(f"egd{d}"), 1)
                for d in range(NDIR):
                    act.wait_ge(D.sem, D.at(n, f"E{d}"))
                    act.activation(Dm[d][:], Dm[d][:], ACT.Exp).then_inc(A(f"E{d}"), 1)
                for d in range(NDIR):
                    act.activation(qg[d][:], B3[d][1][:], ACT.Exp).then_inc(A(f"eGr{d}"), 1)
                for d in range(NDIR):
                    act.wait_ge(T.sem, T.at(n, f"flip{d}"))
                    act.activation(AT[d][:], B3[d][0][:], ACT.Copy).then_inc(A(f"AT{d}"), 1)
                for d in range(NDIR):
                    act.activation(attnT[d][:], B3[d][2][:], ACT.Copy).then_inc(A(f"attnT{d}"), 1)
                for d in range(NDIR):
                    act.wait_ge(T.sem, T.at(n, f"w{d}"))
                    act.activation(WT[d][:], B3[d][1][:], ACT.Copy, scale=-1.0).then_inc(A(f"WT{d}"), 1)
                for d in range(NDIR):
                    act.wait_ge(T.sem, T.at(n, f"v{d}"))
                    act.activation(vnew[d][:], B3[d][0][:], ACT.Copy).then_inc(A(f"vnew{d}"), 1)
            turns(act, body)

        @block.vector
        def _(dve):
            dve.wait_ge(zeroed, 1)
            per_token = lambda col: bcast(col, 2, P)
            per_pair = lambda m: bcast(m, 1, HEADS)

            def decays(n, in_ctx):
                for d in range(NDIR):
                    t = tile(n, in_ctx, d)
                    row = lambda src: src[:, bass.ds(t, 1), d * HEADS:(d + 1) * HEADS].rearrange("p a h -> p (a h)")
                    dve.tensor_copy(beta[d], row(chip.beta_tok))
                    dve.tensor_copy(g_[d], row(chip.decay_tok)).then_inc(DG(f"gb{d}"), 1)

            def body(n, s, ctx):
                for d in range(NDIR):
                    dve.wait_ge(TC.sem, TC.at(n, f"cols{d}"))
                    dve.tensor_copy(Gc[d], B[d][0][:, 0:HEADS]).then_inc(D(f"Gc{d}"), 1)
                for d in range(NDIR):
                    dve.wait_ge(D.sem, D.at(n, f"Gc{d}"))
                    dve.tensor_tensor(gd[d], B3[d][1][:, :, last[d]], Gc[d], ALU.subtract).then_inc(D(f"gd{d}"), 1)
                for d in range(NDIR):
                    dve.scalar_tensor_tensor(out=Dm[d][:], in0=B3[d][1][:], scalar=-1.0, in1=per_token(Gc[d]),
                                             op0=ALU.mult, op1=ALU.add).then_inc(D(f"E0_{d}"), 1)
                for d in range(NDIR):
                    dve.wait_ge(D.sem, D.at(n, f"E0_{d}"))
                    dve.tensor_scalar(Dm[d][:], Dm[d][:], 0.0, None, ALU.min).then_inc(D(f"E{d}"), 1)
                for d in range(NDIR):
                    dve.wait_ge(A.sem, A.at(n, f"egd{d}"))
                    dve.wait_ge(TK.sem, TK.at(n, f"tok{d}"))
                    dve.tensor_tensor(beg[d], eGc[d], beta[d], ALU.mult)
                    dve.tensor_tensor(kd[d][:], B3[d][2][:], per_token(egd[d]), ALU.mult).then_inc(D(f"kd{d}"), 1)
                for d in range(NDIR):
                    dve.wait_ge(D.sem, D.at(n, f"kd{d}"))
                    dve.tensor_tensor(kbe[d][:], B3[d][2][:], per_token(beg[d]), ALU.mult).then_inc(D(f"kbe{d}"), 1)
                for d in range(NDIR):
                    dve.tensor_tensor(vb[d][:], B3[d][3][:], per_token(beta[d]), ALU.mult).then_inc(D(f"vb{d}"), 1)
                for d in range(NDIR):
                    dve.wait_ge(A.sem, A.at(n, f"eGr{d}"))
                    dve.tensor_copy(eGl[d], qg[d][:, :, last[d]]).then_inc(D(f"eGl{d}"), 1)
                for d in range(NDIR):
                    dve.wait_ge(D.sem, D.at(n, f"eGl{d}"))
                    dve.tensor_tensor(qg[d][:], qg[d][:], qkv[d][s][:, 0:HEADS, :], ALU.mult).then_inc(D(f"qg{d}"), 1)
                for d in range(NDIR):
                    dve.tensor_tensor(Dm[d][:], Dm[d][:], per_pair(seen[d][:]), ALU.mult).then_inc(D(f"Dm{d}"), 1)
                for d in range(NDIR):
                    dve.wait_ge(T.sem, T.at(n, f"gram{d}"))
                    dve.wait_ge(D.sem, D.at(n, f"Dm{d}"))
                    for h in range(HEADS):
                        m = dve.scalar_tensor_tensor(out=A_[d][:, h, :], in0=B3[d][0][:, h, :],
                                                     scalar=beta[d][:, h:h + 1], in1=Dm[d][:, h, :], op0=ALU.mult,
                                                     op1=ALU.mult)
                    m.then_inc(D(f"A{d}"), 1)
                for d in range(NDIR):
                    dve.wait_ge(D.sem, D.at(n, f"A{d}"))
                    dve.tensor_tensor(Dm[d][:], B3[d][1][:], Dm[d][:], ALU.mult).then_inc(D(f"attn{d}"), 1)
                for d in range(NDIR):
                    dve.scalar_tensor_tensor(out=T_[d][:], in0=A_[d][:], scalar=-1.0,
                                             in1=per_pair(chip.off[:, d, 0, :]), op0=ALU.mult, op1=ALU.mult
                                             ).then_inc(D(f"Ti{d}"), 1)
                for d in range(NDIR):
                    dve.wait_ge(D.sem, D.at(n, f"Ti{d}"))
                    dve.tensor_tensor(T_[d][:], T_[d][:], per_pair(chip.ident[:]), ALU.add).then_inc(D(f"T0_{d}"), 1)
                for d in range(NDIR):
                    dve.wait_ge(A.sem, A.at(n, f"AT{d}"))
                    dve.scalar_tensor_tensor(out=TT[d][:], in0=AT[d][:], scalar=-1.0,
                                             in1=per_pair(chip.off[:, 1 - d, 0, :]), op0=ALU.mult, op1=ALU.mult
                                             ).then_inc(D(f"TTi{d}"), 1)
                for d in range(NDIR):
                    dve.wait_ge(D.sem, D.at(n, f"TTi{d}"))
                    dve.tensor_tensor(TT[d][:], TT[d][:], per_pair(chip.ident[:]), ALU.add).then_inc(D(f"TT0_{d}"), 1)
                for lv in LEVELS:
                    for d in range(NDIR):
                        dve.wait_ge(T.sem, T.at(n, f"a{lv}_{d}"))
                        if lv in OWN:
                            off = half(chip.off[:, d, lv:lv + 1, :], lv, d)
                            off = off.broadcast_to([P, HEADS, *off.shape[2:]])
                            dve.tensor_tensor(half(M1[d][lv - 1], lv, d), half(B3[d][0], lv, d), off, ALU.mult
                                              ).then_inc(D(f"M{lv}_{d}"), 1)
                        else:
                            dve.tensor_tensor(M1[d][lv - 1][:], B3[d][0][:], per_pair(chip.off[:, d, lv, :]), ALU.mult
                                              ).then_inc(D(f"M{lv}_{d}"), 1)
                    for d in range(NDIR):
                        if lv < LEVELS[-1]:
                            dve.wait_ge(T.sem, T.at(n, f"t{lv}_{d}"))
                            t = half(T_[d], lv, d)
                            dve.tensor_tensor(t, t, half(B3[d][1], lv, d), ALU.subtract
                                              ).then_inc(D(f"T{lv}_{d}"), 1)
                        dve.wait_ge(T.sem, T.at(n, f"b{lv}_{d}"))
                        t = half(TT[d], lv, 1 - d)
                        dve.tensor_tensor(t, t, half(B3[d][2], lv, 1 - d), ALU.subtract
                                          ).then_inc(D(f"TT{lv}_{d}"), 1)
                if ctx is not LAST:
                    decays(n + 1, ctx if ctx == 0 else None)
                if ctx == 1:
                    dve.wait_ge(o_zeroed, 1)
                for d in range(NDIR):
                    dve.wait_ge(T.sem, T.at(n, f"os{d}"))
                    for h in range(HEADS):
                        m = dve.scalar_tensor_tensor(out=S[d][:, h, :], in0=S[d][:, h, :], scalar=eGl[d][:, h:h + 1],
                                                     in1=B3[d][3][:, h, :], op0=ALU.mult, op1=ALU.add)
                    m.then_inc(D(f"S{d}"), 1)
                for d in range(NDIR):
                    if in_context(ctx):
                        dve.memset(none[:, d:d + 1], 0.0).then_inc(D(f"o{d}"), 1)
                        continue
                    t = o[:, :, bass.ds((tile(n, ctx, d) - CTX // P) * P, P)]
                    dve.tensor_tensor(t, t, B3[d][2][:], ALU.add).then_inc(D(f"o{d}"), 1)
            decays(0, 0)
            turns(dve, body)


def phase_gla(chip, sq_, sv, sk, sg, so_b):
    nc, bank = chip.nc, chip.bank
    HALF = (64, 32, 16)
    with ExitStack() as st:
        sb = lambda n, s: st.enter_context(nc.sbuf_tensor("gla_" + n, s, F32))
        sem = lambda n: st.enter_context(nc.semaphore("gla_" + n))
        mat = lambda n: [sb(f"{n}{d}", [P, HEADS, P]) for d in range(NDIR)]
        qvkg = [[sb(f"qvkg{d}{s}", [P, 4, HEADS, P]) for s in range(2)] for d in range(NDIR)]
        qg, kdT, dq, dk, v, kd, attnT, S = (mat(n) for n in ("qg", "kdT", "dq", "dk", "v", "kd", "attnT", "S"))
        X = [mat(f"X{L}_") for L in HALF]
        eGl = [sb(f"eGl{d}", [P, HEADS]) for d in range(NDIR)]
        o = sb("o", [P, HEADS, SEQ])
        none = sb("none", [P, NDIR])
        num = lambda n: isinstance(n, int)
        loaded = [sem(f"loaded{s}") for s in range(2)]
        zeroed, o_zeroed, o_stored = sem("zeroed"), sem("o_zeroed"), sem("o_stored")
        D = [Stages(sem(f"dve_stage{d}"), "ekd ex0 ex1 ex2 edq qg kd x0 x1 x2 dq dk diag lv0 lv1 lv2")
             for d in range(NDIR)]
        DO = [Stages(sem(f"dve_sums{d}"), "S o") for d in range(NDIR)]
        A = [Stages(sem(f"act_stage{d}"), "qg kd x0 x1 x2 dk dq v kdtok") for d in range(NDIR)]
        T = [Stages(sem(f"pe_stage{d}"), "v kd lv diag") for d in range(NDIR)]
        TO = [Stages(sem(f"pe_sums{d}"), "os") for d in range(NDIR)]
        block = st.enter_context(nc.Block())
        last = (P - 1, 0)
        B = [[bank[:, 4 * d + n, :] for n in range(4)] for d in range(NDIR)]
        B3 = [[b.rearrange("p (h c) -> p h c", h=HEADS) for b in bs] for bs in B]

        def turns(eng, body):
            def turn(n, s):
                for d in range(NDIR):
                    body(n, s, d)
            for n in range(3):
                turn(n, n % 2)
            with eng.Fori(0, (NT - 4) // 2) as i:
                turn(2 * i + 3, 1)
                turn(2 * i + 4, 0)
            turn(NT - 1, 1)

        in_context = lambda n: num(n) and n < 2

        def tile(n, d):
            if d == 0:
                return n
            return 1 - n if in_context(n) else NT + 1 - n

        def before(n, d):
            return (n if d else n - 1), 1 - d

        def halves(m, L):
            return m.rearrange("p h c -> p (h c)").rearrange("p (b e l) -> p b e l", e=2, l=L)

        def where(d, n):
            L = HALF[n]
            b = B[d][3][:, 256 * n:256 * n + 256] if n < 2 else B[d][0][:, 0:256]
            return b.rearrange("p (h b l) -> p h b l", h=HEADS, l=L)

        @block.sync
        def _(sp):
            def load(n, s):
                if not in_context(n):
                    for d in range(NDIR):
                        sp.wait_ge(D[d].sem, D[d].at(n - 2, "dk"))
                        sp.wait_ge(T[d].sem, T[d].at(n - 2, "v"))
                for d in range(NDIR):
                    hs = slice(d * HEADS, (d + 1) * HEADS)
                    for m, src in enumerate((sq_, sv, sk[hs], sg[hs])):
                        sp.dma_start(qvkg[d][s][:, m], src[:, :, bass.ds(tile(n, d) * P, P)].rearrange(
                            "h p t -> p h t")).then_inc(loaded[s], 16)
            turns(sp, lambda n, s, d: load(n, s) if d == 0 else None)
            for d in range(NDIR):
                sp.wait_ge(DO[d].sem, DO[d].at(NT - 1, "o"))
            sp.dma_start(so_b.rearrange("h p t -> p h t"), o[:]).then_inc(o_stored, 16)
            sp.wait_ge(o_stored, 16)

        @block.gpsimd
        def _(pool):
            for d in range(NDIR):
                z = nc.gpsimd.memset(S[d][:], 0.0)
            z.then_inc(zeroed, 1)
            nc.gpsimd.memset(o[:], 0.0).then_inc(o_zeroed, 1)

        def land(eng, n, s):
            eng.wait_ge(loaded[s], (n - s) // 2 * 128 + 128)

        @block.tensor
        def _(pe):
            pe.wait_ge(zeroed, 1)

            def scores(n, s, d):
                land(pe, n, s)
                if not (num(n) and n == 0):
                    pe.wait_ge(D[d].sem, D[d].at(n - 1, "lv2"))
                for h in range(HEADS):
                    m = pe.transpose(B3[d][0][:, h, :], qvkg[d][s][:, 1, h, :], chip.ident[:])
                m.then_inc(T[d]("v"), 1)
                if not (num(n) and n == 0 and d == 0):
                    sums(*before(n, d))
                if not (num(n) and n == 0):
                    pe.wait_ge(DO[d].sem, DO[d].at(n - 1, "o"))
                pe.wait_ge(D[d].sem, D[d].at(n, "kd"))
                for h in range(HEADS):
                    m = pe.transpose(B3[d][1][:, h, :], kdT[d][:, h, :], chip.ident[:])
                m.then_inc(T[d]("kd"), 1)
                pe.wait_ge(A[d].sem, A[d].at(n, "v"))
                for lv, L in enumerate(HALF):
                    pe.wait_ge(D[d].sem, D[d].at(n, f"x{lv}"))
                    xs = X[lv][d][:].rearrange("p h (b e l) -> p h b e l", e=2, l=L)
                    for h in range(HEADS):
                        m = pe.matmul(where(d, lv)[:, h], X[lv][d][:, h, :], xs[:, h, :, 1 - d, :], start=True,
                                      stop=True)
                m.then_inc(T[d]("lv"), 1)
                pe.wait_ge(D[d].sem, D[d].at(n, "dk"))
                for h in range(HEADS):
                    m = pe.matmul(B3[d][2][:, h, :], dk[d][:, h, :], dq[d][:, h, :], start=True, stop=True)
                m.then_inc(T[d]("diag"), 1)

            def sums(n, d):
                pe.wait_ge(A[d].sem, A[d].at(n, "kdtok"))
                pe.wait_ge(D[d].sem, D[d].at(n, "lv2"))
                for h in range(HEADS):
                    pe.matmul(B3[d][1][:, h, :], S[d][:, h, :], qg[d][:, h, :], start=True, stop=False)
                    pe.matmul(B3[d][1][:, h, :], v[d][:, h, :], attnT[d][:, h, :], start=False, stop=True)
                for h in range(HEADS):
                    m = pe.matmul(B3[d][2][:, h, :], kd[d][:, h, :], v[d][:, h, :], start=True, stop=True)
                m.then_inc(TO[d]("os"), 1)

            turns(pe, scores)
            sums(NT - 1, 1)

        @block.scalar
        def _(act):
            def body(n, s, d):
                land(act, n, s)
                if not (num(n) and n == 0):
                    act.wait_ge(TO[d].sem, TO[d].at(n - 1, "os"))
                act.activation(qg[d][:], qvkg[d][s][:, 3], ACT.Exp).then_inc(A[d]("qg"), 1)
                act.wait_ge(D[d].sem, D[d].at(n, "ekd"))
                act.activation(kdT[d][:], kdT[d][:], ACT.Exp).then_inc(A[d]("kd"), 1)
                for lv in range(3):
                    act.wait_ge(D[d].sem, D[d].at(n, f"ex{lv}"))
                    act.activation(X[lv][d][:], X[lv][d][:], ACT.Exp).then_inc(A[d](f"x{lv}"), 1)
                act.wait_ge(D[d].sem, D[d].at(n, "edq"))
                act.activation(dk[d][:], dq[d][:], ACT.Exp, scale=-1.0).then_inc(A[d]("dk"), 1)
                act.wait_ge(A[d].sem, A[d].at(n, "dk"))
                act.activation(dq[d][:], dq[d][:], ACT.Exp).then_inc(A[d]("dq"), 1)
                act.wait_ge(T[d].sem, T[d].at(n, "v"))
                act.activation(v[d][:], B3[d][0][:], ACT.Copy).then_inc(A[d]("v"), 1)
                act.wait_ge(T[d].sem, T[d].at(n, "kd"))
                act.activation(kd[d][:], B3[d][1][:], ACT.Copy).then_inc(A[d]("kdtok"), 1)
            turns(act, body)

        @block.vector
        def _(dve):
            dve.wait_ge(zeroed, 1)

            def reference(n, s, d, lv):
                L = HALF[lv]
                if not (num(n) and n == 0):
                    dve.wait_ge(T[d].sem, T[d].at(n - 1, "lv"))
                g, x = halves(qvkg[d][s][:, 3], L), halves(X[lv][d][:], L)
                nb = HEADS * P // (2 * L)
                ref = (g[:, :, 0, L - 1:L] if d == 0 else g[:, :, 1, 0:1]).broadcast_to([P, nb, L])
                ask, key = 1 - d, d
                dve.tensor_tensor(x[:, :, ask, :], g[:, :, ask, :], ref, ALU.subtract)
                dve.tensor_tensor(x[:, :, key, :], ref, g[:, :, key, :], ALU.subtract).then_inc(D[d](f"ex{lv}"), 1)

            def sums(n, d):
                dve.wait_ge(TO[d].sem, TO[d].at(n, "os"))
                for h in range(HEADS):
                    m = dve.scalar_tensor_tensor(out=S[d][:, h, :], in0=S[d][:, h, :], scalar=eGl[d][:, h:h + 1],
                                                 in1=B3[d][2][:, h, :], op0=ALU.mult, op1=ALU.add)
                m.then_inc(DO[d]("S"), 1)
                if in_context(n):
                    dve.memset(none[:, d:d + 1], 0.0).then_inc(DO[d]("o"), 1)
                    if n == 1 and d == 0:
                        dve.wait_ge(o_zeroed, 1)
                    return
                if not (num(n) and n == 2) or d == 1:
                    m, e = before(n, d)
                    dve.wait_ge(DO[e].sem, DO[e].at(m, "o"))
                    dve.nop(nofuse=True)
                t = o[:, :, bass.ds((tile(n, d) - CTX // P) * P, P)]
                dve.tensor_tensor(t, t, B3[d][1][:], ALU.add).then_inc(DO[d]("o"), 1)

            def prepare(n, s, d):
                land(dve, n, s)
                if not (num(n) and n == 0):
                    dve.wait_ge(T[d].sem, T[d].at(n - 1, "kd"))
                G = qvkg[d][s][:, 3]
                dve.tensor_tensor(kdT[d][:], G[:, :, last[d]:last[d] + 1].broadcast_to([P, HEADS, P]), G,
                                  ALU.subtract).then_inc(D[d]("ekd"), 1)
                reference(n, s, d, 0)
                if not (num(n) and n == 0):
                    sums(n - 1, d)
                reference(n, s, d, 1)
                reference(n, s, d, 2)
                g = qvkg[d][s][:, 3].rearrange("p h c -> p (h c)").rearrange("p (b l) -> p b l", l=16)
                x = dq[d][:].rearrange("p h c -> p (h c)").rearrange("p (b l) -> p b l", l=16)
                e = 15 * d
                if not (num(n) and n == 0):
                    dve.wait_ge(T[d].sem, T[d].at(n - 1, "diag"))
                dve.tensor_tensor(x, g, g[:, :, e:e + 1].broadcast_to([P, HEADS * 8, 16]), ALU.subtract
                                  ).then_inc(D[d]("edq"), 1)
                if not (num(n) and n == 0 and d == 0):
                    gather(*before(n, d))
                dve.wait_ge(A[d].sem, A[d].at(n, "qg"))
                if not (num(n) and n == 0):
                    dve.wait_ge(DO[d].sem, DO[d].at(n - 1, "S"))
                dve.tensor_copy(eGl[d][:], qg[d][:, :, last[d]]).then_inc(D[d]("qg"), 1)
                dve.wait_ge(A[d].sem, A[d].at(n, "kd"))
                dve.wait_ge(D[d].sem, D[d].at(n, "qg"))
                dve.tensor_tensor(qg[d][:], qg[d][:], qvkg[d][s][:, 0], ALU.mult)
                dve.tensor_tensor(kdT[d][:], kdT[d][:], qvkg[d][s][:, 2], ALU.mult).then_inc(D[d]("kd"), 1)
                for lv, L in enumerate(HALF):
                    dve.wait_ge(A[d].sem, A[d].at(n, f"x{lv}"))
                    x = halves(X[lv][d][:], L)
                    dve.tensor_tensor(x[:, :, 1 - d, :], x[:, :, 1 - d, :],
                                      halves(qvkg[d][s][:, 0], L)[:, :, 1 - d, :], ALU.mult)
                    dve.tensor_tensor(x[:, :, d, :], x[:, :, d, :], halves(qvkg[d][s][:, 2], L)[:, :, d, :],
                                      ALU.mult).then_inc(D[d](f"x{lv}"), 1)
                dve.wait_ge(A[d].sem, A[d].at(n, "dq"))
                dve.tensor_tensor(dq[d][:], dq[d][:], qvkg[d][s][:, 0], ALU.mult).then_inc(D[d]("dq"), 1)
                dve.tensor_tensor(dk[d][:], dk[d][:], qvkg[d][s][:, 2], ALU.mult).then_inc(D[d]("dk"), 1)

            def gather(n, d):
                dve.wait_ge(T[d].sem, T[d].at(n, "diag"))
                dve.tensor_tensor(attnT[d][:], B3[d][2][:], bcast(chip.diag16[:, d, :], 1, HEADS), ALU.mult
                                  ).then_inc(D[d]("diag"), 1)
                for lv, L in enumerate(HALF):
                    ask = 1 - d
                    dve.wait_ge(D[d].sem, D[d].at(n, f"lv{lv - 1}" if lv else "diag"))
                    dve.nop(nofuse=True)
                    mask = chip.off[:, 1 - d, 6 - lv, :].bitcast(U32).rearrange("p (b e l) -> p b e l", e=2, l=L)
                    out = attnT[d][:].rearrange("p h (b e l) -> p h b e l", e=2, l=L)[:, :, :, ask, :]
                    dve.copy_predicated(out, bcast(mask[:, :, ask, :], 1, HEADS), where(d, lv)
                                        ).then_inc(D[d](f"lv{lv}"), 1)

            turns(dve, prepare)
            sums(NT - 1, 0)
            gather(NT - 1, 1)
            sums(NT - 1, 1)


def phase_branch_gates(chip, uT, w_in, so_a, so_b, a_norm_g, b_norm_g, yT):
    nc, bank = chip.nc, chip.bank
    NF = 2 * HEADS
    NB = LATENT_BLOCKS
    with ExitStack() as st:
        sb = lambda n, s: st.enter_context(nc.sbuf_tensor("gates_" + n, s, F32))
        sem = lambda n: st.enter_context(nc.semaphore("gates_" + n))
        W = sb("W", [P, 2, KT, P])
        o = sb("o", [P, 2, SEQ])
        sq = sb("sq", [P, SEQ])
        inv = sb("inv", [P, SEQ])
        silu = sb("silu", [P, SEQ])
        gain = sb("gain", [P, 2])
        w_loaded = [sem(f"w_loaded{s}") for s in range(2)]
        o_loaded = [sem(f"o_loaded{s}") for s in range(2)]
        gain_loaded = sem("gain_loaded")
        T = Stages(sem("pe_stage"), " ".join([f"proj{b}" for b in range(NB)] + [f"sum{b}" for b in range(NB)]))
        A = Stages(sem("act_stage"), "sq " + " ".join(f"silu{b}" for b in range(NB)) + " rinv")
        D = Stages(sem("dve_stage"), " ".join(f"ss{b}" for b in range(NB)) + " inv o y")
        block = st.enter_context(nc.Block())

        def turns(eng, body):
            body(0, 0, 0)
            body(0, 1, 0)
            for br in range(2):
                with eng.Fori(max(1, br * HEADS // 2), (br + 1) * HEADS // 2) as i:
                    for s in range(2):
                        body(i, s, br)

        def first(i):
            return isinstance(i, int) and i == 0

        @block.sync
        def _(sp):
            for br, g in enumerate((a_norm_g, b_norm_g)):
                sp.dma_start(gain[:, br:br + 1], g[0].rearrange("(p a) -> p a", a=1)).then_inc(gain_loaded, 16)

            def body(i, s, br):
                f = 2 * i + s
                if not first(i):
                    sp.wait_ge(T.sem, T.at(f - 2, f"proj{NB - 1}"))
                base = (C_AGATE, C_BGATE - HD)[br]
                sp.dma_start(W[:, s], w_in[:, bass.ds(f * P + base, P)].rearrange("(k p) n -> p k n", p=P)
                             ).then_inc(w_loaded[s], 16)
                if not first(i):
                    sp.wait_ge(D.sem, D.at(f - 2, "y"))
                sp.dma_start(o[:, s, :], (so_a, so_b)[br][bass.ds(f - br * HEADS, 1)].rearrange("a p t -> (a p) t")
                             ).then_inc(o_loaded[s], 16)
            turns(sp, body)

        @block.tensor
        def _(pe):
            def body(i, s, br):
                f = 2 * i + s
                pe.wait_ge(w_loaded[s], i * 16 + 16)
                for b in range(NB):
                    if not (first(i) and s == 0):
                        pe.wait_ge(A.sem, A.at(f - 1, f"silu{b}"))
                    for k in range(KT):
                        mm = pe.matmul(bank[:, b, :], W[:, s, k, :], uT[:, k, CTX + b * BANK:CTX + (b + 1) * BANK],
                                       start=(k == 0), stop=(k == KT - 1))
                    mm.then_inc(T(f"proj{b}"), 1)
                pe.wait_ge(A.sem, A.at(f, "sq"))
                for b in range(NB):
                    if not (first(i) and s == 0):
                        pe.wait_ge(D.sem, D.at(f - 1, f"ss{b}"))
                    pe.matmul(bank[:, 4 + b, :], chip.ones[:], sq[:, b * BANK:(b + 1) * BANK], start=True, stop=True
                              ).then_inc(T(f"sum{b}"), 1)
            turns(pe, body)

        @block.scalar
        def _(act):
            def body(i, s, br):
                f = 2 * i + s
                act.wait_ge(o_loaded[s], i * 16 + 16)
                if not (first(i) and s == 0):
                    act.wait_ge(T.sem, T.at(f - 1, f"sum{NB - 1}"))
                act.activation(sq[:], o[:, s, :], ACT.Square).then_inc(A("sq"), 1)
                for b in range(NB):
                    act.wait_ge(T.sem, T.at(f, f"proj{b}"))
                    if not (first(i) and s == 0):
                        act.wait_ge(D.sem, D.at(f - 1, "y"))
                    act.activation(silu[:, b * BANK:(b + 1) * BANK], bank[:, b, :], ACT.Silu).then_inc(A(f"silu{b}"), 1)
                act.wait_ge(D.sem, D.at(f, "inv"))
                act.activation(inv[:], inv[:], ACT.Sqrt).then_inc(A("rinv"), 1)
            turns(act, body)

        @block.vector
        def _(dve):
            dve.wait_ge(gain_loaded, 32)

            def body(i, s, br):
                f = 2 * i + s
                if not (first(i) and s == 0):
                    dve.wait_ge(D.sem, D.at(f - 1, "o"))
                for b in range(NB):
                    dve.wait_ge(T.sem, T.at(f, f"sum{b}"))
                    dve.tensor_scalar(inv[:, b * BANK:(b + 1) * BANK], bank[:, 4 + b, :], 1.0 / P, EPS1, ALU.mult,
                                      ALU.add).then_inc(D(f"ss{b}"), 1)
                dve.wait_ge(D.sem, D.at(f, f"ss{NB - 1}"))
                dve.reciprocal(inv[:], inv[:]).then_inc(D("inv"), 1)
                dve.wait_ge(A.sem, A.at(f, "rinv"))
                dve.scalar_tensor_tensor(out=o[:, s, :], in0=o[:, s, :], scalar=gain[:, br:br + 1], in1=inv[:],
                                         op0=ALU.mult, op1=ALU.mult).then_inc(D("o"), 1)
                dve.wait_ge(D.sem, D.at(f, "o"))
                grid = lambda v: v.rearrange("p (r w) -> p r w", w=GRID_W)
                by_row = grid(o[:, s, :]) if br == 0 else o[:, s, :].rearrange("p (w r) -> p r w", r=ROWS)
                dve.tensor_tensor(grid(yT[:, bass.ds(f, 1), :].rearrange("p a t -> p (a t)")), by_row, grid(silu[:]),
                                  ALU.mult).then_inc(D("y"), 1)
            turns(dve, body)


def phase_merge(chip, uT, w_in, yT, w_a_out, w_b_out, smT):
    nc, bank = chip.nc, chip.bank
    NB = LATENT_BLOCKS
    with ExitStack() as st:
        sb = lambda n, s: st.enter_context(nc.sbuf_tensor("merge_" + n, s, F32))
        sem = lambda n: st.enter_context(nc.semaphore("merge_" + n))
        WG = sb("WG", [P, 2, 2, KT, P])
        WY = sb("WY", [P, 2, 2, HEADS, P])
        sig = sb("sig", [P, 2, 2, BANK])
        row = sb("row", [P, 2, SEQ])
        loaded = [sem(f"loaded{s}") for s in range(2)]
        stored = [sem(f"stored{s}") for s in range(2)]
        T = Stages(sem("pe_stage"), " ".join(f"gate{b} y{b}" for b in range(NB)))
        A = Stages(sem("act_stage"), " ".join(f"sig{b}" for b in range(NB)))
        D = Stages(sem("dve_stage"), " ".join(f"a{b} b{b} sum{b}" for b in range(NB)))
        block = st.enter_context(nc.Block())

        def turns(eng, body):
            body(0, 0)
            body(0, 1)
            with eng.Fori(1, KT // 2) as i:
                for s in range(2):
                    body(i, s)

        first = lambda i: isinstance(i, int) and i == 0

        @block.sync
        def _(sp):
            def body(i, s):
                j = 2 * i + s
                if not first(i):
                    sp.wait_ge(T.sem, T.at(j - 2, f"y{NB - 1}"))
                for br in range(2):
                    sp.dma_start(WG[:, s, br], w_in[:, bass.ds(j * P + C_MERGE + br * DM, P)].rearrange(
                        "(k p) n -> p k n", p=P)).then_inc(loaded[s], 16)
                    sp.dma_start(WY[:, s, br], (w_a_out, w_b_out)[br][:, bass.ds(j * P, P)].rearrange(
                        "(k p) n -> p k n", p=P)).then_inc(loaded[s], 16)
            turns(sp, body)

        @block.gpsimd
        def _(pool):
            def body(i, s):
                j = 2 * i + s
                pool.wait_ge(D.sem, D.at(j, f"sum{NB - 1}"))
                pool.dma_start(smT[bass.ds(j, 1)].rearrange("a p t -> (a p) t"), row[:, s, :]).then_inc(stored[s], 16)
            turns(pool, body)
            for s in range(2):
                pool.wait_ge(stored[s], 16 * KT // 2)

        @block.tensor
        def _(pe):
            def body(i, s):
                j = 2 * i + s
                pe.wait_ge(loaded[s], i * 64 + 64)
                for b in range(NB):
                    q = 4 * (b % 2)
                    if b >= 2:
                        pe.wait_ge(D.sem, D.at(j, f"sum{b - 2}"))
                    elif not (first(i) and s == 0):
                        pe.wait_ge(D.sem, D.at(j - 1, f"sum{b + 2}"))
                    t = slice(CTX + b * BANK, CTX + (b + 1) * BANK)
                    for br in range(2):
                        for k in range(KT):
                            mm = pe.matmul(bank[:, q + br, :], WG[:, s, br, k, :], uT[:, k, t], start=(k == 0),
                                           stop=(k == KT - 1))
                    mm.then_inc(T(f"gate{b}"), 1)
                    for br in range(2):
                        for k in range(HEADS):
                            mm = pe.matmul(bank[:, q + 2 + br, :], WY[:, s, br, k, :],
                                           yT[:, br * HEADS + k, b * BANK:(b + 1) * BANK], start=(k == 0),
                                           stop=(k == HEADS - 1))
                    mm.then_inc(T(f"y{b}"), 1)
            turns(pe, body)

        @block.scalar
        def _(act):
            def body(i, s):
                j = 2 * i + s
                for b in range(NB):
                    act.wait_ge(T.sem, T.at(j, f"gate{b}"))
                    for br in range(2):
                        m = act.activation(sig[:, b % 2, br, :], bank[:, 4 * (b % 2) + br, :], ACT.Sigmoid)
                    m.then_inc(A(f"sig{b}"), 1)
            turns(act, body)

        @block.vector
        def _(dve):
            def body(i, s):
                j = 2 * i + s
                if not first(i):
                    dve.wait_ge(stored[s], i * 16)
                for b in range(NB):
                    q, t = b % 2, slice(b * BANK, (b + 1) * BANK)
                    dve.wait_ge(A.sem, A.at(j, f"sig{b}"))
                    dve.wait_ge(T.sem, T.at(j, f"y{b}"))
                    dve.tensor_tensor(row[:, s, t], bank[:, 4 * q + 2, :], sig[:, q, 0, :], ALU.mult
                                      ).then_inc(D(f"a{b}"), 1)
                    dve.tensor_tensor(sig[:, q, 1, :], bank[:, 4 * q + 3, :], sig[:, q, 1, :], ALU.mult
                                      ).then_inc(D(f"b{b}"), 1)
                    dve.wait_ge(D.sem, D.at(j, f"b{b}"))
                    dve.tensor_tensor(row[:, s, t], row[:, s, t], sig[:, q, 1, :], ALU.add).then_inc(D(f"sum{b}"), 1)
            turns(dve, body)


def layer_norm_steps(dve, D, A, t, x, stats, mv, inv, rstd, eps, g_row):
    width = x.shape[-1]
    for n in range(width // BANK):
        m = dve.bn_stats(stats[:, 6 * n:6 * n + 6], x[:, n * BANK:(n + 1) * BANK])
    m.then_inc(D("stats"), 1)
    dve.wait_ge(D.sem, D.at(t, "stats"))
    dve.nop(nofuse=True)
    dve.bn_aggr(mv, stats[:, 0:6 * (width // BANK)]).then_inc(D("mv"), 1)
    dve.wait_ge(D.sem, D.at(t, "mv"))
    dve.tensor_scalar(mv[:, 1:2], mv[:, 1:2], eps, None, ALU.add).then_inc(D("var"), 1)
    dve.wait_ge(D.sem, D.at(t, "var"))
    dve.reciprocal(inv, mv[:, 1:2]).then_inc(D("inv"), 1)
    dve.wait_ge(A.sem, A.at(t, "rstd"))
    dve.tensor_scalar(x, x, mv[:, 0:1], rstd, ALU.subtract, ALU.mult).then_inc(D("n"), 1)
    dve.wait_ge(D.sem, D.at(t, "n"))
    dve.tensor_tensor(x, x, g_row, ALU.mult).then_inc(D("scaled"), 1)
    dve.wait_ge(D.sem, D.at(t, "scaled"))


def phase_residual(chip, x, smT, w_out, ln_g, ln_b, sh, hT):
    nc, bank = chip.nc, chip.bank
    NTL = SEQ // P
    with ExitStack() as st:
        sb = lambda n, s: st.enter_context(nc.sbuf_tensor("residual_" + n, s, F32))
        sem = lambda n: st.enter_context(nc.semaphore("residual_" + n))
        W = sb("W", [P, KT, DM])
        mT = sb("mT", [P, 2, KT, P])
        xs = sb("xs", [P, 2, DM])
        r = sb("r", [P, 2, DM])
        h = sb("h", [P, 2, DM])
        rows = sb("rows", [P, 2, DM])
        stats, mv, inv, rstd = (sb(n, [P, w]) for n, w in (("stats", 12), ("mv", 2), ("inv", 1), ("rstd", 1)))
        once = sem("once")
        w_loaded = [sem(f"w_loaded{n}") for n in range(4)]
        loaded = [sem(f"loaded{s}") for s in range(2)]
        stored = [sem(f"stored{s}") for s in range(2)]
        T, TU = Stages(sem("pe_mm"), "mm"), Stages(sem("pe_turned"), "turned")
        A = Stages(sem("act_stage"), "rstd hT")
        D = Stages(sem("dve_stage"), "gated sum stats mv var inv n scaled h")
        block = st.enter_context(nc.Block())

        def turns(eng, body):
            body(0, 0)
            body(0, 1)
            with eng.Fori(1, NTL // 2) as i:
                for s in range(2):
                    body(i, s)

        first = lambda i: isinstance(i, int) and i == 0

        @block.sync
        def _(sp):
            def weights():
                for n, w in enumerate(w_loaded):
                    k = slice(2 * n, 2 * n + 2)
                    sp.dma_start(W[:, k, :], w_out.rearrange("(k p) n -> p k n", p=P)[:, k, :]).then_inc(w, 16)
                for n, src in enumerate((ln_g, ln_b)):
                    sp.dma_start(rows[:, n, :], src.broadcast_to([P, DM])).then_inc(once, 16)

            def body(i, s):
                t = 2 * i + s
                if not first(i):
                    sp.wait_ge(T.sem, T.at(t - 2, "mm"))
                    sp.wait_ge(D.sem, D.at(t - 2, "sum"))
                sp.dma_start(mT[:, s], smT[:, :, bass.ds(t * P, P)].rearrange("k p t -> p k t")).then_inc(loaded[s], 16)
                sp.dma_start(xs[:, s], x[bass.ds(t * P, P), :]).then_inc(loaded[s], 16)
                if first(i) and s == 0:
                    weights()
            turns(sp, body)

        @block.gpsimd
        def _(pool):
            def body(i, s):
                t = 2 * i + s
                pool.wait_ge(D.sem, D.at(t, "h"))
                pool.dma_start(sh[bass.ds(t * P, P), :], h[:, s, :]).then_inc(stored[s], 16)
            turns(pool, body)
            for s in range(2):
                pool.wait_ge(stored[s], 16 * NTL // 2)

        @block.tensor
        def _(pe):
            def mm(i, s):
                t = 2 * i + s
                pe.wait_ge(loaded[s], i * 32 + 32)
                if not first(i):
                    pe.wait_ge(D.sem, D.at(t - 2, "gated"))
                for n in range(2):
                    for k in range(KT):
                        if first(i) and s == 0 and n == 0 and k % 2 == 0:
                            pe.wait_ge(w_loaded[k // 2], 16)
                        m = pe.matmul(bank[:, 2 * s + n, :], mT[:, s, k, :], W[:, k, n * BANK:(n + 1) * BANK],
                                      start=(k == 0), stop=(k == KT - 1))
                m.then_inc(T("mm"), 1)

            def turn(i, s):
                t = 2 * i + s
                pe.wait_ge(D.sem, D.at(t, "h"))
                if not first(i):
                    pe.wait_ge(A.sem, A.at(t - 2, "hT"))
                for k in range(KT):
                    m = pe.transpose(bank[:, 4 + 2 * s + k // 4, (k % 4) * P:(k % 4 + 1) * P],
                                     h[:, s, k * P:(k + 1) * P], chip.ident[:])
                m.then_inc(TU("turned"), 1)

            mm(0, 0)
            mm(0, 1)
            turn(0, 0)
            with pe.Fori(1, NTL // 2) as i:
                mm(i, 0)
                turn(i - 1, 1)
                mm(i, 1)
                turn(i, 0)
            turn(NTL // 2 - 1, 1)

        @block.scalar
        def _(act):
            def body(i, s):
                t = 2 * i + s
                act.wait_ge(D.sem, D.at(t, "inv"))
                act.activation(rstd[:], inv[:], ACT.Sqrt).then_inc(A("rstd"), 1)
                act.wait_ge(TU.sem, TU.at(t, "turned"))
                for n in range(2):
                    m = act.activation(hT[:, 4 * n:4 * n + 4, bass.ds(t * P, P)],
                                       bank[:, 4 + 2 * s + n, :].rearrange("p (k t) -> p k t", k=4), ACT.Copy)
                m.then_inc(A("hT"), 1)
            turns(act, body)

        @block.vector
        def _(dve):
            dve.wait_ge(once, 32)

            def body(i, s):
                t = 2 * i + s
                dve.wait_ge(T.sem, T.at(t, "mm"))
                for n in range(2):
                    c = slice(n * BANK, (n + 1) * BANK)
                    m = dve.tensor_tensor(r[:, s, c], bank[:, 2 * s + n, :], chip.gate_rows[:, c], ALU.mult)
                m.then_inc(D("gated"), 1)
                dve.wait_ge(D.sem, D.at(t, "gated"))
                dve.scalar_tensor_tensor(out=r[:, s, :], in0=xs[:, s, :], scalar=ALPHA, in1=r[:, s, :], op0=ALU.mult,
                                         op1=ALU.add).then_inc(D("sum"), 1)
                dve.wait_ge(D.sem, D.at(t, "sum"))
                layer_norm_steps(dve, D, A, t, r[:, s, :], stats[:], mv[:], inv[:], rstd[:], EPS1, rows[:, 0, :])
                if not first(i):
                    dve.wait_ge(stored[s], i * 16)
                    dve.wait_ge(TU.sem, TU.at(t - 2, "turned"))
                dve.tensor_tensor(h[:, s, :], r[:, s, :], rows[:, 1, :], ALU.add).then_inc(D("h"), 1)
            turns(dve, body)


EPS2 = 1e-5
Q_LORA, KV_LORA, ROPE, NOPE = 256, 128, 32, 64
QK = NOPE + ROPE
AH = 8
DV = 64
WIDTH = AH * DV
C_KV, C_KR, C_ZA = Q_LORA, Q_LORA + KV_LORA, Q_LORA + KV_LORA + ROPE
C_U, C_V, C_ZB = C_ZA + WIDTH, C_ZA + 2 * WIDTH, C_ZA + 3 * WIDTH
QT = SEQ // P
NEG = -1e30
TWO_PI = 6.283185307179586


def phase_rotation(chip, positions, inv_freq, rot):
    nc, bank = chip.nc, chip.bank
    R = slice(NOPE, QK)
    HALF = ROPE // 2
    with ExitStack() as st:
        sb = lambda n, s, dt=F32: st.enter_context(nc.sbuf_tensor("rotation_" + n, s, dt))
        sem = lambda n: st.enter_context(nc.semaphore("rotation_" + n))
        consts = sb("consts", [1, 2, QK])
        cols = sb("cols", [QK, 2])
        pos = sb("pos", [QK, SEQ], I32)
        ang, turns_, tmp = (sb(n, [QK, SEQ]) for n in ("ang", "turns", "tmp"))
        pos_loaded, consts_ready, cols_turned = sem("pos_loaded"), sem("consts_ready"), sem("cols_turned")
        table, table_act = sem("table"), sem("table_act")
        block = st.enter_context(nc.Block())

        @block.sync
        def _(sp):
            sp.dma_start(pos[R, :], positions.broadcast_to([ROPE, SEQ])).then_inc(pos_loaded, 16)
            sp.dma_start(consts[:, 0, NOPE:NOPE + HALF], inv_freq).then_inc(pos_loaded, 16)
            sp.dma_start(consts[:, 0, NOPE + HALF:QK], inv_freq).then_inc(pos_loaded, 16)

        @block.gpsimd
        def _(pool):
            nc.gpsimd.memset(consts[:, 1, NOPE:NOPE + HALF], -1.0)
            nc.gpsimd.memset(consts[:, 1, NOPE + HALF:QK], 1.0)
            nc.gpsimd.memset(consts[:, :, 0:NOPE], 0.0).then_inc(consts_ready, 1)

        @block.tensor
        def _(pe):
            pe.wait_ge(consts_ready, 1)
            pe.wait_ge(pos_loaded, 48)
            for n in range(2):
                m = pe.transpose(bank[0:QK, 7, n:n + 1], consts[:, n, :], chip.ident[0:1, 0:1])
            m.then_inc(cols_turned, 1)

        @block.scalar
        def _(act):
            for n in range(2):
                act.wait_ge(table, (9, 13)[n])
                act.activation((tmp, ang)[n][R, :], (tmp, ang)[n][R, :], ACT.Sin).then_inc(table_act, 1)

        @block.vector
        def _(dve):
            count = [0]

            def link(ins):
                count[0] += 1
                ins.then_inc(table, 1)
                dve.wait_ge(table, count[0])
            dve.wait_ge(cols_turned, 1)
            dve.wait_ge(pos_loaded, 48)
            link(dve.tensor_copy(cols[:], bank[0:QK, 7, 0:2]))
            link(dve.tensor_copy(ang[R, :], pos[R, :]))
            link(dve.tensor_scalar(ang[R, :], ang[R, :], cols[R, 0:1], None, ALU.mult))
            link(dve.tensor_scalar(turns_[R, :], ang[R, :], 1.0 / TWO_PI, 12582912.0, ALU.mult, ALU.add))
            link(dve.tensor_scalar(turns_[R, :], turns_[R, :], 12582912.0, None, ALU.subtract))
            parts = (6.28125, 1.9340515136718750e-3, TWO_PI - 6.28125 - 1.9340515136718750e-3)
            for part in parts:
                link(dve.scalar_tensor_tensor(out=ang[R, :], in0=turns_[R, :], scalar=-part, in1=ang[R, :],
                                              op0=ALU.mult, op1=ALU.add))
            PI = 3.1415925
            link(dve.tensor_scalar(tmp[R, :], ang[R, :], PI, -PI, ALU.min, ALU.max))
            link(dve.tensor_scalar(ang[R, :], ang[R, :], TWO_PI / 4, None, ALU.add))
            link(dve.tensor_scalar(turns_[R, :], ang[R, :], PI, -TWO_PI, ALU.is_gt, ALU.mult))
            link(dve.tensor_tensor(ang[R, :], ang[R, :], turns_[R, :], ALU.add))
            link(dve.tensor_scalar(ang[R, :], ang[R, :], PI, -PI, ALU.min, ALU.max))
            dve.wait_ge(table_act, 1)
            link(dve.tensor_scalar(rot[R, 1, :], tmp[R, :], cols[R, 1:2], None, ALU.mult))
            dve.wait_ge(table_act, 2)
            link(dve.tensor_copy(rot[R, 0, :], ang[R, :]))


def phase_latents(chip, hT, w_in, q_norm_g, kv_norm_g, cqT, ckvT, kT, rot, shT):
    nc, bank = chip.nc, chip.bank
    NB = LATENT_BLOCKS
    R = slice(NOPE, QK)
    HALF = ROPE // 2
    with ExitStack() as st:
        sb = lambda n, s, dt=F32: st.enter_context(nc.sbuf_tensor("latents_" + n, s, dt))
        sem = lambda n: st.enter_context(nc.semaphore("latents_" + n))
        W = sb("W", [P, KT, 3 * P])
        WR = sb("WR", [P, KT, 2, QK])
        gains = sb("gains", [P, 3])
        sq = sb("sq", [P, 3, BANK])
        v = sb("v", [P, 2, BANK])
        kr = sb("kr", [QK, 2, BANK])
        once, shT_stored = sem("once"), sem("shT_stored")
        T = Stages(sem("pe_stage"), "proj0 proj1 proj2 kr krs sumq sumkv")
        A = Stages(sem("act_stage"), "raw0 raw1 raw2 sq0 sq1 sq2 rinv")
        D = Stages(sem("dve_stage"), "vq vkv inv q0 q1 kv krc krs kr")
        block = st.enter_context(nc.Block())

        @block.sync
        def _(sp):
            v_ = lambda ap: ap.rearrange("(k p) n -> p k n", p=P)
            sp.dma_start(W[:], v_(w_in[:, 0:3 * P])).then_inc(once, 16)
            sp.dma_start(WR[:, :, 0, :], v_(w_in[:, C_KR - NOPE:C_KR + ROPE])).then_inc(once, 16)
            sp.dma_start(WR[:, :, 1, 0:NOPE], v_(w_in[:, C_KR - NOPE:C_KR])).then_inc(once, 16)
            for half in range(2):
                sp.dma_start(WR[:, :, 1, NOPE + half * HALF:NOPE + (half + 1) * HALF],
                             v_(w_in[:, C_KR + (1 - half) * HALF:C_KR + (2 - half) * HALF])).then_inc(once, 16)
            for f in range(2):
                sp.dma_start(gains[:, f:f + 1], q_norm_g[f * P:(f + 1) * P].rearrange("(p a) -> p a", a=1)
                             ).then_inc(once, 16)
            sp.dma_start(gains[:, 2:3], kv_norm_g.rearrange("(p a) -> p a", a=1)).then_inc(once, 16)
            with sp.Fori(0, QT) as t:
                sp.dma_start(shT[bass.ds(t, 1)].rearrange("a p (k c) -> (a p) k c", k=KT),
                             hT[:, :, bass.ds(t * P, P)]).then_inc(shT_stored, 16)
            sp.wait_ge(shT_stored, 16 * QT)

        @block.tensor
        def _(pe):
            pe.wait_ge(once, 16 * 8)

            def body(b, first):
                rhs = lambda k: hT[:, k, bass.ds(b * BANK, BANK)]
                for f in range(3):
                    if not first:
                        pe.wait_ge(A.sem, A.at(b - 1, f"raw{f}"))
                        pe.wait_ge(A.sem, A.at(b - 1, f"sq{f}"))
                    for k in range(KT):
                        m = pe.matmul(bank[:, f, :], W[:, k, f * P:(f + 1) * P], rhs(k), start=(k == 0),
                                      stop=(k == KT - 1))
                    m.then_inc(T(f"proj{f}"), 1)
                for n, name in enumerate(("kr", "krs")):
                    if not first:
                        pe.wait_ge(D.sem, D.at(b - 1, name if n else "krc"))
                    for k in range(KT):
                        m = pe.matmul(bank[0:QK, 3 + n, :], WR[:, k, n, :], rhs(k), start=(k == 0),
                                      stop=(k == KT - 1))
                    m.then_inc(T(name), 1)
                pe.wait_ge(A.sem, A.at(b, "sq1"))
                if not first:
                    pe.wait_ge(D.sem, D.at(b - 1, "vkv"))
                for f in range(2):
                    m = pe.matmul(bank[:, 5, :], chip.ones[:], sq[:, f, :], start=(f == 0), stop=(f == 1))
                m.then_inc(T("sumq"), 1)
                pe.wait_ge(A.sem, A.at(b, "sq2"))
                pe.matmul(bank[:, 6, :], chip.ones[:], sq[:, 2, :], start=True, stop=True).then_inc(T("sumkv"), 1)
            body(0, True)
            with pe.Fori(1, NB) as b:
                body(b, False)

        @block.scalar
        def _(act):
            def body(b, first):
                for f in range(3):
                    act.wait_ge(T.sem, T.at(b, f"proj{f}"))
                    out = cqT[:, f, bass.ds(b * BANK, BANK)] if f < 2 else ckvT[:, bass.ds(b * BANK, BANK)]
                    act.activation(out, bank[:, f, :], ACT.Copy).then_inc(A(f"raw{f}"), 1)
                for f in range(3):
                    if not first and f == 0:
                        act.wait_ge(T.sem, T.at(b - 1, "sumkv"))
                    act.activation(sq[:, f, :], bank[:, f, :], ACT.Square).then_inc(A(f"sq{f}"), 1)
                act.wait_ge(D.sem, D.at(b, "inv"))
                act.activation(v[:], v[:], ACT.Sqrt).then_inc(A("rinv"), 1)
            body(0, True)
            with act.Fori(1, NB) as b:
                body(b, False)

        @block.vector
        def _(dve):
            dve.wait_ge(once, 16 * 8)

            def body(b, first):
                t = bass.ds(b * BANK, BANK)
                dve.wait_ge(T.sem, T.at(b, "sumq"))
                if not first:
                    dve.wait_ge(D.sem, D.at(b - 1, "kv"))
                dve.tensor_scalar(v[:, 0, :], bank[:, 5, :], 1.0 / Q_LORA, EPS2, ALU.mult, ALU.add
                                  ).then_inc(D("vq"), 1)
                dve.wait_ge(T.sem, T.at(b, "sumkv"))
                dve.tensor_scalar(v[:, 1, :], bank[:, 6, :], 1.0 / KV_LORA, EPS2, ALU.mult, ALU.add
                                  ).then_inc(D("vkv"), 1)
                dve.wait_ge(D.sem, D.at(b, "vkv"))
                dve.reciprocal(v[:], v[:]).then_inc(D("inv"), 1)
                dve.wait_ge(A.sem, A.at(b, "rinv"))
                for f in range(3):
                    c = cqT[:, f, t] if f < 2 else ckvT[:, t]
                    dve.scalar_tensor_tensor(out=c, in0=c, scalar=gains[:, f:f + 1], in1=v[:, f // 2, :],
                                             op0=ALU.mult, op1=ALU.mult).then_inc(D(("q0", "q1", "kv")[f]), 1)
                dve.tensor_tensor(kr[R, 0, :], bank[R, 3, :], rot[R, 0, t], ALU.mult).then_inc(D("krc"), 1)
                dve.tensor_tensor(kr[R, 1, :], bank[R, 4, :], rot[R, 1, t], ALU.mult).then_inc(D("krs"), 1)
                dve.wait_ge(D.sem, D.at(b, "krs"))
                dve.tensor_tensor(kT[R, t], kr[R, 0, :], kr[R, 1, :], ALU.add).then_inc(D("kr"), 1)
            body(0, True)
            with dve.Fori(1, NB) as b:
                body(b, False)


def phase_attention(chip, cqT, ckvT, kT, rot, w_uq, w_ukv, vall, oall):
    nc, bank = chip.nc, chip.bank
    NB = LATENT_BLOCKS
    R = slice(NOPE, QK)
    HALF = ROPE // 2
    SCALE = QK ** -0.5
    AHEAD, NSC = 2, 3
    NS, NTB = 3, 3
    SC0, TB0, OB0 = 0, 3, 6
    chunks = {i: (i + 4) // 4 for i in range(QT)}
    with ExitStack() as st:
        sb = lambda n, s: st.enter_context(nc.sbuf_tensor("attn_" + n, s, F32))
        sem = lambda n: st.enter_context(nc.semaphore("attn_" + n))
        WQ = sb("WQ", [P, 2, 2, QK])
        WK = sb("WK", [P, NOPE])
        WV = sb("WV", [P, AH, DV])
        qT = sb("qT", [QK, SEQ])
        v = sb("v", [P, QT, DV])
        ahead = sb("ahead", [P, P])
        sc = sb("sc", [P, NSC, SEQ])
        pT = sb("pT", [P, NTB, BANK])
        tmp = sb("tmp", [QK, 2, 2, BANK])
        mx = sb("mx", [P, NSC, 4])
        top = sb("top", [P, NSC])
        total = sb("total", [P, NSC])
        share = sb("share", [P, NSC])
        w_loaded, mask_ready = sem("w_loaded"), sem("mask_ready")
        wv_loaded, vall_ready, vall_copied = sem("wv_loaded"), sem("vall_ready"), sem("vall_copied")
        order = [i for n in range(QT // 2) for i in (QT - 1 - n, n)]
        at = {i: n for n, i in enumerate(order)}
        slot = {i: n % NSC for i, n in at.items()}
        steps = [(order[n] if n < QT else None, order[n - AHEAD] if n >= AHEAD else None) for n in range(QT + AHEAD)]
        groups = [(i, g) for i in order for g in range(chunks[i])]
        gi = {ig: n for n, ig in enumerate(groups)}
        T = Stages(sem("pe_stage"), " ".join([f"q{b} k{b}" for b in range(NB)])
                   + " " + " ".join(x for i, j in steps for x in (
                       [f"s{i}_{g}" for g in range(chunks.get(i, 0))]
                       + ([y for g in range(chunks[j] + 2) for y in (
                           ([f"t{j}_{g}"] if g < chunks[j] else []) + ([f"o{j}_{g - 2}"] if g > 1 else []))]
                          if j is not None else []))))
        D = Stages(sem("dve_stage"), " ".join(f"qc{b} qs{b} q{b}" for b in range(NB)) + " " + " ".join(
            x for i, j in steps for x in (
                ([f"m{i}_{g}" for g in range(chunks[i])] + [f"top{i}"] if i is not None else [])
                + ([f"share{j}", f"o{j}"] if j is not None else []))))
        A = Stages(sem("act_stage"), "v " + " ".join(f"q{b} k{b}" for b in range(NB)) + " " + " ".join(
            x for i, j in steps for x in (([f"t{j}_{g}" for g in range(chunks[j])] if j is not None else [])
                                          + ([f"e{i}"] if i is not None else []))))
        ended = lambda f: f"o{f}_{chunks[f] - 1}"
        block = st.enter_context(nc.Block())

        def turns(eng, body):
            body(0, True)
            with eng.Fori(1, AH) as h:
                body(h, False)

        @block.sync
        def _(sp):
            sp.dma_start(WV[:], w_ukv.rearrange("k (h n) -> k h n", h=AH)[:, :, NOPE:NOPE + DV]).then_inc(wv_loaded, 16)

            def body(h, first):
                if not first:
                    sp.wait_ge(T.sem, T.at(h - 1, f"k{NB - 1}"))
                q = w_uq.rearrange("(k p) n -> p k n", p=P)
                sp.dma_start(WQ[:, :, 0, :], q[:, :, bass.ds(h * QK, QK)]).then_inc(w_loaded, 16)
                sp.dma_start(WQ[:, :, 1, 0:NOPE], q[:, :, bass.ds(h * QK, NOPE)]).then_inc(w_loaded, 16)
                for half in range(2):
                    sp.dma_start(WQ[:, :, 1, NOPE + half * HALF:NOPE + (half + 1) * HALF],
                                 q[:, :, bass.ds(h * QK + NOPE + (1 - half) * HALF, HALF)]).then_inc(w_loaded, 16)
                sp.dma_start(WK[:], w_ukv[:, bass.ds(h * (NOPE + DV), NOPE)]).then_inc(w_loaded, 16)
            turns(sp, body)

        @block.gpsimd
        def _(pool):
            nc.gpsimd.memset(ahead[:], 0.0).then_inc(mask_ready, 1)
            pool.wait_ge(mask_ready, 1)
            nc.gpsimd.affine_select(out=ahead[:], in_=ahead[:], compare_op=ALU.is_ge, fill=NEG, base=0,
                                    pattern=[[-1, P]], channel_multiplier=1).then_inc(mask_ready, 1)

        @block.tensor
        def _(pe):
            pe.wait_ge(mask_ready, 2)
            pe.wait_ge(wv_loaded, 16)
            for t in range(QT):
                if t >= 4:
                    pe.wait_ge(vall_copied, t - 3)
                pe.matmul(bank[:, 4 + t % 4, :], ckvT[:, t * P:(t + 1) * P], WV[:].rearrange("p h n -> p (h n)"),
                          start=True, stop=True).then_inc(vall_ready, 1)

            def body(h, first):
                pe.wait_ge(w_loaded, h * 80 + 80)
                for b in range(NB):
                    t = slice(b * BANK, (b + 1) * BANK)
                    b0 = 3 * (b % 2)
                    if b >= 2:
                        pe.wait_ge(A.sem, A.at(h, f"k{b - 2}"))
                        pe.wait_ge(D.sem, D.at(h, f"qs{b - 2}"))
                    elif not first:
                        pe.wait_ge(D.sem, D.at(h - 1, ("m%d_%d" % groups[-1], f"o{order[-1]}")[b]))
                    elif b == 1:
                        pe.wait_ge(vall_copied, QT)
                    for n in range(2):
                        for k in range(2):
                            m = pe.matmul(bank[0:QK, b0 + n, :], WQ[:, k, n, :], cqT[:, k, t], start=(k == 0),
                                          stop=(k == 1))
                    m.then_inc(T(f"q{b}"), 1)
                    pe.matmul(bank[0:NOPE, b0 + 2, :], WK[:], ckvT[:, t], start=True, stop=True).then_inc(T(f"k{b}"), 1)

                def scores(i):
                    q = qT[:, i * P:(i + 1) * P]
                    for g in range(chunks[i]):
                        n = gi[i, g]
                        if n >= NS:
                            pe.wait_ge(D.sem, D.at(h, "m%d_%d" % groups[n - NS]))
                        else:
                            pe.wait_ge(A.sem, A.at(h, f"k{NB - 1}"))
                            pe.wait_ge(D.sem, D.at(h, f"q{NB - 1}"))
                        lo, hi = g * BANK, min((g + 1) * BANK, i * P)
                        bk = bank[:, SC0 + n % NS, :]
                        if hi > lo:
                            m = pe.matmul(bk[:, 0:hi - lo], q, kT[:, lo:hi], start=True, stop=True)
                        if (i + 1) * P <= (g + 1) * BANK:
                            d = slice(i * P - lo, (i + 1) * P - lo)
                            pe.matmul(bk[:, d], q, kT[:, i * P:(i + 1) * P], start=True, stop=False)
                            m = pe.matmul(bk[:, d], chip.ident[:], ahead[:], start=False, stop=True)
                        m.then_inc(T(f"s{i}_{g}"), 1)

                def rest(i):
                    for g in range(chunks[i] + 2):
                        if g < chunks[i]:
                            n = gi[i, g]
                            if g == 0:
                                pe.wait_ge(A.sem, A.at(h, f"e{i}"))
                            if n >= NTB:
                                pe.wait_ge(A.sem, A.at(h, "t%d_%d" % groups[n - NTB]))
                            for c in range(4 * g, min(4 * g + 4, i + 1)):
                                m = pe.transpose(bank[:, TB0 + n % NTB, (c % 4) * P:(c % 4 + 1) * P],
                                                 sc[:, slot[i], c * P:(c + 1) * P], chip.ident[:])
                            m.then_inc(T(f"t{i}_{g}"), 1)
                        if g > 1:
                            n = gi[i, g - 2]
                            pe.wait_ge(A.sem, A.at(h, f"t{i}_{g - 2}"))
                            if g == 2 and at[i] >= 2:
                                pe.wait_ge(D.sem, D.at(h, f"o{order[at[i] - 2]}"))
                            if g == 2 and at[i] == 0:
                                pe.wait_ge(A.sem, A.at(h, "v"))
                            for c in range(4 * (g - 2), min(4 * g - 4, i + 1)):
                                m = pe.matmul(bank[:, OB0 + at[i] % 2, 0:DV], pT[:, n % NTB, (c % 4) * P:(c % 4 + 1) * P],
                                              v[:, c, :], start=(c == 0), stop=(c == i))
                            m.then_inc(T(f"o{i}_{g - 2}"), 1)
                for i, j in steps:
                    if i is not None:
                        scores(i)
                    if j is not None:
                        rest(j)
            turns(pe, body)

        @block.scalar
        def _(act):
            for t in range(QT):
                act.wait_ge(vall_ready, t + 1)
                act.activation(vall[:, t, :], bank[:, 4 + t % 4, :], ACT.Copy).then_inc(vall_copied, 1)

            def body(h, first):
                if first:
                    act.wait_ge(vall_copied, QT)
                else:
                    act.wait_ge(T.sem, T.at(h - 1, ended(order[-1])))
                act.activation(v[:], vall[:, :, bass.ds(h * DV, DV)], ACT.Copy).then_inc(A("v"), 1)
                for b in range(NB):
                    t = slice(b * BANK, (b + 1) * BANK)
                    act.wait_ge(T.sem, T.at(h, f"q{b}"))
                    act.activation(qT[0:NOPE, t], bank[0:NOPE, 3 * (b % 2), :], ACT.Copy).then_inc(A(f"q{b}"), 1)
                    act.wait_ge(T.sem, T.at(h, f"k{b}"))
                    act.activation(kT[0:NOPE, t], bank[0:NOPE, 3 * (b % 2) + 2, :], ACT.Copy).then_inc(A(f"k{b}"), 1)
                for i, j in steps:
                    for g in range(chunks[j] if j is not None else 0):
                        n = gi[j, g]
                        w = min(BANK, (j + 1) * P - g * BANK)
                        act.wait_ge(T.sem, T.at(h, f"t{j}_{g}"))
                        if n >= NTB:
                            act.wait_ge(T.sem, T.at(h, "o%d_%d" % groups[n - NTB]))
                        act.activation(pT[:, n % NTB, 0:w], bank[:, TB0 + n % NTB, 0:w], ACT.Copy
                                       ).then_inc(A(f"t{j}_{g}"), 1)
                    if i is None:
                        continue
                    act.wait_ge(D.sem, D.at(h, f"top{i}"))
                    n = (i + 1) * P
                    act.activation(sc[:, slot[i], 0:n], sc[:, slot[i], 0:n], ACT.Exp,
                                   bias=top[:, slot[i]:slot[i] + 1], accum_out=total[:, slot[i]:slot[i] + 1]
                                   ).then_inc(A(f"e{i}"), 1)
            turns(act, body)

        @block.vector
        def _(dve):
            def body(h, first):
                for b in range(NB):
                    t = slice(b * BANK, (b + 1) * BANK)
                    dve.wait_ge(T.sem, T.at(h, f"q{b}"))
                    dve.wait_ge(A.sem, A.at(h, f"q{b}"))
                    if b or not first:
                        prev = D.at(h, f"q{b - 1}") if b else D.at(h - 1, f"q{NB - 1}")
                        dve.wait_ge(D.sem, prev)
                    dve.tensor_tensor(tmp[R, b % 2, 0, :], bank[R, 3 * (b % 2), :], rot[R, 0, t], ALU.mult
                                      ).then_inc(D(f"qc{b}"), 1)
                    dve.tensor_tensor(tmp[R, b % 2, 1, :], bank[R, 3 * (b % 2) + 1, :], rot[R, 1, t], ALU.mult
                                      ).then_inc(D(f"qs{b}"), 1)
                    dve.wait_ge(D.sem, D.at(h, f"qs{b}"))
                    dve.tensor_tensor(qT[R, t], tmp[R, b % 2, 0, :], tmp[R, b % 2, 1, :], ALU.add
                                      ).then_inc(D(f"q{b}"), 1)
                for i, j in steps:
                    if i is not None:
                        for g in range(chunks[i]):
                            n = gi[i, g]
                            w = min(BANK, (i + 1) * P - g * BANK)
                            dve.wait_ge(T.sem, T.at(h, f"s{i}_{g}"))
                            dve.tensor_scalar(sc[:, slot[i], g * BANK:g * BANK + w], bank[:, SC0 + n % NS, 0:w], SCALE,
                                              None, ALU.mult, ALU.max, accum_out=mx[:, slot[i], g:g + 1]
                                              ).then_inc(D(f"m{i}_{g}"), 1)
                        dve.wait_ge(D.sem, D.at(h, f"m{i}_{chunks[i] - 1}"))
                        dve.tensor_reduce(top[:, slot[i]:slot[i] + 1], mx[:, slot[i], 0:chunks[i]], AX.X, ALU.max,
                                          negate=True).then_inc(D(f"top{i}"), 1)
                    if j is not None:
                        u = slice(slot[j], slot[j] + 1)
                        dve.wait_ge(T.sem, T.at(h, f"o{j}_{chunks[j] - 1}"))
                        dve.reciprocal(share[:, u], total[:, u]).then_inc(D(f"share{j}"), 1)
                        dve.wait_ge(D.sem, D.at(h, f"share{j}"))
                        dve.tensor_scalar(oall[:, j, bass.ds(h * DV, DV)], bank[:, OB0 + at[j] % 2, 0:DV],
                                          share[:, u], None, ALU.mult).then_inc(D(f"o{j}"), 1)
            turns(dve, body)


def phase_output(chip, oall, WO, shT, sh, w_in, sgu_g, sgu_b, w_spatial, b_spatial, w_out, ln_g, ln_b, out):
    nc, bank = chip.nc, chip.bank
    COLS = (C_V, C_U, C_ZB, C_ZA)
    with ExitStack() as st:
        sb = lambda n, s: st.enter_context(nc.sbuf_tensor("out_" + n, s, F32))
        sem = lambda n: st.enter_context(nc.semaphore("out_" + n))
        W = sb("W", [P, KT, 4, WIDTH])
        wsT = sb("wsT", [P, AH, P])
        bs = sb("bs", [AH, P])
        bsT = sb("bsT", [P, AH])
        srows = sb("srows", [P, 2, WIDTH])
        rows = sb("rows", [P, 2, DM])
        xT = sb("xT", [P, 2, KT, P])
        hs = sb("hs", [P, DM])
        v, u, zb, za = (sb(n, [P, 2, WIDTH]) for n in ("v", "u", "zb", "za"))
        m_ = sb("m", [P, 2 * WIDTH])
        ws = m_[:].rearrange("p (h s) -> p h s", h=AH)
        mT = sb("mT", [P, KT, P])
        r = sb("r", [P, DM])
        stats, mv, inv, rstd = (sb(n, [P, 2, w]) for n, w in (("stats", 12), ("mv", 2), ("inv", 1), ("rstd", 1)))
        once, rows_loaded, wo_loaded, prep, prep_pe = (sem(n) for n in ("once", "rows_loaded", "wo_loaded", "prep",
                                                                        "prep_pe"))
        w_loaded = [sem(f"w_loaded{n}") for n in range(4)]
        x_loaded = [sem(f"x_loaded{s}") for s in range(2)]
        h_loaded, stored = sem("h_loaded"), sem("stored")
        TH_ = Stages(sem("pe_head"), "proj0 proj1 proj2 proj3")
        TT_ = Stages(sem("pe_tail"), "spatial turned mm")
        AH_ = Stages(sem("act_head"), "v u zb rstd za")
        AT_ = Stages(sem("act_tail"), "mT rstd")
        DH_ = Stages(sem("dve_head"), "stats mv var inv n scaled vn")
        DT_ = Stages(sem("dve_tail"), "sv su b a sum stats mv var inv n scaled y")
        block = st.enter_context(nc.Block())

        def steps(eng, step):
            step(0, 0, True, False)
            step(1, 1, True, True)
            with eng.Fori(1, QT // 2) as i:
                step(2 * i, 0, True, True)
                step(2 * i + 1, 1, True, True)
            step(QT, 0, False, True)
        early = lambda t: isinstance(t, int) and t < 2

        @block.sync
        def _(sp):
            sp.dma_start(ws, w_spatial.rearrange("h t s -> t h s")).then_inc(once, 16)
            sp.dma_start(bs[:], b_spatial).then_inc(once, 16)
            for s in range(2):
                sp.dma_start(xT[:, s], shT[s:s + 1].rearrange("a p (k c) -> (a p) k c", k=KT)).then_inc(x_loaded[s], 16)
            for n, c in enumerate(COLS):
                sp.dma_start(W[:, :, n, :], w_in[:, c:c + WIDTH].rearrange("(k p) n -> p k n", p=P)
                             ).then_inc(w_loaded[n], 16)
            for n, src in enumerate((sgu_g, sgu_b)):
                sp.dma_start(srows[:, n, :], src.broadcast_to([P, WIDTH])).then_inc(rows_loaded, 16)
            for n, src in enumerate((ln_g, ln_b)):
                sp.dma_start(rows[:, n, :], src.broadcast_to([P, DM])).then_inc(rows_loaded, 16)
            sp.dma_start(WO, w_out.rearrange("(k p) n -> p k n", p=P)).then_inc(wo_loaded, 16)

            def step(t, s, new, old):
                if new and not early(t):
                    sp.wait_ge(TH_.sem, TH_.at(t - 2, "proj3"))
                    sp.dma_start(xT[:, s], shT[bass.ds(t, 1)].rearrange("a p (k c) -> (a p) k c", k=KT)
                                 ).then_inc(x_loaded[s], 16)
                if old:
                    if not early(t):
                        sp.wait_ge(DT_.sem, DT_.at(t - 2, "sum"))
                    sp.dma_start(hs[:], sh[bass.ds((t - 1) * P, P), :]).then_inc(h_loaded, 16)
            steps(sp, step)

        @block.gpsimd
        def _(pool):
            def step(t, s, new, old):
                if old:
                    pool.wait_ge(DT_.sem, DT_.at(t - 1, "y"))
                    pool.dma_start(out[bass.ds((t - 1) * P, P), :], r[:]).then_inc(stored, 16)
            steps(pool, step)
            pool.wait_ge(stored, 16 * QT)

        @block.tensor
        def _(pe):
            pe.wait_ge(once, 32)
            pe.transpose(bank[:, 7, 0:AH], bs[:], chip.ident[0:AH, 0:AH]).then_inc(prep_pe, 1)
            pe.wait_ge(prep, 1)
            for h in range(AH):
                m = pe.transpose(bank[:, 5 + h // 4, (h % 4) * P:(h % 4 + 1) * P], ws[:, h, :], chip.ident[:])
            m.then_inc(prep_pe, 1)

            def step(t, s, new, old):
                def project(n):
                    if not new:
                        return
                    if isinstance(t, int) and t == 0:
                        pe.wait_ge(w_loaded[n], 16)
                    else:
                        pe.wait_ge(AH_.sem, AH_.at(t - 1, ("v", "u", "zb", "za")[n]))
                    for k in range(KT):
                        m = pe.matmul(bank[:, n, :], xT[:, s, k, :], W[:, k, n, :], start=(k == 0), stop=(k == KT - 1))
                    m.then_inc(TH_(f"proj{n}"), 1)

                if new:
                    pe.wait_ge(x_loaded[s], (t - s) // 2 * 16 + 16)
                project(0)
                if old:
                    pe.wait_ge(DH_.sem, DH_.at(t - 1, "vn"))
                    if early(t):
                        pe.wait_ge(prep, 3)
                    else:
                        pe.wait_ge(DT_.sem, DT_.at(t - 2, "sum"))
                    for h in range(AH):
                        m = pe.matmul(bank[:, 4, h * DV:(h + 1) * DV], wsT[:, h, :], v[:, 1 - s, h * DV:(h + 1) * DV],
                                      start=True, stop=True)
                    m.then_inc(TT_("spatial"), 1)
                project(1)
                project(2)
                if old:
                    pe.wait_ge(DT_.sem, DT_.at(t - 1, "a"))
                    for k in range(KT):
                        m = pe.transpose(bank[:, 5 + k // 4, (k % 4) * P:(k % 4 + 1) * P], m_[:, k * P:(k + 1) * P],
                                         chip.ident[:])
                    m.then_inc(TT_("turned"), 1)
                project(3)
                if old:
                    if early(t):
                        pe.wait_ge(wo_loaded, 16)
                    pe.wait_ge(AT_.sem, AT_.at(t - 1, "mT"))
                    for n in range(2):
                        for k in range(KT):
                            m = pe.matmul(bank[:, (7, 4)[n], :], mT[:, k, :], WO[:, k, n * BANK:(n + 1) * BANK],
                                          start=(k == 0), stop=(k == KT - 1))
                    m.then_inc(TT_("mm"), 1)
            steps(pe, step)

        @block.scalar
        def _(act):
            def step(t, s, new, old):
                if new:
                    if not early(t):
                        act.wait_ge(TT_.sem, TT_.at(t - 2, "spatial"))
                    act.wait_ge(TH_.sem, TH_.at(t, "proj0"))
                    act.activation(v[:, s], bank[:, 0, :], ACT.Gelu).then_inc(AH_("v"), 1)
                    if not early(t):
                        act.wait_ge(DT_.sem, DT_.at(t - 2, "a"))
                    act.wait_ge(TH_.sem, TH_.at(t, "proj1"))
                    act.activation(u[:, s], bank[:, 1, :], ACT.Gelu).then_inc(AH_("u"), 1)
                    act.wait_ge(TH_.sem, TH_.at(t, "proj2"))
                    act.activation(zb[:, s], bank[:, 2, :], ACT.Silu).then_inc(AH_("zb"), 1)
                    act.wait_ge(DH_.sem, DH_.at(t, "inv"))
                    act.activation(rstd[:, 0, :], inv[:, 0, :], ACT.Sqrt).then_inc(AH_("rstd"), 1)
                if old:
                    act.wait_ge(TT_.sem, TT_.at(t - 1, "turned"))
                    for n in range(2):
                        m = act.activation(mT[:, 4 * n:4 * n + 4, :],
                                           bank[:, 5 + n, :].rearrange("p (k c) -> p k c", k=4), ACT.Copy)
                    m.then_inc(AT_("mT"), 1)
                if new:
                    act.wait_ge(TH_.sem, TH_.at(t, "proj3"))
                    act.activation(za[:, s], bank[:, 3, :], ACT.Silu).then_inc(AH_("za"), 1)
                if old:
                    act.wait_ge(DT_.sem, DT_.at(t - 1, "inv"))
                    act.activation(rstd[:, 1, :], inv[:, 1, :], ACT.Sqrt).then_inc(AT_("rstd"), 1)
            steps(act, step)

        @block.vector
        def _(dve):
            dve.wait_ge(once, 32)
            dve.tensor_tensor(ws, ws, bcast(chip.low[:], 1, AH), ALU.mult).then_inc(prep, 1)
            dve.wait_ge(prep_pe, 1)
            dve.tensor_copy(bsT[:], bank[:, 7, 0:AH]).then_inc(prep, 1)
            dve.wait_ge(prep_pe, 2)
            for n in range(2):
                m = dve.tensor_copy(wsT[:, 4 * n:4 * n + 4, :], bank[:, 5 + n, :].rearrange("p (h c) -> p h c", h=4))
            m.then_inc(prep, 1)
            dve.wait_ge(rows_loaded, 64)
            dve.wait_ge(prep, 3)

            def step(t, s, new, old):
                by_head = lambda ap: ap.rearrange("p (h d) -> p h d", h=AH)
                a, b = m_[:, 0:WIDTH], m_[:, WIDTH:2 * WIDTH]
                if old:
                    dve.wait_ge(TT_.sem, TT_.at(t - 1, "spatial"))
                    if not early(t):
                        dve.wait_ge(TT_.sem, TT_.at(t - 2, "turned"))
                    dve.tensor_tensor(by_head(b), by_head(bank[:, 4, :]), bcast(bsT[:], 2, DV), ALU.add
                                      ).then_inc(DT_("sv"), 1)
                    dve.wait_ge(AH_.sem, AH_.at(t - 1, "za"))
                    dve.wait_ge(DT_.sem, DT_.at(t - 1, "sv"))
                    dve.tensor_tensor(b, b, u[:, 1 - s], ALU.mult).then_inc(DT_("su"), 1)
                    dve.wait_ge(DT_.sem, DT_.at(t - 1, "su"))
                    dve.tensor_tensor(b, b, zb[:, 1 - s], ALU.mult).then_inc(DT_("b"), 1)
                    dve.tensor_tensor(a, oall[:, bass.ds(t - 1, 1), :].rearrange("p a n -> p (a n)"), za[:, 1 - s],
                                      ALU.mult).then_inc(DT_("a"), 1)
                if new:
                    dve.wait_ge(AH_.sem, AH_.at(t, "v"))
                    layer_norm_steps(dve, DH_, AH_, t, v[:, s], stats[:, 0], mv[:, 0], inv[:, 0], rstd[:, 0], EPS2,
                                     srows[:, 0, :])
                    dve.tensor_tensor(v[:, s], v[:, s], srows[:, 1, :], ALU.add).then_inc(DH_("vn"), 1)
                if old:
                    dve.wait_ge(TT_.sem, TT_.at(t - 1, "mm"))
                    dve.wait_ge(h_loaded, t * 16)
                    if not early(t):
                        dve.wait_ge(stored, (t - 1) * 16)
                    for n in range(2):
                        c = slice(n * BANK, (n + 1) * BANK)
                        m = dve.scalar_tensor_tensor(out=r[:, c], in0=hs[:, c], scalar=ALPHA,
                                                     in1=bank[:, (7, 4)[n], :], op0=ALU.mult, op1=ALU.add)
                    m.then_inc(DT_("sum"), 1)
                    dve.wait_ge(DT_.sem, DT_.at(t - 1, "sum"))
                    layer_norm_steps(dve, DT_, AT_, t - 1, r[:], stats[:, 1], mv[:, 1], inv[:, 1], rstd[:, 1], EPS2,
                                     rows[:, 0, :])
                    dve.tensor_tensor(r[:], r[:], rows[:, 1, :], ALU.add).then_inc(DT_("y"), 1)
            steps(dve, step)


def build(nc, a, out):
    def scratch(name, shape):
        return nc.dram_tensor(name, shape, F32, kind="Internal").ap()

    sa = scratch("delta_qkv", [3 * HEADS, P, TOK])
    sq_, sv = scratch("gla_queries", [HEADS, P, TOK]), scratch("gla_values", [HEADS, P, TOK])
    sk, sg = scratch("gla_keys", [2 * HEADS, P, TOK]), scratch("gla_decays", [2 * HEADS, P, TOK])
    so_a, so_b = scratch("delta_outputs", [HEADS, P, SEQ]), scratch("gla_outputs", [HEADS, P, SEQ])
    smT = scratch("merged", [KT, P, SEQ])
    sh = scratch("hidden", [SEQ, DM])
    shT = scratch("hidden_turned", [QT, P, DM])
    with ExitStack() as stack:
        chip = Chip(nc, stack)
        w_in = a["w_in"][0]
        with ExitStack() as st:
            uT = st.enter_context(nc.sbuf_tensor("uT", [P, KT, TOK], F32))
            phase_constants(chip, a["c"], a["c_ctx"], a["w_mod"], a["b_mod"], a["lb_param"])
            phase_modulated_norm(chip, uT, a["x"][0], a["ctx"][0])
            phase_conv(chip, uT, w_in, a["conv_w"], sa)
            phase_decay_beta(chip, uT, w_in, a["a_log"], a["dt_bias"])
            phase_gla_inputs(chip, uT, w_in, sq_, sv, sk, sg)
            phase_delta_rule(chip, sa, so_a)
            phase_gla(chip, sq_, sv, sk, sg, so_b)
            yT = st.enter_context(nc.sbuf_tensor("yT", [P, 2 * HEADS, SEQ], F32))
            phase_branch_gates(chip, uT, w_in, so_a, so_b, a["a_norm_g"], a["b_norm_g"], yT)
            phase_merge(chip, uT, w_in, yT, a["w_a_out"][0], a["w_b_out"][0], smT)
        hT = stack.enter_context(nc.sbuf_tensor("hT", [P, KT, SEQ], F32))
        oall = hT[:, 0:KT // 2, :].rearrange("p k t -> p (k t)").rearrange("p (a n) -> p a n", n=WIDTH)
        vall = hT[:, KT // 2:KT, :].rearrange("p k t -> p (k t)").rearrange("p (a n) -> p a n", n=WIDTH)
        WO = hT[:, KT // 2:KT, :].rearrange("p k t -> p (k t)").rearrange("p (a n) -> p a n", n=DM)
        phase_residual(chip, a["x"][0], smT, a["w_out"][0], a["ln_g"], a["ln_b"], sh, hT)
        with ExitStack() as st:
            sb = lambda n, s: st.enter_context(nc.sbuf_tensor(n, s, F32))
            cqT, ckvT = sb("cqT", [P, 2, SEQ]), sb("ckvT", [P, SEQ])
            kT, rot = sb("kT", [QK, SEQ]), sb("rot", [QK, 2, SEQ])
            phase_rotation(chip, a["positions_2"], a["inv_freq"], rot)
            phase_latents(chip, hT, a["w_in_2"], a["q_norm_g_2"], a["kv_norm_g_2"], cqT, ckvT, kT, rot, shT)
            phase_attention(chip, cqT, ckvT, kT, rot, a["w_uq_2"], a["w_ukv_2"], vall, oall)
        row = lambda n: a[n].rearrange("(a n) -> a n", a=1)
        phase_output(chip, oall, WO, shT, sh, a["w_in_2"], row("sgu_norm_g_2"), row("sgu_norm_b_2"), a["w_spatial_2"],
                     a["b_spatial_2"], a["w_out_2"], row("ln_g_2"), row("ln_b_2"), out[0])


INPUTS = ["x", "c", "ctx", "c_ctx", "w_mod", "b_mod", "w_in", "conv_w", "a_log", "dt_bias", "lb_param", "a_norm_g",
          "b_norm_g", "w_a_out", "w_b_out", "w_out", "ln_g", "ln_b", "positions_2", "w_in_2", "q_norm_g_2", "w_uq_2",
          "kv_norm_g_2", "w_ukv_2", "sgu_norm_g_2", "sgu_norm_b_2", "w_spatial_2", "b_spatial_2", "w_out_2", "ln_g_2",
          "ln_b_2"]


def kernel(**inputs):
    import numpy as np
    import concourse.bacc as bacc
    from concourse.bass_utils import run_bass_kernel_spmd

    arrays = {name: np.ascontiguousarray(inputs[name]) for name in INPUTS}
    half = ROPE // 2
    arrays["inv_freq"] = (np.float32(1.0) / np.float32(10000.0) ** (np.arange(half, dtype=np.float32)
                                                                   / np.float32(half))).reshape(1, half)
    nc = bacc.Bacc("TRN2", target_bir_lowering=False, num_devices=1)
    aps = {name: nc.dram_tensor(f"in_{name}", v.shape, mybir.dt.from_np(v.dtype), kind="ExternalInput").ap()
           for name, v in arrays.items()}
    out = nc.dram_tensor("out", (1, SEQ, DM), F32, kind="ExternalOutput").ap()
    build(nc, aps, out)
    result = run_bass_kernel_spmd(nc, [{f"in_{name}": v for name, v in arrays.items()}], core_ids=[0])
    return result.results[0]["out"]
```
